# Optimizing a Trainium2 kernel written in Bass

```python
import math
import jax, jax.numpy as jnp
from jax import lax
import numpy as np

D_MODEL = 1024
BATCH = 1
SEQ = 256
DEPTH = 4

GRID_W = 64
CTX_LEN = 256
N_MIXERS = 3
D_FF = 4 * D_MODEL
RMS_EPS = 1e-6
ROPE_BASE = 10000.0
Q_BLOCK = 128
FOURIER_GROUPS = 4
DIFF_HEADS = D_MODEL // 128
DIFF_HEAD_DIM = D_MODEL // (2 * DIFF_HEADS)
DIFF_V_DIM = 2 * DIFF_HEAD_DIM
MLA_HEADS = 16
MLA_NOPE_DIM = 64
MLA_ROPE_DIM = 32
MLA_V_DIM = 64
MLA_Q_RANK = 256
MLA_KV_RANK = 128
MLA_DOWN = MLA_Q_RANK + MLA_KV_RANK + MLA_ROPE_DIM
N_FOURIER = (DEPTH + 2) // 3
N_DIFF = (DEPTH + 1) // 3
N_MLA = DEPTH // 3


def rms_norm(x, g, eps=RMS_EPS):
    x32 = x.astype(jnp.float32)
    y = x32 * lax.rsqrt(jnp.mean(x32 * x32, axis=-1, keepdims=True) + eps)
    return y.astype(x.dtype) * g

def modulate(x, g, shift, scale):
    return rms_norm(x, g) * (1 + scale) + shift

def axial_rope_tables(rows, dim):
    n_freq = dim // 4
    inv_freq = ROPE_BASE ** (-jnp.arange(n_freq, dtype=jnp.float32) / n_freq)
    t = jnp.arange(rows * GRID_W)
    row = (t // GRID_W).astype(jnp.float32)
    col = (t % GRID_W).astype(jnp.float32)
    ang = jnp.stack([row[:, None] * inv_freq, col[:, None] * inv_freq], axis=1)
    return jnp.cos(ang), jnp.sin(ang)

def apply_axial_rope(x, cos, sin):
    shp = x.shape
    n_freq = shp[-1] // 4
    xs = x.reshape(shp[:-1] + (2, 2, n_freq))
    x1, x2 = xs[..., 0, :], xs[..., 1, :]
    cb = cos[None, :, None].astype(x.dtype)
    sb = sin[None, :, None].astype(x.dtype)
    out = jnp.stack([x1 * cb - x2 * sb, x2 * cb + x1 * sb], axis=-2)
    return out.reshape(shp)

def sweep_query_blocks(fn, *qs):
    b, s = qs[0].shape[:2]
    nb = s // Q_BLOCK
    blocks = tuple(jnp.moveaxis(q.reshape((b, nb, Q_BLOCK) + q.shape[2:]), 1, 0) for q in qs)
    out = lax.map(lambda blk: fn(*blk), blocks)
    return jnp.moveaxis(out, 0, 1).reshape((b, s) + out.shape[3:])

def sq_relu_mlp(h, w1, w2):
    return jnp.square(jax.nn.relu(h @ w1)) @ w2

def fourier_mixer(h, w, bias):
    b, s, d = h.shape
    hg = h.astype(jnp.float32).reshape(b, s, FOURIER_GROUPS, d // FOURIER_GROUPS)
    f = jnp.fft.fft2(hg, axes=(1, 3), norm="ortho").real
    return f.reshape(b, s, d).astype(h.dtype) @ w + bias

def diff_project(h, w_qkv, rope):
    b, s, _ = h.shape
    q, k, v = jnp.split(h @ w_qkv, 3, axis=-1)
    q = q.reshape(b, s, 2 * DIFF_HEADS, DIFF_HEAD_DIM)
    k = k.reshape(b, s, 2 * DIFF_HEADS, DIFF_HEAD_DIM)
    if rope is not None:
        q = apply_axial_rope(q, *rope)
        k = apply_axial_rope(k, *rope)
    q = q.reshape(b, s, DIFF_HEADS, 2, DIFF_HEAD_DIM)
    k = k.reshape(b, s, DIFF_HEADS, 2, DIFF_HEAD_DIM)
    v = v.reshape(b, s, DIFF_HEADS, DIFF_V_DIM)
    return q[..., 0, :], q[..., 1, :], k[..., 0, :], k[..., 1, :], v

def diff_attend(q1, q2, k1, k2, v, lam):
    scale = DIFF_HEAD_DIM ** -0.5
    s1 = jnp.einsum("bqhd,bkhd->bhqk", q1, k1).astype(jnp.float32) * scale
    s2 = jnp.einsum("bqhd,bkhd->bhqk", q2, k2).astype(jnp.float32) * scale
    p = jax.nn.softmax(s1, axis=-1) - lam * jax.nn.softmax(s2, axis=-1)
    return jnp.einsum("bhqk,bkhe->bqhe", p.astype(v.dtype), v)

def diff_attention_mixer(h_lat, h_ctx, w_qkv, lq1, lk1, lq2, lk2, subln_g, w_o, layer_idx, rope, with_ctx):
    lam_init = 0.8 - 0.6 * math.exp(-0.3 * layer_idx)
    lam = (jnp.exp(jnp.sum(lq1.astype(jnp.float32) * lk1.astype(jnp.float32)))
           - jnp.exp(jnp.sum(lq2.astype(jnp.float32) * lk2.astype(jnp.float32))) + lam_init)
    q1l, q2l, k1l, k2l, vl = diff_project(h_lat, w_qkv, rope)
    q1c, q2c, k1c, k2c, vc = diff_project(h_ctx, w_qkv, None)
    k1a = jnp.concatenate([k1c, k1l], axis=1)
    k2a = jnp.concatenate([k2c, k2l], axis=1)
    va = jnp.concatenate([vc, vl], axis=1)

    def finish(o):
        b, s = o.shape[:2]
        return (rms_norm(o, subln_g) * (1 - lam_init)).reshape(b, s, D_MODEL) @ w_o

    o_lat = sweep_query_blocks(lambda a, bq: diff_attend(a, bq, k1a, k2a, va, lam), q1l, q2l)
    y_lat = finish(o_lat)
    y_ctx = finish(diff_attend(q1c, q2c, k1c, k2c, vc, lam)) if with_ctx else None
    return y_lat, y_ctx

def mla_project(h, w_down, q_norm_g, kv_norm_g, w_uq, w_ukv, rope):
    b, s, _ = h.shape
    cq, ckv, k_rope = jnp.split(h @ w_down, [MLA_Q_RANK, MLA_Q_RANK + MLA_KV_RANK], axis=-1)
    q = (rms_norm(cq, q_norm_g) @ w_uq).reshape(b, s, MLA_HEADS, MLA_NOPE_DIM + MLA_ROPE_DIM)
    q_nope, q_rope = jnp.split(q, [MLA_NOPE_DIM], axis=-1)
    kv = (rms_norm(ckv, kv_norm_g) @ w_ukv).reshape(b, s, MLA_HEADS, MLA_NOPE_DIM + MLA_V_DIM)
    k_nope, v = jnp.split(kv, [MLA_NOPE_DIM], axis=-1)
    k_rope = k_rope[:, :, None, :]
    if rope is not None:
        q_rope = apply_axial_rope(q_rope, *rope)
        k_rope = apply_axial_rope(k_rope, *rope)
    return q_nope, q_rope, k_nope, k_rope[:, :, 0], v

def mla_attend(q_nope, q_rope, k_nope, k_rope, v):
    scale = (MLA_NOPE_DIM + MLA_ROPE_DIM) ** -0.5
    s = (jnp.einsum("bqhd,bkhd->bhqk", q_nope, k_nope)
         + jnp.einsum("bqhr,bkr->bhqk", q_rope, k_rope)).astype(jnp.float32) * scale
    p = jax.nn.softmax(s, axis=-1)
    return jnp.einsum("bhqk,bkhe->bqhe", p.astype(v.dtype), v)

def mla_mixer(h_lat, h_ctx, w_down, q_norm_g, kv_norm_g, w_uq, w_ukv, w_o, rope, with_ctx):
    qn_l, qr_l, kn_l, kr_l, v_l = mla_project(h_lat, w_down, q_norm_g, kv_norm_g, w_uq, w_ukv, rope)
    qn_c, qr_c, kn_c, kr_c, v_c = mla_project(h_ctx, w_down, q_norm_g, kv_norm_g, w_uq, w_ukv, None)
    kn_a = jnp.concatenate([kn_c, kn_l], axis=1)
    kr_a = jnp.concatenate([kr_c, kr_l], axis=1)
    v_a = jnp.concatenate([v_c, v_l], axis=1)
    o_lat = sweep_query_blocks(lambda qn, qr: mla_attend(qn, qr, kn_a, kr_a, v_a), qn_l, qr_l)
    b, s = o_lat.shape[:2]
    y_lat = o_lat.reshape(b, s, MLA_HEADS * MLA_V_DIM) @ w_o
    y_ctx = None
    if with_ctx:
        o_ctx = mla_attend(qn_c, qr_c, kn_c, kr_c, v_c)
        y_ctx = o_ctx.reshape(o_ctx.shape[0], o_ctx.shape[1], MLA_HEADS * MLA_V_DIM) @ w_o
    return y_lat, y_ctx

def first_inputs(seed: int = 0) -> dict:
    key = jax.random.key(seed)
    ks = jax.random.split(key, 26)

    def nrm(k, shape, scale):
        return jax.random.normal(k, shape, jnp.float32) * scale

    def gain(k, shape):
        return 1.0 + 0.05 * jax.random.normal(k, shape, jnp.float32)

    d = D_MODEL
    return {
        "x": nrm(ks[0], (BATCH, SEQ, d), 1.0),
        "c": nrm(ks[1], (BATCH, d), 1.0),
        "ctx": nrm(ks[2], (BATCH, CTX_LEN, d), 1.0),
        "c_ctx": nrm(ks[3], (d,), 1.0),
        "mod_w": nrm(ks[4], (DEPTH, d, 6 * d), 0.5 * d ** -0.5),
        "mod_b": nrm(ks[5], (DEPTH, 6 * d), 0.02),
        "norm_mix_g": gain(ks[6], (DEPTH, d)),
        "norm_mlp_g": gain(ks[7], (DEPTH, d)),
        "final_g": gain(ks[8], (d,)),
        "mlp_w1": nrm(ks[9], (DEPTH, d, D_FF), d ** -0.5),
        "mlp_w2": nrm(ks[10], (DEPTH, D_FF, d), D_FF ** -0.5),
        "fourier_w": nrm(ks[11], (N_FOURIER, d, d), d ** -0.5),
        "fourier_b": nrm(ks[12], (N_FOURIER, d), 0.02),
        "diff_w_qkv": nrm(ks[13], (N_DIFF, d, 3 * d), d ** -0.5),
        "diff_lambda_q1": nrm(ks[14], (N_DIFF, DIFF_HEAD_DIM), 0.1),
        "diff_lambda_k1": nrm(ks[15], (N_DIFF, DIFF_HEAD_DIM), 0.1),
        "diff_lambda_q2": nrm(ks[16], (N_DIFF, DIFF_HEAD_DIM), 0.1),
        "diff_lambda_k2": nrm(ks[17], (N_DIFF, DIFF_HEAD_DIM), 0.1),
        "diff_subln_g": gain(ks[18], (N_DIFF, DIFF_V_DIM)),
        "diff_w_o": nrm(ks[19], (N_DIFF, d, d), d ** -0.5),
        "mla_w_down": nrm(ks[20], (N_MLA, d, MLA_DOWN), d ** -0.5),
        "mla_q_norm_g": gain(ks[21], (N_MLA, MLA_Q_RANK)),
        "mla_kv_norm_g": gain(ks[22], (N_MLA, MLA_KV_RANK)),
        "mla_w_uq": nrm(ks[23], (N_MLA, MLA_Q_RANK, MLA_HEADS * (MLA_NOPE_DIM + MLA_ROPE_DIM)), MLA_Q_RANK ** -0.5),
        "mla_w_ukv": nrm(ks[24], (N_MLA, MLA_KV_RANK, MLA_HEADS * (MLA_NOPE_DIM + MLA_V_DIM)), MLA_KV_RANK ** -0.5),
        "mla_w_o": nrm(ks[25], (N_MLA, MLA_HEADS * MLA_V_DIM, d), (MLA_HEADS * MLA_V_DIM) ** -0.5),
    }

def first_block(x, c, ctx, c_ctx, mod_w, mod_b, norm_mix_g, norm_mlp_g, final_g, mlp_w1, mlp_w2,
              fourier_w, fourier_b, diff_w_qkv, diff_lambda_q1, diff_lambda_k1, diff_lambda_q2,
              diff_lambda_k2, diff_subln_g, diff_w_o, mla_w_down, mla_q_norm_g, mla_kv_norm_g,
              mla_w_uq, mla_w_ukv, mla_w_o):
    rows = x.shape[1] // GRID_W
    rope_diff = axial_rope_tables(rows, DIFF_HEAD_DIM)
    rope_mla = axial_rope_tables(rows, MLA_ROPE_DIM)
    silu_c = jax.nn.silu(c)[:, None, :]
    silu_cc = jax.nn.silu(c_ctx)
    x_lat, x_ctx = x, ctx
    for i in range(DEPTH):
        kind, j = i % N_MIXERS, i // N_MIXERS
        update_ctx = i < DEPTH - 1
        ctx_feeds_mixer = update_ctx or kind != 0
        sh_a, sc_a, g_a, sh_m, sc_m, g_m = jnp.split(silu_c @ mod_w[i] + mod_b[i], 6, axis=-1)
        h_lat = modulate(x_lat, norm_mix_g[i], sh_a, sc_a)
        if ctx_feeds_mixer:
            csh_a, csc_a, cg_a, csh_m, csc_m, cg_m = jnp.split(silu_cc @ mod_w[i] + mod_b[i], 6, axis=-1)
            h_ctx = modulate(x_ctx, norm_mix_g[i], csh_a, csc_a)
        if kind == 0:
            y_lat = fourier_mixer(h_lat, fourier_w[j], fourier_b[j])
            y_ctx = fourier_mixer(h_ctx, fourier_w[j], fourier_b[j]) if update_ctx else None
        elif kind == 1:
            y_lat, y_ctx = diff_attention_mixer(
                h_lat, h_ctx, diff_w_qkv[j], diff_lambda_q1[j], diff_lambda_k1[j], diff_lambda_q2[j],
                diff_lambda_k2[j], diff_subln_g[j], diff_w_o[j], i, rope_diff, update_ctx)
        else:
            y_lat, y_ctx = mla_mixer(
                h_lat, h_ctx, mla_w_down[j], mla_q_norm_g[j], mla_kv_norm_g[j], mla_w_uq[j],
                mla_w_ukv[j], mla_w_o[j], rope_mla, update_ctx)
        x_lat = x_lat + g_a * y_lat
        x_lat = x_lat + g_m * sq_relu_mlp(modulate(x_lat, norm_mlp_g[i], sh_m, sc_m), mlp_w1[i], mlp_w2[i])
        if update_ctx:
            x_ctx = x_ctx + cg_a * y_ctx
            x_ctx = x_ctx + cg_m * sq_relu_mlp(modulate(x_ctx, norm_mlp_g[i], csh_m, csc_m), mlp_w1[i], mlp_w2[i])
    return rms_norm(x_lat, final_g)


DEPTH_2 = 1

N_META = 16
MIX_WIDTH = D_MODEL
POOL_WIDTH = MIX_WIDTH // 2
POOL_WINDOWS = (2, 4, 8, 16)
N_POOL_GROUPS = 4
POOL_GROUP = POOL_WIDTH // N_POOL_GROUPS
GLA_HEADS = 4
GLA_VDIM = MIX_WIDTH - POOL_WIDTH
GLA_HEAD_V = GLA_VDIM // GLA_HEADS
GLA_KDIM = GLA_VDIM // 2
GLA_HEAD_K = GLA_KDIM // GLA_HEADS
GATE_RANK = 16
GATE_NORMALIZER = 16.0
CHUNK = 64
N_GROUPS = 4
EXPERTS_PER_GROUP = 4
N_EXPERTS = N_GROUPS * EXPERTS_PER_GROUP
TOP_K_IN_GROUP = 2
EXPERT_HIDDEN = D_MODEL // 4
EPS = 1e-6
IN_COLS = POOL_WIDTH + 2 * GLA_KDIM + 2 * GLA_VDIM + GATE_RANK
SPLIT_POINTS = (POOL_WIDTH,
                POOL_WIDTH + GLA_KDIM,
                POOL_WIDTH + 2 * GLA_KDIM,
                POOL_WIDTH + 2 * GLA_KDIM + GLA_VDIM,
                POOL_WIDTH + 2 * GLA_KDIM + 2 * GLA_VDIM)


def rmsnorm(x, w):
    xf = x.astype(jnp.float32)
    y = xf * lax.rsqrt(jnp.mean(xf * xf, axis=-1, keepdims=True) + EPS)
    return (y * w.astype(jnp.float32)).astype(x.dtype)

def pool_mixer(u, pool_w, pool_scale):
    B, L, _ = u.shape
    uf = u.astype(jnp.float32).reshape(B, L, N_POOL_GROUPS, POOL_GROUP)
    cs = jnp.concatenate([jnp.zeros((B, 1, N_POOL_GROUPS, POOL_GROUP), jnp.float32),
                          jnp.cumsum(uf, axis=1)], axis=1)
    t = jnp.arange(L)
    outs = []
    for g, w in enumerate(POOL_WINDOWS):
        lo = jnp.maximum(t + 1 - w, 0)
        cs_g = cs[:, :, g]
        win_sum = cs_g[:, 1:] - cs_g[:, lo]
        cnt = (t + 1 - lo).astype(jnp.float32)[None, :, None]
        outs.append(win_sum / cnt - uf[:, :, g])
    pooled = jnp.stack(outs, axis=2)
    mixed = jnp.einsum('blgc,gcd->blgd', pooled, pool_w.astype(jnp.float32))
    y = mixed.reshape(B, L, POOL_WIDTH) * pool_scale.astype(jnp.float32)
    return y.astype(u.dtype)

def gla_mixer(q, k, v, r, g_lr, w_gate_up, b_gate, gla_norm_w):
    B, L, _ = q.shape
    f32 = jnp.float32
    log_a = jax.nn.log_sigmoid(g_lr.astype(f32) @ w_gate_up.astype(f32)
                               + b_gate.astype(f32)) / GATE_NORMALIZER
    pad = CHUNK - N_META

    def heads(a, dh):
        a = jnp.pad(a.astype(f32), ((0, 0), (pad, 0), (0, 0)))
        return a.reshape(B, -1, CHUNK, GLA_HEADS, dh).transpose(0, 3, 1, 2, 4)

    qh = heads(q, GLA_HEAD_K) * (GLA_HEAD_K ** -0.5)
    kh = heads(k, GLA_HEAD_K)
    vh = heads(v, GLA_HEAD_V)
    gh = heads(log_a, GLA_HEAD_K)
    b = jnp.cumsum(gh, axis=3)
    b_last = b[:, :, :, -1:, :]
    q_t = qh * jnp.exp(b)
    k_t = kh * jnp.exp(-b)
    k_end = kh * jnp.exp(b_last - b)
    causal = jnp.tril(jnp.ones((CHUNK, CHUNK), dtype=bool))
    scores = jnp.where(causal, jnp.einsum('bhncd,bhnsd->bhncs', q_t, k_t), 0.0)
    o_intra = jnp.einsum('bhncs,bhnsv->bhncv', scores, vh)
    dS = jnp.einsum('bhncd,bhncv->bhndv', k_end, vh)
    decay = jnp.exp(b_last[:, :, :, 0, :])

    def step(S, inp):
        dS_n, dec_n = inp
        return dec_n[..., None] * S + dS_n, S

    S0 = jnp.zeros((B, GLA_HEADS, GLA_HEAD_K, GLA_HEAD_V), f32)
    _, S_start = lax.scan(step, S0, (jnp.moveaxis(dS, 2, 0), jnp.moveaxis(decay, 2, 0)))
    S_start = jnp.moveaxis(S_start, 0, 2)
    o_inter = jnp.einsum('bhncd,bhndv->bhncv', q_t, S_start)
    o = (o_intra + o_inter).transpose(0, 2, 3, 1, 4).reshape(B, -1, GLA_HEADS, GLA_HEAD_V)[:, pad:]
    o = o * lax.rsqrt(jnp.mean(o * o, axis=-1, keepdims=True) + EPS) * gla_norm_w.astype(f32)
    o = o.reshape(B, L, GLA_VDIM) * jax.nn.silu(r.astype(f32))
    return o.astype(q.dtype)

def hier_moe(x, w_rg, b_rg, w_re, b_re, w_gate, w_up, w_down):
    B, L, D = x.shape
    f32 = jnp.float32
    xt = x.reshape(-1, D)
    xf = xt.astype(f32)
    g_logits = xf @ w_rg.astype(f32) + b_rg.astype(f32)
    g_prob = jax.nn.softmax(g_logits, axis=-1)
    g_sel = jnp.argmax(g_logits, axis=-1)
    p_g = jnp.take_along_axis(g_prob, g_sel[:, None], axis=-1)
    e_logits = (xf @ w_re.astype(f32) + b_re.astype(f32)).reshape(-1, N_GROUPS, EXPERTS_PER_GROUP)
    e_logits = jnp.take_along_axis(e_logits, g_sel[:, None, None], axis=1)[:, 0]
    e_prob = jax.nn.softmax(e_logits, axis=-1)
    top_p, top_i = lax.top_k(e_prob, TOP_K_IN_GROUP)
    top_p = top_p / jnp.sum(top_p, axis=-1, keepdims=True)
    weights = p_g * top_p
    expert_id = g_sel[:, None] * EXPERTS_PER_GROUP + top_i
    combine = jnp.sum(jax.nn.one_hot(expert_id, N_EXPERTS, dtype=f32) * weights[..., None], axis=1)
    y = jnp.zeros(xf.shape, f32)
    for e in range(N_EXPERTS):
        h = jax.nn.silu(xt @ w_gate[e]) * (xt @ w_up[e])
        y = y + combine[:, e:e + 1] * (h @ w_down[e]).astype(f32)
    return y.reshape(B, L, D).astype(x.dtype)

def second_inputs(seed: int = 0) -> dict:
    key = jax.random.key(seed)
    ks = jax.random.split(key, 20)
    n = jax.random.normal
    D = D_MODEL
    return {
        "x": n(ks[0], (BATCH, SEQ, D), jnp.float32),
        "meta_tokens": n(ks[1], (N_META, D), jnp.float32),
        "norm_mix_w": 1.0 + 0.05 * n(ks[2], (DEPTH_2, D), jnp.float32),
        "w_in": n(ks[3], (DEPTH_2, D, IN_COLS), jnp.float32) * D ** -0.5,
        "w_gate_up": n(ks[4], (DEPTH_2, GATE_RANK, GLA_KDIM), jnp.float32) * GATE_RANK ** -0.5,
        "b_gate": 0.1 * n(ks[5], (DEPTH_2, GLA_KDIM), jnp.float32),
        "gla_norm_w": 1.0 + 0.05 * n(ks[6], (DEPTH_2, GLA_HEAD_V), jnp.float32),
        "pool_w": n(ks[7], (DEPTH_2, N_POOL_GROUPS, POOL_GROUP, POOL_GROUP), jnp.float32) * POOL_GROUP ** -0.5,
        "pool_scale": 1.0 + 0.05 * n(ks[8], (DEPTH_2, POOL_WIDTH), jnp.float32),
        "w_out": n(ks[9], (DEPTH_2, MIX_WIDTH, D), jnp.float32) * MIX_WIDTH ** -0.5,
        "norm_ffn_w": 1.0 + 0.05 * n(ks[10], (DEPTH_2, D), jnp.float32),
        "w_router_group": n(ks[11], (DEPTH_2, D, N_GROUPS), jnp.float32) * D ** -0.5,
        "b_router_group": 0.01 * n(ks[12], (DEPTH_2, N_GROUPS), jnp.float32),
        "w_router_expert": n(ks[13], (DEPTH_2, D, N_EXPERTS), jnp.float32) * D ** -0.5,
        "b_router_expert": 0.01 * n(ks[14], (DEPTH_2, N_EXPERTS), jnp.float32),
        "w_expert_gate": n(ks[15], (DEPTH_2, N_EXPERTS, D, EXPERT_HIDDEN), jnp.float32) * D ** -0.5,
        "w_expert_up": n(ks[16], (DEPTH_2, N_EXPERTS, D, EXPERT_HIDDEN), jnp.float32) * D ** -0.5,
        "w_expert_down": n(ks[17], (DEPTH_2, N_EXPERTS, EXPERT_HIDDEN, D), jnp.float32) * EXPERT_HIDDEN ** -0.5,
        "final_norm_w": 1.0 + 0.05 * n(ks[18], (D,), jnp.float32),
    }

def second_block(x, meta_tokens, norm_mix_w, w_in, w_gate_up, b_gate, gla_norm_w, pool_w,
              pool_scale, w_out, norm_ffn_w, w_router_group, b_router_group,
              w_router_expert, b_router_expert, w_expert_gate, w_expert_up,
              w_expert_down, final_norm_w):
    B = x.shape[0]
    meta = jnp.broadcast_to(meta_tokens[None].astype(x.dtype), (B, N_META, D_MODEL))
    h = jnp.concatenate([meta, x], axis=1)
    for l in range(DEPTH_2):
        u = rmsnorm(h, norm_mix_w[l])
        proj = u @ w_in[l]
        pool_v, q, k, v, r, g_lr = jnp.split(proj, SPLIT_POINTS, axis=-1)
        y_pool = pool_mixer(pool_v, pool_w[l], pool_scale[l])
        y_gla = gla_mixer(q, k, v, r, g_lr, w_gate_up[l], b_gate[l], gla_norm_w[l])
        h = h + jnp.concatenate([y_pool, y_gla], axis=-1) @ w_out[l]
        h = h + hier_moe(rmsnorm(h, norm_ffn_w[l]), w_router_group[l], b_router_group[l],
                         w_router_expert[l], b_router_expert[l], w_expert_gate[l],
                         w_expert_up[l], w_expert_down[l])
    return rmsnorm(h, final_norm_w)[:, N_META:]


def setup_inputs(seed=0):
    out = dict(first_inputs(seed))
    for name, value in second_inputs(seed + 1).items():
        if name != "x":
            out[name + "_2"] = value
    return out


def reference(
    x, c, ctx, c_ctx, mod_w, mod_b, norm_mix_g, norm_mlp_g, final_g, mlp_w1, mlp_w2, fourier_w,
    fourier_b, diff_w_qkv, diff_lambda_q1, diff_lambda_k1, diff_lambda_q2, diff_lambda_k2,
    diff_subln_g, diff_w_o, mla_w_down, mla_q_norm_g, mla_kv_norm_g, mla_w_uq, mla_w_ukv,
    mla_w_o, meta_tokens_2, norm_mix_w_2, w_in_2, w_gate_up_2, b_gate_2, gla_norm_w_2, pool_w_2,
    pool_scale_2, w_out_2, norm_ffn_w_2, w_router_group_2, b_router_group_2, w_router_expert_2,
    b_router_expert_2, w_expert_gate_2, w_expert_up_2, w_expert_down_2, final_norm_w_2,
):
    x = first_block(
        x, c, ctx, c_ctx, mod_w, mod_b, norm_mix_g, norm_mlp_g, final_g, mlp_w1, mlp_w2,
        fourier_w, fourier_b, diff_w_qkv, diff_lambda_q1, diff_lambda_k1, diff_lambda_q2,
        diff_lambda_k2, diff_subln_g, diff_w_o, mla_w_down, mla_q_norm_g, mla_kv_norm_g,
        mla_w_uq, mla_w_ukv, mla_w_o,
    )
    return second_block(
        x, meta_tokens_2, norm_mix_w_2, w_in_2, w_gate_up_2, b_gate_2, gla_norm_w_2, pool_w_2,
        pool_scale_2, w_out_2, norm_ffn_w_2, w_router_group_2, b_router_group_2,
        w_router_expert_2, b_router_expert_2, w_expert_gate_2, w_expert_up_2, w_expert_down_2,
        final_norm_w_2,
    )


_drawn_inputs = setup_inputs


def setup_inputs(seed=0):
    import zlib

    import numpy as np

    out = dict(_drawn_inputs(seed))
    spreads = {}
    factors = {'diff_lambda_q1': 7.6,
     'diff_subln_g': 3.131,
     'mla_q_norm_g': 8.0,
     'mla_kv_norm_g': 8.0,
     'b_router_group_2': 21.829,
     'b_router_expert_2': 4.819}
    for name, (base, spread) in spreads.items():
        noise = np.random.default_rng([zlib.crc32(name.encode()), seed]).standard_normal(out[name].shape)
        drawn = base * np.exp(spread * noise) if base else spread * noise
        out[name] = __import__('jax').numpy.asarray(drawn.astype(out[name].dtype))
    for name, factor in factors.items():
        out[name] = (out[name] * factor).astype(out[name].dtype)
    return out
```

```python
from contextlib import ExitStack

import numpy as np
import concourse.bass as bass
from concourse import mybir

F32 = mybir.dt.float32
F32R = mybir.dt.float32r
ACT = mybir.ActivationFunctionType
ALU = mybir.AluOpType
AX = mybir.AxisListType

P = 128
D = 1024
KT = D // P
LAT = 256
CTX = 256
TOK = LAT + CTX
META = 16
TOK2 = LAT + META
DEPTH = 4
FF = 4 * D
FF_BLOCK = 1024
BLOCKS = FF // FF_BLOCK
MOD_TILES = 6 * KT
EPS = 1e-6
LAM_INIT = 0.8 - 0.6 * float(np.exp(-0.3))
HEADS = 8
HALF = 64
MLA_HEADS = 16
NOPE, ROPE = 64, 32
QD = NOPE + ROPE
Q_RANK, KV_RANK = 256, 128
GLA_HEADS = 4
CHUNK = 64
EXPERTS = 16
E_GROUPS = 4
E_PER = 4
E_HID = 256

RING = 4
RAW = 4
AHEAD = RING - 1
BANKS = 4
AUX = 3
PANEL = KT * P

VEC_ROWS = {}
VEC_TILES = 3


def place_vectors():
    rows = [0] * VEC_TILES
    plan = [("mod_b_lo", 0, 96), ("c", 0, 8), ("c_ctx", 0, 8), ("mod_b_hi", 1, 96),
            ("norm_mix_g", 2, 32), ("norm_mlp_g", 2, 32), ("final_g", 2, 8), ("fourier_b", 2, 16),
            ("norm_mix_w_2", 2, 8), ("norm_ffn_w_2", 2, 8), ("final_norm_w_2", 2, 8),
            ("pool_scale_2", 2, 4), ("gla_norm_w_2", 2, 1), ("b_gate_2", 2, 2), ("diff_subln_g", 2, 1),
            ("mla_q_norm_g", 2, 2), ("mla_kv_norm_g", 2, 1)]
    for name, tile, n in plan:
        VEC_ROWS[name] = (tile, rows[tile], n)
        rows[tile] += n
    return rows


VEC_COUNT = place_vectors()


class Plan:

    def __init__(self):
        self.tiles = []
        self.aux = []
        self.loaded = [0] * RAW
        self.at = {}
        self.units = []
        self.panels = []

    def phase(self, name, units=(), tiles=(), aux=(), frees=()):
        self.at[name] = {"unit": len(self.units), "panel": len(self.panels), "tile": len(self.tiles), "aux": len(self.aux)}
        k = 0
        first = len(self.panels)
        self.panels += [None] * len(frees)
        for panels, dmas in units:
            if isinstance(panels, int):
                panels = range(k, k + panels)
            slot = len(self.units) % RAW
            self.loaded[slot] += 16 * dmas
            for place, panel in enumerate(panels):
                free = frees[panel]
                if isinstance(free, int):
                    free = ("tile_done", len(self.tiles) + free + 1)
                self.panels[first + panel] = (len(self.units), place, free)
                k += 1
            self.units.append((first + max(panels) + 1, slot, self.loaded[slot]))
        assert k == len(frees)
        self.tiles += tiles
        self.aux += aux


AUX_AT = {}


def diff_aux():
    tiles = []

    def add(what, h, i, signal, value):
        AUX_AT["diff", what, h, i] = len(tiles)
        tiles.append((signal, value))

    for turn in range(HEADS + 1):
        h = turn - 1
        if h >= 0:
            for i in range(8):
                add("score", h, i, "p_exp", 8 * h + i + 1)
            for i in range(3):
                add("turn_p", h, i, "pt_lo", 3 * h + i + 1)
            add("pv", h, 0, "o_out", h + 1)
        if turn < HEADS:
            add("turn_v", turn, 0, "v_lo", turn + 1)
        if h >= 0:
            add("square", h, 0, "o_root", h + 1)
    return tiles


def mla_aux():
    tiles = []

    def add(what, h, i, signal, value):
        AUX_AT["mla", what, h, i] = len(tiles)
        tiles.append((signal, value))

    for turn in range(MLA_HEADS + 1):
        h = turn - 1
        if h >= 0:
            for i in range(2):
                add("score", h, i, "mla_exp", 2 * h + i + 1)
        if turn < MLA_HEADS:
            add("turn_v", turn, 0, "mla_v_lo", turn + 1)
        if h >= 0:
            for i in range(2):
                add("turn_p", h, i, "mla_pt_lo", 2 * h + i + 1)
    return tiles


EXPERT_TURNS = 4
WIN_ORDER = [16, 4, 5, 6, 7, 8, 9, 10, 11, 0, 1, 2, 3, 12, 13, 14, 15]
POOL_AT, Q_AT, K_AT, V_AT, R_AT, GATE_AT = 0, 4, 6, 8, 12, 16
GATE_RANK = 16
CHUNKS = [(0, META)] + [(META + CHUNK * n, CHUNK) for n in range(LAT // CHUNK)]
MLP_TILES = 2 * KT


def signals(name, first, n):
    return [(name, first + i + 1) for i in range(n)]


X_AT = {"four0": 0, "mlp0": 8, "diffo": 40, "mlp1": 48, "mlao": 80, "mlp2": 88, "four3": 120,
        "mlp3": 128, "wout": 160, "moe": 168}


def mlp_tiles(layer):
    tiles = []
    for b in range(BLOCKS):
        tiles += signals("relu", KT * (BLOCKS * layer + b), KT)
        tiles += signals("x_done", X_AT[f"mlp{layer}"] + KT * b, KT)
    return tiles


def make_plan():
    p = Plan()
    p.phase("vec", tiles=[("vec", 1), ("lam_col", 1)])
    p.phase("xin", tiles=signals("x_cols", 0, KT))
    p.phase("four0", [(2, 1)] * 4, signals("four_lo", 0, 24) + signals("x_done", 0, KT), frees=[24 + m for m in range(KT)])
    p.phase("mlp0", [(2, 1)] * 32, mlp_tiles(0), frees=range(64))
    pairs = [([h + j, h + j + 3], 1) for h in range(0, 3 * HEADS, 6) for j in range(3)]
    p.phase("diff", pairs, signals("qkv", 0, 24), diff_aux(), frees=range(24))
    p.phase("diffo", [(2, 1)] * 4, signals("x_done", X_AT["diffo"], KT), frees=range(8))
    p.phase("mlp1", [(2, 1)] * 32, mlp_tiles(1), frees=range(64))
    p.phase("mlad", [(2, 1), (1, 1), (1, 1)], signals("down_out", 0, 4), frees=range(4))
    p.phase("mla", [(2, 4), (2, 2), (2, 4)], signals("mla_qkv", 0, 2 * MLA_HEADS), mla_aux(),
            frees=[6, 14, 15, 31, 22, 30])
    p.phase("mlao", [(2, 1)] * 4, signals("x_done", X_AT["mlao"], KT), frees=range(8))
    p.phase("mlp2", [(2, 1)] * 32, mlp_tiles(2), frees=range(64))
    p.phase("four3", [(2, 1)] * 4, signals("four_lo", 24, 16) + signals("x_done", X_AT["four3"], KT),
            frees=[16 + m for m in range(KT)])
    p.phase("mlp3", [(2, 1)] * 32, mlp_tiles(3), frees=range(64))
    p.phase("meta", tiles=[("meta_cols", 1)])
    p.phase("win", [(1, 1)] + [(2, 1)] * 8, signals("proj", 0, 17), frees=range(17))
    p.phase("wout", [(2, 1)] * 4, signals("x_done", X_AT["wout"], KT), frees=range(8))
    panels = 6 * EXPERTS
    p.phase("moe", [(2, 1)] * (panels // 2), frees=[("expert_done", i + 1) for i in range(panels)])
    return p


PLAN = make_plan()

MIX_TILES = []
MIX_AT = {}
for _what, _n, _signal in (("gate", 2, "z_in"), ("turn_v", 5, "v_rows"), ("turn_k", 2, "k_rows"),
                           ("pool", 2, "pool_in"), ("score", 2, "sc_in"), ("state", 2, "states"),
                           ("out", 2, "go_in"), ("square", 2, "go_root")):
    for _i in range(_n):
        MIX_AT[_what, _i] = len(MIX_TILES)
        MIX_TILES.append((_signal, _i + 1 if _signal != "states" else 4 * (_i + 1)))



NORMS = [("mix0", True, TOK), ("mlp0", True, TOK), ("mix1", True, TOK), ("mlp1", True, TOK),
         ("mix2", True, TOK), ("mlp2", True, LAT), ("mix3", True, LAT), ("mlp3", True, LAT),
         ("final", False, LAT), ("mix_2", True, TOK2), ("ffn_2", True, LAT), ("final_2", False, LAT)]
NORM_AT = {name: i for i, (name, _, _) in enumerate(NORMS)}
SPLIT_AT = {name: sum(s for _, s, _ in NORMS[:i]) for i, (name, _, _) in enumerate(NORMS)}
MOD_UNITS = 6
MOD_AFTER = {2: 0, 5: 1, 7: 2, 9: 3, 12: 4, 14: 5}


def build_program(nc, a, out):
    ctx = ExitStack()
    sems = {}

    def s(name):
        if name not in sems:
            sems[name] = ctx.enter_context(nc.semaphore(name))
        return sems[name]

    with ctx:
        base = 16512
        at = {}

        def sb(name, shape, dtype=F32, over=None):
            nonlocal base
            size = int(np.prod(shape[1:])) * 4
            size = (size + 31) // 32 * 32
            if over is None:
                place, base = base, base + size
            else:
                place = over
            at[name] = place
            return nc.alloc_sbuf_tensor_at(name, list(shape), dtype, offset=place)

        X = sb("x", [P, KT, TOK])
        H_hi = sb("h_hi", [P, KT, TOK], F32R)
        H_lo = sb("h_lo", [P, KT, TOK], F32R)
        G_hi = sb("g_hi", [P, KT, TOK], F32R)
        G_lo = sb("g_lo", [P, KT, TOK], F32R)
        x_rows = sb("x_rows", [P, 4, D], over=at["g_hi"])
        W_hi = [sb(f"w_hi{r}", [P, PANEL], F32R) for r in range(RING)]
        W_lo = [sb(f"w_lo{r}", [P, PANEL], F32R) for r in range(RING)]
        w_raw = [sb(f"w_raw{r}", [P, KT, 2, P]) for r in range(RAW)]
        ident = sb("ident", [P, P])
        ones = sb("ones", [P, P])
        eps = sb("eps", [P, 1])
        vec_rows = sb("vec_rows", [P, VEC_TILES, P])
        vec = sb("vec", [P, VEC_TILES, P])
        lam_in = sb("lam_in", [1, 4, HALF])
        lam_prod = sb("lam_prod", [1, 2, HALF])
        lam_row = sb("lam_row", [1, 4])
        lam_col = sb("lam_col", [P, 2])
        subln = sb("subln", [P, 1])
        silu_c = sb("silu_c", [P, 2, KT])
        silu_t = sb("silu_t", [P, 2, KT])
        mod = [sb(f"mod{r}", [P, MOD_TILES, 2]) for r in range(2)]
        scale_mix = sb("scale_mix", [P, KT, 2])
        scale_mlp = sb("scale_mlp", [P, KT, 2])
        gated_b = sb("gated_b", [P, KT, 2])
        norm_buf = [sb(f"norm{r}", [P, TOK]) for r in range(6)]
        work = base
        mod_raw = [sb(f"mod_raw{r}", [P, KT, 2, P]) for r in range(2)]
        mlp_work = base
        relu = [sb(f"relu{r}", [P, TOK]) for r in range(2)]
        square = [sb(f"square{r}", [P, TOK]) for r in range(2)]
        base = mlp_work
        dft = sb("dft", [P, 2, 2 * 256])
        dft_hi = sb("dft_hi", [P, 2, 2 * 256], F32R)
        dft_lo = sb("dft_lo", [P, 2, 2 * 256], F32R)
        base = work
        rope = sb("rope", [P, 2, LAT])
        q_f = sb("q_f", [P, TOK])
        k_f = sb("k_f", [P, TOK])
        v_f = q_f
        q_hi, q_lo = sb("q_hi", [P, TOK], F32R), sb("q_lo", [P, TOK], F32R)
        k_hi, k_lo = sb("k_hi", [P, TOK], F32R), sb("k_lo", [P, TOK], F32R)
        v_hi, v_lo = sb("v_hi", [P, 4, P], F32R), sb("v_lo", [P, 4, P], F32R)
        p_raw = [[sb(f"p_raw{r}{j}", [P, TOK]) for j in range(2)] for r in range(2)]
        p_all = sb("p_all", [P, 2 * TOK + 2 * CTX])
        pt_hi, pt_lo = sb("pt_hi", [P, 6, LAT], F32R), sb("pt_lo", [P, 6, LAT], F32R)
        neg_max = sb("neg_max", [P, 8])
        z = sb("z", [P, 8])
        z_inv = sb("z_inv", [P, 8])
        z_mix = sb("z_mix", [P, 8])
        o_f, o_sq, o_inv, o_t, o_g = norm_buf[0], norm_buf[1], norm_buf[2], norm_buf[3], norm_buf[4]
        turned, straight = norm_buf[5][:, 0:LAT], norm_buf[5][:, LAT:TOK]
        assert base <= 229344, base
        base = work
        rope32 = sb("rope32", [P, 2, LAT])
        cq_f = sb("cq_f", [P, 2, LAT])
        ckv_f = sb("ckv_f", [P, TOK])
        cq_hi, cq_lo = sb("cq_hi", [P, 2, LAT], F32R), sb("cq_lo", [P, 2, LAT], F32R)
        ckv_hi, ckv_lo = sb("ckv_hi", [P, TOK], F32R), sb("ckv_lo", [P, TOK], F32R)
        mq_f = sb("mq_f", [P, LAT])
        kv_f = sb("kv_f", [P, TOK])
        mq_hi, mq_lo = sb("mq_hi", [P, LAT], F32R), sb("mq_lo", [P, LAT], F32R)
        mk_hi, mk_lo = sb("mk_hi", [P, TOK], F32R), sb("mk_lo", [P, TOK], F32R)
        mv_hi = [sb(f"mv_hi{j}", [P, 4, P], F32R) for j in range(2)]
        mv_lo = [sb(f"mv_lo{j}", [P, 4, P], F32R) for j in range(2)]
        mp_raw = [sb(f"mp_raw{r}", [P, TOK], over=at[("cq_f", "ckv_f")[r]]) for r in range(2)]
        mp_all = sb("mp_all", [P, 2, TOK])
        mpt_hi, mpt_lo = sb("mpt_hi", [P, 4, LAT], F32R), sb("mpt_lo", [P, 4, LAT], F32R)
        m_max = sb("m_max", [P, 2])
        m_z = sb("m_z", [P, 2])
        m_zinv = sb("m_zinv", [P, 2])
        assert base <= 229344, base

        base = work
        meta_rows = sb("meta_rows", [META, D])
        pool_w = sb("pool_w", [P, 4, P])
        gate_up = sb("gate_up", [GATE_RANK, 2 * P])
        route_w = sb("route_w", [P, KT, 4 + EXPERTS])
        route_b = sb("route_b", [1, 4 + EXPERTS])
        chunk_mask = sb("chunk_mask", [P, TOK2])
        S_all = sb("S_all", [P, 2, 4, P])
        assert base <= mlp_work
        base = at["g_hi"]
        proj = sb("proj", [P, 17, TOK2])
        pooled = sb("pooled", [P, 4, LAT])
        win_a = sb("win_a", [P, 4, TOK2])
        win_b = sb("win_b", [P, 4, TOK2])
        assert base <= at["w_hi0"]
        base = at["h_hi"]
        Y_hi, Y_lo = sb("Y_hi", [P, KT, LAT], F32R), sb("Y_lo", [P, KT, LAT], F32R)
        go_f = sb("go_f", [P, GLA_HEADS, LAT])
        r_silu = sb("r_silu", [P, GLA_HEADS, LAT])
        y_f = sb("y_f", [P, 4, LAT])
        sc = sb("sc", [CHUNK, GLA_HEADS, 4, CHUNK])
        assert base <= at["g_hi"]
        base = at["norm0"]
        z_f = sb("z_f", [P, 2, TOK2])
        z_abs = sb("z_abs", [P, 2, TOK2])
        log_a = sb("log_a", [P, 2, TOK2])
        b_cum = sb("b_cum", [P, 2, TOK2])
        e_pos = sb("e_pos", [P, 2, TOK2])
        assert base <= work
        base = mlp_work
        e_neg = sb("e_neg", [P, 2, LAT])
        e_end = sb("e_end", [P, 2, TOK2])
        q_pad = [sb(f"q_pad{j}", [P, 2, LAT]) for j in range(2)]
        k_t = sb("k_t", [P, 2, LAT])
        k_end = sb("k_end", [P, 2, TOK2])
        v_rows_m = sb("v_rows_m", [META, GLA_HEADS, P])
        k_rows_m = sb("k_rows_m", [META, 2, P])
        b_last = sb("b_last", [P, 2, 4])
        decay = sb("decay", [P, 2, 4])
        v_rows = sb("v_rows", [CHUNK, GLA_HEADS, 4, P])
        k_rows = sb("k_rows", [CHUNK, 2, 3, P])
        go_sq, go_inv = win_a[:, :, 0:LAT], win_b[:, :, 0:LAT]
        assert base <= 229344, base
        base = mlp_work
        logits = sb("logits", [P, 2, 4 + EXPERTS])
        r4 = [sb(f"r4_{i}", [P, 2, 4]) for i in range(12)]
        r1 = [sb(f"r1_{i}", [P, 2]) for i in range(8)]
        r16 = sb("r16", [P, 2, 4, 4])
        rank = sb("rank", [P, 2, 4])
        combine = sb("combine", [P, 2, EXPERTS])
        diag = [sb(f"diag{j}", [P, 2, P]) for j in range(2)]
        e_exp = sb("e_exp", [P, 2, LAT])
        e_inv = sb("e_inv", [P, 2, LAT])
        e_hid = [sb(f"e_hid{j}", [P, 2, LAT]) for j in range(2)]
        E_hi = [sb(f"E_hi{j}", [P, 2, LAT], F32R) for j in range(2)]
        E_lo = [sb(f"E_lo{j}", [P, 2, LAT], F32R) for j in range(2)]
        zero_row = sb("zero_row", [1, TOK])
        out_rows = sb("out_rows", [P, 2, D])
        assert base <= 229344, base

        psum = [ctx.enter_context(nc.psum_tensor(f"bank{b}", [P, 512], F32)) for b in range(8)]
        bank = psum[:BANKS]
        mod_ps = psum[4]
        pv_ps = psum[4]
        mix_ps = psum[4:8]
        aux = psum[5:8]
        sum_ps = psum[7]

        def vcol(name, k=0):
            tile, row, _ = VEC_ROWS[name]
            return vec[:, tile, row + k:row + k + 1]

        def vcols(name, first=0, n=None):
            tile, row, count = VEC_ROWS[name]
            n = count if n is None else n
            return vec[:, tile, row + first:row + first + n]

        def later(value, i, step):
            return value if i is None else value + i * step

        w1 = a["mlp_w1"].rearrange("l (k p) (b u c) -> l b u p k c", p=P, b=BLOCKS, u=4)
        w2 = a["mlp_w2"].rearrange("l (b k p) (u c) -> l b u p k c", p=P, b=BLOCKS, u=4)
        mod_w = a["mod_w"].rearrange("l (k p) (b u c) -> l b u p k c", p=P, b=BLOCKS, u=MOD_UNITS)

        block = ctx.enter_context(nc.Block())

        @block.sync
        def _(sp):
            def wait_raw_free(u, i=None, step=0):
                if u >= RAW:
                    sp.wait_ge(s("panel_ready"), later(PLAN.units[u - RAW][0], i, step))

            def load_unit(u, parts, i=None, step=0):
                wait_raw_free(u, i, step)
                slot = PLAN.units[u][1]
                for dst, src in parts:
                    sp.dma_start(dst(w_raw[slot]), src).then_inc(s(f"raw_in{slot}"), 16)

            def whole(raw):
                return raw[:, :, :, :].rearrange("p k j c -> p k (j c)")

            def load_square(name, w):
                v = w.rearrange("(k p) (u c) -> u p k c", p=P, c=2 * P)
                for u in range(4):
                    load_unit(PLAN.at[name]["unit"] + u, [(whole, v[u])])

            def load_mlp(layer):
                u0 = PLAN.at[f"mlp{layer}"]["unit"]
                with sp.Fori(0, BLOCKS) as b:
                    for u in range(4):
                        load_unit(u0 + u, [(whole, w1[layer, b, u])], b, 2 * KT)
                    for u in range(4):
                        load_unit(u0 + 4 + u, [(whole, w2[layer, b, u])], b, 2 * KT)

            sp.dma_start(x_rows[:, 0:2, :], a["x"][0].rearrange("(t p) d -> p t d", p=P)).then_inc(s("x_in"), 16)
            sp.dma_start(x_rows[:, 2:4, :], a["ctx"][0].rearrange("(t p) d -> p t d", p=P)).then_inc(s("x_in"), 16)
            mod_b = a["mod_b"].rearrange("l (r c) -> (l r) c", c=P)
            rows = {"mod_b_lo": mod_b[0:96], "mod_b_hi": mod_b[96:192],
                    "c": a["c"].rearrange("o (r c) -> (o r) c", c=P),
                    "c_ctx": a["c_ctx"].rearrange("(r c) -> r c", c=P),
                    "final_g": a["final_g"].rearrange("(r c) -> r c", c=P),
                    "final_norm_w_2": a["final_norm_w_2"].rearrange("(r c) -> r c", c=P)}
            for name, (tile, row, n) in VEC_ROWS.items():
                src = rows[name] if name in rows else a[name].rearrange("l (r c) -> (l r) c", c=P)
                sp.dma_start(vec_rows[row:row + n, tile, :], src).then_inc(s("vec_in"), 16)
            for n, name in enumerate(["diff_lambda_q1", "diff_lambda_q2", "diff_lambda_k1", "diff_lambda_k2"]):
                sp.dma_start(lam_in[:, n, :], a[name]).then_inc(s("vec_in"), 16)
            sp.dma_start(dft[:, :, :], a["dft"].rearrange("(k p) c -> p k c", p=P)).then_inc(s("dft_in"), 16)
            load_square("four0", a["fourier_w"][0])
            load_mlp(0)
            w_qkv = a["diff_w_qkv"][0].rearrange("(k p) (three m c) -> m three p k c", p=P, three=3, c=2 * P)
            sp.wait_ge(s("mod_used"), 2 * BLOCKS * MOD_UNITS)
            sp.dma_start(rope[:, :, :], a["rope_diff"]).then_inc(s("rope_in"), 16)
            for h in range(HEADS // 2):
                for j in range(3):
                    load_unit(PLAN.at["diff"]["unit"] + 3 * h + j, [(whole, w_qkv[h, j])])
            load_square("diffo", a["diff_w_o"][0])
            load_mlp(1)
            sp.wait_ge(s("mod_used"), 3 * BLOCKS * MOD_UNITS)
            sp.dma_start(rope32[HALF:HALF + ROPE, :, :], a["rope_mla"]).then_inc(s("rope_in"), 16)
            down = a["mla_w_down"][0].rearrange("(k p) c -> p k c", p=P)
            u = PLAN.at["mlad"]["unit"]
            load_unit(u, [(whole, down[:, :, 0:Q_RANK])])
            load_unit(u + 1, [(lambda raw: raw[:, :, 0, :], down[:, :, Q_RANK:Q_RANK + KV_RANK])])
            load_unit(u + 2, [(lambda raw: raw[:, :, 0, 0:QD], down[:, :, Q_RANK + KV_RANK - NOPE:])])
            uq = a["mla_w_uq"][0].rearrange("(k p) (g h c) -> g k p h c", p=P, g=4, c=QD)
            ukv = a["mla_w_ukv"][0].rearrange("p (j h c) -> j p h c", j=2, c=P)
            u = PLAN.at["mla"]["unit"]

            def load_uq(u, g0):
                load_unit(u, [(lambda raw, j=j, k=k: raw[:, 4 * k:4 * k + 4, j, 0:QD], uq[g0 + j, k])
                              for j in range(2) for k in range(2)])

            load_uq(u, 0)
            load_unit(u + 1, [(lambda raw, j=j: raw[:, :, j, :], ukv[j]) for j in range(2)])
            load_uq(u + 2, 2)
            load_square("mlao", a["mla_w_o"][0])
            load_mlp(2)
            sp.wait_ge(s("g_lo"), 3 * KT * BLOCKS)
            sp.dma_start(dft[:, :, :], a["dft"].rearrange("(k p) c -> p k c", p=P)).then_inc(s("dft_in"), 16)
            load_square("four3", a["fourier_w"][1])
            load_mlp(3)
            sp.wait_ge(s("mod_used"), DEPTH * BLOCKS * MOD_UNITS)
            small = [(meta_rows[:, :], a["meta_tokens_2"]),
                     (pool_w[:, :, :], a["pool_w_2"][0].rearrange("g c d -> c g d")),
                     (gate_up[:, :], a["w_gate_up_2"][0]),
                     (route_w[:, :, 0:4], a["w_router_group_2"][0].rearrange("(k p) c -> p k c", p=P)),
                     (route_w[:, :, 4:], a["w_router_expert_2"][0].rearrange("(k p) c -> p k c", p=P)),
                     (route_b[:, 0:4], a["b_router_group_2"]),
                     (route_b[:, 4:], a["b_router_expert_2"])]
            for dst, src in small:
                sp.dma_start(dst, src).then_inc(s("small_in"), 16)
            w_in = a["w_in_2"][0].rearrange("(k p) c -> p k c", p=P)
            u = PLAN.at["win"]["unit"]
            load_unit(u, [(lambda raw: raw[:, :, 0, 0:GATE_RANK], w_in[:, :, GATE_AT * P:])])
            for i in range(8):
                c = WIN_ORDER[1 + 2 * i] * P
                load_unit(u + 1 + i, [(whole, w_in[:, :, c:c + 2 * P])])
            load_square("wout", a["w_out_2"][0])
            w_gate = a["w_expert_gate_2"][0].rearrange("e (k p) c -> e p k c", p=P)
            w_up = a["w_expert_up_2"][0].rearrange("e (k p) c -> e p k c", p=P)
            w_down = a["w_expert_down_2"][0].rearrange("e (k p) c -> e p k c", p=P)

            def down_rows(raw):
                return raw[:, :, :, :].rearrange("p (k a) j c -> p k (a j c)", k=2)

            u = PLAN.at["moe"]["unit"]

            def load_experts(x, place, i=None):
                first = u + 3 * place - 1 if place else u
                step = 6 * EXPERT_TURNS
                load_unit(first, [(whole, w_gate[x])], i, step)
                load_unit(first + 1, [(whole, w_up[x])], i, step)
                if place:
                    load_unit(first + 2, [(down_rows, w_down[x - 1])], i, step)

            load_experts(0, 0)
            with sp.Fori(0, 3) as i:
                for j in range(EXPERT_TURNS):
                    load_experts(i * EXPERT_TURNS + (1 + j), 1 + j, i)
            for x in range(1 + 3 * EXPERT_TURNS, EXPERTS):
                load_experts(x, x)
            load_unit(u + 3 * EXPERTS - 1, [(down_rows, w_down[EXPERTS - 1])])
            out_v = out[0].rearrange("(t p) d -> p t d", p=P)
            for tt in range(2):
                sp.wait_ge(s("out_rows"), 2 * tt + 2)
                sp.dma_start(out_v[:, tt, :], out_rows[:, tt, :]).then_inc(s("out"), 16)
            sp.wait_ge(s("out"), 32)

        @block.gpsimd
        def _(pool):
            pool.memset(ident[:, :], 0.0).then_inc(s("const"), 1)
            pool.memset(ones[:, :], 1.0).then_inc(s("const"), 1)
            pool.memset(eps[:, :], EPS).then_inc(s("const"), 1)
            pool.wait_ge(s("const"), 3)
            pool.affine_select(out=ident[:, :], in_=ident[:, :], compare_op=ALU.not_equal, fill=1.0,
                               base=0, pattern=[[-1, P]], channel_multiplier=1).then_inc(s("const"), 1)

            def load_mod(layer, b, i):
                for u in range(MOD_UNITS):
                    n = BLOCKS * MOD_UNITS * layer + u
                    if layer or i is not None or u >= 2:
                        pool.wait_ge(s("mod_used"), later(n - 1, i, MOD_UNITS))
                    pool.dma_start(mod_raw[u % 2][:, :, :, :].rearrange("p k j c -> p k (j c)"),
                                   mod_w[layer, b, u]).then_inc(s(f"mod_in{u % 2}"), 16)

            load_mod(0, 0, None)
            with pool.Fori(1, BLOCKS) as b:
                load_mod(0, b, b)
            for layer in range(1, DEPTH):
                if layer > 1:
                    pool.wait_ge(s("x_done"), X_AT[f"mlp{layer - 1}"])
                with pool.Fori(0, BLOCKS) as b:
                    load_mod(layer, b, b)
            for i in range(2):
                pool.wait_ge(s("sc_in"), i + 1)
                pool.affine_select(out=sc[:, 2 * i:2 * i + 2, :, :].rearrange("p h n c -> p (h n) c"),
                                   in_=sc[:, 2 * i:2 * i + 2, :, :].rearrange("p h n c -> p (h n) c"),
                                   compare_op=ALU.is_ge, fill=0.0, base=0, pattern=[[0, 8], [1, CHUNK]],
                                   channel_multiplier=-1).then_inc(s("sc_masked"), 1)

        @block.scalar
        def _(act):
            def split_hi(n, i=None, tiles=0, raws=0):
                if isinstance(i, int):
                    n, i = n + i * MLP_TILES, None
                unit, place, _ = PLAN.panels[n]
                _, slot, value = PLAN.units[unit]
                act.wait_ge(s(f"raw_in{slot}"), later(value, i, raws))
                if n >= RING:
                    name, freed = PLAN.panels[n - RING][2]
                    act.wait_ge(s(name), later(freed, i, tiles))
                act.activation(W_hi[n % RING][:, :].rearrange("p (k c) -> p k c", c=P),
                               w_raw[slot][:, :, place, :], ACT.Copy).then_inc(s("w_hi"), 1)

            def norm(name, n_cols, segments, pairs):
                ni = NORM_AT[name]
                c = slice(0, n_cols)
                if name in ("mix_2", "final_2"):
                    act.wait_ge(s("h"), KT * ni)
                for k in range(KT):
                    if k >= 2:
                        act.wait_ge(s("sq_added"), KT * ni + k - 1)
                    act.activation(norm_buf[k % 2][:, c], X[:, k, c], ACT.Square).then_inc(s("sq"), 1)
                act.wait_ge(s("sum"), ni + 1)
                act.activation(norm_buf[3][:, c], sum_ps[:, c], ACT.Sqrt, bias=eps[:, 0:1],
                               scale=1.0 / D).then_inc(s("root"), 1)
                for k in range(KT):
                    act.wait_ge(s("t"), KT * ni + k + 1)
                    if pairs is not None and k >= 2:
                        act.wait_ge(s("h_lo"), KT * pairs + k - 1)
                    for c0, cn, scale, shift, *to in segments:
                        d0 = to[0] if to else c0
                        dst = norm_buf[4 + k % 2][:, d0:d0 + cn] if pairs is not None else X[:, k, c0:c0 + cn]
                        ins = act.activation(dst, norm_buf[k % 2][:, c0:c0 + cn], ACT.Identity,
                                             bias=shift(k) if shift else 0.0, scale=scale(k))
                    ins.then_inc(s("h"), 1)
                    if pairs is not None:
                        act.wait_ge(s("h"), KT * ni + k + 1)
                        act.activation(H_hi[:, k, c], norm_buf[4 + k % 2][:, c], ACT.Copy).then_inc(s("h_hi"), 1)

            def mod_norm(name, layer, n_cols):
                m = mod[layer % 2]
                act.wait_ge(s("scales"), layer + 1)
                shift_at = 0 if name.startswith("mix") else 3 * KT
                scales = scale_mix if name.startswith("mix") else scale_mlp
                segs = [(st * LAT, LAT, lambda k, st=st: scales[:, k, st:st + 1],
                         lambda k, st=st: m[:, shift_at + k, st:st + 1]) for st in range(n_cols // LAT)]
                norm(name, n_cols, segs, SPLIT_AT[name])

            def fourier(name, streams):
                t = PLAN.at[name]["tile"]
                n_tok = 2 * streams
                for g in range(4):
                    for tt in range(n_tok):
                        act.wait_ge(s("tile_done"), t + 1)
                        act.activation(G_hi[:, 4 * (g % 2) + tt, 0:256], bank[t % BANKS][:, 0:256], ACT.Copy)
                        act.activation(G_hi[:, 4 * (g % 2) + tt, 256:512], bank[t % BANKS][:, 256:512],
                                       ACT.Copy, scale=-1.0).then_inc(s("four_hi"), 1)
                        t += 1
                    for m in range(2):
                        act.wait_ge(s("tile_done"), t + 1)
                        act.activation(H_hi[:, 2 * g + m, 0:streams * LAT], bank[t % BANKS][:, 0:streams * LAT],
                                       ACT.Copy).then_inc(s("four_hi"), 1)
                        t += 1

            def mlp(layer, n_cols):
                at0 = PLAN.at[f"mlp{layer}"]
                p0, t0 = at0["panel"], at0["tile"]
                h0 = KT * BLOCKS * layer
                def hidden_block(b):
                    for j in range(MLP_TILES):
                        split_hi(p0 + j + AHEAD, b, MLP_TILES, 2 * 16)
                        if j < KT:
                            act.wait_ge(s("tile_done"), later(t0 + j + 1, b, MLP_TILES))
                            if layer or j >= 2:
                                act.wait_ge(s("g_sq"), later(h0 + j - 1, b, KT))
                            act.activation(relu[j % 2][:, 0:n_cols], bank[(t0 + j) % BANKS][:, 0:n_cols],
                                           ACT.Relu).then_inc(s("relu"), 1)
                            act.wait_ge(s("relu"), later(h0 + j + 1, b, KT))
                            act.activation(G_hi[:, j, 0:n_cols], relu[j % 2][:, 0:n_cols],
                                           ACT.Square).then_inc(s("g_hi"), 1)

                with act.Fori(0, BLOCKS - 1) as b:
                    hidden_block(b)
                hidden_block(BLOCKS - 1)

            act.wait_ge(s("tile_done"), 1)
            for v in range(VEC_TILES):
                ins = act.activation(vec[:, v, 0:VEC_COUNT[v]], bank[0][:, v * P:v * P + VEC_COUNT[v]], ACT.Copy)
            ins.then_inc(s("vec"), 1)
            act.wait_ge(s("vec"), 1)
            act.activation(silu_t[:, :, :], vcols("c", 0, 16).rearrange("p (s k) -> p s k", s=2),
                           ACT.Exp, scale=-1.0).then_inc(s("silu_exp"), 1)
            act.wait_ge(s("lam"), 2)
            act.activation(lam_row[:, 2:4], lam_row[:, 0:2], ACT.Exp).then_inc(s("lam_exp"), 1)
            t0 = PLAN.at["xin"]["tile"]
            for k in range(KT):
                act.wait_ge(s("tile_done"), t0 + k + 1)
                act.activation(X[:, k, :], bank[(t0 + k) % BANKS][:, :], ACT.Copy).then_inc(s("x_cols"), 1)
            act.wait_ge(s("dft_in"), 16)
            act.activation(dft_hi[:, :, :], dft[:, :, :], ACT.Copy).then_inc(s("dft_hi"), 1)
            p0 = PLAN.at["four0"]["panel"]
            for n in range(AHEAD):
                split_hi(p0 + n)
            act.wait_ge(s("x_cols"), KT)
            act.wait_ge(s("scales"), 1)
            mod_norm("mix0", 0, TOK)
            fourier("four0", 2)
            for m in range(KT):
                split_hi(p0 + m + AHEAD)
            act.wait_ge(s("x_done"), X_AT["mlp0"])
            mod_norm("mlp0", 0, TOK)
            mlp(0, TOK)
            def exps(h):
                def scaled(qt):
                    n = TOK if qt < 2 else CTX
                    act.wait_ge(s("z_mix"), 4 * h + qt + 1)
                    act.activation(p_raw[qt % 2][1][:, 0:n], p_raw[qt % 2][1][:, 0:n], ACT.Identity,
                                   scale=z_mix[:, 2 * qt + 1:2 * qt + 2]).then_inc(s("p_scaled"), 1)

                for qt in range(4):
                    n = TOK if qt < 2 else CTX
                    for j in range(2):
                        i = 2 * qt + j
                        act.wait_ge(s("neg_max"), 8 * h + i + 1)
                        if 4 * h + qt >= 2:
                            act.wait_ge(s("p_mix"), 4 * h + qt - 1)
                        x = PLAN.at["diff"]["aux"] + AUX_AT["diff", "score", h, i]
                        act.activation(p_raw[qt % 2][j][:, 0:n], aux[x % AUX][:, 0:n], ACT.Exp,
                                       bias=neg_max[:, i:i + 1], accum_out=z[:, i:i + 1]).then_inc(s("p_exp"), 1)
                    if qt:
                        scaled(qt - 1)
                scaled(3)

            def diff_attention():
                t0, p0, x0 = PLAN.at["diff"]["tile"], PLAN.at["diff"]["panel"], PLAN.at["diff"]["aux"]
                for turn in range(HEADS + 1):
                    h = turn - 1
                    if h >= 0:
                        exps(h)
                    if turn < HEADS:
                        for j, (dst, scale) in enumerate(((q_f, HALF ** -0.5), (k_f, 1.0))):
                            t = t0 + 3 * turn + j
                            split_hi(p0 + 3 * turn + j + AHEAD)
                            act.wait_ge(s("tile_done"), t + 1)
                            if turn:
                                act.wait_ge(s("qk_lo"), 2 * turn - 1 + j)
                            act.activation(dst[:, :], bank[t % BANKS][:, :], ACT.Copy, scale=scale).then_inc(s("qkv"), 1)
                        for j, (dst, src) in enumerate(((q_hi, q_f), (k_hi, k_f))):
                            act.wait_ge(s("roped"), 2 * turn + j + 1)
                            act.activation(dst[:, :], src[:, :], ACT.Copy).then_inc(s("qk_hi"), 1)
                    if h >= 0:
                        for i in range(3):
                            x = x0 + AUX_AT["diff", "turn_p", h, i]
                            act.wait_ge(s("aux_done"), x + 1)
                            act.activation(pt_hi[:, 2 * i:2 * i + 2, :].rearrange("p a b -> p (a b)"), aux[x % AUX][:, :],
                                           ACT.Copy).then_inc(s("pt_hi"), 1)
                    if turn < HEADS:
                        t = t0 + 3 * turn + 2
                        split_hi(p0 + 3 * turn + 2 + AHEAD)
                        act.wait_ge(s("tile_done"), t + 1)
                        act.wait_ge(s("qk_lo"), 2 * turn + 1)
                        act.activation(v_f[:, :], bank[t % BANKS][:, :], ACT.Copy).then_inc(s("qkv"), 1)
                    if h >= 0:
                        x = x0 + AUX_AT["diff", "pv", h, 0]
                        act.wait_ge(s("aux_done"), x + 1)
                        act.activation(o_f[:, :], aux[x % AUX][:, :], ACT.Copy).then_inc(s("o_out"), 1)
                        act.wait_ge(s("o_out"), h + 1)
                        act.activation(o_sq[:, :], o_f[:, :], ACT.Square).then_inc(s("o_sq"), 1)
                    if turn < HEADS:
                        x = x0 + AUX_AT["diff", "turn_v", turn, 0]
                        act.wait_ge(s("aux_done"), x + 1)
                        act.activation(v_hi[:, :, :].rearrange("p a b -> p (a b)"), aux[x % AUX][:, :],
                                       ACT.Copy).then_inc(s("v_hi"), 1)
                    if h >= 0:
                        x = x0 + AUX_AT["diff", "square", h, 0]
                        act.wait_ge(s("aux_done"), x + 1)
                        act.activation(o_inv[:, :], aux[x % AUX][:, :], ACT.Sqrt, bias=eps[:, 0:1],
                                       scale=1.0 / P).then_inc(s("o_root"), 1)
                        act.wait_ge(s("o_t"), h + 1)
                        act.activation(o_g[:, :], o_t[:, :], ACT.Identity,
                                       scale=subln[:, 0:1]).then_inc(s("o_g"), 1)
                        act.wait_ge(s("o_g"), h + 1)
                        act.activation(G_hi[:, h, :], o_g[:, :], ACT.Copy).then_inc(s("o_hi"), 1)

            mod_norm("mix1", 1, TOK)
            diff_attention()
            for m in range(KT):
                split_hi(PLAN.at["diffo"]["panel"] + m + AHEAD)
            act.wait_ge(s("x_done"), X_AT["mlp1"])
            mod_norm("mlp1", 1, TOK)
            mlp(1, TOK)
            def down_outputs():
                t0, p0 = PLAN.at["mlad"]["tile"], PLAN.at["mlad"]["panel"]
                rotary = slice(HALF, HALF + ROPE)
                outs = [cq_f[:, 0, :], cq_f[:, 1, :], ckv_f[:, :], kv_f[rotary, :]]
                for j, dst in enumerate(outs):
                    split_hi(p0 + j + AHEAD)
                    b = bank[(t0 + j) % BANKS]
                    act.wait_ge(s("tile_done"), t0 + j + 1)
                    src = b[:, 0:LAT] if j < 2 else b[:, :] if j == 2 else b[rotary, :]
                    act.activation(dst, src, ACT.Copy).then_inc(s("down_out"), 1)
                act.wait_ge(s("down_out"), 3)
                act.activation(norm_buf[0][:, :], cq_f[:, :, :].rearrange("p a b -> p (a b)"), ACT.Square).then_inc(s("down_sq"), 1)
                act.activation(norm_buf[1][:, :], ckv_f[:, :], ACT.Square).then_inc(s("down_sq"), 1)
                act.wait_ge(s("down_sum"), 1)
                act.activation(norm_buf[2][:, 0:LAT], pv_ps[:, 0:LAT], ACT.Sqrt, bias=eps[:, 0:1],
                               scale=1.0 / Q_RANK).then_inc(s("down_root"), 1)
                act.wait_ge(s("down_sum"), 2)
                act.activation(norm_buf[3][:, :], sum_ps[:, :], ACT.Sqrt, bias=eps[:, 0:1],
                               scale=1.0 / KV_RANK).then_inc(s("down_root"), 1)
                act.wait_ge(s("rope32_done"), 1)
                act.activation(mk_hi[rotary, :], kv_f[rotary, :], ACT.Copy).then_inc(s("key_hi"), 1)
                act.wait_ge(s("down_t"), 1)
                for k in range(2):
                    ins = act.activation(cq_f[:, k, :], norm_buf[4][:, k * LAT:(k + 1) * LAT], ACT.Identity,
                                         scale=vcol("mla_q_norm_g", k))
                ins.then_inc(s("down_g"), 1)
                act.wait_ge(s("down_g"), 1)
                act.activation(cq_hi[:, :, :], cq_f[:, :, :], ACT.Copy).then_inc(s("down_hi"), 1)
                act.wait_ge(s("down_t"), 2)
                act.activation(ckv_f[:, :], norm_buf[5][:, :], ACT.Identity,
                               scale=vcol("mla_kv_norm_g")).then_inc(s("down_g"), 1)
                act.wait_ge(s("down_g"), 2)
                act.activation(ckv_hi[:, :], ckv_f[:, :], ACT.Copy).then_inc(s("down_hi"), 1)

            def mla_attention():
                t0, p0, x0 = PLAN.at["mla"]["tile"], PLAN.at["mla"]["panel"], PLAN.at["mla"]["aux"]
                split_after = {0: [3], 3: [4], 7: [5, 6], 11: [], 15: [7]}
                for turn in range(MLA_HEADS + 1):
                    h = turn - 1
                    if h >= 0:
                        for i in range(2):
                            x = x0 + AUX_AT["mla", "score", h, i]
                            act.wait_ge(s("mla_max"), 2 * h + i + 1)
                            if h:
                                act.wait_ge(s("mla_mix"), 2 * h + i - 1)
                            act.activation(mp_raw[i][:, :], aux[x % AUX][:, :], ACT.Exp, bias=m_max[:, i:i + 1],
                                           accum_out=m_z[:, i:i + 1]).then_inc(s("mla_exp"), 1)
                    if turn < MLA_HEADS:
                        t = t0 + 2 * turn
                        act.wait_ge(s("tile_done"), t + 1)
                        if turn:
                            act.wait_ge(s("mla_q_lo"), turn)
                        act.activation(mq_f[0:QD, :], bank[t % BANKS][0:QD, 0:LAT], ACT.Copy,
                                       scale=QD ** -0.5).then_inc(s("mla_qkv"), 1)
                        act.wait_ge(s("tile_done"), t + 2)
                        act.wait_ge(s("mla_k_lo"), turn + 1)
                        act.activation(kv_f[:, :], bank[(t + 1) % BANKS][:, :], ACT.Copy).then_inc(s("mla_qkv"), 1)
                        act.wait_ge(s("rope32_done"), turn + 2)
                        act.activation(mq_hi[0:QD, :], mq_f[0:QD, :], ACT.Copy).then_inc(s("mla_q_hi"), 1)
                        act.wait_ge(s("mla_qkv"), 2 * turn + 2)
                        act.activation(mk_hi[0:NOPE, :], kv_f[0:NOPE, :], ACT.Copy).then_inc(s("mla_k_hi"), 1)
                        for n in split_after.get(turn, []):
                            split_hi(p0 + n)
                        x = x0 + AUX_AT["mla", "turn_v", turn, 0]
                        j = turn % 2
                        act.wait_ge(s("aux_done"), x + 1)
                        act.activation(mv_hi[j][:, :, j * HALF:(j + 1) * HALF],
                                       aux[x % AUX][:, :].rearrange("p (t c) -> p t c", c=P)[:, :, HALF:P],
                                       ACT.Copy).then_inc(s("mla_v_hi"), 1)
                    if h >= 0:
                        for i in range(2):
                            x = x0 + AUX_AT["mla", "turn_p", h, i]
                            act.wait_ge(s("aux_done"), x + 1)
                            act.activation(mpt_hi[:, 2 * i:2 * i + 2, :].rearrange("p a b -> p (a b)"), aux[x % AUX][:, :],
                                           ACT.Copy).then_inc(s("mla_pt_hi"), 1)
                        if h % 2:
                            m = h // 2
                            act.wait_ge(s("pv_done"), m + 1)
                            act.activation(G_hi[:, m, 0:LAT], pv_ps[:, (m % 2) * LAT:(m % 2 + 1) * LAT],
                                           ACT.Copy).then_inc(s("mla_o_hi"), 1)
                split_hi(p0 + 8)

            mod_norm("mix2", 2, TOK)
            down_outputs()
            mla_attention()
            for m in range(KT):
                split_hi(PLAN.at["mlao"]["panel"] + m + AHEAD)
            act.wait_ge(s("x_done"), X_AT["mlp2"])
            mod_norm("mlp2", 2, LAT)
            mlp(2, LAT)
            act.wait_ge(s("dft_in"), 32)
            act.activation(dft_hi[:, :, :], dft[:, :, :], ACT.Copy).then_inc(s("dft_hi"), 1)
            mod_norm("mix3", 3, LAT)
            fourier("four3", 1)
            for m in range(KT):
                split_hi(PLAN.at["four3"]["panel"] + m + AHEAD)
            act.wait_ge(s("x_done"), X_AT["mlp3"])
            mod_norm("mlp3", 3, LAT)
            mlp(3, LAT)
            act.wait_ge(s("x_done"), X_AT["wout"])
            norm("final", LAT, [(0, LAT, lambda k: vcol("final_g", k), None)], None)
            act.wait_ge(s("tile_done"), PLAN.at["meta"]["tile"] + 1)
            b = bank[PLAN.at["meta"]["tile"] % BANKS]
            act.activation(X[:, :, LAT:TOK2], b[:, 0:KT * META].rearrange("p (k t) -> p k t", t=META),
                           ACT.Copy).then_inc(s("meta_cols"), 1)
            act.wait_ge(s("meta_cols"), 1)
            w = lambda k: vcol("norm_mix_w_2", k)
            norm("mix_2", TOK2, [(0, LAT, w, None, META), (LAT, META, w, None, 0)], SPLIT_AT["mix_2"])

            def projections():
                t0, p0 = PLAN.at["win"]["tile"], PLAN.at["win"]["panel"]
                for i, col in enumerate(WIN_ORDER):
                    split_hi(p0 + i + AHEAD)
                    act.wait_ge(s("tile_done"), t0 + i + 1)
                    rows = slice(0, GATE_RANK if col == GATE_AT else P)
                    act.activation(proj[rows, col, :], bank[(t0 + i) % BANKS][rows, 0:TOK2], ACT.Copy).then_inc(s("proj"), 1)
                    if i == 3:
                        gates()
                    if i == 10:
                        turned_values()
                    if i == 14:
                        turned_keys()

            def mix_tile(what, i):
                n = MIX_AT[what, i]
                act.wait_ge(s("mix_done_ps"), n + 1)
                return mix_ps[n % 4]

            def gates():
                for j in range(2):
                    ps = mix_tile("gate", j)
                    act.activation(z_f[:, j, :], ps[:, 0:TOK2], ACT.Identity, bias=vcol("b_gate_2", j)).then_inc(s("z_in"), 1)
                act.wait_ge(s("z_in"), 2)
                act.activation(z_abs[:, :, :], z_f[:, :, :], ACT.Abs).then_inc(s("z_step"), 1)
                act.wait_ge(s("z_step"), 1)
                act.activation(z_abs[:, :, :], z_abs[:, :, :], ACT.Exp, scale=-1.0).then_inc(s("z_step"), 1)
                act.wait_ge(s("z_step"), 2)
                act.activation(z_abs[:, :, :], z_abs[:, :, :], ACT.Ln, bias=1.0).then_inc(s("z_ln"), 1)
                act.wait_ge(s("b_last"), 1)
                act.activation(e_pos[:, :, :], b_cum[:, :, :], ACT.Exp, scale=1.0 / 16).then_inc(s("e_pos"), 1)
                act.activation(e_neg[:, :, :], b_cum[:, :, META:], ACT.Exp, scale=-1.0 / 16).then_inc(s("e_neg"), 1)
                for j in range(2):
                    for n in range(4):
                        c0, cn = CHUNKS[n]
                        act.activation(e_end[:, j, c0:c0 + cn], b_cum[:, j, c0:c0 + cn], ACT.Exp,
                                       bias=b_last[:, j, n:n + 1], scale=-1.0 / 16)
                act.activation(decay[:, :, :], b_last[:, :, :], ACT.Exp).then_inc(s("e_end"), 1)

            def turned_values():
                for i in range(5):
                    ps = mix_tile("turn_v", i)
                    if i < 4:
                        act.activation(v_rows[:, i, :, :].rearrange("p n c -> p (n c)"), ps[0:CHUNK, :], ACT.Copy).then_inc(s("v_rows"), 1)
                    else:
                        act.activation(v_rows_m[:, :, :].rearrange("p n c -> p (n c)"), ps[0:META, :], ACT.Copy).then_inc(s("v_rows"), 1)

            def turned_keys():
                for j in range(2):
                    ps = mix_tile("turn_k", j)
                    act.activation(k_rows[:, j, :, :].rearrange("p n c -> p (n c)"), ps[0:CHUNK, 0:3 * P], ACT.Copy)
                    act.activation(k_rows_m[:, j, :], ps[0:META, 3 * P:4 * P], ACT.Copy).then_inc(s("k_rows"), 1)

            def mixer_rest():
                act.wait_ge(s("proj"), 17)
                act.activation(r_silu[:, :, :], proj[:, R_AT:R_AT + 4, META:], ACT.Exp, scale=-1.0).then_inc(s("r_exp"), 1)
                for i in range(2):
                    ps = mix_tile("pool", i)
                    for g in range(2):
                        ins = act.activation(y_f[:, 2 * i + g, :], ps[:, g * LAT:(g + 1) * LAT], ACT.Identity,
                                             scale=vcol("pool_scale_2", 2 * i + g))
                    ins.then_inc(s("pool_in"), 1)
                act.wait_ge(s("pool_in"), 2)
                act.activation(Y_hi[:, 0:4, :], y_f[:, :, :], ACT.Copy).then_inc(s("y_hi"), 1)
                for i in range(2):
                    ps = mix_tile("score", i)
                    act.activation(sc[:, 2 * i:2 * i + 2, :, :].rearrange("p h n c -> p (h n c)"), ps[0:CHUNK, :],
                                   ACT.Copy).then_inc(s("sc_in"), 1)
                for i in range(2):
                    ps = mix_tile("out", i)
                    act.activation(go_f[:, 2 * i:2 * i + 2, :], ps[:, :].rearrange("p (h c) -> p h c", h=2), ACT.Copy).then_inc(s("go_in"), 1)
                act.wait_ge(s("go_in"), 2)
                act.activation(go_sq, go_f[:, :, :], ACT.Square).then_inc(s("go_sq"), 1)
                for i in range(2):
                    ps = mix_tile("square", i)
                    act.activation(go_inv[:, 2 * i:2 * i + 2, :], ps[:, :].rearrange("p (h c) -> p h c", h=2), ACT.Sqrt,
                                   bias=eps[:, 0:1], scale=1.0 / P).then_inc(s("go_root"), 1)
                act.wait_ge(s("go_t"), 1)
                act.activation(y_f[:, :, :], go_f[:, :, :], ACT.Identity, scale=vcol("gla_norm_w_2")).then_inc(s("go_g"), 1)
                act.wait_ge(s("go_g"), 1)
                act.activation(Y_hi[:, 4:8, :], y_f[:, :, :], ACT.Copy).then_inc(s("y_hi"), 1)

            projections()
            mixer_rest()
            for m in range(KT):
                split_hi(PLAN.at["wout"]["panel"] + m + AHEAD)
            act.wait_ge(s("x_done"), X_AT["moe"])
            norm("ffn_2", LAT, [(0, LAT, lambda k: vcol("norm_ffn_w_2", k), None)], SPLIT_AT["ffn_2"])

            def router():
                act.wait_ge(s("logit_done"), 1)
                act.activation(logits[:, :, :], psum[2][:, 0:2 * (4 + EXPERTS)].rearrange("p (t c) -> p t c", t=2),
                               ACT.Copy).then_inc(s("logits"), 1)
                for i in range(2):
                    act.wait_ge(s("shifted"), i + 1)
                    act.activation(r4[4 * i + 1][:, :, :], r4[4 * i][:, :, :], ACT.Exp).then_inc(s("route_exp"), 1)

            def gated(x, i=None, step=0):
                done = 6 * x + 2
                act.wait_ge(s("expert_done"), later(done, i, 6 * step))
                if x:
                    act.wait_ge(s("e_hid"), later(x, i, step))
                act.activation(e_exp[:, :, :].rearrange("p m c -> p (m c)"), psum[3 * (x % 2)][:, :], ACT.Exp,
                               scale=-1.0).then_inc(s("e_exp"), 1)
                act.wait_ge(s("e_hid"), later(x + 1, i, step))
                act.activation(E_hi[x % 2][:, :, :], e_hid[x % 2][:, :, :], ACT.Copy).then_inc(s("e_hi"), 1)

            p0 = PLAN.at["moe"]["panel"]

            def expert_split(n, i=None):
                if n < 6 * EXPERTS:
                    step = 6 * EXPERT_TURNS
                    split_hi(p0 + n, i, step, 16 * 3)

            def expert_turn(x, i=None):
                n = 6 * x - 2 if x else 0
                for j in range(4):
                    expert_split(n + j + AHEAD, i)
                gated(x, i, EXPERT_TURNS)
                if x:
                    for j in range(4, 6):
                        expert_split(n + j + AHEAD, i)

            router()
            expert_turn(0)
            with act.Fori(0, 3) as i:
                for j in range(EXPERT_TURNS):
                    expert_turn(1 + j, i)
            for x in range(1 + 3 * EXPERT_TURNS, EXPERTS):
                expert_turn(x)
            act.wait_ge(s("y_added"), 1)
            norm("final_2", LAT, [(0, LAT, lambda k: vcol("final_norm_w_2", k), None)], None)
            for n in range(4):
                act.wait_ge(s("out_turned"), n + 1)
                act.activation(out_rows[:, n // 2, 512 * (n % 2):512 * (n % 2 + 1)], psum[n][:, :], ACT.Copy).then_inc(s("out_rows"), 1)

        @block.tensor
        def _(pe):
            def split_product(dst, w_hi, w_lo, r_hi, r_lo, start, stop):
                pe.matmul(dst, w_hi, r_hi, start=start, stop=False)
                pe.matmul(dst, w_hi, r_lo, start=False, stop=False)
                return pe.matmul(dst, w_lo, r_hi, start=False, stop=stop)

            def wait_bank(t, i=None, step=KT):
                if t >= BANKS:
                    name, value = PLAN.tiles[t - BANKS]
                    pe.wait_ge(s(name), later(value, i, step))

            def panel_product(n, t, r_hi, r_lo, c, i=None, ready=None, rows=P):
                if isinstance(i, int):
                    n, t, i = n + i * MLP_TILES, t + i * MLP_TILES, None
                pe.wait_ge(s("panel_ready"), later(n + 1, i, MLP_TILES))
                wait_bank(t, i)
                dst = bank[t % BANKS][0:rows, 0:c.stop - c.start]
                for k in range(KT):
                    if ready:
                        ready(k)
                    w = slice(k * P, k * P + rows)
                    ins = split_product(dst, W_hi[n % RING][:, w], W_lo[n % RING][:, w], r_hi[:, k, c],
                                        r_lo[:, k, c], k == 0, k == KT - 1)
                ins.then_inc(s("tile_done"), 1)

            def mod_unit(u, n, i=None):
                pe.wait_ge(s(f"mod_in{u % 2}"), later(16 * (n // 2 + 1), i, 16 * MOD_UNITS // 2))
                for j in range(2):
                    for k in range(KT):
                        ins = pe.matmul(mod_ps[:, 2 * (2 * u + j):2 * (2 * u + j) + 2], mod_raw[u % 2][:, k, j, :],
                                        silu_c[:, :, k], start=(k == 0), stop=(k == KT - 1))
                ins.then_inc(s("mod_used"), 1)

            def norm_sum(name, n_cols):
                ni = NORM_AT[name]
                pe.wait_ge(s("sq_added"), KT * ni + KT)
                pe.matmul(sum_ps[:, 0:n_cols], ones[:, :], norm_buf[2][:, 0:n_cols], start=True,
                          stop=True).then_inc(s("sum"), 1)

            def h_ready(name):
                split = SPLIT_AT[name]
                return lambda k: pe.wait_ge(s("h_lo"), KT * split + k + 1)

            def fourier(name, streams, norm_name):
                t = PLAN.at[name]["tile"]
                f0 = 0 if name == "four0" else 24
                n_tok = 2 * streams
                for g in range(4):
                    for tt in range(n_tok):
                        wait_bank(t)
                        if g >= 2:
                            pe.wait_ge(s("tile_done"), t - tt - (n_tok + 2))
                        tok = slice(tt * P, (tt + 1) * P)
                        for k in range(2):
                            h_ready(norm_name)(2 * g + k)
                            ins = split_product(bank[t % BANKS][:, :], H_hi[:, 2 * g + k, tok], H_lo[:, 2 * g + k, tok],
                                                dft_hi[:, k, :], dft_lo[:, k, :], k == 0, k == 1)
                        ins.then_inc(s("tile_done"), 1)
                        t += 1
                    for m in range(2):
                        wait_bank(t)
                        for st in range(streams):
                            for q in range(4):
                                part, k = q // 2, q % 2
                                if m == 0:
                                    pe.wait_ge(s("four_lo"), f0 + (n_tok + 2) * g + 2 * st + k + 1)
                                col = slice(part * 256 + m * P, part * 256 + (m + 1) * P)
                                row = 4 * (g % 2) + 2 * st + k
                                trig = slice(part * 256, part * 256 + 256)
                                ins = split_product(bank[t % BANKS][:, st * LAT:(st + 1) * LAT],
                                                    G_hi[:, row, col], G_lo[:, row, col], dft_hi[:, k, trig],
                                                    dft_lo[:, k, trig], q == 0, q == 3)
                        ins.then_inc(s("tile_done"), 1)
                        t += 1
                for m in range(KT):
                    n = PLAN.at[name]["panel"] + m
                    panel_product(n, t + m, H_hi, H_lo, slice(0, streams * LAT),
                                  ready=lambda k: pe.wait_ge(s("four_lo"), f0 + (n_tok + 2) * (k // 2) + n_tok + k % 2 + 1))

            def mlp(layer, n_cols, with_mod):
                at0 = PLAN.at[f"mlp{layer}"]
                p0, t0 = at0["panel"], at0["tile"]
                h0 = KT * BLOCKS * layer
                ready = h_ready(f"mlp{layer}")

                def hidden_block(b):
                    for j in range(MLP_TILES):
                        if j < KT:
                            panel_product(p0 + j, t0 + j, H_hi, H_lo, slice(0, n_cols), b,
                                          ready if j == 0 else None)
                        else:
                            panel_product(p0 + j, t0 + j, G_hi, G_lo, slice(0, n_cols), b,
                                          (lambda k: pe.wait_ge(s("g_lo"), later(h0 + k + 1, b, KT))) if j == KT else None)
                        if with_mod and j in MOD_AFTER:
                            u = MOD_AFTER[j]
                            if u == 0:
                                pe.wait_ge(s("mod_read"), later(BLOCKS * (layer + 1), b, 1))
                            mod_unit(u, BLOCKS * MOD_UNITS * (layer + 1) + u, b)

                with pe.Fori(0, BLOCKS - 1) as b:
                    hidden_block(b)
                hidden_block(BLOCKS - 1)

            pe.wait_ge(s("const"), 4)
            pe.wait_ge(s("vec_in"), 16 * (len(VEC_ROWS) + 4))
            for v in range(VEC_TILES):
                ins = pe.transpose(bank[0][:, v * P:v * P + VEC_COUNT[v]], vec_rows[0:VEC_COUNT[v], v, :],
                                   ident[0:VEC_COUNT[v], 0:VEC_COUNT[v]])
            ins.then_inc(s("tile_done"), 1)
            pe.wait_ge(s("lam"), 3)
            pe.matmul(bank[1][:, 0:2], ones[0:1, :], lam_row[:, 0:2], start=True, stop=True).then_inc(s("tile_done"), 1)
            pe.wait_ge(s("x_in"), 32)
            t0 = PLAN.at["xin"]["tile"]
            for k in range(KT):
                wait_bank(t0 + k)
                for tt in range(4):
                    ins = pe.transpose(bank[(t0 + k) % BANKS][:, tt * P:(tt + 1) * P],
                                       x_rows[:, tt, k * P:(k + 1) * P], ident[:, :])
                ins.then_inc(s("tile_done"), 1)
            pe.wait_ge(s("silu_c"), 1)
            for u in range(MOD_UNITS):
                mod_unit(u, u)
            with pe.Fori(1, BLOCKS) as b:
                pe.wait_ge(s("mod_read"), b)
                for u in range(MOD_UNITS):
                    mod_unit(u, u, b)
            norm_sum("mix0", TOK)
            pe.wait_ge(s("dft_lo"), 1)
            fourier("four0", 2, "mix0")
            norm_sum("mlp0", TOK)
            mlp(0, TOK, True)
            def take_aux(x):
                if x >= AUX:
                    name, value = PLAN.aux[x - AUX]
                    pe.wait_ge(s(name), value)
                return aux[x % AUX]

            def diff_attention():
                t0, p0, x0 = PLAN.at["diff"]["tile"], PLAN.at["diff"]["panel"], PLAN.at["diff"]["aux"]
                full = slice(0, TOK)
                for turn in range(HEADS + 1):
                    h = turn - 1
                    if h >= 0:
                        pe.wait_ge(s("qk_lo"), 2 * h + 2)
                        for i in range(8):
                            qt, j = i // 2, i % 2
                            dst = take_aux(x0 + AUX_AT["diff", "score", h, i])
                            half = slice(j * HALF, (j + 1) * HALF)
                            keys = full if qt < 2 else slice(LAT, TOK)
                            q = slice(qt * P, (qt + 1) * P)
                            split_product(dst[:, 0:keys.stop - keys.start], q_hi[half, q], q_lo[half, q], k_hi[half, keys],
                                          k_lo[half, keys], True, True).then_inc(s("aux_done"), 1)
                    if turn < HEADS:
                        ready = h_ready("mix1") if turn == 0 else None
                        panel_product(p0 + 3 * turn, t0 + 3 * turn, H_hi, H_lo, full, ready=ready)
                        panel_product(p0 + 3 * turn + 1, t0 + 3 * turn + 1, H_hi, H_lo, full)
                    if h >= 0:
                        pe.wait_ge(s("p_mix"), 4 * h + 4)
                        for i in range(3):
                            dst = take_aux(x0 + AUX_AT["diff", "turn_p", h, i])
                            for j in range(2):
                                for q in range(2):
                                    key = q * TOK + (2 * i + j) * P if i < 2 else 2 * TOK + q * CTX + j * P
                                    ins = pe.transpose(dst[:, j * LAT + q * P:j * LAT + (q + 1) * P],
                                                       p_all[:, key:key + P], ident[:, :])
                            ins.then_inc(s("aux_done"), 1)
                    if turn < HEADS:
                        panel_product(p0 + 3 * turn + 2, t0 + 3 * turn + 2, H_hi, H_lo, full)
                    if h >= 0:
                        dst = take_aux(x0 + AUX_AT["diff", "pv", h, 0])
                        pe.wait_ge(s("v_lo"), h + 1)
                        pe.wait_ge(s("pt_lo"), 3 * h + 3)
                        for kt in range(4):
                            split_product(dst[:, 0:LAT], v_hi[:, kt, :], v_lo[:, kt, :], pt_hi[:, kt, :],
                                          pt_lo[:, kt, :], kt == 0, kt == 3)
                        for kt in range(2):
                            ins = split_product(dst[:, LAT:TOK], v_hi[:, 2 + kt, :], v_lo[:, 2 + kt, :],
                                                pt_hi[:, 4 + kt, :], pt_lo[:, 4 + kt, :], kt == 0, kt == 1)
                        ins.then_inc(s("aux_done"), 1)
                    if turn < HEADS:
                        dst = take_aux(x0 + AUX_AT["diff", "turn_v", turn, 0])
                        pe.wait_ge(s("qkv"), 3 * turn + 3)
                        for tt in range(4):
                            ins = pe.transpose(dst[:, tt * P:(tt + 1) * P], v_f[:, tt * P:(tt + 1) * P], ident[:, :])
                        ins.then_inc(s("aux_done"), 1)
                    if h >= 0:
                        dst = take_aux(x0 + AUX_AT["diff", "square", h, 0])
                        pe.wait_ge(s("o_sq"), h + 1)
                        pe.matmul(dst[:, :], ones[:, :], o_sq[:, :], start=True, stop=True).then_inc(s("aux_done"), 1)

            def output_product(name, signal, first, c):
                for m in range(KT):
                    panel_product(PLAN.at[name]["panel"] + m, PLAN.at[name]["tile"] + m, G_hi, G_lo, c,
                                  ready=(lambda k: pe.wait_ge(s(signal), first + k + 1)) if m == 0 else None)

            norm_sum("mix1", TOK)
            diff_attention()
            output_product("diffo", "o_lo", 0, slice(0, TOK))
            norm_sum("mlp1", TOK)
            mlp(1, TOK, True)
            def down_products():
                t0, p0 = PLAN.at["mlad"]["tile"], PLAN.at["mlad"]["panel"]
                for j in range(4):
                    c = slice(0, LAT if j < 2 else TOK)
                    panel_product(p0 + j, t0 + j, H_hi, H_lo, c, ready=h_ready("mix2") if j == 0 else None,
                                  rows=P if j < 3 else QD)
                pe.wait_ge(s("down_sq"), 1)
                for k in range(2):
                    ins = pe.matmul(pv_ps[:, 0:LAT], ones[:, :], norm_buf[0][:, k * LAT:(k + 1) * LAT], start=(k == 0), stop=(k == 1))
                ins.then_inc(s("down_sum"), 1)
                pe.wait_ge(s("down_sq"), 2)
                pe.matmul(sum_ps[:, :], ones[:, :], norm_buf[1][:, :], start=True, stop=True).then_inc(s("down_sum"), 1)

            def mla_attention():
                t0, p0, x0 = PLAN.at["mla"]["tile"], PLAN.at["mla"]["panel"], PLAN.at["mla"]["aux"]
                pe.wait_ge(s("mv_zero"), 1)
                for turn in range(MLA_HEADS + 1):
                    h = turn - 1
                    if h >= 0:
                        pe.wait_ge(s("mla_q_lo"), h + 1)
                        pe.wait_ge(s("mla_k_lo"), h + 2)
                        for i in range(2):
                            dst = take_aux(x0 + AUX_AT["mla", "score", h, i])
                            q = slice(i * P, (i + 1) * P)
                            split_product(dst[:, :], mq_hi[0:QD, q], mq_lo[0:QD, q], mk_hi[0:QD, :], mk_lo[0:QD, :],
                                          True, True).then_inc(s("aux_done"), 1)
                    if turn < MLA_HEADS:
                        t = t0 + 2 * turn
                        n = p0 + [0, 1, 4, 5][turn // 4]
                        pe.wait_ge(s("panel_ready"), n + 1)
                        pe.wait_ge(s("down_lo"), 1)
                        wait_bank(t)
                        for k in range(2):
                            w = slice((4 * k + turn % 4) * P, (4 * k + turn % 4) * P + QD)
                            ins = split_product(bank[t % BANKS][0:QD, 0:LAT], W_hi[n % RING][:, w], W_lo[n % RING][:, w],
                                                cq_hi[:, k, :], cq_lo[:, k, :], k == 0, k == 1)
                        ins.then_inc(s("tile_done"), 1)
                        n = p0 + 2 + turn // 8
                        pe.wait_ge(s("panel_ready"), n + 1)
                        pe.wait_ge(s("down_lo"), 2)
                        wait_bank(t + 1)
                        w = slice(turn % 8 * P, (turn % 8 + 1) * P)
                        split_product(bank[(t + 1) % BANKS][:, :], W_hi[n % RING][:, w], W_lo[n % RING][:, w], ckv_hi[:, :],
                                      ckv_lo[:, :], True, True).then_inc(s("tile_done"), 1)
                        dst = take_aux(x0 + AUX_AT["mla", "turn_v", turn, 0])
                        pe.wait_ge(s("mla_qkv"), 2 * turn + 2)
                        for tt in range(4):
                            ins = pe.transpose(dst[:, tt * P:(tt + 1) * P], kv_f[:, tt * P:(tt + 1) * P], ident[:, :])
                        ins.then_inc(s("aux_done"), 1)
                    if h >= 0:
                        pe.wait_ge(s("mla_mix"), 2 * h + 2)
                        for i in range(2):
                            dst = take_aux(x0 + AUX_AT["mla", "turn_p", h, i])
                            for j in range(2):
                                for q in range(2):
                                    ins = pe.transpose(dst[:, j * LAT + q * P:j * LAT + (q + 1) * P],
                                                       mp_all[:, q, (2 * i + j) * P:(2 * i + j + 1) * P], ident[:, :])
                            ins.then_inc(s("aux_done"), 1)
                        m, j = h // 2, h % 2
                        if j == 0 and m >= 2:
                            pe.wait_ge(s("mla_o_lo"), m - 1)
                        pe.wait_ge(s("mla_v_lo"), h + 1)
                        pe.wait_ge(s("mla_pt_lo"), 2 * h + 2)
                        for kt in range(4):
                            ins = split_product(pv_ps[:, (m % 2) * LAT:(m % 2 + 1) * LAT], mv_hi[j][:, kt, :], mv_lo[j][:, kt, :],
                                                mpt_hi[:, kt, :], mpt_lo[:, kt, :], j == 0 and kt == 0, j == 1 and kt == 3)
                        if j:
                            ins.then_inc(s("pv_done"), 1)

            norm_sum("mix2", TOK)
            down_products()
            mla_attention()
            output_product("mlao", "mla_o_lo", 0, slice(0, LAT))
            norm_sum("mlp2", LAT)
            mlp(2, LAT, True)
            norm_sum("mix3", LAT)
            pe.wait_ge(s("dft_lo"), 2)
            fourier("four3", 1, "mix3")
            norm_sum("mlp3", LAT)
            mlp(3, LAT, False)
            norm_sum("final", LAT)
            pe.wait_ge(s("small_in"), 16 * 7)
            t = PLAN.at["meta"]["tile"]
            wait_bank(t)
            for k in range(KT):
                ins = pe.transpose(bank[t % BANKS][:, k * META:(k + 1) * META], meta_rows[:, k * P:(k + 1) * P],
                                   ident[0:META, 0:META])
            ins.then_inc(s("tile_done"), 1)
            norm_sum("mix_2", TOK2)

            def mix_tile(what, i):
                n = MIX_AT[what, i]
                if n >= 4:
                    name, value = MIX_TILES[n - 4]
                    pe.wait_ge(s(name), value)
                return mix_ps[n % 4]

            def done(ins):
                ins.then_inc(s("mix_done_ps"), 1)

            def gates():
                pe.wait_ge(s("proj"), 1)
                for j in range(2):
                    ps = mix_tile("gate", j)
                    done(pe.matmul(ps[:, 0:TOK2], gate_up[:, j * P:(j + 1) * P], proj[0:GATE_RANK, GATE_AT, :],
                                   start=True, stop=True))

            def turned_values():
                pe.wait_ge(s("proj"), 9)
                for h in range(GLA_HEADS):
                    ps = mix_tile("turn_v", h)
                    for n in range(4):
                        c0, cn = CHUNKS[n + 1]
                        ins = pe.transpose(ps[0:cn, n * P:(n + 1) * P], proj[:, V_AT + h, c0:c0 + cn], ident[:, :])
                    done(ins)
                ps = mix_tile("turn_v", 4)
                for h in range(GLA_HEADS):
                    ins = pe.transpose(ps[0:META, h * P:(h + 1) * P], proj[:, V_AT + h, 0:META], ident[:, :])
                done(ins)

            def turned_keys():
                pe.wait_ge(s("k_end"), 1)
                for j in range(2):
                    ps = mix_tile("turn_k", j)
                    for n in range(3):
                        c0, cn = CHUNKS[n + 1]
                        pe.transpose(ps[0:cn, n * P:(n + 1) * P], k_end[:, j, c0:c0 + cn], ident[:, :])
                    done(pe.transpose(ps[0:META, 3 * P:4 * P], k_end[:, j, 0:META], ident[:, :]))

            def mixer_rest():
                for i in range(2):
                    ps = mix_tile("pool", i)
                    pe.wait_ge(s("pooled"), 2 * i + 2)
                    for g in range(2):
                        ins = pe.matmul(ps[:, g * LAT:(g + 1) * LAT], pool_w[:, 2 * i + g, :], pooled[:, 2 * i + g, :],
                                        start=True, stop=True)
                    done(ins)
                pe.wait_ge(s("qk_t"), 1)
                for i in range(2):
                    ps = mix_tile("score", i)
                    for j in range(2):
                        for n in range(4):
                            c = slice(n * CHUNK, (n + 1) * CHUNK)
                            ins = pe.matmul(ps[0:CHUNK, j * LAT + n * CHUNK:j * LAT + (n + 1) * CHUNK], k_t[:, i, c],
                                            q_pad[j][:, i, c], start=True, stop=True)
                    done(ins)
                pe.wait_ge(s("v_rows"), 5)
                pe.wait_ge(s("k_rows"), 2)
                for i in range(2):
                    ps = mix_tile("state", i)
                    for n in range(4):
                        for j in range(2):
                            half = slice(j * HALF, (j + 1) * HALF)
                            h = 2 * i + j
                            keys = k_rows_m[:, i, half] if n == 0 else k_rows[:, i, n - 1, half]
                            values = v_rows_m[:, h, :] if n == 0 else v_rows[:, h, n - 1, :]
                            ins = pe.matmul(ps[half, n * P:(n + 1) * P], keys, values, start=True, stop=True)
                    done(ins)
                for i in range(2):
                    ps = mix_tile("out", i)
                    pe.wait_ge(s("sc_masked"), i + 1)
                    pe.wait_ge(s("states"), 4 * i + 4)
                    for j in range(2):
                        h = 2 * i + j
                        for n in range(4):
                            dst = ps[:, j * LAT + n * CHUNK:j * LAT + (n + 1) * CHUNK]
                            pe.matmul(dst, v_rows[:, h, n, :], sc[:, h, n, :], start=True, stop=False)
                            ins = pe.matmul(dst, S_all[:, i, n, :], q_pad[j][:, i, n * CHUNK:(n + 1) * CHUNK],
                                            start=False, stop=True)
                    done(ins)
                pe.wait_ge(s("go_sq"), 1)
                for i in range(2):
                    ps = mix_tile("square", i)
                    for j in range(2):
                        ins = pe.matmul(ps[:, j * LAT:(j + 1) * LAT], ones[:, :], go_sq[:, 2 * i + j, :], start=True, stop=True)
                    done(ins)

            for i in range(len(WIN_ORDER)):
                panel_product(PLAN.at["win"]["panel"] + i, PLAN.at["win"]["tile"] + i, H_hi, H_lo, slice(0, TOK2),
                              ready=h_ready("mix_2") if i == 0 else None)
                if i == 2:
                    gates()
                if i == 10:
                    turned_values()
                if i == 14:
                    turned_keys()
            mixer_rest()
            for m in range(KT):
                panel_product(PLAN.at["wout"]["panel"] + m, PLAN.at["wout"]["tile"] + m, Y_hi, Y_lo, slice(0, LAT),
                              ready=(lambda k: pe.wait_ge(s("y_lo"), 1 + k // 4)) if m == 0 else None)
            norm_sum("ffn_2", LAT)
            pe.wait_ge(s("h_lo"), KT * SPLIT_AT["ffn_2"] + KT)
            pe.wait_ge(s("x_done"), X_AT["moe"])
            for tt in range(2):
                dst = psum[2][:, tt * (4 + EXPERTS):(tt + 1) * (4 + EXPERTS)]
                pe.matmul(dst, ones[0:1, :], route_b[:, :], start=True, stop=False)
                for k in range(KT):
                    tok = slice(tt * P, (tt + 1) * P)
                    pe.matmul(dst, H_hi[:, k, tok].bitcast(F32), route_w[:, k, :], start=False, stop=False)
                    ins = pe.matmul(dst, H_lo[:, k, tok].bitcast(F32), route_w[:, k, :], start=False, stop=(k == KT - 1))
            ins.then_inc(s("logit_done"), 1)
            p0 = PLAN.at["moe"]["panel"]

            def expert_panel(n, i):
                pe.wait_ge(s("panel_ready"), later(p0 + n + 1, i, 6 * EXPERT_TURNS))
                r = (p0 + n) % RING
                return W_hi[r], W_lo[r]

            def expert_in(x, n, what, i=None):
                if what == 0 and x >= 2:
                    pe.wait_ge(s("e_hid"), later(x - 1, i, EXPERT_TURNS))
                if what == 1 and x >= 1:
                    pe.wait_ge(s("e_hid"), later(x, i, EXPERT_TURNS))
                ps = psum[3 * (x % 2)] if what == 0 else psum[1]
                for j in range(2):
                    hi, lo = expert_panel(n + j, i)
                    for k in range(KT):
                        w = slice(k * P, (k + 1) * P)
                        ins = split_product(ps[:, j * LAT:(j + 1) * LAT], hi[:, w], lo[:, w], H_hi[:, k, 0:LAT],
                                            H_lo[:, k, 0:LAT], k == 0, k == KT - 1)
                    ins.then_inc(s("expert_done"), 1)

            def weight_row(x, i=None):
                pe.wait_ge(s("diag"), later(x + 1, i, EXPERT_TURNS))
                if x:
                    pe.wait_ge(s("e_hid"), later(x, i, EXPERT_TURNS))
                else:
                    pe.wait_ge(s("logits"), 1)
                for tt in range(2):
                    ins = pe.matmul(psum[2][:, tt * P:(tt + 1) * P], ones[:, :], diag[x % 2][:, tt, :], start=True, stop=True)
                ins.then_inc(s("weight_row"), 1)

            def expert_out(x, n, i=None):
                pe.wait_ge(s("e_lo"), later(x + 1, i, EXPERT_TURNS))
                for j in range(2):
                    hi, lo = expert_panel(n + j, i)
                    for a4 in range(4):
                        m = 2 * a4 + j
                        dst = psum[4 + m // 2][:, (m % 2) * LAT:(m % 2 + 1) * LAT]
                        for k in range(2):
                            w = slice((4 * k + a4) * P, (4 * k + a4 + 1) * P)
                            last = x == EXPERTS - 1 and k == 1
                            for q, (wp, rp) in enumerate(((hi, E_hi), (hi, E_lo), (lo, E_hi))):
                                ins = pe.matmul(dst, wp[:, w], rp[x % 2][:, k, :], start=False,
                                                stop=last and q == 2, skip_group_check=True)
                    ins.then_inc(s("expert_done"), 1)

            def expert_turn(x, i=None):
                n = 6 * x - 2 if x else 0
                expert_in(x, n, 0, i)
                expert_in(x, n + 2, 1, i)
                weight_row(x, i)
                if x:
                    expert_out(x - 1, n + 4, i)

            pe.wait_ge(s("zero_row"), 1)
            pe.wait_ge(s("x_done"), X_AT["moe"])
            for b in range(4):
                pe.matmul(psum[4 + b][:, :], ones[0:1, :], zero_row[:, :], start=True, stop=False, skip_group_check=True)
            expert_turn(0)
            with pe.Fori(0, 3) as i:
                for j in range(EXPERT_TURNS):
                    expert_turn(1 + j, i)
            for x in range(1 + 3 * EXPERT_TURNS, EXPERTS):
                expert_turn(x)
            expert_out(EXPERTS - 1, 6 * EXPERTS - 2)
            norm_sum("final_2", LAT)
            for tt in range(2):
                for half in range(2):
                    n = 2 * tt + half
                    for k in range(4):
                        pe.wait_ge(s("h"), KT * NORM_AT["final_2"] + 4 * half + k + 1)
                        ins = pe.transpose(psum[n][:, k * P:(k + 1) * P], X[:, 4 * half + k, tt * P:(tt + 1) * P], ident[:, :])
                    ins.then_inc(s("out_turned"), 1)

        @block.vector
        def _(dve):
            def split_lo(n):
                unit, place, _ = PLAN.panels[n]
                slot = PLAN.units[unit][1]
                dve.tensor_tensor(W_lo[n % RING][:, :].rearrange("p (k c) -> p k c", c=P), w_raw[slot][:, :, place, :],
                                  W_hi[n % RING][:, :].bitcast(F32).rearrange("p (k c) -> p k c", c=P),
                                  ALU.subtract).then_inc(s("panel_ready"), 1)

            def split_lo_at(n, i=None):
                if isinstance(i, int):
                    n, i = n + i * MLP_TILES, None
                dve.wait_ge(s("w_hi"), later(n + 1, i, MLP_TILES))
                split_lo(n)

            def norm(name, n_cols, pairs):
                ni = NORM_AT[name]
                c = slice(0, n_cols)
                for k in range(KT):
                    dve.wait_ge(s("sq"), KT * ni + k + 1)
                    if k == 0:
                        dve.tensor_copy(norm_buf[2][:, c], norm_buf[0][:, c]).then_inc(s("sq_added"), 1)
                    else:
                        dve.wait_ge(s("sq_added"), KT * ni + k)
                        dve.tensor_tensor(norm_buf[2][:, c], norm_buf[2][:, c], norm_buf[k % 2][:, c],
                                          ALU.add).then_inc(s("sq_added"), 1)
                dve.wait_ge(s("root"), ni + 1)
                dve.reciprocal(norm_buf[3][:, c], norm_buf[3][:, c]).then_inc(s("rstd"), 1)
                dve.wait_ge(s("rstd"), ni + 1)

                def lo(k):
                    dve.wait_ge(s("h_hi"), KT * pairs + k + 1)
                    dve.tensor_tensor(H_lo[:, k, c], norm_buf[4 + k % 2][:, c], H_hi[:, k, c].bitcast(F32),
                                      ALU.subtract).then_inc(s("h_lo"), 1)

                for k in range(KT):
                    if k >= 2:
                        dve.wait_ge(s("h"), KT * ni + k - 1)
                    dve.tensor_tensor(norm_buf[k % 2][:, c], X[:, k, c], norm_buf[3][:, c], ALU.mult).then_inc(s("t"), 1)
                    if pairs is not None and k >= 1:
                        lo(k - 1)
                if pairs is not None:
                    lo(KT - 1)

            def mod_read(i, n, layer):
                dve.wait_ge(s("mod_used"), later(MOD_UNITS * (n + 1), i, MOD_UNITS))
                m = mod[layer % 2][:, :, :].rearrange("p t s -> p (t s)")
                cols = bass.ds(i * (4 * MOD_UNITS), 4 * MOD_UNITS)
                dve.tensor_copy(m[:, cols], mod_ps[:, 0:4 * MOD_UNITS]).then_inc(s("mod_read"), 1)

            def mod_finish(layer):
                m = mod[layer % 2]
                half, row = ("mod_b_lo", 48 * layer) if layer < 2 else ("mod_b_hi", 48 * (layer - 2))
                dve.wait_ge(s("mod_read"), BLOCKS * (layer + 1))
                bias = vcols(half, row, MOD_TILES).rearrange("p (m o) -> p m o", o=1).to_broadcast([P, MOD_TILES, 2])
                dve.tensor_tensor(m[:, :, :], m[:, :, :], bias, ALU.add).then_inc(s("mod_sum"), 1)
                dve.wait_ge(s("mod_sum"), layer + 1)
                for name, scales, first in (("norm_mix_g", scale_mix, KT), ("norm_mlp_g", scale_mlp, 4 * KT)):
                    g = vcols(name, KT * layer, KT).rearrange("p (m o) -> p m o", o=1).to_broadcast([P, KT, 2])
                    ins = dve.scalar_tensor_tensor(scales[:, :, :], m[:, first:first + KT, :], 1.0, g,
                                                   ALU.add, ALU.mult)
                ins.then_inc(s("scales"), 1)

            def add_gated(m, t, xn, layer, gate_at, streams, i=None, step=0):
                dve.wait_ge(s("tile_done"), later(t + 1, i, MLP_TILES))
                if xn:
                    dve.wait_ge(s("x_done"), later(xn, i, step))
                for st in range(streams):
                    c = slice(st * LAT, (st + 1) * LAT)
                    ins = dve.scalar_tensor_tensor(X[:, m, c], bank[t % BANKS][:, c],
                                                   mod[layer % 2][:, gate_at + m, st:st + 1], X[:, m, c],
                                                   ALU.mult, ALU.add)
                ins.then_inc(s("x_done"), 1)

            def fourier(name, layer, streams):
                t = PLAN.at[name]["tile"]
                p0 = PLAN.at[name]["panel"]
                f0 = 0 if name == "four0" else 24
                n_tok = 2 * streams
                for g in range(4):
                    for tt in range(n_tok):
                        row = 4 * (g % 2) + tt
                        dve.wait_ge(s("four_hi"), f0 + t - PLAN.at[name]["tile"] + 1)
                        dve.tensor_tensor(G_lo[:, row, 0:256], bank[t % BANKS][:, 0:256],
                                          G_hi[:, row, 0:256].bitcast(F32), ALU.subtract)
                        dve.scalar_tensor_tensor(G_lo[:, row, 256:512], bank[t % BANKS][:, 256:512], -1.0,
                                                 G_hi[:, row, 256:512].bitcast(F32), ALU.mult,
                                                 ALU.subtract).then_inc(s("four_lo"), 1)
                        t += 1
                    for m in range(2):
                        c = slice(0, streams * LAT)
                        dve.wait_ge(s("four_hi"), f0 + t - PLAN.at[name]["tile"] + 1)
                        dve.tensor_tensor(H_lo[:, 2 * g + m, c], bank[t % BANKS][:, c],
                                          H_hi[:, 2 * g + m, c].bitcast(F32), ALU.subtract).then_inc(s("four_lo"), 1)
                        t += 1
                bias = vcols("fourier_b", KT * (layer // 3), KT).rearrange("p (m o) -> p m o", o=1).to_broadcast([P, KT, 2])
                dve.tensor_tensor(gated_b[:, :, :], mod[layer % 2][:, 2 * KT:3 * KT, :], bias,
                                  ALU.mult).then_inc(s("gated_b"), 1)
                dve.wait_ge(s("gated_b"), layer // 3 + 1)
                for m in range(KT):
                    for st in range(streams):
                        c = slice(st * LAT, (st + 1) * LAT)
                        ins = dve.tensor_scalar(X[:, m, c], X[:, m, c], gated_b[:, m, st:st + 1], None, ALU.add)
                ins.then_inc(s("x_bias"), 1)
                dve.wait_ge(s("x_bias"), layer // 3 + 1)
                for m in range(KT):
                    split_lo_at(p0 + m + AHEAD)
                    add_gated(m, t + m, 0, layer, 2 * KT, streams)

            def mlp(layer, streams, with_mod):
                at0 = PLAN.at[f"mlp{layer}"]
                p0, t0 = at0["panel"], at0["tile"]
                h0 = KT * BLOCKS * layer
                xn = X_AT[f"mlp{layer}"]
                c = slice(0, streams * LAT)

                def lo(j, b):
                    dve.wait_ge(s("g_hi"), later(h0 + j + 1, b, KT))
                    dve.wait_ge(s("g_sq"), later(h0 + j + 1, b, KT))
                    dve.tensor_tensor(G_lo[:, j, c], square[j % 2][:, c], G_hi[:, j, c].bitcast(F32),
                                      ALU.subtract).then_inc(s("g_lo"), 1)

                def hidden_block(b):
                    for j in range(MLP_TILES):
                        split_lo_at(p0 + j + AHEAD, b)
                        if j < KT:
                            dve.wait_ge(s("relu"), later(h0 + j + 1, b, KT))
                            dve.tensor_tensor(square[j % 2][:, c], relu[j % 2][:, c], relu[j % 2][:, c],
                                              ALU.mult).then_inc(s("g_sq"), 1)
                            lo(j, b)
                        else:
                            add_gated(j - KT, t0 + j, xn + j - KT, layer, 5 * KT, streams, b, KT)
                        if with_mod and j == MLP_TILES - 1:
                            mod_read(b, BLOCKS * (layer + 1), layer + 1)

                with dve.Fori(0, BLOCKS - 1) as b:
                    hidden_block(b)
                hidden_block(BLOCKS - 1)
                if with_mod:
                    mod_finish(layer + 1)

            dve.wait_ge(s("vec_in"), 16 * (len(VEC_ROWS) + 4))
            dve.tensor_tensor(lam_prod[:, :, :], lam_in[:, 0:2, :], lam_in[:, 2:4, :], ALU.mult).then_inc(s("lam"), 1)
            dve.wait_ge(s("lam"), 1)
            dve.tensor_reduce(lam_row[:, 0:2], lam_prod[:, :, :], AX.X, ALU.add).then_inc(s("lam"), 1)
            dve.wait_ge(s("silu_exp"), 1)
            dve.tensor_scalar(silu_t[:, :, :], silu_t[:, :, :], 1.0, None, ALU.add).then_inc(s("silu_add"), 1)
            dve.wait_ge(s("silu_add"), 1)
            dve.reciprocal(silu_t[:, :, :], silu_t[:, :, :]).then_inc(s("silu_add"), 1)
            dve.wait_ge(s("silu_add"), 2)
            dve.tensor_tensor(silu_c[:, :, :], silu_t[:, :, :], vcols("c", 0, 16).rearrange("p (s k) -> p s k", s=2),
                              ALU.mult).then_inc(s("silu_c"), 1)
            dve.wait_ge(s("lam_exp"), 1)
            dve.scalar_tensor_tensor(lam_row[:, 1:2], lam_row[:, 3:4], LAM_INIT, lam_row[:, 2:3], ALU.subtract,
                                     ALU.subtract)
            dve.memset(lam_row[:, 0:1], 1.0).then_inc(s("lam"), 1)
            dve.wait_ge(s("tile_done"), 2)
            dve.tensor_copy(lam_col[:, :], bank[1][:, 0:2]).then_inc(s("lam_col"), 1)
            dve.wait_ge(s("dft_hi"), 1)
            dve.tensor_tensor(dft_lo[:, :, :], dft[:, :, :], dft_hi[:, :, :].bitcast(F32), ALU.subtract).then_inc(s("dft_lo"), 1)
            for n in range(AHEAD):
                split_lo_at(PLAN.at["four0"]["panel"] + n)
            mod_read(0, 0, 0)
            with dve.Fori(1, BLOCKS) as b:
                mod_read(b, 0, 0)
            mod_finish(0)
            norm("mix0", TOK, SPLIT_AT["mix0"])
            fourier("four0", 0, 2)
            norm("mlp0", TOK, SPLIT_AT["mlp0"])
            mlp(0, 2, True)
            def mixes(h):
                def mix(qt):
                    n = TOK if qt < 2 else CTX
                    pair = slice(2 * qt, 2 * qt + 2)
                    dve.wait_ge(s("p_exp"), 8 * h + 2 * qt + 2)
                    dve.reciprocal(z_inv[:, pair], z[:, pair]).then_inc(s("z_inv"), 1)
                    dve.wait_ge(s("z_inv"), 4 * h + qt + 1)
                    dve.tensor_tensor(z_mix[:, pair], z_inv[:, pair], lam_col[:, :], ALU.mult).then_inc(s("z_mix"), 1)
                    dve.wait_ge(s("p_scaled"), 4 * h + qt + 1)
                    first = qt * TOK if qt < 2 else 2 * TOK + (qt - 2) * CTX
                    dve.scalar_tensor_tensor(p_all[:, first:first + n], p_raw[qt % 2][0][:, 0:n],
                                             z_mix[:, 2 * qt:2 * qt + 1], p_raw[qt % 2][1][:, 0:n], ALU.mult,
                                             ALU.add).then_inc(s("p_mix"), 1)

                for qt in range(4):
                    n = TOK if qt < 2 else CTX
                    for j in range(2):
                        x = PLAN.at["diff"]["aux"] + AUX_AT["diff", "score", h, 2 * qt + j]
                        dve.wait_ge(s("aux_done"), x + 1)
                        dve.tensor_reduce(neg_max[:, 2 * qt + j:2 * qt + j + 1], aux[x % AUX][:, 0:n], AX.X, ALU.max,
                                          negate=True).then_inc(s("neg_max"), 1)
                    if qt:
                        mix(qt - 1)
                mix(3)

            swap16 = [i ^ 16 for i in range(32)]

            def diff_attention():
                p0, x0 = PLAN.at["diff"]["panel"], PLAN.at["diff"]["aux"]
                for turn in range(HEADS + 1):
                    h = turn - 1
                    if h >= 0:
                        mixes(h)
                    if turn < HEADS:
                        for j, f in enumerate((q_f, k_f)):
                            split_lo_at(p0 + 3 * turn + j + AHEAD)
                            dve.wait_ge(s("qkv"), 3 * turn + j + 1)
                            r = 2 * turn + j
                            if r:
                                dve.wait_ge(s("roped"), r)
                            dve.stream_shuffle(turned, f[:, 0:LAT], swap16).then_inc(s("rope_step"), 1)
                            dve.tensor_tensor(straight, f[:, 0:LAT], rope[:, 0, :], ALU.mult)
                            dve.wait_ge(s("rope_step"), 2 * r + 1)
                            dve.tensor_tensor(turned, turned, rope[:, 1, :], ALU.mult).then_inc(s("rope_step"), 1)
                            dve.wait_ge(s("rope_step"), 2 * r + 2)
                            dve.tensor_tensor(f[:, 0:LAT], straight, turned, ALU.add).then_inc(s("roped"), 1)
                        for j, (lo, hi, f) in enumerate(((q_lo, q_hi, q_f), (k_lo, k_hi, k_f))):
                            dve.wait_ge(s("qk_hi"), 2 * turn + j + 1)
                            dve.tensor_tensor(lo[:, :], f[:, :], hi[:, :].bitcast(F32), ALU.subtract).then_inc(s("qk_lo"), 1)
                    if h >= 0:
                        for i in range(3):
                            x = x0 + AUX_AT["diff", "turn_p", h, i]
                            dve.wait_ge(s("pt_hi"), 3 * h + i + 1)
                            dve.tensor_tensor(pt_lo[:, 2 * i:2 * i + 2, :].rearrange("p a b -> p (a b)"), aux[x % AUX][:, :],
                                              pt_hi[:, 2 * i:2 * i + 2, :].rearrange("p a b -> p (a b)").bitcast(F32),
                                              ALU.subtract).then_inc(s("pt_lo"), 1)
                    if turn < HEADS:
                        split_lo_at(p0 + 3 * turn + 2 + AHEAD)
                        x = x0 + AUX_AT["diff", "turn_v", turn, 0]
                        dve.wait_ge(s("v_hi"), turn + 1)
                        dve.tensor_tensor(v_lo[:, :, :].rearrange("p a b -> p (a b)"), aux[x % AUX][:, :],
                                          v_hi[:, :, :].rearrange("p a b -> p (a b)").bitcast(F32),
                                          ALU.subtract).then_inc(s("v_lo"), 1)
                    if h >= 0:
                        dve.wait_ge(s("o_root"), h + 1)
                        dve.reciprocal(o_inv[:, :], o_inv[:, :]).then_inc(s("o_inv"), 1)
                        dve.wait_ge(s("o_inv"), h + 1)
                        dve.tensor_tensor(o_t[:, :], o_f[:, :], o_inv[:, :], ALU.mult).then_inc(s("o_t"), 1)
                        dve.wait_ge(s("o_hi"), h + 1)
                        dve.tensor_tensor(G_lo[:, h, :], o_g[:, :], G_hi[:, h, :].bitcast(F32),
                                          ALU.subtract).then_inc(s("o_lo"), 1)

            def output_added(name, layer, streams):
                for m in range(KT):
                    split_lo_at(PLAN.at[name]["panel"] + m + AHEAD)
                    add_gated(m, PLAN.at[name]["tile"] + m, 0, layer, 2 * KT, streams)

            dve.tensor_scalar(subln[:, :], vcol("diff_subln_g"), 1.0 - LAM_INIT, None, ALU.mult).then_inc(s("subln"), 1)
            norm("mix1", TOK, SPLIT_AT["mix1"])
            dve.wait_ge(s("rope_in"), 16)
            diff_attention()
            output_added("diffo", 1, 2)
            norm("mlp1", TOK, SPLIT_AT["mlp1"])
            mlp(1, 2, True)
            def down_outputs():
                t0, p0 = PLAN.at["mlad"]["tile"], PLAN.at["mlad"]["panel"]
                for j in range(4):
                    split_lo_at(p0 + j + AHEAD)
                rotary = slice(HALF, HALF + ROPE)
                dve.wait_ge(s("rope_in"), 32)
                dve.wait_ge(s("down_out"), 4)
                rotate(kv_f[rotary, 0:LAT], rotary, 0, mp_all[:, 0, :])
                dve.wait_ge(s("key_hi"), 1)
                dve.tensor_tensor(mk_lo[rotary, :], kv_f[rotary, :], mk_hi[rotary, :].bitcast(F32),
                                  ALU.subtract).then_inc(s("mla_k_lo"), 1)
                dve.wait_ge(s("down_root"), 2)
                dve.reciprocal(norm_buf[2][:, 0:LAT], norm_buf[2][:, 0:LAT])
                dve.reciprocal(norm_buf[3][:, :], norm_buf[3][:, :]).then_inc(s("down_inv"), 1)
                dve.wait_ge(s("down_inv"), 1)
                for k in range(2):
                    ins = dve.tensor_tensor(norm_buf[4][:, k * LAT:(k + 1) * LAT], cq_f[:, k, :], norm_buf[2][:, 0:LAT], ALU.mult)
                ins.then_inc(s("down_t"), 1)
                dve.tensor_tensor(norm_buf[5][:, :], ckv_f[:, :], norm_buf[3][:, :], ALU.mult).then_inc(s("down_t"), 1)
                dve.wait_ge(s("down_hi"), 1)
                dve.tensor_tensor(cq_lo[:, :, :], cq_f[:, :, :], cq_hi[:, :, :].bitcast(F32), ALU.subtract).then_inc(s("down_lo"), 1)
                dve.wait_ge(s("down_hi"), 2)
                dve.tensor_tensor(ckv_lo[:, :], ckv_f[:, :], ckv_hi[:, :].bitcast(F32), ALU.subtract).then_inc(s("down_lo"), 1)

            swap8 = [i ^ 8 for i in range(32)]

            def rotate(x, rows, r, buf):
                m_turned, m_straight = buf[:, 0:LAT], buf[:, LAT:TOK]
                if r:
                    dve.wait_ge(s("rope32_done"), r)
                dve.stream_shuffle(m_turned[rows, 0:LAT], x, swap8).then_inc(s("rope32_step"), 1)
                dve.tensor_tensor(m_straight[rows, 0:LAT], x, rope32[rows, 0, :], ALU.mult)
                dve.wait_ge(s("rope32_step"), 2 * r + 1)
                dve.tensor_tensor(m_turned[rows, 0:LAT], m_turned[rows, 0:LAT], rope32[rows, 1, :],
                                  ALU.mult).then_inc(s("rope32_step"), 1)
                dve.wait_ge(s("rope32_step"), 2 * r + 2)
                dve.tensor_tensor(x, m_straight[rows, 0:LAT], m_turned[rows, 0:LAT], ALU.add).then_inc(s("rope32_done"), 1)

            def mla_attention():
                p0, x0 = PLAN.at["mla"]["panel"], PLAN.at["mla"]["aux"]
                split_after = {0: [3], 3: [4], 7: [5, 6], 11: [], 15: [7]}
                rotary = slice(HALF, HALF + ROPE)
                for turn in range(MLA_HEADS + 1):
                    h = turn - 1
                    if h >= 0:
                        for i in range(2):
                            x = x0 + AUX_AT["mla", "score", h, i]
                            dve.wait_ge(s("aux_done"), x + 1)
                            dve.tensor_reduce(m_max[:, i:i + 1], aux[x % AUX][:, :], AX.X, ALU.max,
                                              negate=True).then_inc(s("mla_max"), 1)
                        dve.wait_ge(s("mla_exp"), 2 * h + 2)
                        dve.reciprocal(m_zinv[:, :], m_z[:, :]).then_inc(s("mla_zinv"), 1)
                        dve.wait_ge(s("mla_zinv"), h + 1)
                        for i in range(2):
                            dve.tensor_scalar(mp_all[:, i, :], mp_raw[i][:, :], m_zinv[:, i:i + 1], None,
                                              ALU.mult).then_inc(s("mla_mix"), 1)
                    if turn < MLA_HEADS:
                        dve.wait_ge(s("mla_qkv"), 2 * turn + 1)
                        rotate(mq_f[rotary, :], rotary, turn + 1, norm_buf[0])
                        dve.wait_ge(s("mla_q_hi"), turn + 1)
                        dve.tensor_tensor(mq_lo[0:QD, :], mq_f[0:QD, :], mq_hi[0:QD, :].bitcast(F32),
                                          ALU.subtract).then_inc(s("mla_q_lo"), 1)
                        dve.wait_ge(s("mla_k_hi"), turn + 1)
                        dve.tensor_tensor(mk_lo[0:NOPE, :], kv_f[0:NOPE, :], mk_hi[0:NOPE, :].bitcast(F32),
                                          ALU.subtract).then_inc(s("mla_k_lo"), 1)
                        for n in split_after.get(turn, []):
                            split_lo_at(p0 + n)
                        x = x0 + AUX_AT["mla", "turn_v", turn, 0]
                        j = turn % 2
                        half = slice(j * HALF, (j + 1) * HALF)
                        dve.wait_ge(s("mla_v_hi"), turn + 1)
                        dve.tensor_tensor(mv_lo[j][:, :, half], aux[x % AUX][:, :].rearrange("p (t c) -> p t c", c=P)[:, :, HALF:P],
                                          mv_hi[j][:, :, half].bitcast(F32), ALU.subtract).then_inc(s("mla_v_lo"), 1)
                    if h >= 0:
                        for i in range(2):
                            x = x0 + AUX_AT["mla", "turn_p", h, i]
                            dve.wait_ge(s("mla_pt_hi"), 2 * h + i + 1)
                            dve.tensor_tensor(mpt_lo[:, 2 * i:2 * i + 2, :].rearrange("p a b -> p (a b)"), aux[x % AUX][:, :],
                                              mpt_hi[:, 2 * i:2 * i + 2, :].rearrange("p a b -> p (a b)").bitcast(F32),
                                              ALU.subtract).then_inc(s("mla_pt_lo"), 1)
                        if h % 2:
                            m = h // 2
                            dve.wait_ge(s("mla_o_hi"), m + 1)
                            dve.tensor_tensor(G_lo[:, m, 0:LAT], pv_ps[:, (m % 2) * LAT:(m % 2 + 1) * LAT],
                                              G_hi[:, m, 0:LAT].bitcast(F32), ALU.subtract).then_inc(s("mla_o_lo"), 1)
                split_lo_at(p0 + 8)

            norm("mix2", TOK, SPLIT_AT["mix2"])
            for j in range(2):
                dve.memset(mv_hi[j][:, :, :].bitcast(F32), 0.0)
                ins = dve.memset(mv_lo[j][:, :, :].bitcast(F32), 0.0)
            ins.then_inc(s("mv_zero"), 1)
            dve.wait_ge(s("mv_zero"), 1)
            down_outputs()
            mla_attention()
            output_added("mlao", 2, 1)
            norm("mlp2", LAT, SPLIT_AT["mlp2"])
            mlp(2, 1, True)
            dve.wait_ge(s("dft_hi"), 2)
            dve.tensor_tensor(dft_lo[:, :, :], dft[:, :, :], dft_hi[:, :, :].bitcast(F32), ALU.subtract).then_inc(s("dft_lo"), 1)
            norm("mix3", LAT, SPLIT_AT["mix3"])
            fourier("four3", 3, 1)
            norm("mlp3", LAT, SPLIT_AT["mlp3"])
            mlp(3, 1, False)
            norm("final", LAT, None)
            dve.wait_ge(s("small_in"), 16 * 7)
            dve.memset(chunk_mask[:, :], 1.0).then_inc(s("mask"), 1)
            dve.wait_ge(s("mask"), 1)
            for c0, _ in CHUNKS:
                ins = dve.memset(chunk_mask[:, c0:c0 + 1], 0.0)
            ins.then_inc(s("mask"), 1)
            norm("mix_2", TOK2, SPLIT_AT["mix_2"])

            def gates():
                dve.wait_ge(s("z_ln"), 1)
                dve.scalar_tensor_tensor(log_a[:, :, :], z_f[:, :, :], 0.0, z_abs[:, :, :], ALU.min,
                                         ALU.subtract).then_inc(s("log_a"), 1)
                dve.wait_ge(s("log_a"), 1)
                dve.wait_ge(s("mask"), 2)
                for j in range(2):
                    ins = dve.tensor_tensor_scan(b_cum[:, j, :], chunk_mask[:, :], log_a[:, j, :], 0.0, ALU.mult, ALU.add)
                ins.then_inc(s("b_cum"), 1)
                dve.wait_ge(s("b_cum"), 1)
                for n in range(4):
                    end = CHUNKS[n][0] + CHUNKS[n][1] - 1
                    ins = dve.tensor_scalar(b_last[:, :, n:n + 1], b_cum[:, :, end:end + 1], 1.0 / 16, None, ALU.mult)
                ins.then_inc(s("b_last"), 1)

            def gated_qk():
                for j in range(2):
                    dve.memset(q_pad[j][:, :, :], 0.0).then_inc(s("q_zero"), 1)
                dve.wait_ge(s("q_zero"), 2)
                dve.wait_ge(s("e_end"), 1)
                dve.wait_ge(s("proj"), 5)
                dve.tensor_tensor(k_end[:, :, 0:CHUNKS[4][0]], proj[:, K_AT:K_AT + 2, 0:CHUNKS[4][0]],
                                  e_end[:, :, 0:CHUNKS[4][0]], ALU.mult).then_inc(s("k_end"), 1)
                for j in range(2):
                    half = slice(j * HALF, (j + 1) * HALF)
                    dve.scalar_tensor_tensor(q_pad[j][half, :, :], proj[half, Q_AT:Q_AT + 2, META:], HALF ** -0.5,
                                             e_pos[half, :, META:], ALU.mult, ALU.mult)
                dve.tensor_tensor(k_t[:, :, :], proj[:, K_AT:K_AT + 2, META:], e_neg[:, :, :], ALU.mult).then_inc(s("qk_t"), 1)

            def pooling():
                dve.wait_ge(s("proj"), 13)
                u = proj[:, POOL_AT:POOL_AT + 4, :]
                src, width = u, 1
                for g, dst in enumerate((win_a, win_b, win_a, win_b)):
                    lo = 2 * width - 1
                    dve.tensor_tensor(dst[:, g:, lo:], src[:, g:, lo:], src[:, g:, lo - width:TOK2 - width],
                                      ALU.add).then_inc(s("window"), 1)
                    dve.wait_ge(s("window"), g + 1)
                    width *= 2
                    dve.scalar_tensor_tensor(pooled[:, g, :], dst[:, g, META:], 1.0 / width, u[:, g, META:], ALU.mult,
                                             ALU.subtract).then_inc(s("pooled"), 1)
                    if g < 3:
                        dve.wait_ge(s("pooled"), g + 1)
                    src = dst

            def mixer_rest():
                dve.wait_ge(s("r_exp"), 1)
                dve.tensor_scalar(r_silu[:, :, :], r_silu[:, :, :], 1.0, None, ALU.add).then_inc(s("r_step"), 1)
                dve.wait_ge(s("r_step"), 1)
                dve.reciprocal(r_silu[:, :, :], r_silu[:, :, :]).then_inc(s("r_step"), 1)
                dve.wait_ge(s("r_step"), 2)
                dve.tensor_tensor(r_silu[:, :, :], r_silu[:, :, :], proj[:, R_AT:R_AT + 4, META:], ALU.mult).then_inc(s("r_step"), 1)
                dve.wait_ge(s("y_hi"), 1)
                dve.tensor_tensor(Y_lo[:, 0:4, :], y_f[:, :, :], Y_hi[:, 0:4, :].bitcast(F32), ALU.subtract).then_inc(s("y_lo"), 1)
                for i in range(2):
                    n = MIX_AT["state", i]
                    ps = mix_ps[n % 4]
                    dve.wait_ge(s("mix_done_ps"), n + 1)
                    dve.tensor_copy(S_all[:, i, 0, :], ps[:, 0:P]).then_inc(s("states"), 1)
                    for c in range(1, 4):
                        dve.wait_ge(s("states"), 4 * i + c)
                        dve.scalar_tensor_tensor(S_all[:, i, c, :], S_all[:, i, c - 1, :], decay[:, i, c:c + 1],
                                                 ps[:, c * P:(c + 1) * P], ALU.mult, ALU.add).then_inc(s("states"), 1)
                dve.wait_ge(s("go_root"), 2)
                dve.reciprocal(go_inv, go_inv).then_inc(s("go_step"), 1)
                dve.wait_ge(s("go_step"), 1)
                dve.tensor_tensor(go_inv, go_inv, r_silu[:, :, :], ALU.mult).then_inc(s("go_step"), 1)
                dve.wait_ge(s("go_step"), 2)
                dve.tensor_tensor(go_f[:, :, :], go_f[:, :, :], go_inv, ALU.mult).then_inc(s("go_t"), 1)
                dve.wait_ge(s("y_hi"), 2)
                dve.tensor_tensor(Y_lo[:, 4:8, :], y_f[:, :, :], Y_hi[:, 4:8, :].bitcast(F32), ALU.subtract).then_inc(s("y_lo"), 1)

            for i in range(len(WIN_ORDER)):
                split_lo_at(PLAN.at["win"]["panel"] + i + AHEAD)
                if i == 3:
                    gates()
                if i == 6:
                    gated_qk()
                if i == 13:
                    pooling()
            mixer_rest()
            for m in range(KT):
                split_lo_at(PLAN.at["wout"]["panel"] + m + AHEAD)
                t = PLAN.at["wout"]["tile"] + m
                dve.wait_ge(s("tile_done"), t + 1)
                dve.tensor_tensor(X[:, m, 0:LAT], X[:, m, 0:LAT], bank[t % BANKS][:, 0:LAT], ALU.add).then_inc(s("x_done"), 1)
            dve.memset(zero_row[:, :], 0.0).then_inc(s("zero_row"), 1)
            norm("ffn_2", LAT, SPLIT_AT["ffn_2"])

            steps = [0]

            def step(ins):
                ins.then_inc(s("route"), 1)
                steps[0] += 1
                dve.wait_ge(s("route"), steps[0])

            def spread(x, n=4):
                return x[:, :].rearrange("p (t o) -> p t o", o=1).to_broadcast([P, 2, n])

            def first_largest(choice, top, values, scratch):
                step(dve.tensor_reduce(top[:, :], values, AX.X, ALU.max))
                step(dve.tensor_tensor(choice, values, spread(top), ALU.is_equal))
                step(dve.tensor_tensor(choice, choice, rank[:, :, :], ALU.mult))
                step(dve.tensor_reduce(scratch[:, :], choice, AX.X, ALU.max))
                step(dve.tensor_tensor(choice, choice, spread(scratch), ALU.is_equal))

            def router():
                for j in range(4):
                    step(dve.memset(rank[:, :, j:j + 1], float(4 - j)))
                dve.wait_ge(s("logits"), 1)
                groups = logits[:, :, 0:4]
                g_one, e_sel, e_one, e_two = r4[2][:, :, :], r4[3][:, :, :], r4[6][:, :, :], r4[7][:, :, :]
                first_largest(g_one, r1[0], groups, r1[1])
                dve.tensor_tensor(r4[0][:, :, :], groups, spread(r1[0]), ALU.subtract).then_inc(s("shifted"), 1)
                experts = logits[:, :, 4:].rearrange("p t (g j) -> p t g j", g=4)
                for t in range(2):
                    dve.tensor_tensor(r16[:, t, :, :], experts[:, t, :, :],
                                      r4[2][:, t, :].rearrange("p (g o) -> p g o", o=1).to_broadcast([P, 4, 4]), ALU.mult)
                step(dve.memset(r1[7][:, :], 0.0))
                step(dve.tensor_tensor(r4[8][:, :, :], r16[:, :, 0, :], r16[:, :, 1, :], ALU.add))
                step(dve.tensor_tensor(r4[9][:, :, :], r16[:, :, 2, :], r16[:, :, 3, :], ALU.add))
                step(dve.tensor_tensor(e_sel, r4[8][:, :, :], r4[9][:, :, :], ALU.add))
                first_largest(e_one, r1[2], e_sel, r1[3])
                dve.tensor_tensor(r4[4][:, :, :], e_sel, spread(r1[2]), ALU.subtract).then_inc(s("shifted"), 1)
                step(dve.scalar_tensor_tensor(r4[8][:, :, :], e_one, -3e38, e_sel, ALU.mult, ALU.add))
                first_largest(e_two, r1[4], r4[8][:, :, :], r1[5])
                step(dve.tensor_tensor(e_one, e_one, e_two, ALU.add))
                dve.wait_ge(s("route_exp"), 2)
                step(dve.tensor_reduce(r1[0][:, :], r4[1][:, :, :], AX.X, ALU.add))
                step(dve.tensor_tensor(r4[9][:, :, :], r4[5][:, :, :], e_one, ALU.mult))
                step(dve.tensor_reduce(r1[1][:, :], r4[9][:, :, :], AX.X, ALU.add))
                step(dve.tensor_tensor(r1[2][:, :], r1[0][:, :], r1[1][:, :], ALU.mult))
                step(dve.reciprocal(r1[3][:, :], r1[2][:, :]))
                step(dve.tensor_tensor(r4[9][:, :, :], r4[9][:, :, :], spread(r1[3]), ALU.mult))
                for g in range(4):
                    step(dve.tensor_tensor(combine[:, :, 4 * g:4 * g + 4], r4[9][:, :, :],
                                           r4[2][:, :, g:g + 1].to_broadcast([P, 2, 4]), ALU.mult))

            p0 = PLAN.at["moe"]["panel"]

            def expert_split(n, i=None):
                if n < 6 * EXPERTS:
                    dve.wait_ge(s("w_hi"), later(p0 + n + 1, i, 6 * EXPERT_TURNS))
                    split_lo(p0 + n)

            def diagonal(x, i=None):
                if x >= 2:
                    dve.wait_ge(s("weight_row"), later(x - 1, i, EXPERT_TURNS))
                for tt in range(2):
                    col = combine[:, tt, x:x + 1] if i is None else combine[:, tt, bass.ds(i * EXPERT_TURNS + x, 1)]
                    ins = dve.tensor_scalar(diag[x % 2][:, tt, :], ident[:, :], col, None, ALU.mult)
                ins.then_inc(s("diag"), 1)

            def gated(x, i=None):
                st = EXPERT_TURNS
                h = e_hid[x % 2]
                flat = lambda v: v[:, :, :].rearrange("p m c -> p (m c)")
                dve.wait_ge(s("e_exp"), later(x + 1, i, st))
                dve.tensor_scalar(e_inv[:, :, :], e_exp[:, :, :], 1.0, None, ALU.add).then_inc(s("e_step"), 1)
                dve.wait_ge(s("e_step"), later(4 * x + 1, i, 4 * st))
                dve.reciprocal(e_inv[:, :, :], e_inv[:, :, :]).then_inc(s("e_step"), 1)
                dve.wait_ge(s("e_step"), later(4 * x + 2, i, 4 * st))
                dve.tensor_tensor(flat(e_inv), flat(e_inv), psum[3 * (x % 2)][:, :], ALU.mult).then_inc(s("e_step"), 1)
                dve.wait_ge(s("e_step"), later(4 * x + 3, i, 4 * st))
                dve.wait_ge(s("expert_done"), later(6 * x + 2 if x else 4, i, 6 * st))
                dve.tensor_tensor(flat(e_inv), flat(e_inv), psum[1][:, :], ALU.mult).then_inc(s("e_step"), 1)
                dve.wait_ge(s("e_step"), later(4 * x + 4, i, 4 * st))
                dve.wait_ge(s("weight_row"), later(x + 1, i, st))
                row = psum[2][:, 0:LAT].rearrange("p (o c) -> p o c", o=1).to_broadcast([P, 2, LAT])
                dve.tensor_tensor(h[:, :, :], e_inv[:, :, :], row, ALU.mult).then_inc(s("e_hid"), 1)
                dve.wait_ge(s("e_hi"), later(x + 1, i, st))
                dve.tensor_tensor(E_lo[x % 2][:, :, :], h[:, :, :], E_hi[x % 2][:, :, :].bitcast(F32),
                                  ALU.subtract).then_inc(s("e_lo"), 1)

            def expert_turn(x, i=None):
                n = 6 * x - 2 if x else 0
                diagonal(x, i)
                for j in range(4):
                    expert_split(n + j + AHEAD, i)
                gated(x, i)
                if x:
                    for j in range(4, 6):
                        expert_split(n + j + AHEAD, i)

            router()
            expert_turn(0)
            with dve.Fori(0, 3) as i:
                for j in range(EXPERT_TURNS):
                    expert_turn(1 + j, i)
            for x in range(1 + 3 * EXPERT_TURNS, EXPERTS):
                expert_turn(x)
            dve.wait_ge(s("expert_done"), 6 * EXPERTS)
            for b in range(4):
                ins = dve.tensor_tensor(X[:, 2 * b:2 * b + 2, 0:LAT], X[:, 2 * b:2 * b + 2, 0:LAT],
                                        psum[4 + b][:, :].rearrange("p (m c) -> p m c", m=2), ALU.add)
            ins.then_inc(s("y_added"), 1)
            norm("final_2", LAT, None)


DFT_N = 256


def tables():
    n = np.arange(DFT_N)
    angle = 2 * np.pi * ((n[:, None] * n[None, :]) % DFT_N) / DFT_N
    dft = np.concatenate([np.cos(angle), np.sin(angle)], axis=1) / np.sqrt(DFT_N)
    def rope(width, reps):
        n_freq = width // 4
        inv_freq = (np.float32(10000.0) ** (-np.arange(n_freq, dtype=np.float32) / n_freq)).astype(np.float32)
        t = np.arange(LAT)
        where = np.stack([t // 64, t % 64]).astype(np.float32)
        f = np.arange(width)
        turn = where[f // (2 * n_freq)] * inv_freq[f % n_freq][:, None]
        sign = np.where(f // n_freq % 2 == 0, -1.0, 1.0)[:, None]
        both = np.stack([np.cos(turn), np.sin(turn) * sign], axis=1)
        return np.tile(both, (reps, 1, 1)).astype(np.float32)

    return {"dft": dft.astype(np.float32), "rope_diff": rope(HALF, 2), "rope_mla": rope(ROPE, 1)}


def kernel(**inputs):
    import concourse.bacc as bacc
    from concourse.bass_utils import run_bass_kernel_spmd

    nc = bacc.Bacc("TRN2", target_bir_lowering=False, num_devices=1)
    arrays = {f"in_{name}": np.ascontiguousarray(value) for name, value in {**inputs, **tables()}.items()}
    aps = {name[3:]: nc.dram_tensor(name, v.shape, mybir.dt.from_np(v.dtype), kind="ExternalInput").ap()
           for name, v in arrays.items()}
    out = nc.dram_tensor("out", (1, LAT, D), F32, kind="ExternalOutput").ap()
    build_program(nc, aps, out)
    result = run_bass_kernel_spmd(nc, [arrays], core_ids=[0])
    return result.results[0]["out"]
```

```python
from contextlib import ExitStack

import numpy as np
import concourse.bass as bass
from concourse import mybir

F32 = mybir.dt.float32
F32R = mybir.dt.float32r
ACT = mybir.ActivationFunctionType
ALU = mybir.AluOpType
AX = mybir.AxisListType

P = 128
D = 1024
KT = D // P
LAT = 256
CTX = 256
TOK = LAT + CTX
META = 16
TOK2 = LAT + META
DEPTH = 4
FF = 4 * D
FF_BLOCK = 1024
BLOCKS = FF // FF_BLOCK
MOD_TILES = 6 * KT
EPS = 1e-6
LAM_INIT = 0.8 - 0.6 * float(np.exp(-0.3))
HEADS = 8
HALF = 64
MLA_HEADS = 16
NOPE, ROPE = 64, 32
QD = NOPE + ROPE
Q_RANK, KV_RANK = 256, 128
GLA_HEADS = 4
CHUNK = 64
EXPERTS = 16
E_GROUPS = 4
E_PER = 4
E_HID = 256

RING = 4
RAW = 4
AHEAD = RING - 1
BANKS = 4
AUX = 3
PANEL = KT * P

VEC_ROWS = {}
VEC_TILES = 3


def place_vectors():
    rows = [0] * VEC_TILES
    plan = [("mod_b_lo", 0, 96), ("c", 0, 8), ("c_ctx", 0, 8), ("mod_b_hi", 1, 96),
            ("norm_mix_g", 2, 32), ("norm_mlp_g", 2, 32), ("final_g", 2, 8), ("fourier_b", 2, 16),
            ("norm_mix_w_2", 2, 8), ("norm_ffn_w_2", 2, 8), ("final_norm_w_2", 2, 8),
            ("pool_scale_2", 2, 4), ("gla_norm_w_2", 2, 1), ("b_gate_2", 2, 2), ("diff_subln_g", 2, 1),
            ("mla_q_norm_g", 2, 2), ("mla_kv_norm_g", 2, 1)]
    for name, tile, n in plan:
        VEC_ROWS[name] = (tile, rows[tile], n)
        rows[tile] += n
    return rows


VEC_COUNT = place_vectors()


class Plan:

    def __init__(self):
        self.tiles = []
        self.aux = []
        self.loaded = [0] * RAW
        self.at = {}
        self.units = []
        self.panels = []

    def phase(self, name, units=(), tiles=(), aux=(), frees=()):
        self.at[name] = {"unit": len(self.units), "panel": len(self.panels), "tile": len(self.tiles), "aux": len(self.aux)}
        k = 0
        first = len(self.panels)
        self.panels += [None] * len(frees)
        for panels, dmas in units:
            if isinstance(panels, int):
                panels = range(k, k + panels)
            slot = len(self.units) % RAW
            self.loaded[slot] += 16 * dmas
            for place, panel in enumerate(panels):
                free = frees[panel]
                if isinstance(free, int):
                    free = ("tile_done", len(self.tiles) + free + 1)
                self.panels[first + panel] = (len(self.units), place, free)
                k += 1
            self.units.append((first + max(panels) + 1, slot, self.loaded[slot]))
        assert k == len(frees)
        self.tiles += tiles
        self.aux += aux


AUX_AT = {}


def diff_aux():
    tiles = []

    def add(what, h, i, signal, value):
        AUX_AT["diff", what, h, i] = len(tiles)
        tiles.append((signal, value))

    for turn in range(HEADS + 1):
        h = turn - 1
        if h >= 0:
            for i in range(8):
                add("score", h, i, "p_exp", 8 * h + i + 1)
            for i in range(3):
                add("turn_p", h, i, "pt_lo", 3 * h + i + 1)
            add("pv", h, 0, "o_out", h + 1)
        if turn < HEADS:
            add("turn_v", turn, 0, "v_lo", turn + 1)
        if h >= 0:
            add("square", h, 0, "o_root", h + 1)
    return tiles


def mla_aux():
    tiles = []

    def add(what, h, i, signal, value):
        AUX_AT["mla", what, h, i] = len(tiles)
        tiles.append((signal, value))

    for turn in range(MLA_HEADS + 1):
        h = turn - 1
        if h >= 0:
            for i in range(2):
                add("score", h, i, "mla_exp", 2 * h + i + 1)
        if turn < MLA_HEADS:
            add("turn_v", turn, 0, "mla_v_lo", turn + 1)
        if h >= 0:
            for i in range(2):
                add("turn_p", h, i, "mla_pt_lo", 2 * h + i + 1)
    return tiles


EXPERT_TURNS = 4
WIN_ORDER = [16, 4, 5, 6, 7, 8, 9, 10, 11, 0, 1, 2, 3, 12, 13, 14, 15]
POOL_AT, Q_AT, K_AT, V_AT, R_AT, GATE_AT = 0, 4, 6, 8, 12, 16
GATE_RANK = 16
CHUNKS = [(0, META)] + [(META + CHUNK * n, CHUNK) for n in range(LAT // CHUNK)]
MLP_TILES = 2 * KT


def signals(name, first, n):
    return [(name, first + i + 1) for i in range(n)]


X_AT = {"four0": 0, "mlp0": 8, "diffo": 40, "mlp1": 48, "mlao": 80, "mlp2": 88, "four3": 120,
        "mlp3": 128, "wout": 160, "moe": 168}


def mlp_tiles(layer):
    tiles = []
    for b in range(BLOCKS):
        tiles += signals("relu", KT * (BLOCKS * layer + b), KT)
        tiles += signals("x_done", X_AT[f"mlp{layer}"] + KT * b, KT)
    return tiles


def make_plan():
    p = Plan()
    p.phase("vec", tiles=[("vec", 1), ("lam_col", 1)])
    p.phase("xin", tiles=signals("x_cols", 0, KT))
    p.phase("four0", [(2, 1)] * 4, signals("four_lo", 0, 24) + signals("x_done", 0, KT), frees=[24 + m for m in range(KT)])
    p.phase("mlp0", [(2, 1)] * 32, mlp_tiles(0), frees=range(64))
    pairs = [([h + j, h + j + 3], 1) for h in range(0, 3 * HEADS, 6) for j in range(3)]
    p.phase("diff", pairs, signals("qkv", 0, 24), diff_aux(), frees=range(24))
    p.phase("diffo", [(2, 1)] * 4, signals("x_done", X_AT["diffo"], KT), frees=range(8))
    p.phase("mlp1", [(2, 1)] * 32, mlp_tiles(1), frees=range(64))
    p.phase("mlad", [(2, 1), (1, 1), (1, 1)], signals("down_out", 0, 4), frees=range(4))
    p.phase("mla", [(2, 4), (2, 2), (2, 4)], signals("mla_qkv", 0, 2 * MLA_HEADS), mla_aux(),
            frees=[6, 14, 15, 31, 22, 30])
    p.phase("mlao", [(2, 1)] * 4, signals("x_done", X_AT["mlao"], KT), frees=range(8))
    p.phase("mlp2", [(2, 1)] * 32, mlp_tiles(2), frees=range(64))
    p.phase("four3", [(2, 1)] * 4, signals("four_lo", 24, 16) + signals("x_done", X_AT["four3"], KT),
            frees=[16 + m for m in range(KT)])
    p.phase("mlp3", [(2, 1)] * 32, mlp_tiles(3), frees=range(64))
    p.phase("meta", tiles=[("meta_cols", 1)])
    p.phase("win", [(1, 1)] + [(2, 1)] * 8, signals("proj", 0, 17), frees=range(17))
    p.phase("wout", [(2, 1)] * 4, signals("x_done", X_AT["wout"], KT), frees=range(8))
    panels = 6 * EXPERTS
    p.phase("moe", [(2, 1)] * (panels // 2), frees=[("expert_done", i + 1) for i in range(panels)])
    return p


PLAN = make_plan()

MIX_TILES = []
MIX_AT = {}
for _what, _n, _signal in (("gate", 2, "z_in"), ("turn_v", 5, "v_rows"), ("turn_k", 2, "k_rows"),
                           ("pool", 2, "pool_in"), ("score", 2, "sc_in"), ("state", 2, "states"),
                           ("out", 2, "go_in"), ("square", 2, "go_root")):
    for _i in range(_n):
        MIX_AT[_what, _i] = len(MIX_TILES)
        MIX_TILES.append((_signal, _i + 1 if _signal != "states" else 4 * (_i + 1)))



NORMS = [("mix0", True, TOK), ("mlp0", True, TOK), ("mix1", True, TOK), ("mlp1", True, TOK),
         ("mix2", True, TOK), ("mlp2", True, LAT), ("mix3", True, LAT), ("mlp3", True, LAT),
         ("final", False, LAT), ("mix_2", True, TOK2), ("ffn_2", True, LAT), ("final_2", False, LAT)]
SPLIT_NORMS = {name for name, split, _ in NORMS if split}
NORM_AT = {name: i for i, (name, _, _) in enumerate(NORMS)}
SPLIT_AT = {name: sum(s for _, s, _ in NORMS[:i]) for i, (name, _, _) in enumerate(NORMS)}
MOD_RING = 4
MOD_COLS = 6 * D // BLOCKS
MOD_UNITS = KT
MOD_PART = MOD_COLS // 4
MOD_AFTER = {1: 0, 2: 1, 4: 2, 5: 3, 7: 4, 8: 5, 10: 6, 11: 7}
MOD_ROWS_AT, MOD_TURN_AT = 12, 14


def build_program(nc, a, out):
    ctx = ExitStack()
    sems = {}

    def s(name):
        if name not in sems:
            sems[name] = ctx.enter_context(nc.semaphore(name))
        return sems[name]

    with ctx:
        base = 16512
        at = {}

        def sb(name, shape, dtype=F32, over=None):
            nonlocal base
            size = int(np.prod(shape[1:])) * 4
            size = (size + 31) // 32 * 32
            if over is None:
                place, base = base, base + size
            else:
                place = over
            at[name] = place
            return nc.alloc_sbuf_tensor_at(name, list(shape), dtype, offset=place)

        X = sb("x", [P, KT, TOK])
        H_hi = sb("h_hi", [P, KT, TOK], F32R)
        H_lo = sb("h_lo", [P, KT, TOK], F32R)
        G_hi = sb("g_hi", [P, KT, TOK], F32R)
        G_lo = sb("g_lo", [P, KT, TOK], F32R)
        x_rows = sb("x_rows", [P, 4, D], over=at["g_hi"])
        W_hi = [sb(f"w_hi{r}", [P, PANEL], F32R) for r in range(RING)]
        W_lo = [sb(f"w_lo{r}", [P, PANEL], F32R) for r in range(RING)]
        w_raw = [sb(f"w_raw{r}", [P, KT, 2, P]) for r in range(RAW)]
        ident = sb("ident", [P, P])
        ones = sb("ones", [P, P])
        eps = sb("eps", [P, 1])
        vec_rows = sb("vec_rows", [P, VEC_TILES, P])
        vec = sb("vec", [P, VEC_TILES, P])
        lam_in = sb("lam_in", [1, 4, HALF])
        lam_prod = sb("lam_prod", [1, 2, HALF])
        lam_row = sb("lam_row", [1, 4])
        lam_col = sb("lam_col", [P, 2])
        subln = sb("subln", [P, 1])
        silu_c = sb("silu_c", [P, KT, 32])
        silu_t = sb("silu_t", [P, 2, KT])
        mod = [sb(f"mod{r}", [P, MOD_TILES, 2]) for r in range(2)]
        scale_mix = sb("scale_mix", [P, KT, 2])
        scale_mlp = sb("scale_mlp", [P, KT, 2])
        gated_b = sb("gated_b", [P, KT, 2])
        norm_buf = [sb(f"norm{r}", [P, TOK]) for r in range(6)]
        work = base
        mod_raw = [sb(f"mod_raw{r}", [P, MOD_COLS]) for r in range(MOD_RING)]
        mod_rows = sb("mod_rows", [P, MOD_PART])
        mlp_work = base
        relu = [sb(f"relu{r}", [P, TOK]) for r in range(2)]
        square = [sb(f"square{r}", [P, TOK]) for r in range(2)]
        base = mlp_work
        dft = sb("dft", [P, 2, 2 * 256])
        dft_hi = sb("dft_hi", [P, 2, 2 * 256], F32R)
        dft_lo = sb("dft_lo", [P, 2, 2 * 256], F32R)
        base = work
        rope = sb("rope", [P, 2, LAT])
        q_f = sb("q_f", [P, TOK])
        k_f = sb("k_f", [P, TOK])
        v_f = q_f
        q_hi, q_lo = sb("q_hi", [P, TOK], F32R), sb("q_lo", [P, TOK], F32R)
        k_hi, k_lo = sb("k_hi", [P, TOK], F32R), sb("k_lo", [P, TOK], F32R)
        v_hi, v_lo = sb("v_hi", [P, 4, P], F32R), sb("v_lo", [P, 4, P], F32R)
        p_raw = [[sb(f"p_raw{r}{j}", [P, TOK]) for j in range(2)] for r in range(2)]
        p_all = sb("p_all", [P, 2 * TOK + 2 * CTX])
        pt_hi, pt_lo = sb("pt_hi", [P, 6, LAT], F32R), sb("pt_lo", [P, 6, LAT], F32R)
        neg_max = sb("neg_max", [P, 8])
        z = sb("z", [P, 8])
        z_inv = sb("z_inv", [P, 8])
        z_mix = sb("z_mix", [P, 8])
        o_f, o_sq, o_inv, o_t, o_g = norm_buf[0], norm_buf[1], norm_buf[2], norm_buf[3], norm_buf[4]
        turned, straight = norm_buf[5][:, 0:LAT], norm_buf[5][:, LAT:TOK]
        assert base <= 229344, base
        base = work
        rope32 = sb("rope32", [P, 2, LAT])
        cq_f = sb("cq_f", [P, 2, LAT])
        ckv_f = sb("ckv_f", [P, TOK])
        cq_hi, cq_lo = sb("cq_hi", [P, 2, LAT], F32R), sb("cq_lo", [P, 2, LAT], F32R)
        ckv_hi, ckv_lo = sb("ckv_hi", [P, TOK], F32R), sb("ckv_lo", [P, TOK], F32R)
        mq_f = sb("mq_f", [P, LAT])
        kv_f = sb("kv_f", [P, TOK])
        mq_hi, mq_lo = sb("mq_hi", [P, LAT], F32R), sb("mq_lo", [P, LAT], F32R)
        mk_hi, mk_lo = sb("mk_hi", [P, TOK], F32R), sb("mk_lo", [P, TOK], F32R)
        mv_hi = [sb(f"mv_hi{j}", [P, 4, P], F32R) for j in range(2)]
        mv_lo = [sb(f"mv_lo{j}", [P, 4, P], F32R) for j in range(2)]
        mp_raw = [sb(f"mp_raw{r}", [P, TOK], over=at[("cq_f", "ckv_f")[r]]) for r in range(2)]
        mp_all = sb("mp_all", [P, 2, TOK])
        mpt_hi, mpt_lo = sb("mpt_hi", [P, 4, LAT], F32R), sb("mpt_lo", [P, 4, LAT], F32R)
        m_max = sb("m_max", [P, 2])
        m_z = sb("m_z", [P, 2])
        m_zinv = sb("m_zinv", [P, 2])
        assert base <= 229344, base

        base = work
        meta_rows = sb("meta_rows", [META, D])
        pool_w = sb("pool_w", [P, 4, P])
        gate_up = sb("gate_up", [GATE_RANK, 2 * P])
        route_w = sb("route_w", [P, KT, 4 + EXPERTS])
        route_b = sb("route_b", [1, 4 + EXPERTS])
        chunk_mask = sb("chunk_mask", [P, TOK2])
        S_all = sb("S_all", [P, 2, 4, P])
        second_work = base
        base = at["g_hi"]
        proj = sb("proj", [P, 17, TOK2])
        pooled = sb("pooled", [P, 4, LAT])
        win_a = sb("win_a", [P, 4, TOK2])
        win_b = sb("win_b", [P, 4, TOK2])
        assert base <= at["w_hi0"]
        base = at["h_hi"]
        Y_hi, Y_lo = sb("Y_hi", [P, KT, LAT], F32R), sb("Y_lo", [P, KT, LAT], F32R)
        go_f = sb("go_f", [P, GLA_HEADS, LAT])
        r_silu = sb("r_silu", [P, GLA_HEADS, LAT])
        y_f = sb("y_f", [P, 4, LAT])
        sc = sb("sc", [CHUNK, GLA_HEADS, 4, CHUNK])
        assert base <= at["g_hi"]
        base = at["norm0"]
        z_f = sb("z_f", [P, 2, TOK2])
        z_abs = sb("z_abs", [P, 2, TOK2])
        log_a = sb("log_a", [P, 2, TOK2])
        b_cum = sb("b_cum", [P, 2, TOK2])
        e_pos = sb("e_pos", [P, 2, TOK2])
        assert base <= work
        base = second_work
        e_neg = sb("e_neg", [P, 2, LAT])
        e_end = sb("e_end", [P, 2, TOK2])
        q_pad = [sb(f"q_pad{j}", [P, 2, LAT]) for j in range(2)]
        k_t = sb("k_t", [P, 2, LAT])
        k_end = sb("k_end", [P, 2, TOK2])
        v_rows_m = sb("v_rows_m", [META, GLA_HEADS, P])
        k_rows_m = sb("k_rows_m", [META, 2, P])
        b_last = sb("b_last", [P, 2, 4])
        decay = sb("decay", [P, 2, 4])
        v_rows = sb("v_rows", [CHUNK, GLA_HEADS, 4, P])
        k_rows = sb("k_rows", [CHUNK, 2, 3, P])
        go_sq, go_inv = win_a[:, :, 0:LAT], win_b[:, :, 0:LAT]
        assert base <= 229344, base
        base = second_work
        logits = sb("logits", [P, 2, 4 + EXPERTS])
        r4 = [sb(f"r4_{i}", [P, 2, 4]) for i in range(12)]
        r1 = [sb(f"r1_{i}", [P, 2]) for i in range(8)]
        r16 = sb("r16", [P, 2, 4, 4])
        rank = sb("rank", [P, 2, 4])
        combine = sb("combine", [P, 2, EXPERTS])
        diag = [sb(f"diag{j}", [P, 2, P]) for j in range(2)]
        e_exp = sb("e_exp", [P, 2, LAT])
        e_inv = sb("e_inv", [P, 2, LAT])
        e_hid = [sb(f"e_hid{j}", [P, 2, LAT]) for j in range(2)]
        E_hi = [sb(f"E_hi{j}", [P, 2, LAT], F32R) for j in range(2)]
        E_lo = [sb(f"E_lo{j}", [P, 2, LAT], F32R) for j in range(2)]
        zero_row = sb("zero_row", [1, TOK])
        out_rows = sb("out_rows", [P, 2, D])
        assert base <= 229344, base

        psum = [ctx.enter_context(nc.psum_tensor(f"bank{b}", [P, 512], F32)) for b in range(8)]
        bank = psum[:BANKS]
        mod_ps = psum[4]
        pv_ps = psum[4]
        mix_ps = psum[4:8]
        aux = psum[5:8]
        sum_ps = psum[7]

        def vcol(name, k=0):
            tile, row, _ = VEC_ROWS[name]
            return vec[:, tile, row + k:row + k + 1]

        def vcols(name, first=0, n=None):
            tile, row, count = VEC_ROWS[name]
            n = count if n is None else n
            return vec[:, tile, row + first:row + first + n]

        def later(value, i, step):
            return value if i is None else value + i * step

        w1 = a["mlp_w1"].rearrange("l (k p) (b u c) -> l b u p k c", p=P, b=BLOCKS, u=4)
        w2 = a["mlp_w2"].rearrange("l (b k p) (u c) -> l b u p k c", p=P, b=BLOCKS, u=4)
        mod_w = a["mod_w"].rearrange("l (k p) (b c) -> l b k p c", p=P, b=BLOCKS)

        block = ctx.enter_context(nc.Block())

        @block.sync
        def _(sp):
            def wait_raw_free(u, i=None, step=0):
                if u >= RAW:
                    sp.wait_ge(s("panel_ready"), later(PLAN.units[u - RAW][0], i, step))

            def load_unit(u, parts, i=None, step=0):
                wait_raw_free(u, i, step)
                slot = PLAN.units[u][1]
                for dst, src in parts:
                    sp.dma_start(dst(w_raw[slot]), src).then_inc(s(f"raw_in{slot}"), 16)

            def whole(raw):
                return raw[:, :, :, :].rearrange("p k j c -> p k (j c)")

            def load_square(name, w):
                v = w.rearrange("(k p) (u c) -> u p k c", p=P, c=2 * P)
                for u in range(4):
                    load_unit(PLAN.at[name]["unit"] + u, [(whole, v[u])])

            def load_mod(layer, block, u, n0, i=None):
                n = n0 + u
                if n >= MOD_RING:
                    sp.wait_ge(s("mod_used"), later(n - MOD_RING + 1, i, MOD_UNITS))
                sp.dma_start(mod_raw[u % MOD_RING][:, :], mod_w[layer, block, u]).then_inc(s(f"mod_in{u % MOD_RING}"), 16)

            def load_mlp(layer, with_mod):
                u0 = PLAN.at[f"mlp{layer}"]["unit"]
                n0 = BLOCKS * MOD_UNITS * (layer + 1)

                def weights(u, b, i):
                    w = w1[layer, b, u] if u < 4 else w2[layer, b, u - 4]
                    load_unit(u0 + u, [(whole, w)], i, 2 * KT)

                def block(b, order, i):
                    for what, u in order:
                        if what == "w":
                            weights(u, b, i)
                        elif what == "M":
                            load_mod(layer + 1, 0, u, n0)
                        else:
                            load_mod(layer + 1, b + 1, u, n0 + MOD_UNITS, i)

                def order(text):
                    return [(x[0], int(x[1])) for x in text.split()]

                if with_mod:
                    block(0, order("M0 M1 M2 M3 w0 w1 w2 w3 w4 M4 M5 M6 M7 m0 w5 m1 w6 m2 m3 w7 m4 m5 m6 m7"), None)
                    with sp.Fori(1, BLOCKS - 1) as b:
                        block(b, order("w0 m0 w1 m1 w2 m2 m3 w3 w4 w5 m4 w6 m5 m6 w7 m7"), b)
                    with sp.Fori(BLOCKS - 1, BLOCKS) as b:
                        block(b, order("w0 w1 w2 w3 w4 w5 w6 w7"), b)
                else:
                    with sp.Fori(0, BLOCKS) as b:
                        block(b, order("w0 w1 w2 w3 w4 w5 w6 w7"), b)

            sp.dma_start(x_rows[:, 0:2, :], a["x"][0].rearrange("(t p) d -> p t d", p=P)).then_inc(s("x_in"), 16)
            sp.dma_start(x_rows[:, 2:4, :], a["ctx"][0].rearrange("(t p) d -> p t d", p=P)).then_inc(s("x_in"), 16)
            mod_b = a["mod_b"].rearrange("l (r c) -> (l r) c", c=P)
            rows = {"mod_b_lo": mod_b[0:96], "mod_b_hi": mod_b[96:192],
                    "c": a["c"].rearrange("o (r c) -> (o r) c", c=P),
                    "c_ctx": a["c_ctx"].rearrange("(r c) -> r c", c=P),
                    "final_g": a["final_g"].rearrange("(r c) -> r c", c=P),
                    "final_norm_w_2": a["final_norm_w_2"].rearrange("(r c) -> r c", c=P)}
            for name, (tile, row, n) in VEC_ROWS.items():
                src = rows[name] if name in rows else a[name].rearrange("l (r c) -> (l r) c", c=P)
                sp.dma_start(vec_rows[row:row + n, tile, :], src).then_inc(s("vec_in"), 16)
            for n, name in enumerate(["diff_lambda_q1", "diff_lambda_q2", "diff_lambda_k1", "diff_lambda_k2"]):
                sp.dma_start(lam_in[:, n, :], a[name]).then_inc(s("vec_in"), 16)
            sp.dma_start(dft[:, :, :], a["dft"].rearrange("(k p) c -> p k c", p=P)).then_inc(s("dft_in"), 16)

            for b in range(BLOCKS):
                if b == 2:
                    load_square("four0", a["fourier_w"][0])
                for u in range(MOD_UNITS):
                    load_mod(0, b, u, MOD_UNITS * b)
            load_mlp(0, True)
            w_qkv = a["diff_w_qkv"][0].rearrange("(k p) (three m c) -> m three p k c", p=P, three=3, c=2 * P)
            sp.wait_ge(s("mod_used"), 2 * BLOCKS * MOD_UNITS)
            sp.dma_start(rope[:, :, :], a["rope_diff"]).then_inc(s("rope_in"), 16)
            for h in range(HEADS // 2):
                for j in range(3):
                    load_unit(PLAN.at["diff"]["unit"] + 3 * h + j, [(whole, w_qkv[h, j])])
            load_square("diffo", a["diff_w_o"][0])
            sp.wait_ge(s("o_lo"), KT)
            load_mlp(1, True)
            sp.wait_ge(s("mod_used"), 3 * BLOCKS * MOD_UNITS)
            sp.dma_start(rope32[HALF:HALF + ROPE, :, :], a["rope_mla"]).then_inc(s("rope_in"), 16)
            down = a["mla_w_down"][0].rearrange("(k p) c -> p k c", p=P)
            u = PLAN.at["mlad"]["unit"]
            load_unit(u, [(whole, down[:, :, 0:Q_RANK])])
            load_unit(u + 1, [(lambda raw: raw[:, :, 0, :], down[:, :, Q_RANK:Q_RANK + KV_RANK])])
            load_unit(u + 2, [(lambda raw: raw[:, :, 0, 0:QD], down[:, :, Q_RANK + KV_RANK - NOPE:])])
            uq = a["mla_w_uq"][0].rearrange("(k p) (g h c) -> g k p h c", p=P, g=4, c=QD)
            ukv = a["mla_w_ukv"][0].rearrange("p (j h c) -> j p h c", j=2, c=P)
            u = PLAN.at["mla"]["unit"]

            def load_uq(u, g0):
                load_unit(u, [(lambda raw, j=j, k=k: raw[:, 4 * k:4 * k + 4, j, 0:QD], uq[g0 + j, k])
                              for j in range(2) for k in range(2)])

            load_uq(u, 0)
            load_unit(u + 1, [(lambda raw, j=j: raw[:, :, j, :], ukv[j]) for j in range(2)])
            load_uq(u + 2, 2)
            load_square("mlao", a["mla_w_o"][0])
            sp.wait_ge(s("mla_o_lo"), KT)
            load_mlp(2, True)
            sp.wait_ge(s("g_lo"), 3 * KT * BLOCKS)
            sp.dma_start(dft[:, :, :], a["dft"].rearrange("(k p) c -> p k c", p=P)).then_inc(s("dft_in"), 16)
            load_square("four3", a["fourier_w"][1])
            load_mlp(3, False)
            sp.wait_ge(s("mod_used"), DEPTH * BLOCKS * MOD_UNITS)
            small = [(meta_rows[:, :], a["meta_tokens_2"]),
                     (pool_w[:, :, :], a["pool_w_2"][0].rearrange("g c d -> c g d")),
                     (gate_up[:, :], a["w_gate_up_2"][0]),
                     (route_w[:, :, 0:4], a["w_router_group_2"][0].rearrange("(k p) c -> p k c", p=P)),
                     (route_w[:, :, 4:], a["w_router_expert_2"][0].rearrange("(k p) c -> p k c", p=P)),
                     (route_b[:, 0:4], a["b_router_group_2"]),
                     (route_b[:, 4:], a["b_router_expert_2"])]
            for dst, src in small:
                sp.dma_start(dst, src).then_inc(s("small_in"), 16)
            w_in = a["w_in_2"][0].rearrange("(k p) c -> p k c", p=P)
            u = PLAN.at["win"]["unit"]
            load_unit(u, [(lambda raw: raw[:, :, 0, 0:GATE_RANK], w_in[:, :, GATE_AT * P:])])
            for i in range(8):
                c = WIN_ORDER[1 + 2 * i] * P
                load_unit(u + 1 + i, [(whole, w_in[:, :, c:c + 2 * P])])
            load_square("wout", a["w_out_2"][0])
            w_gate = a["w_expert_gate_2"][0].rearrange("e (k p) c -> e p k c", p=P)
            w_up = a["w_expert_up_2"][0].rearrange("e (k p) c -> e p k c", p=P)
            w_down = a["w_expert_down_2"][0].rearrange("e (k p) c -> e p k c", p=P)

            def down_rows(raw):
                return raw[:, :, :, :].rearrange("p (k a) j c -> p k (a j c)", k=2)

            u = PLAN.at["moe"]["unit"]

            def load_experts(x, place, i=None):
                first = u + 3 * place - 1 if place else u
                step = 6 * EXPERT_TURNS
                load_unit(first, [(whole, w_gate[x])], i, step)
                load_unit(first + 1, [(whole, w_up[x])], i, step)
                if place:
                    load_unit(first + 2, [(down_rows, w_down[x - 1])], i, step)

            load_experts(0, 0)
            with sp.Fori(0, 3) as i:
                for j in range(EXPERT_TURNS):
                    load_experts(i * EXPERT_TURNS + (1 + j), 1 + j, i)
            for x in range(1 + 3 * EXPERT_TURNS, EXPERTS):
                load_experts(x, x)
            load_unit(u + 3 * EXPERTS - 1, [(down_rows, w_down[EXPERTS - 1])])
            out_v = out[0].rearrange("(t p) d -> p t d", p=P)
            for tt in range(2):
                sp.wait_ge(s("out_rows"), 2 * tt + 2)
                sp.dma_start(out_v[:, tt, :], out_rows[:, tt, :]).then_inc(s("out"), 16)
            sp.wait_ge(s("out"), 32)

        @block.gpsimd
        def _(pool):
            pool.memset(ident[:, :], 0.0).then_inc(s("const"), 1)
            pool.memset(ones[:, :], 1.0).then_inc(s("const"), 1)
            pool.memset(eps[:, :], EPS).then_inc(s("const"), 1)
            pool.memset(silu_c[:, :, :], 0.0).then_inc(s("const"), 1)
            pool.wait_ge(s("const"), 4)
            pool.affine_select(out=ident[:, :], in_=ident[:, :], compare_op=ALU.not_equal, fill=1.0,
                               base=0, pattern=[[-1, P]], channel_multiplier=1).then_inc(s("const"), 1)

            for i in range(2):
                pool.wait_ge(s("sc_in"), i + 1)
                pool.affine_select(out=sc[:, 2 * i:2 * i + 2, :, :].rearrange("p h n c -> p (h n) c"),
                                   in_=sc[:, 2 * i:2 * i + 2, :, :].rearrange("p h n c -> p (h n) c"),
                                   compare_op=ALU.is_ge, fill=0.0, base=0, pattern=[[0, 8], [1, CHUNK]],
                                   channel_multiplier=-1).then_inc(s("sc_masked"), 1)

        @block.scalar
        def _(act):
            def split_hi(n, i=None, tiles=0, raws=0):
                if isinstance(i, int):
                    n, i = n + i * MLP_TILES, None
                unit, place, _ = PLAN.panels[n]
                _, slot, value = PLAN.units[unit]
                act.wait_ge(s(f"raw_in{slot}"), later(value, i, raws))
                if n >= RING:
                    name, freed = PLAN.panels[n - RING][2]
                    act.wait_ge(s(name), later(freed, i, tiles))
                act.activation(W_hi[n % RING][:, :].rearrange("p (k c) -> p k c", c=P),
                               w_raw[slot][:, :, place, :], ACT.Copy).then_inc(s("w_hi"), 1)

            def square(name, n_cols, k, x_done=None):
                ni, c = NORM_AT[name], slice(0, n_cols)
                if x_done is not None:
                    act.wait_ge(s("x_done"), x_done)
                if k >= 2:
                    act.wait_ge(s("sq_added"), KT * ni + k - 1)
                elif ni:
                    act.wait_ge(s("h"), KT * ni)
                act.activation(norm_buf[k % 2][:, c], X[:, k, c], ACT.Square).then_inc(s("sq"), 1)

            def root(name, n_cols):
                ni, c = NORM_AT[name], slice(0, n_cols)
                act.wait_ge(s("sum"), ni + 1)
                act.activation(norm_buf[3][:, c], sum_ps[:, c], ACT.Sqrt, bias=eps[:, 0:1],
                               scale=1.0 / D).then_inc(s("root"), 1)

            def apply(name, n_cols, segments, pairs):
                ni, c = NORM_AT[name], slice(0, n_cols)
                for k in range(KT):
                    act.wait_ge(s("t"), KT * ni + k + 1)
                    if pairs is not None and k >= 2:
                        act.wait_ge(s("h_lo"), KT * pairs + k - 1)
                    for c0, cn, scale, shift, *to in segments:
                        d0 = to[0] if to else c0
                        dst = norm_buf[4 + k % 2][:, d0:d0 + cn] if pairs is not None else X[:, k, c0:c0 + cn]
                        ins = act.activation(dst, norm_buf[k % 2][:, c0:c0 + cn], ACT.Identity,
                                             bias=shift(k) if shift else 0.0, scale=scale(k))
                    ins.then_inc(s("h"), 1)
                    if pairs is not None:
                        act.wait_ge(s("h"), KT * ni + k + 1)
                        act.activation(H_hi[:, k, c], norm_buf[4 + k % 2][:, c], ACT.Copy).then_inc(s("h_hi"), 1)

            def norm(name, n_cols, segments, pairs):
                for k in range(KT):
                    square(name, n_cols, k)
                root(name, n_cols)
                apply(name, n_cols, segments, pairs)

            def mod_apply(name, layer, n_cols):
                m = mod[layer % 2]
                mix = name.startswith("mix")
                act.wait_ge(s("scales_mix" if mix else "scales_mlp"), layer + 1)
                shift_at = 0 if mix else 3 * KT
                scales = scale_mix if mix else scale_mlp
                segs = [(st * LAT, LAT, lambda k, st=st: scales[:, k, st:st + 1],
                         lambda k, st=st: m[:, shift_at + k, st:st + 1]) for st in range(n_cols // LAT)]
                apply(name, n_cols, segs, SPLIT_AT[name])

            def mod_norm(name, layer, n_cols):
                root(name, n_cols)
                mod_apply(name, layer, n_cols)

            def copy_mod_rows(g, i=None):
                act.wait_ge(s("mod_used"), later(MOD_UNITS * (g + 1), i, MOD_UNITS))
                act.activation(mod_rows[:, :], mod_ps[:, 0:MOD_PART], ACT.Copy).then_inc(s("mod_rows_in"), 1)

            def output_splits(name, norm_name, n_cols):
                for m in range(KT):
                    split_hi(PLAN.at[name]["panel"] + m + AHEAD)
                    if m:
                        square(norm_name, n_cols, m - 1, X_AT[name] + m)
                square(norm_name, n_cols, KT - 1, X_AT[name] + KT)

            def fourier(name, streams):
                t = PLAN.at[name]["tile"]
                n_tok = 2 * streams
                for g in range(4):
                    if name == "four0" and g == 3:
                        for n in range(AHEAD):
                            split_hi(PLAN.at[name]["panel"] + n)
                    for tt in range(n_tok):
                        act.wait_ge(s("tile_done"), t + 1)
                        act.activation(G_hi[:, 4 * (g % 2) + tt, 0:256], bank[t % BANKS][:, 0:256], ACT.Copy)
                        act.activation(G_hi[:, 4 * (g % 2) + tt, 256:512], bank[t % BANKS][:, 256:512],
                                       ACT.Copy, scale=-1.0).then_inc(s("four_hi"), 1)
                        t += 1
                    if name == "four0" and g % 2:
                        copy_mod_rows(2 + g // 2)
                    for m in range(2):
                        act.wait_ge(s("tile_done"), t + 1)
                        act.activation(H_hi[:, 2 * g + m, 0:streams * LAT], bank[t % BANKS][:, 0:streams * LAT],
                                       ACT.Copy).then_inc(s("four_hi"), 1)
                        t += 1

            def mlp(layer, n_cols, with_mod, next_norm):
                at0 = PLAN.at[f"mlp{layer}"]
                p0, t0 = at0["panel"], at0["tile"]
                h0 = KT * BLOCKS * layer
                def hidden_block(b, last=False):
                    for j in range(MLP_TILES):
                        split_hi(p0 + j + AHEAD, b, MLP_TILES, 2 * 16)
                        if with_mod and not last and j == MOD_ROWS_AT:
                            copy_mod_rows(BLOCKS * (layer + 1) + 1, b)
                        if last and j > KT:
                            square(*next_norm, j - KT - 1, X_AT[f"mlp{layer}"] + KT * (BLOCKS - 2) + j)
                        if j < KT:
                            act.wait_ge(s("tile_done"), later(t0 + j + 1, b, MLP_TILES))
                            if layer or j >= 2:
                                act.wait_ge(s("g_sq"), later(h0 + j - 1, b, KT))
                            act.activation(relu[j % 2][:, 0:n_cols], bank[(t0 + j) % BANKS][:, 0:n_cols],
                                           ACT.Relu).then_inc(s("relu"), 1)
                            act.wait_ge(s("relu"), later(h0 + j + 1, b, KT))
                            act.activation(G_hi[:, j, 0:n_cols], relu[j % 2][:, 0:n_cols],
                                           ACT.Square).then_inc(s("g_hi"), 1)

                if with_mod:
                    copy_mod_rows(BLOCKS * (layer + 1))
                with act.Fori(0, BLOCKS - 1) as b:
                    hidden_block(b)
                hidden_block(BLOCKS - 1, True)
                square(*next_norm, KT - 1, X_AT[f"mlp{layer}"] + KT * BLOCKS)

            act.wait_ge(s("tile_done"), 1)
            for v in range(VEC_TILES):
                ins = act.activation(vec[:, v, 0:VEC_COUNT[v]], bank[0][:, v * P:v * P + VEC_COUNT[v]], ACT.Copy)
            ins.then_inc(s("vec"), 1)
            act.wait_ge(s("vec"), 1)
            act.activation(silu_t[:, :, :], vcols("c", 0, 16).rearrange("p (s k) -> p s k", s=2),
                           ACT.Exp, scale=-1.0).then_inc(s("silu_exp"), 1)
            act.wait_ge(s("lam"), 2)
            act.activation(lam_row[:, 2:4], lam_row[:, 0:2], ACT.Exp).then_inc(s("lam_exp"), 1)
            t0 = PLAN.at["xin"]["tile"]
            for k in range(KT):
                act.wait_ge(s("tile_done"), t0 + k + 1)
                act.activation(X[:, k, :], bank[(t0 + k) % BANKS][:, :], ACT.Copy).then_inc(s("x_cols"), 1)
            act.wait_ge(s("dft_in"), 16)
            act.activation(dft_hi[:, :, :], dft[:, :, :], ACT.Copy).then_inc(s("dft_hi"), 1)
            act.wait_ge(s("x_cols"), KT)
            for k in range(KT):
                square("mix0", TOK, k)
            copy_mod_rows(0)
            root("mix0", TOK)
            copy_mod_rows(1)
            mod_apply("mix0", 0, TOK)
            fourier("four0", 2)
            output_splits("four0", "mlp0", TOK)
            mod_norm("mlp0", 0, TOK)
            mlp(0, TOK, True, ("mix1", TOK))
            def exps(h):
                def scaled(qt):
                    n = TOK if qt < 2 else CTX
                    act.wait_ge(s("z_mix"), 4 * h + qt + 1)
                    act.activation(p_raw[qt % 2][1][:, 0:n], p_raw[qt % 2][1][:, 0:n], ACT.Identity,
                                   scale=z_mix[:, 2 * qt + 1:2 * qt + 2]).then_inc(s("p_scaled"), 1)

                for qt in range(4):
                    n = TOK if qt < 2 else CTX
                    for j in range(2):
                        i = 2 * qt + j
                        act.wait_ge(s("neg_max"), 8 * h + i + 1)
                        if 4 * h + qt >= 2:
                            act.wait_ge(s("p_mix"), 4 * h + qt - 1)
                        x = PLAN.at["diff"]["aux"] + AUX_AT["diff", "score", h, i]
                        act.activation(p_raw[qt % 2][j][:, 0:n], aux[x % AUX][:, 0:n], ACT.Exp,
                                       bias=neg_max[:, i:i + 1], accum_out=z[:, i:i + 1]).then_inc(s("p_exp"), 1)
                    if qt:
                        scaled(qt - 1)
                scaled(3)

            def diff_attention():
                t0, p0, x0 = PLAN.at["diff"]["tile"], PLAN.at["diff"]["panel"], PLAN.at["diff"]["aux"]
                for turn in range(HEADS + 1):
                    h = turn - 1
                    if h >= 0:
                        exps(h)
                    if turn < HEADS:
                        for j, (dst, scale) in enumerate(((q_f, HALF ** -0.5), (k_f, 1.0))):
                            t = t0 + 3 * turn + j
                            split_hi(p0 + 3 * turn + j + AHEAD)
                            act.wait_ge(s("tile_done"), t + 1)
                            if turn:
                                act.wait_ge(s("qk_lo"), 2 * turn - 1 + j)
                            act.activation(dst[:, :], bank[t % BANKS][:, :], ACT.Copy, scale=scale).then_inc(s("qkv"), 1)
                        for j, (dst, src) in enumerate(((q_hi, q_f), (k_hi, k_f))):
                            act.wait_ge(s("roped"), 2 * turn + j + 1)
                            act.activation(dst[:, :], src[:, :], ACT.Copy).then_inc(s("qk_hi"), 1)
                    if h >= 0:
                        for i in range(3):
                            x = x0 + AUX_AT["diff", "turn_p", h, i]
                            act.wait_ge(s("aux_done"), x + 1)
                            act.activation(pt_hi[:, 2 * i:2 * i + 2, :].rearrange("p a b -> p (a b)"), aux[x % AUX][:, :],
                                           ACT.Copy).then_inc(s("pt_hi"), 1)
                    if turn < HEADS:
                        t = t0 + 3 * turn + 2
                        split_hi(p0 + 3 * turn + 2 + AHEAD)
                        act.wait_ge(s("tile_done"), t + 1)
                        act.wait_ge(s("qk_lo"), 2 * turn + 1)
                        act.activation(v_f[:, :], bank[t % BANKS][:, :], ACT.Copy).then_inc(s("qkv"), 1)
                    if h >= 0:
                        x = x0 + AUX_AT["diff", "pv", h, 0]
                        act.wait_ge(s("aux_done"), x + 1)
                        act.activation(o_f[:, :], aux[x % AUX][:, :], ACT.Copy).then_inc(s("o_out"), 1)
                        act.wait_ge(s("o_out"), h + 1)
                        act.activation(o_sq[:, :], o_f[:, :], ACT.Square).then_inc(s("o_sq"), 1)
                    if turn < HEADS:
                        x = x0 + AUX_AT["diff", "turn_v", turn, 0]
                        act.wait_ge(s("aux_done"), x + 1)
                        act.activation(v_hi[:, :, :].rearrange("p a b -> p (a b)"), aux[x % AUX][:, :],
                                       ACT.Copy).then_inc(s("v_hi"), 1)
                    if h >= 0:
                        x = x0 + AUX_AT["diff", "square", h, 0]
                        act.wait_ge(s("aux_done"), x + 1)
                        act.activation(o_inv[:, :], aux[x % AUX][:, :], ACT.Sqrt, bias=eps[:, 0:1],
                                       scale=1.0 / P).then_inc(s("o_root"), 1)
                        act.wait_ge(s("o_t"), h + 1)
                        act.activation(o_g[:, :], o_t[:, :], ACT.Identity,
                                       scale=subln[:, 0:1]).then_inc(s("o_g"), 1)
                        act.wait_ge(s("o_g"), h + 1)
                        act.activation(G_hi[:, h, :], o_g[:, :], ACT.Copy).then_inc(s("o_hi"), 1)

            mod_norm("mix1", 1, TOK)
            diff_attention()
            output_splits("diffo", "mlp1", TOK)
            mod_norm("mlp1", 1, TOK)
            mlp(1, TOK, True, ("mix2", TOK))
            def down_outputs():
                t0, p0 = PLAN.at["mlad"]["tile"], PLAN.at["mlad"]["panel"]
                rotary = slice(HALF, HALF + ROPE)
                outs = [cq_f[:, 0, :], cq_f[:, 1, :], ckv_f[:, :], kv_f[rotary, :]]
                for j, dst in enumerate(outs):
                    split_hi(p0 + j + AHEAD)
                    b = bank[(t0 + j) % BANKS]
                    act.wait_ge(s("tile_done"), t0 + j + 1)
                    src = b[:, 0:LAT] if j < 2 else b[:, :] if j == 2 else b[rotary, :]
                    act.activation(dst, src, ACT.Copy).then_inc(s("down_out"), 1)
                act.wait_ge(s("down_out"), 3)
                act.activation(norm_buf[0][:, :], cq_f[:, :, :].rearrange("p a b -> p (a b)"), ACT.Square).then_inc(s("down_sq"), 1)
                act.activation(norm_buf[1][:, :], ckv_f[:, :], ACT.Square).then_inc(s("down_sq"), 1)
                act.wait_ge(s("down_sum"), 1)
                act.activation(norm_buf[2][:, 0:LAT], pv_ps[:, 0:LAT], ACT.Sqrt, bias=eps[:, 0:1],
                               scale=1.0 / Q_RANK).then_inc(s("down_root"), 1)
                act.wait_ge(s("down_sum"), 2)
                act.activation(norm_buf[3][:, :], sum_ps[:, :], ACT.Sqrt, bias=eps[:, 0:1],
                               scale=1.0 / KV_RANK).then_inc(s("down_root"), 1)
                act.wait_ge(s("rope32_done"), 1)
                act.activation(mk_hi[rotary, :], kv_f[rotary, :], ACT.Copy).then_inc(s("key_hi"), 1)
                act.wait_ge(s("down_t"), 1)
                for k in range(2):
                    ins = act.activation(cq_f[:, k, :], norm_buf[4][:, k * LAT:(k + 1) * LAT], ACT.Identity,
                                         scale=vcol("mla_q_norm_g", k))
                ins.then_inc(s("down_g"), 1)
                act.wait_ge(s("down_g"), 1)
                act.activation(cq_hi[:, :, :], cq_f[:, :, :], ACT.Copy).then_inc(s("down_hi"), 1)
                act.wait_ge(s("down_t"), 2)
                act.activation(ckv_f[:, :], norm_buf[5][:, :], ACT.Identity,
                               scale=vcol("mla_kv_norm_g")).then_inc(s("down_g"), 1)
                act.wait_ge(s("down_g"), 2)
                act.activation(ckv_hi[:, :], ckv_f[:, :], ACT.Copy).then_inc(s("down_hi"), 1)

            def mla_attention():
                t0, p0, x0 = PLAN.at["mla"]["tile"], PLAN.at["mla"]["panel"], PLAN.at["mla"]["aux"]
                split_after = {0: [3], 3: [4], 7: [5, 6], 11: [], 15: [7]}
                for turn in range(MLA_HEADS + 1):
                    h = turn - 1
                    if h >= 0:
                        for i in range(2):
                            x = x0 + AUX_AT["mla", "score", h, i]
                            act.wait_ge(s("mla_max"), 2 * h + i + 1)
                            if h:
                                act.wait_ge(s("mla_mix"), 2 * h + i - 1)
                            act.activation(mp_raw[i][:, :], aux[x % AUX][:, :], ACT.Exp, bias=m_max[:, i:i + 1],
                                           accum_out=m_z[:, i:i + 1]).then_inc(s("mla_exp"), 1)
                    if turn < MLA_HEADS:
                        t = t0 + 2 * turn
                        act.wait_ge(s("tile_done"), t + 1)
                        if turn:
                            act.wait_ge(s("mla_q_lo"), turn)
                        act.activation(mq_f[0:QD, :], bank[t % BANKS][0:QD, 0:LAT], ACT.Copy,
                                       scale=QD ** -0.5).then_inc(s("mla_qkv"), 1)
                        act.wait_ge(s("tile_done"), t + 2)
                        act.wait_ge(s("mla_k_lo"), turn + 1)
                        act.activation(kv_f[:, :], bank[(t + 1) % BANKS][:, :], ACT.Copy).then_inc(s("mla_qkv"), 1)
                        act.wait_ge(s("rope32_done"), turn + 2)
                        act.activation(mq_hi[0:QD, :], mq_f[0:QD, :], ACT.Copy).then_inc(s("mla_q_hi"), 1)
                        act.wait_ge(s("mla_qkv"), 2 * turn + 2)
                        act.activation(mk_hi[0:NOPE, :], kv_f[0:NOPE, :], ACT.Copy).then_inc(s("mla_k_hi"), 1)
                        for n in split_after.get(turn, []):
                            split_hi(p0 + n)
                        x = x0 + AUX_AT["mla", "turn_v", turn, 0]
                        j = turn % 2
                        act.wait_ge(s("aux_done"), x + 1)
                        act.activation(mv_hi[j][:, :, j * HALF:(j + 1) * HALF],
                                       aux[x % AUX][:, :].rearrange("p (t c) -> p t c", c=P)[:, :, HALF:P],
                                       ACT.Copy).then_inc(s("mla_v_hi"), 1)
                    if h >= 0:
                        for i in range(2):
                            x = x0 + AUX_AT["mla", "turn_p", h, i]
                            act.wait_ge(s("aux_done"), x + 1)
                            act.activation(mpt_hi[:, 2 * i:2 * i + 2, :].rearrange("p a b -> p (a b)"), aux[x % AUX][:, :],
                                           ACT.Copy).then_inc(s("mla_pt_hi"), 1)
                        if h % 2:
                            m = h // 2
                            act.wait_ge(s("pv_done"), m + 1)
                            act.activation(G_hi[:, m, 0:LAT], pv_ps[:, (m % 2) * LAT:(m % 2 + 1) * LAT],
                                           ACT.Copy).then_inc(s("mla_o_hi"), 1)
                split_hi(p0 + 8)

            mod_norm("mix2", 2, TOK)
            down_outputs()
            mla_attention()
            output_splits("mlao", "mlp2", LAT)
            mod_norm("mlp2", 2, LAT)
            mlp(2, LAT, True, ("mix3", LAT))
            act.wait_ge(s("dft_in"), 32)
            act.activation(dft_hi[:, :, :], dft[:, :, :], ACT.Copy).then_inc(s("dft_hi"), 1)
            mod_norm("mix3", 3, LAT)
            fourier("four3", 1)
            output_splits("four3", "mlp3", LAT)
            mod_norm("mlp3", 3, LAT)
            mlp(3, LAT, False, ("final", LAT))
            root("final", LAT)
            apply("final", LAT, [(0, LAT, lambda k: vcol("final_g", k), None)], None)
            act.wait_ge(s("tile_done"), PLAN.at["meta"]["tile"] + 1)
            b = bank[PLAN.at["meta"]["tile"] % BANKS]
            act.activation(X[:, :, LAT:TOK2], b[:, 0:KT * META].rearrange("p (k t) -> p k t", t=META),
                           ACT.Copy).then_inc(s("meta_cols"), 1)
            act.wait_ge(s("meta_cols"), 1)
            w = lambda k: vcol("norm_mix_w_2", k)
            norm("mix_2", TOK2, [(0, LAT, w, None, META), (LAT, META, w, None, 0)], SPLIT_AT["mix_2"])

            def projections():
                t0, p0 = PLAN.at["win"]["tile"], PLAN.at["win"]["panel"]
                for i, col in enumerate(WIN_ORDER):
                    split_hi(p0 + i + AHEAD)
                    act.wait_ge(s("tile_done"), t0 + i + 1)
                    rows = slice(0, GATE_RANK if col == GATE_AT else P)
                    act.activation(proj[rows, col, :], bank[(t0 + i) % BANKS][rows, 0:TOK2], ACT.Copy).then_inc(s("proj"), 1)
                    if i == 3:
                        gates()
                    if i == 10:
                        turned_values()
                    if i == 14:
                        turned_keys()

            def mix_tile(what, i):
                n = MIX_AT[what, i]
                act.wait_ge(s("mix_done_ps"), n + 1)
                return mix_ps[n % 4]

            def gates():
                for j in range(2):
                    ps = mix_tile("gate", j)
                    act.activation(z_f[:, j, :], ps[:, 0:TOK2], ACT.Identity, bias=vcol("b_gate_2", j)).then_inc(s("z_in"), 1)
                act.wait_ge(s("z_in"), 2)
                act.activation(z_abs[:, :, :], z_f[:, :, :], ACT.Abs).then_inc(s("z_step"), 1)
                act.wait_ge(s("z_step"), 1)
                act.activation(z_abs[:, :, :], z_abs[:, :, :], ACT.Exp, scale=-1.0).then_inc(s("z_step"), 1)
                act.wait_ge(s("z_step"), 2)
                act.activation(z_abs[:, :, :], z_abs[:, :, :], ACT.Ln, bias=1.0).then_inc(s("z_ln"), 1)
                act.wait_ge(s("b_last"), 1)
                act.activation(e_pos[:, :, :], b_cum[:, :, :], ACT.Exp, scale=1.0 / 16)
                act.activation(e_neg[:, :, :], b_cum[:, :, META:], ACT.Exp, scale=-1.0 / 16)
                for j in range(2):
                    for n in range(4):
                        c0, cn = CHUNKS[n]
                        act.activation(e_end[:, j, c0:c0 + cn], b_cum[:, j, c0:c0 + cn], ACT.Exp,
                                       bias=b_last[:, j, n:n + 1], scale=-1.0 / 16)
                act.activation(decay[:, :, :], b_last[:, :, :], ACT.Exp).then_inc(s("e_end"), 1)

            def turned_values():
                for i in range(5):
                    ps = mix_tile("turn_v", i)
                    if i < 4:
                        act.activation(v_rows[:, i, :, :].rearrange("p n c -> p (n c)"), ps[0:CHUNK, :], ACT.Copy).then_inc(s("v_rows"), 1)
                    else:
                        act.activation(v_rows_m[:, :, :].rearrange("p n c -> p (n c)"), ps[0:META, :], ACT.Copy).then_inc(s("v_rows"), 1)

            def turned_keys():
                for j in range(2):
                    ps = mix_tile("turn_k", j)
                    act.activation(k_rows[:, j, :, :].rearrange("p n c -> p (n c)"), ps[0:CHUNK, 0:3 * P], ACT.Copy)
                    act.activation(k_rows_m[:, j, :], ps[0:META, 3 * P:4 * P], ACT.Copy).then_inc(s("k_rows"), 1)

            def mixer_rest():
                act.wait_ge(s("proj"), 17)
                act.activation(r_silu[:, :, :], proj[:, R_AT:R_AT + 4, META:], ACT.Exp, scale=-1.0).then_inc(s("r_exp"), 1)
                for i in range(2):
                    ps = mix_tile("pool", i)
                    for g in range(2):
                        ins = act.activation(y_f[:, 2 * i + g, :], ps[:, g * LAT:(g + 1) * LAT], ACT.Identity,
                                             scale=vcol("pool_scale_2", 2 * i + g))
                    ins.then_inc(s("pool_in"), 1)
                act.wait_ge(s("pool_in"), 2)
                act.activation(Y_hi[:, 0:4, :], y_f[:, :, :], ACT.Copy).then_inc(s("y_hi"), 1)
                for i in range(2):
                    ps = mix_tile("score", i)
                    act.activation(sc[:, 2 * i:2 * i + 2, :, :].rearrange("p h n c -> p (h n c)"), ps[0:CHUNK, :],
                                   ACT.Copy).then_inc(s("sc_in"), 1)
                for i in range(2):
                    ps = mix_tile("out", i)
                    act.activation(go_f[:, 2 * i:2 * i + 2, :], ps[:, :].rearrange("p (h c) -> p h c", h=2), ACT.Copy).then_inc(s("go_in"), 1)
                act.wait_ge(s("go_in"), 2)
                act.activation(go_sq, go_f[:, :, :], ACT.Square).then_inc(s("go_sq"), 1)
                for i in range(2):
                    ps = mix_tile("square", i)
                    act.activation(go_inv[:, 2 * i:2 * i + 2, :], ps[:, :].rearrange("p (h c) -> p h c", h=2), ACT.Sqrt,
                                   bias=eps[:, 0:1], scale=1.0 / P).then_inc(s("go_root"), 1)
                act.wait_ge(s("go_t"), 1)
                act.activation(y_f[:, :, :], go_f[:, :, :], ACT.Identity, scale=vcol("gla_norm_w_2")).then_inc(s("go_g"), 1)
                act.wait_ge(s("go_g"), 1)
                act.activation(Y_hi[:, 4:8, :], y_f[:, :, :], ACT.Copy).then_inc(s("y_hi"), 1)

            projections()
            mixer_rest()
            output_splits("wout", "ffn_2", LAT)
            root("ffn_2", LAT)
            apply("ffn_2", LAT, [(0, LAT, lambda k: vcol("norm_ffn_w_2", k), None)], SPLIT_AT["ffn_2"])

            def router():
                act.wait_ge(s("logit_done"), 1)
                act.activation(logits[:, :, :], psum[2][:, 0:2 * (4 + EXPERTS)].rearrange("p (t c) -> p t c", t=2),
                               ACT.Copy).then_inc(s("logits"), 1)
                for i in range(2):
                    act.wait_ge(s("shifted"), i + 1)
                    act.activation(r4[4 * i + 1][:, :, :], r4[4 * i][:, :, :], ACT.Exp).then_inc(s("route_exp"), 1)

            def gated(x, i=None, step=0):
                done = 6 * x + 2
                act.wait_ge(s("expert_done"), later(done, i, 6 * step))
                if x:
                    act.wait_ge(s("e_hid"), later(x, i, step))
                act.activation(e_exp[:, :, :].rearrange("p m c -> p (m c)"), psum[3 * (x % 2)][:, :], ACT.Exp,
                               scale=-1.0).then_inc(s("e_exp"), 1)
                act.wait_ge(s("e_hid"), later(x + 1, i, step))
                act.activation(E_hi[x % 2][:, :, :], e_hid[x % 2][:, :, :], ACT.Copy).then_inc(s("e_hi"), 1)

            p0 = PLAN.at["moe"]["panel"]

            def expert_split(n, i=None):
                if n < 6 * EXPERTS:
                    step = 6 * EXPERT_TURNS
                    split_hi(p0 + n, i, step, 16 * 3)

            def expert_turn(x, i=None):
                n = 6 * x - 2 if x else 0
                for j in range(4):
                    expert_split(n + j + AHEAD, i)
                gated(x, i, EXPERT_TURNS)
                if x:
                    for j in range(4, 6):
                        expert_split(n + j + AHEAD, i)

            router()
            expert_turn(0)
            with act.Fori(0, 3) as i:
                for j in range(EXPERT_TURNS):
                    expert_turn(1 + j, i)
            for x in range(1 + 3 * EXPERT_TURNS, EXPERTS):
                expert_turn(x)
            act.wait_ge(s("y_added"), 1)
            norm("final_2", LAT, [(0, LAT, lambda k: vcol("final_norm_w_2", k), None)], None)
            for n in range(4):
                act.wait_ge(s("out_turned"), n + 1)
                act.activation(out_rows[:, n // 2, 512 * (n % 2):512 * (n % 2 + 1)], psum[n][:, :], ACT.Copy).then_inc(s("out_rows"), 1)

        @block.tensor
        def _(pe):
            def split_product(dst, w_hi, w_lo, r_hi, r_lo, start, stop):
                pe.matmul(dst, w_hi, r_hi, start=start, stop=False)
                pe.matmul(dst, w_hi, r_lo, start=False, stop=False)
                return pe.matmul(dst, w_lo, r_hi, start=False, stop=stop)

            def wait_bank(t, i=None, step=KT):
                if t >= BANKS:
                    name, value = PLAN.tiles[t - BANKS]
                    pe.wait_ge(s(name), later(value, i, step))

            def panel_product(n, t, r_hi, r_lo, c, i=None, ready=None, rows=P):
                if isinstance(i, int):
                    n, t, i = n + i * MLP_TILES, t + i * MLP_TILES, None
                pe.wait_ge(s("panel_ready"), later(n + 1, i, MLP_TILES))
                wait_bank(t, i)
                dst = bank[t % BANKS][0:rows, 0:c.stop - c.start]
                for k in range(KT):
                    if ready:
                        ready(k)
                    w = slice(k * P, k * P + rows)
                    ins = split_product(dst, W_hi[n % RING][:, w], W_lo[n % RING][:, w], r_hi[:, k, c],
                                        r_lo[:, k, c], k == 0, k == KT - 1)
                ins.then_inc(s("tile_done"), 1)

            def first_products(panels, t, r_hi, r_lo, c, ready, rows=P):
                for j, n in enumerate(panels):
                    pe.wait_ge(s("panel_ready"), n + 1)
                    wait_bank(t + j)
                for k in range(KT):
                    ready(k)
                    for j, n in enumerate(panels):
                        m = rows[j] if isinstance(rows, list) else rows
                        cols = c[j] if isinstance(c, list) else c
                        w = slice(k * P, k * P + m)
                        ins = split_product(bank[(t + j) % BANKS][0:m, 0:cols.stop], W_hi[n % RING][:, w], W_lo[n % RING][:, w],
                                            r_hi[:, k, cols], r_lo[:, k, cols], k == 0, k == KT - 1)
                        if k == KT - 1:
                            ins.then_inc(s("tile_done"), 1)

            def mod_unit(u, g, i=None):
                if u == 0 and (g or i is not None):
                    pe.wait_ge(s("mod_read"), later(g, i, 1))
                uses = MOD_UNITS // MOD_RING
                pe.wait_ge(s(f"mod_in{u % MOD_RING}"), later(16 * (uses * g + u // MOD_RING + 1), i, 16 * uses))
                for j in range(4):
                    ins = pe.matmul(mod_ps[32 * j:32 * (j + 1), 0:MOD_PART], silu_c[:, u, :],
                                    mod_raw[u % MOD_RING][:, j * MOD_PART:(j + 1) * MOD_PART],
                                    start=(u == 0), stop=(u == MOD_UNITS - 1))
                ins.then_inc(s("mod_used"), 1)

            def turn_mod(g, i=None):
                pe.wait_ge(s("mod_rows_in"), later(g + 1, i, 1))
                for j in range(MOD_PART // P):
                    ins = pe.transpose(mod_ps[:, j * P:(j + 1) * P], mod_rows[:, j * P:(j + 1) * P], ident[:, :])
                ins.then_inc(s("mod_turned"), 1)

            def mod_block(g):
                for u in range(MOD_UNITS):
                    mod_unit(u, g)
                turn_mod(g)

            def norm_sum(name, n_cols):
                ni = NORM_AT[name]
                pe.wait_ge(s("sq_added"), KT * ni + KT)
                pe.matmul(sum_ps[:, 0:n_cols], ones[:, :], norm_buf[2][:, 0:n_cols], start=True,
                          stop=True).then_inc(s("sum"), 1)

            def h_ready(name):
                split = SPLIT_AT[name]
                return lambda k: pe.wait_ge(s("h_lo"), KT * split + k + 1)

            def fourier(name, streams, norm_name):
                t = PLAN.at[name]["tile"]
                f0 = 0 if name == "four0" else 24
                n_tok = 2 * streams
                for g in range(4):
                    for tt in range(n_tok):
                        wait_bank(t)
                        if g >= 2:
                            pe.wait_ge(s("tile_done"), t - tt - (n_tok + 2))
                        tok = slice(tt * P, (tt + 1) * P)
                        for k in range(2):
                            h_ready(norm_name)(2 * g + k)
                            ins = split_product(bank[t % BANKS][:, :], H_hi[:, 2 * g + k, tok], H_lo[:, 2 * g + k, tok],
                                                dft_hi[:, k, :], dft_lo[:, k, :], k == 0, k == 1)
                        ins.then_inc(s("tile_done"), 1)
                        if name == "four0":
                            mod_unit((4 * g + tt) % MOD_UNITS, 2 + g // 2)
                        t += 1
                    for m in range(2):
                        wait_bank(t)
                        for st in range(streams):
                            for q in range(4):
                                part, k = q // 2, q % 2
                                if m == 0:
                                    pe.wait_ge(s("four_lo"), f0 + (n_tok + 2) * g + 2 * st + k + 1)
                                col = slice(part * 256 + m * P, part * 256 + (m + 1) * P)
                                row = 4 * (g % 2) + 2 * st + k
                                trig = slice(part * 256, part * 256 + 256)
                                ins = split_product(bank[t % BANKS][:, st * LAT:(st + 1) * LAT],
                                                    G_hi[:, row, col], G_lo[:, row, col], dft_hi[:, k, trig],
                                                    dft_lo[:, k, trig], q == 0, q == 3)
                        ins.then_inc(s("tile_done"), 1)
                        t += 1
                    if name == "four0" and g % 2:
                        turn_mod(2 + g // 2)
                for m in range(KT):
                    n = PLAN.at[name]["panel"] + m
                    panel_product(n, t + m, H_hi, H_lo, slice(0, streams * LAT),
                                  ready=lambda k: pe.wait_ge(s("four_lo"), f0 + (n_tok + 2) * (k // 2) + n_tok + k % 2 + 1))

            def mlp(layer, n_cols, with_mod):
                at0 = PLAN.at[f"mlp{layer}"]
                p0, t0 = at0["panel"], at0["tile"]
                h0 = KT * BLOCKS * layer
                ready = h_ready(f"mlp{layer}")
                for u in range(MOD_UNITS):
                    if u == MOD_UNITS // 2 - 1:
                        norm_sum(f"mlp{layer}", n_cols)
                    if with_mod:
                        mod_unit(u, BLOCKS * (layer + 1))

                def hidden_block(b, first=False, last=False):
                    if first:
                        first_products([p0, p0 + 1], t0, H_hi, H_lo, slice(0, n_cols), ready)
                        if with_mod:
                            turn_mod(BLOCKS * (layer + 1))
                    for j in range(MLP_TILES):
                        if j < KT:
                            if not first or j >= 2:
                                panel_product(p0 + j, t0 + j, H_hi, H_lo, slice(0, n_cols), b)
                        else:
                            panel_product(p0 + j, t0 + j, G_hi, G_lo, slice(0, n_cols), b,
                                          (lambda k: pe.wait_ge(s("g_lo"), later(h0 + k + 1, b, KT))) if j == KT else None)
                        if with_mod and not last and j in MOD_AFTER:
                            mod_unit(MOD_AFTER[j], BLOCKS * (layer + 1) + 1, b)
                        if with_mod and not last and j == MOD_TURN_AT:
                            turn_mod(BLOCKS * (layer + 1) + 1, b)

                hidden_block(0, first=True)
                with pe.Fori(1, BLOCKS - 1) as b:
                    hidden_block(b)
                hidden_block(BLOCKS - 1, last=True)

            pe.wait_ge(s("const"), 5)
            pe.wait_ge(s("vec_in"), 16 * (len(VEC_ROWS) + 4))
            for v in range(VEC_TILES):
                ins = pe.transpose(bank[0][:, v * P:v * P + VEC_COUNT[v]], vec_rows[0:VEC_COUNT[v], v, :],
                                   ident[0:VEC_COUNT[v], 0:VEC_COUNT[v]])
            ins.then_inc(s("tile_done"), 1)
            pe.wait_ge(s("lam"), 3)
            pe.matmul(bank[1][:, 0:2], ones[0:1, :], lam_row[:, 0:2], start=True, stop=True).then_inc(s("tile_done"), 1)
            pe.wait_ge(s("x_in"), 32)
            t0 = PLAN.at["xin"]["tile"]
            for k in range(KT):
                wait_bank(t0 + k)
                for tt in range(4):
                    ins = pe.transpose(bank[(t0 + k) % BANKS][:, tt * P:(tt + 1) * P],
                                       x_rows[:, tt, k * P:(k + 1) * P], ident[:, :])
                ins.then_inc(s("tile_done"), 1)
            pe.wait_ge(s("silu_c"), 1)
            mod_block(0)
            norm_sum("mix0", TOK)
            mod_block(1)
            pe.wait_ge(s("dft_lo"), 1)
            fourier("four0", 2, "mix0")
            mlp(0, TOK, True)
            def take_aux(x):
                if x >= AUX:
                    name, value = PLAN.aux[x - AUX]
                    pe.wait_ge(s(name), value)
                return aux[x % AUX]

            def diff_attention():
                t0, p0, x0 = PLAN.at["diff"]["tile"], PLAN.at["diff"]["panel"], PLAN.at["diff"]["aux"]
                full = slice(0, TOK)
                for turn in range(HEADS + 1):
                    h = turn - 1
                    if h >= 0:
                        pe.wait_ge(s("qk_lo"), 2 * h + 2)
                        for i in range(8):
                            qt, j = i // 2, i % 2
                            dst = take_aux(x0 + AUX_AT["diff", "score", h, i])
                            half = slice(j * HALF, (j + 1) * HALF)
                            keys = full if qt < 2 else slice(LAT, TOK)
                            q = slice(qt * P, (qt + 1) * P)
                            split_product(dst[:, 0:keys.stop - keys.start], q_hi[half, q], q_lo[half, q], k_hi[half, keys],
                                          k_lo[half, keys], True, True).then_inc(s("aux_done"), 1)
                    if turn < HEADS:
                        if turn == 0:
                            first_products([p0, p0 + 1], t0, H_hi, H_lo, full, h_ready("mix1"))
                        else:
                            panel_product(p0 + 3 * turn, t0 + 3 * turn, H_hi, H_lo, full)
                            panel_product(p0 + 3 * turn + 1, t0 + 3 * turn + 1, H_hi, H_lo, full)
                    if h >= 0:
                        pe.wait_ge(s("p_mix"), 4 * h + 4)
                        for i in range(3):
                            dst = take_aux(x0 + AUX_AT["diff", "turn_p", h, i])
                            for j in range(2):
                                for q in range(2):
                                    key = q * TOK + (2 * i + j) * P if i < 2 else 2 * TOK + q * CTX + j * P
                                    ins = pe.transpose(dst[:, j * LAT + q * P:j * LAT + (q + 1) * P],
                                                       p_all[:, key:key + P], ident[:, :])
                            ins.then_inc(s("aux_done"), 1)
                    if turn < HEADS:
                        panel_product(p0 + 3 * turn + 2, t0 + 3 * turn + 2, H_hi, H_lo, full)
                    if h >= 0:
                        dst = take_aux(x0 + AUX_AT["diff", "pv", h, 0])
                        pe.wait_ge(s("v_lo"), h + 1)
                        pe.wait_ge(s("pt_lo"), 3 * h + 3)
                        for kt in range(4):
                            split_product(dst[:, 0:LAT], v_hi[:, kt, :], v_lo[:, kt, :], pt_hi[:, kt, :],
                                          pt_lo[:, kt, :], kt == 0, kt == 3)
                        for kt in range(2):
                            ins = split_product(dst[:, LAT:TOK], v_hi[:, 2 + kt, :], v_lo[:, 2 + kt, :],
                                                pt_hi[:, 4 + kt, :], pt_lo[:, 4 + kt, :], kt == 0, kt == 1)
                        ins.then_inc(s("aux_done"), 1)
                    if turn < HEADS:
                        dst = take_aux(x0 + AUX_AT["diff", "turn_v", turn, 0])
                        pe.wait_ge(s("qkv"), 3 * turn + 3)
                        for tt in range(4):
                            ins = pe.transpose(dst[:, tt * P:(tt + 1) * P], v_f[:, tt * P:(tt + 1) * P], ident[:, :])
                        ins.then_inc(s("aux_done"), 1)
                    if h >= 0:
                        dst = take_aux(x0 + AUX_AT["diff", "square", h, 0])
                        pe.wait_ge(s("o_sq"), h + 1)
                        pe.matmul(dst[:, :], ones[:, :], o_sq[:, :], start=True, stop=True).then_inc(s("aux_done"), 1)

            def output_product(name, signal, first, c):
                for m in range(KT):
                    panel_product(PLAN.at[name]["panel"] + m, PLAN.at[name]["tile"] + m, G_hi, G_lo, c,
                                  ready=(lambda k: pe.wait_ge(s(signal), first + k + 1)) if m == 0 else None)

            norm_sum("mix1", TOK)
            diff_attention()
            output_product("diffo", "o_lo", 0, slice(0, TOK))
            mlp(1, TOK, True)
            def down_products():
                t0, p0 = PLAN.at["mlad"]["tile"], PLAN.at["mlad"]["panel"]
                first_products([p0, p0 + 1, p0 + 2], t0, H_hi, H_lo, [slice(0, LAT), slice(0, LAT), slice(0, TOK)],
                               h_ready("mix2"))
                panel_product(p0 + 3, t0 + 3, H_hi, H_lo, slice(0, TOK), rows=QD)
                pe.wait_ge(s("down_sq"), 1)
                for k in range(2):
                    ins = pe.matmul(pv_ps[:, 0:LAT], ones[:, :], norm_buf[0][:, k * LAT:(k + 1) * LAT], start=(k == 0), stop=(k == 1))
                ins.then_inc(s("down_sum"), 1)
                pe.wait_ge(s("down_sq"), 2)
                pe.matmul(sum_ps[:, :], ones[:, :], norm_buf[1][:, :], start=True, stop=True).then_inc(s("down_sum"), 1)

            def mla_attention():
                t0, p0, x0 = PLAN.at["mla"]["tile"], PLAN.at["mla"]["panel"], PLAN.at["mla"]["aux"]
                pe.wait_ge(s("mv_zero"), 1)
                for turn in range(MLA_HEADS + 1):
                    h = turn - 1
                    if h >= 0:
                        pe.wait_ge(s("mla_q_lo"), h + 1)
                        pe.wait_ge(s("mla_k_lo"), h + 2)
                        for i in range(2):
                            dst = take_aux(x0 + AUX_AT["mla", "score", h, i])
                            q = slice(i * P, (i + 1) * P)
                            split_product(dst[:, :], mq_hi[0:QD, q], mq_lo[0:QD, q], mk_hi[0:QD, :], mk_lo[0:QD, :],
                                          True, True).then_inc(s("aux_done"), 1)
                    if turn < MLA_HEADS:
                        t = t0 + 2 * turn
                        n = p0 + [0, 1, 4, 5][turn // 4]
                        pe.wait_ge(s("panel_ready"), n + 1)
                        pe.wait_ge(s("down_lo"), 1)
                        wait_bank(t)
                        for k in range(2):
                            w = slice((4 * k + turn % 4) * P, (4 * k + turn % 4) * P + QD)
                            ins = split_product(bank[t % BANKS][0:QD, 0:LAT], W_hi[n % RING][:, w], W_lo[n % RING][:, w],
                                                cq_hi[:, k, :], cq_lo[:, k, :], k == 0, k == 1)
                        ins.then_inc(s("tile_done"), 1)
                        n = p0 + 2 + turn // 8
                        pe.wait_ge(s("panel_ready"), n + 1)
                        pe.wait_ge(s("down_lo"), 2)
                        wait_bank(t + 1)
                        w = slice(turn % 8 * P, (turn % 8 + 1) * P)
                        split_product(bank[(t + 1) % BANKS][:, :], W_hi[n % RING][:, w], W_lo[n % RING][:, w], ckv_hi[:, :],
                                      ckv_lo[:, :], True, True).then_inc(s("tile_done"), 1)
                        dst = take_aux(x0 + AUX_AT["mla", "turn_v", turn, 0])
                        pe.wait_ge(s("mla_qkv"), 2 * turn + 2)
                        for tt in range(4):
                            ins = pe.transpose(dst[:, tt * P:(tt + 1) * P], kv_f[:, tt * P:(tt + 1) * P], ident[:, :])
                        ins.then_inc(s("aux_done"), 1)
                    if h >= 0:
                        pe.wait_ge(s("mla_mix"), 2 * h + 2)
                        for i in range(2):
                            dst = take_aux(x0 + AUX_AT["mla", "turn_p", h, i])
                            for j in range(2):
                                for q in range(2):
                                    ins = pe.transpose(dst[:, j * LAT + q * P:j * LAT + (q + 1) * P],
                                                       mp_all[:, q, (2 * i + j) * P:(2 * i + j + 1) * P], ident[:, :])
                            ins.then_inc(s("aux_done"), 1)
                        m, j = h // 2, h % 2
                        if j == 0 and m >= 2:
                            pe.wait_ge(s("mla_o_lo"), m - 1)
                        pe.wait_ge(s("mla_v_lo"), h + 1)
                        pe.wait_ge(s("mla_pt_lo"), 2 * h + 2)
                        for kt in range(4):
                            ins = split_product(pv_ps[:, (m % 2) * LAT:(m % 2 + 1) * LAT], mv_hi[j][:, kt, :], mv_lo[j][:, kt, :],
                                                mpt_hi[:, kt, :], mpt_lo[:, kt, :], j == 0 and kt == 0, j == 1 and kt == 3)
                        if j:
                            ins.then_inc(s("pv_done"), 1)

            norm_sum("mix2", TOK)
            down_products()
            mla_attention()
            output_product("mlao", "mla_o_lo", 0, slice(0, LAT))
            mlp(2, LAT, True)
            norm_sum("mix3", LAT)
            pe.wait_ge(s("dft_lo"), 2)
            fourier("four3", 1, "mix3")
            mlp(3, LAT, False)
            norm_sum("final", LAT)
            pe.wait_ge(s("small_in"), 16 * 7)
            t = PLAN.at["meta"]["tile"]
            wait_bank(t)
            for k in range(KT):
                ins = pe.transpose(bank[t % BANKS][:, k * META:(k + 1) * META], meta_rows[:, k * P:(k + 1) * P],
                                   ident[0:META, 0:META])
            ins.then_inc(s("tile_done"), 1)
            norm_sum("mix_2", TOK2)

            def mix_tile(what, i):
                n = MIX_AT[what, i]
                if n >= 4:
                    name, value = MIX_TILES[n - 4]
                    pe.wait_ge(s(name), value)
                return mix_ps[n % 4]

            def done(ins):
                ins.then_inc(s("mix_done_ps"), 1)

            def gates():
                pe.wait_ge(s("proj"), 1)
                for j in range(2):
                    ps = mix_tile("gate", j)
                    done(pe.matmul(ps[:, 0:TOK2], gate_up[:, j * P:(j + 1) * P], proj[0:GATE_RANK, GATE_AT, :],
                                   start=True, stop=True))

            def turned_values():
                pe.wait_ge(s("proj"), 9)
                for h in range(GLA_HEADS):
                    ps = mix_tile("turn_v", h)
                    for n in range(4):
                        c0, cn = CHUNKS[n + 1]
                        ins = pe.transpose(ps[0:cn, n * P:(n + 1) * P], proj[:, V_AT + h, c0:c0 + cn], ident[:, :])
                    done(ins)
                ps = mix_tile("turn_v", 4)
                for h in range(GLA_HEADS):
                    ins = pe.transpose(ps[0:META, h * P:(h + 1) * P], proj[:, V_AT + h, 0:META], ident[:, :])
                done(ins)

            def turned_keys():
                pe.wait_ge(s("k_end"), 1)
                for j in range(2):
                    ps = mix_tile("turn_k", j)
                    for n in range(3):
                        c0, cn = CHUNKS[n + 1]
                        pe.transpose(ps[0:cn, n * P:(n + 1) * P], k_end[:, j, c0:c0 + cn], ident[:, :])
                    done(pe.transpose(ps[0:META, 3 * P:4 * P], k_end[:, j, 0:META], ident[:, :]))

            def mixer_rest():
                for i in range(2):
                    ps = mix_tile("pool", i)
                    pe.wait_ge(s("pooled"), 2 * i + 2)
                    for g in range(2):
                        ins = pe.matmul(ps[:, g * LAT:(g + 1) * LAT], pool_w[:, 2 * i + g, :], pooled[:, 2 * i + g, :],
                                        start=True, stop=True)
                    done(ins)
                pe.wait_ge(s("qk_t"), 1)
                for i in range(2):
                    ps = mix_tile("score", i)
                    for j in range(2):
                        for n in range(4):
                            c = slice(n * CHUNK, (n + 1) * CHUNK)
                            ins = pe.matmul(ps[0:CHUNK, j * LAT + n * CHUNK:j * LAT + (n + 1) * CHUNK], k_t[:, i, c],
                                            q_pad[j][:, i, c], start=True, stop=True)
                    done(ins)
                pe.wait_ge(s("v_rows"), 5)
                pe.wait_ge(s("k_rows"), 2)
                for i in range(2):
                    ps = mix_tile("state", i)
                    for n in range(4):
                        for j in range(2):
                            half = slice(j * HALF, (j + 1) * HALF)
                            h = 2 * i + j
                            keys = k_rows_m[:, i, half] if n == 0 else k_rows[:, i, n - 1, half]
                            values = v_rows_m[:, h, :] if n == 0 else v_rows[:, h, n - 1, :]
                            ins = pe.matmul(ps[half, n * P:(n + 1) * P], keys, values, start=True, stop=True)
                    done(ins)
                for i in range(2):
                    ps = mix_tile("out", i)
                    pe.wait_ge(s("sc_masked"), i + 1)
                    pe.wait_ge(s("states"), 4 * i + 4)
                    for j in range(2):
                        h = 2 * i + j
                        for n in range(4):
                            dst = ps[:, j * LAT + n * CHUNK:j * LAT + (n + 1) * CHUNK]
                            pe.matmul(dst, v_rows[:, h, n, :], sc[:, h, n, :], start=True, stop=False)
                            ins = pe.matmul(dst, S_all[:, i, n, :], q_pad[j][:, i, n * CHUNK:(n + 1) * CHUNK],
                                            start=False, stop=True)
                    done(ins)
                pe.wait_ge(s("go_sq"), 1)
                for i in range(2):
                    ps = mix_tile("square", i)
                    for j in range(2):
                        ins = pe.matmul(ps[:, j * LAT:(j + 1) * LAT], ones[:, :], go_sq[:, 2 * i + j, :], start=True, stop=True)
                    done(ins)

            for i in range(len(WIN_ORDER)):
                panel_product(PLAN.at["win"]["panel"] + i, PLAN.at["win"]["tile"] + i, H_hi, H_lo, slice(0, TOK2),
                              ready=h_ready("mix_2") if i == 0 else None)
                if i == 2:
                    gates()
                if i == 10:
                    turned_values()
                if i == 14:
                    turned_keys()
            mixer_rest()
            for m in range(KT):
                panel_product(PLAN.at["wout"]["panel"] + m, PLAN.at["wout"]["tile"] + m, Y_hi, Y_lo, slice(0, LAT),
                              ready=(lambda k: pe.wait_ge(s("y_lo"), 1 + k // 4)) if m == 0 else None)
            norm_sum("ffn_2", LAT)
            pe.wait_ge(s("h_lo"), KT * SPLIT_AT["ffn_2"] + KT)
            pe.wait_ge(s("x_done"), X_AT["moe"])
            for tt in range(2):
                dst = psum[2][:, tt * (4 + EXPERTS):(tt + 1) * (4 + EXPERTS)]
                pe.matmul(dst, ones[0:1, :], route_b[:, :], start=True, stop=False)
                for k in range(KT):
                    tok = slice(tt * P, (tt + 1) * P)
                    pe.matmul(dst, H_hi[:, k, tok].bitcast(F32), route_w[:, k, :], start=False, stop=False)
                    ins = pe.matmul(dst, H_lo[:, k, tok].bitcast(F32), route_w[:, k, :], start=False, stop=(k == KT - 1))
            ins.then_inc(s("logit_done"), 1)
            p0 = PLAN.at["moe"]["panel"]

            def expert_panel(n, i):
                pe.wait_ge(s("panel_ready"), later(p0 + n + 1, i, 6 * EXPERT_TURNS))
                r = (p0 + n) % RING
                return W_hi[r], W_lo[r]

            def expert_in(x, n, what, i=None):
                if what == 0 and x >= 2:
                    pe.wait_ge(s("e_hid"), later(x - 1, i, EXPERT_TURNS))
                if what == 1 and x >= 1:
                    pe.wait_ge(s("e_hid"), later(x, i, EXPERT_TURNS))
                ps = psum[3 * (x % 2)] if what == 0 else psum[1]
                for j in range(2):
                    hi, lo = expert_panel(n + j, i)
                    for k in range(KT):
                        w = slice(k * P, (k + 1) * P)
                        ins = split_product(ps[:, j * LAT:(j + 1) * LAT], hi[:, w], lo[:, w], H_hi[:, k, 0:LAT],
                                            H_lo[:, k, 0:LAT], k == 0, k == KT - 1)
                    ins.then_inc(s("expert_done"), 1)

            def weight_row(x, i=None):
                pe.wait_ge(s("diag"), later(x + 1, i, EXPERT_TURNS))
                if x:
                    pe.wait_ge(s("e_hid"), later(x, i, EXPERT_TURNS))
                else:
                    pe.wait_ge(s("logits"), 1)
                for tt in range(2):
                    ins = pe.matmul(psum[2][:, tt * P:(tt + 1) * P], ones[:, :], diag[x % 2][:, tt, :], start=True, stop=True)
                ins.then_inc(s("weight_row"), 1)

            def expert_out(x, n, i=None):
                pe.wait_ge(s("e_lo"), later(x + 1, i, EXPERT_TURNS))
                for j in range(2):
                    hi, lo = expert_panel(n + j, i)
                    for a4 in range(4):
                        m = 2 * a4 + j
                        dst = psum[4 + m // 2][:, (m % 2) * LAT:(m % 2 + 1) * LAT]
                        for k in range(2):
                            w = slice((4 * k + a4) * P, (4 * k + a4 + 1) * P)
                            last = x == EXPERTS - 1 and k == 1
                            for q, (wp, rp) in enumerate(((hi, E_hi), (hi, E_lo), (lo, E_hi))):
                                ins = pe.matmul(dst, wp[:, w], rp[x % 2][:, k, :], start=False,
                                                stop=last and q == 2, skip_group_check=True)
                    ins.then_inc(s("expert_done"), 1)

            def expert_turn(x, i=None):
                n = 6 * x - 2 if x else 0
                expert_in(x, n, 0, i)
                expert_in(x, n + 2, 1, i)
                weight_row(x, i)
                if x:
                    expert_out(x - 1, n + 4, i)

            pe.wait_ge(s("zero_row"), 1)
            pe.wait_ge(s("x_done"), X_AT["moe"])
            for b in range(4):
                pe.matmul(psum[4 + b][:, :], ones[0:1, :], zero_row[:, :], start=True, stop=False, skip_group_check=True)
            expert_turn(0)
            with pe.Fori(0, 3) as i:
                for j in range(EXPERT_TURNS):
                    expert_turn(1 + j, i)
            for x in range(1 + 3 * EXPERT_TURNS, EXPERTS):
                expert_turn(x)
            expert_out(EXPERTS - 1, 6 * EXPERTS - 2)
            norm_sum("final_2", LAT)
            for tt in range(2):
                for half in range(2):
                    n = 2 * tt + half
                    for k in range(4):
                        pe.wait_ge(s("h"), KT * NORM_AT["final_2"] + 4 * half + k + 1)
                        ins = pe.transpose(psum[n][:, k * P:(k + 1) * P], X[:, 4 * half + k, tt * P:(tt + 1) * P], ident[:, :])
                    ins.then_inc(s("out_turned"), 1)

        @block.vector
        def _(dve):
            def split_lo(n):
                unit, place, _ = PLAN.panels[n]
                slot = PLAN.units[unit][1]
                dve.tensor_tensor(W_lo[n % RING][:, :].rearrange("p (k c) -> p k c", c=P), w_raw[slot][:, :, place, :],
                                  W_hi[n % RING][:, :].bitcast(F32).rearrange("p (k c) -> p k c", c=P),
                                  ALU.subtract).then_inc(s("panel_ready"), 1)

            def split_lo_at(n, i=None):
                if isinstance(i, int):
                    n, i = n + i * MLP_TILES, None
                dve.wait_ge(s("w_hi"), later(n + 1, i, MLP_TILES))
                split_lo(n)

            def add_square(name, n_cols, k):
                ni, c = NORM_AT[name], slice(0, n_cols)
                dve.wait_ge(s("sq"), KT * ni + k + 1)
                if k == 0:
                    dve.tensor_copy(norm_buf[2][:, c], norm_buf[0][:, c]).then_inc(s("sq_added"), 1)
                else:
                    dve.wait_ge(s("sq_added"), KT * ni + k)
                    dve.tensor_tensor(norm_buf[2][:, c], norm_buf[2][:, c], norm_buf[k % 2][:, c],
                                      ALU.add).then_inc(s("sq_added"), 1)

            def invert(name, n_cols):
                ni, c = NORM_AT[name], slice(0, n_cols)
                dve.wait_ge(s("root"), ni + 1)
                dve.reciprocal(norm_buf[3][:, c], norm_buf[3][:, c]).then_inc(s("rstd"), 1)

            def apply(name, n_cols, pairs):
                ni, c = NORM_AT[name], slice(0, n_cols)
                dve.wait_ge(s("rstd"), ni + 1)

                def lo(k):
                    dve.wait_ge(s("h_hi"), KT * pairs + k + 1)
                    dve.tensor_tensor(H_lo[:, k, c], norm_buf[4 + k % 2][:, c], H_hi[:, k, c].bitcast(F32),
                                      ALU.subtract).then_inc(s("h_lo"), 1)

                for k in range(KT):
                    if k >= 2:
                        dve.wait_ge(s("h"), KT * ni + k - 1)
                    dve.tensor_tensor(norm_buf[k % 2][:, c], X[:, k, c], norm_buf[3][:, c], ALU.mult).then_inc(s("t"), 1)
                    if pairs is not None and k >= 1:
                        lo(k - 1)
                if pairs is not None:
                    lo(KT - 1)

            def norm_rest(name, n_cols):
                invert(name, n_cols)
                apply(name, n_cols, SPLIT_AT[name] if name in SPLIT_NORMS else None)

            def norm(name, n_cols):
                for k in range(KT):
                    add_square(name, n_cols, k)
                norm_rest(name, n_cols)

            def mod_read(layer, g, i=None):
                dve.wait_ge(s("mod_turned"), later(g + 1, i, 1))
                turned_tiles = mod_ps[:, 0:MOD_PART].rearrange("p (t j r) -> p j t r", t=MOD_PART // P, j=4)
                b = g % BLOCKS if i is None else i + g % BLOCKS
                dst = mod[layer % 2][:, bass.ds(b * (MOD_TILES // BLOCKS), MOD_TILES // BLOCKS), :] if i is not None else \
                    mod[layer % 2][:, b * (MOD_TILES // BLOCKS):(b + 1) * (MOD_TILES // BLOCKS), :]
                dve.tensor_copy(dst.rearrange("p (j t) s -> p j t s", j=4), turned_tiles[:, :, :, 0:2]).then_inc(s("mod_read"), 1)

            def mod_finish(layer, half):
                n = MOD_TILES // 2
                m = mod[layer % 2][:, half * n:(half + 1) * n, :]
                tile, row = ("mod_b_lo", 48 * layer) if layer < 2 else ("mod_b_hi", 48 * (layer - 2))
                dve.wait_ge(s("mod_read"), BLOCKS * layer + 2 * (half + 1))
                bias = vcols(tile, row + half * n, n).rearrange("p (m o) -> p m o", o=1).to_broadcast([P, n, 2])
                dve.tensor_tensor(m, m, bias, ALU.add).then_inc(s("mod_sum"), 1)
                dve.wait_ge(s("mod_sum"), 2 * layer + half + 1)
                name, scales = (("norm_mix_g", scale_mix), ("norm_mlp_g", scale_mlp))[half]
                g = vcols(name, KT * layer, KT).rearrange("p (m o) -> p m o", o=1).to_broadcast([P, KT, 2])
                dve.scalar_tensor_tensor(scales[:, :, :], m[:, KT:2 * KT, :], 1.0, g, ALU.add,
                                         ALU.mult).then_inc(s(("scales_mix", "scales_mlp")[half]), 1)

            def add_gated(m, t, xn, layer, gate_at, streams, i=None, step=0):
                dve.wait_ge(s("tile_done"), later(t + 1, i, MLP_TILES))
                if xn:
                    dve.wait_ge(s("x_done"), later(xn, i, step))
                for st in range(streams):
                    c = slice(st * LAT, (st + 1) * LAT)
                    ins = dve.scalar_tensor_tensor(X[:, m, c], bank[t % BANKS][:, c],
                                                   mod[layer % 2][:, gate_at + m, st:st + 1], X[:, m, c],
                                                   ALU.mult, ALU.add)
                ins.then_inc(s("x_done"), 1)

            def fourier(name, layer, streams):
                t = PLAN.at[name]["tile"]
                p0 = PLAN.at[name]["panel"]
                f0 = 0 if name == "four0" else 24
                n_tok = 2 * streams
                for g in range(4):
                    if name == "four0" and g == 3:
                        for n in range(AHEAD):
                            split_lo_at(p0 + n)
                    for tt in range(n_tok):
                        row = 4 * (g % 2) + tt
                        dve.wait_ge(s("four_hi"), f0 + t - PLAN.at[name]["tile"] + 1)
                        dve.tensor_tensor(G_lo[:, row, 0:256], bank[t % BANKS][:, 0:256],
                                          G_hi[:, row, 0:256].bitcast(F32), ALU.subtract)
                        dve.scalar_tensor_tensor(G_lo[:, row, 256:512], bank[t % BANKS][:, 256:512], -1.0,
                                                 G_hi[:, row, 256:512].bitcast(F32), ALU.mult,
                                                 ALU.subtract).then_inc(s("four_lo"), 1)
                        t += 1
                    for m in range(2):
                        c = slice(0, streams * LAT)
                        dve.wait_ge(s("four_hi"), f0 + t - PLAN.at[name]["tile"] + 1)
                        dve.tensor_tensor(H_lo[:, 2 * g + m, c], bank[t % BANKS][:, c],
                                          H_hi[:, 2 * g + m, c].bitcast(F32), ALU.subtract).then_inc(s("four_lo"), 1)
                        t += 1
                    if name == "four0" and g % 2:
                        mod_read(0, 2 + g // 2)
                if name == "four0":
                    mod_finish(0, 1)
                bias = vcols("fourier_b", KT * (layer // 3), KT).rearrange("p (m o) -> p m o", o=1).to_broadcast([P, KT, 2])
                dve.tensor_tensor(gated_b[:, :, :], mod[layer % 2][:, 2 * KT:3 * KT, :], bias,
                                  ALU.mult).then_inc(s("gated_b"), 1)
                dve.wait_ge(s("gated_b"), layer // 3 + 1)
                for m in range(KT):
                    for st in range(streams):
                        c = slice(st * LAT, (st + 1) * LAT)
                        ins = dve.tensor_scalar(X[:, m, c], X[:, m, c], gated_b[:, m, st:st + 1], None, ALU.add)
                ins.then_inc(s("x_bias"), 1)
                dve.wait_ge(s("x_bias"), layer // 3 + 1)
                for m in range(KT):
                    split_lo_at(p0 + m + AHEAD)
                    add_gated(m, t + m, 0, layer, 2 * KT, streams)
                    if m:
                        add_square(f"mlp{layer}", streams * LAT, m - 1)
                add_square(f"mlp{layer}", streams * LAT, KT - 1)

            def mlp(layer, streams, with_mod, next_norm):
                at0 = PLAN.at[f"mlp{layer}"]
                p0, t0 = at0["panel"], at0["tile"]
                h0 = KT * BLOCKS * layer
                xn = X_AT[f"mlp{layer}"]
                c = slice(0, streams * LAT)

                def lo(j, b):
                    dve.wait_ge(s("g_hi"), later(h0 + j + 1, b, KT))
                    dve.wait_ge(s("g_sq"), later(h0 + j + 1, b, KT))
                    dve.tensor_tensor(G_lo[:, j, c], square[j % 2][:, c], G_hi[:, j, c].bitcast(F32),
                                      ALU.subtract).then_inc(s("g_lo"), 1)

                def hidden_block(b, last=False):
                    for j in range(MLP_TILES):
                        split_lo_at(p0 + j + AHEAD, b)
                        if j < KT:
                            dve.wait_ge(s("relu"), later(h0 + j + 1, b, KT))
                            dve.tensor_tensor(square[j % 2][:, c], relu[j % 2][:, c], relu[j % 2][:, c],
                                              ALU.mult).then_inc(s("g_sq"), 1)
                            lo(j, b)
                        else:
                            add_gated(j - KT, t0 + j, xn + j - KT, layer, 5 * KT, streams, b, KT)
                        if with_mod and not last and j == MOD_TURN_AT:
                            mod_read(layer + 1, BLOCKS * (layer + 1) + 1, b)
                        if last and j > KT:
                            add_square(*next_norm, j - KT - 1)

                if with_mod:
                    mod_read(layer + 1, BLOCKS * (layer + 1))
                with dve.Fori(0, BLOCKS - 1) as b:
                    hidden_block(b)
                if with_mod:
                    for half in range(2):
                        mod_finish(layer + 1, half)
                hidden_block(BLOCKS - 1, last=True)
                add_square(*next_norm, KT - 1)

            dve.wait_ge(s("vec_in"), 16 * (len(VEC_ROWS) + 4))
            dve.tensor_tensor(lam_prod[:, :, :], lam_in[:, 0:2, :], lam_in[:, 2:4, :], ALU.mult).then_inc(s("lam"), 1)
            dve.wait_ge(s("lam"), 1)
            dve.tensor_reduce(lam_row[:, 0:2], lam_prod[:, :, :], AX.X, ALU.add).then_inc(s("lam"), 1)
            dve.wait_ge(s("silu_exp"), 1)
            dve.tensor_scalar(silu_t[:, :, :], silu_t[:, :, :], 1.0, None, ALU.add).then_inc(s("silu_add"), 1)
            dve.wait_ge(s("silu_add"), 1)
            dve.reciprocal(silu_t[:, :, :], silu_t[:, :, :]).then_inc(s("silu_add"), 1)
            dve.wait_ge(s("silu_add"), 2)
            dve.wait_ge(s("const"), 5)
            dve.tensor_tensor(silu_c[:, :, 0:2].rearrange("p k s -> p s k"), silu_t[:, :, :],
                              vcols("c", 0, 16).rearrange("p (s k) -> p s k", s=2), ALU.mult).then_inc(s("silu_c"), 1)
            dve.wait_ge(s("lam_exp"), 1)
            dve.scalar_tensor_tensor(lam_row[:, 1:2], lam_row[:, 3:4], LAM_INIT, lam_row[:, 2:3], ALU.subtract,
                                     ALU.subtract)
            dve.memset(lam_row[:, 0:1], 1.0).then_inc(s("lam"), 1)
            dve.wait_ge(s("tile_done"), 2)
            dve.tensor_copy(lam_col[:, :], bank[1][:, 0:2]).then_inc(s("lam_col"), 1)
            dve.wait_ge(s("dft_hi"), 1)
            dve.tensor_tensor(dft_lo[:, :, :], dft[:, :, :], dft_hi[:, :, :].bitcast(F32), ALU.subtract).then_inc(s("dft_lo"), 1)
            for k in range(KT):
                add_square("mix0", TOK, k)
            mod_read(0, 0)
            invert("mix0", TOK)
            mod_read(0, 1)
            mod_finish(0, 0)
            apply("mix0", TOK, SPLIT_AT["mix0"])
            fourier("four0", 0, 2)
            norm_rest("mlp0", TOK)
            mlp(0, 2, True, ("mix1", TOK))

            def mixes(h):
                def mix(qt):
                    n = TOK if qt < 2 else CTX
                    pair = slice(2 * qt, 2 * qt + 2)
                    dve.wait_ge(s("p_exp"), 8 * h + 2 * qt + 2)
                    dve.reciprocal(z_inv[:, pair], z[:, pair]).then_inc(s("z_inv"), 1)
                    dve.wait_ge(s("z_inv"), 4 * h + qt + 1)
                    dve.tensor_tensor(z_mix[:, pair], z_inv[:, pair], lam_col[:, :], ALU.mult).then_inc(s("z_mix"), 1)
                    dve.wait_ge(s("p_scaled"), 4 * h + qt + 1)
                    first = qt * TOK if qt < 2 else 2 * TOK + (qt - 2) * CTX
                    dve.scalar_tensor_tensor(p_all[:, first:first + n], p_raw[qt % 2][0][:, 0:n],
                                             z_mix[:, 2 * qt:2 * qt + 1], p_raw[qt % 2][1][:, 0:n], ALU.mult,
                                             ALU.add).then_inc(s("p_mix"), 1)

                for qt in range(4):
                    n = TOK if qt < 2 else CTX
                    for j in range(2):
                        x = PLAN.at["diff"]["aux"] + AUX_AT["diff", "score", h, 2 * qt + j]
                        dve.wait_ge(s("aux_done"), x + 1)
                        dve.tensor_reduce(neg_max[:, 2 * qt + j:2 * qt + j + 1], aux[x % AUX][:, 0:n], AX.X, ALU.max,
                                          negate=True).then_inc(s("neg_max"), 1)
                    if qt:
                        mix(qt - 1)
                mix(3)

            swap16 = [i ^ 16 for i in range(32)]

            def diff_attention():
                p0, x0 = PLAN.at["diff"]["panel"], PLAN.at["diff"]["aux"]
                for turn in range(HEADS + 1):
                    h = turn - 1
                    if h >= 0:
                        mixes(h)
                    if turn < HEADS:
                        for j, f in enumerate((q_f, k_f)):
                            split_lo_at(p0 + 3 * turn + j + AHEAD)
                            dve.wait_ge(s("qkv"), 3 * turn + j + 1)
                            r = 2 * turn + j
                            if r:
                                dve.wait_ge(s("roped"), r)
                            dve.stream_shuffle(turned, f[:, 0:LAT], swap16).then_inc(s("rope_step"), 1)
                            dve.tensor_tensor(straight, f[:, 0:LAT], rope[:, 0, :], ALU.mult)
                            dve.wait_ge(s("rope_step"), 2 * r + 1)
                            dve.tensor_tensor(turned, turned, rope[:, 1, :], ALU.mult).then_inc(s("rope_step"), 1)
                            dve.wait_ge(s("rope_step"), 2 * r + 2)
                            dve.tensor_tensor(f[:, 0:LAT], straight, turned, ALU.add).then_inc(s("roped"), 1)
                        for j, (lo, hi, f) in enumerate(((q_lo, q_hi, q_f), (k_lo, k_hi, k_f))):
                            dve.wait_ge(s("qk_hi"), 2 * turn + j + 1)
                            dve.tensor_tensor(lo[:, :], f[:, :], hi[:, :].bitcast(F32), ALU.subtract).then_inc(s("qk_lo"), 1)
                    if h >= 0:
                        for i in range(3):
                            x = x0 + AUX_AT["diff", "turn_p", h, i]
                            dve.wait_ge(s("pt_hi"), 3 * h + i + 1)
                            dve.tensor_tensor(pt_lo[:, 2 * i:2 * i + 2, :].rearrange("p a b -> p (a b)"), aux[x % AUX][:, :],
                                              pt_hi[:, 2 * i:2 * i + 2, :].rearrange("p a b -> p (a b)").bitcast(F32),
                                              ALU.subtract).then_inc(s("pt_lo"), 1)
                    if turn < HEADS:
                        split_lo_at(p0 + 3 * turn + 2 + AHEAD)
                        x = x0 + AUX_AT["diff", "turn_v", turn, 0]
                        dve.wait_ge(s("v_hi"), turn + 1)
                        dve.tensor_tensor(v_lo[:, :, :].rearrange("p a b -> p (a b)"), aux[x % AUX][:, :],
                                          v_hi[:, :, :].rearrange("p a b -> p (a b)").bitcast(F32),
                                          ALU.subtract).then_inc(s("v_lo"), 1)
                    if h >= 0:
                        dve.wait_ge(s("o_root"), h + 1)
                        dve.reciprocal(o_inv[:, :], o_inv[:, :]).then_inc(s("o_inv"), 1)
                        dve.wait_ge(s("o_inv"), h + 1)
                        dve.tensor_tensor(o_t[:, :], o_f[:, :], o_inv[:, :], ALU.mult).then_inc(s("o_t"), 1)
                        dve.wait_ge(s("o_hi"), h + 1)
                        dve.tensor_tensor(G_lo[:, h, :], o_g[:, :], G_hi[:, h, :].bitcast(F32),
                                          ALU.subtract).then_inc(s("o_lo"), 1)

            def output_added(name, layer, streams):
                for m in range(KT):
                    split_lo_at(PLAN.at[name]["panel"] + m + AHEAD)
                    add_gated(m, PLAN.at[name]["tile"] + m, 0, layer, 2 * KT, streams)
                    if m:
                        add_square(f"mlp{layer}", streams * LAT, m - 1)
                add_square(f"mlp{layer}", streams * LAT, KT - 1)

            dve.tensor_scalar(subln[:, :], vcol("diff_subln_g"), 1.0 - LAM_INIT, None, ALU.mult)
            norm_rest("mix1", TOK)
            dve.wait_ge(s("rope_in"), 16)
            diff_attention()
            output_added("diffo", 1, 2)
            norm_rest("mlp1", TOK)
            mlp(1, 2, True, ("mix2", TOK))

            def down_outputs():
                t0, p0 = PLAN.at["mlad"]["tile"], PLAN.at["mlad"]["panel"]
                for j in range(4):
                    split_lo_at(p0 + j + AHEAD)
                rotary = slice(HALF, HALF + ROPE)
                dve.wait_ge(s("rope_in"), 32)
                dve.wait_ge(s("down_out"), 4)
                rotate(kv_f[rotary, 0:LAT], rotary, 0, mp_all[:, 0, :])
                dve.wait_ge(s("key_hi"), 1)
                dve.tensor_tensor(mk_lo[rotary, :], kv_f[rotary, :], mk_hi[rotary, :].bitcast(F32),
                                  ALU.subtract).then_inc(s("mla_k_lo"), 1)
                dve.wait_ge(s("down_root"), 2)
                dve.reciprocal(norm_buf[2][:, 0:LAT], norm_buf[2][:, 0:LAT])
                dve.reciprocal(norm_buf[3][:, :], norm_buf[3][:, :]).then_inc(s("down_inv"), 1)
                dve.wait_ge(s("down_inv"), 1)
                for k in range(2):
                    ins = dve.tensor_tensor(norm_buf[4][:, k * LAT:(k + 1) * LAT], cq_f[:, k, :], norm_buf[2][:, 0:LAT], ALU.mult)
                ins.then_inc(s("down_t"), 1)
                dve.tensor_tensor(norm_buf[5][:, :], ckv_f[:, :], norm_buf[3][:, :], ALU.mult).then_inc(s("down_t"), 1)
                dve.wait_ge(s("down_hi"), 1)
                dve.tensor_tensor(cq_lo[:, :, :], cq_f[:, :, :], cq_hi[:, :, :].bitcast(F32), ALU.subtract).then_inc(s("down_lo"), 1)
                dve.wait_ge(s("down_hi"), 2)
                dve.tensor_tensor(ckv_lo[:, :], ckv_f[:, :], ckv_hi[:, :].bitcast(F32), ALU.subtract).then_inc(s("down_lo"), 1)

            swap8 = [i ^ 8 for i in range(32)]

            def rotate(x, rows, r, buf):
                m_turned, m_straight = buf[:, 0:LAT], buf[:, LAT:TOK]
                if r:
                    dve.wait_ge(s("rope32_done"), r)
                dve.stream_shuffle(m_turned[rows, 0:LAT], x, swap8).then_inc(s("rope32_step"), 1)
                dve.tensor_tensor(m_straight[rows, 0:LAT], x, rope32[rows, 0, :], ALU.mult)
                dve.wait_ge(s("rope32_step"), 2 * r + 1)
                dve.tensor_tensor(m_turned[rows, 0:LAT], m_turned[rows, 0:LAT], rope32[rows, 1, :],
                                  ALU.mult).then_inc(s("rope32_step"), 1)
                dve.wait_ge(s("rope32_step"), 2 * r + 2)
                dve.tensor_tensor(x, m_straight[rows, 0:LAT], m_turned[rows, 0:LAT], ALU.add).then_inc(s("rope32_done"), 1)

            def mla_attention():
                p0, x0 = PLAN.at["mla"]["panel"], PLAN.at["mla"]["aux"]
                split_after = {0: [3], 3: [4], 7: [5, 6], 11: [], 15: [7]}
                rotary = slice(HALF, HALF + ROPE)
                for turn in range(MLA_HEADS + 1):
                    h = turn - 1
                    if h >= 0:
                        for i in range(2):
                            x = x0 + AUX_AT["mla", "score", h, i]
                            dve.wait_ge(s("aux_done"), x + 1)
                            dve.tensor_reduce(m_max[:, i:i + 1], aux[x % AUX][:, :], AX.X, ALU.max,
                                              negate=True).then_inc(s("mla_max"), 1)
                        dve.wait_ge(s("mla_exp"), 2 * h + 2)
                        dve.reciprocal(m_zinv[:, :], m_z[:, :]).then_inc(s("mla_zinv"), 1)
                        dve.wait_ge(s("mla_zinv"), h + 1)
                        for i in range(2):
                            dve.tensor_scalar(mp_all[:, i, :], mp_raw[i][:, :], m_zinv[:, i:i + 1], None,
                                              ALU.mult).then_inc(s("mla_mix"), 1)
                    if turn < MLA_HEADS:
                        dve.wait_ge(s("mla_qkv"), 2 * turn + 1)
                        rotate(mq_f[rotary, :], rotary, turn + 1, norm_buf[0])
                        dve.wait_ge(s("mla_q_hi"), turn + 1)
                        dve.tensor_tensor(mq_lo[0:QD, :], mq_f[0:QD, :], mq_hi[0:QD, :].bitcast(F32),
                                          ALU.subtract).then_inc(s("mla_q_lo"), 1)
                        dve.wait_ge(s("mla_k_hi"), turn + 1)
                        dve.tensor_tensor(mk_lo[0:NOPE, :], kv_f[0:NOPE, :], mk_hi[0:NOPE, :].bitcast(F32),
                                          ALU.subtract).then_inc(s("mla_k_lo"), 1)
                        for n in split_after.get(turn, []):
                            split_lo_at(p0 + n)
                        x = x0 + AUX_AT["mla", "turn_v", turn, 0]
                        j = turn % 2
                        half = slice(j * HALF, (j + 1) * HALF)
                        dve.wait_ge(s("mla_v_hi"), turn + 1)
                        dve.tensor_tensor(mv_lo[j][:, :, half], aux[x % AUX][:, :].rearrange("p (t c) -> p t c", c=P)[:, :, HALF:P],
                                          mv_hi[j][:, :, half].bitcast(F32), ALU.subtract).then_inc(s("mla_v_lo"), 1)
                    if h >= 0:
                        for i in range(2):
                            x = x0 + AUX_AT["mla", "turn_p", h, i]
                            dve.wait_ge(s("mla_pt_hi"), 2 * h + i + 1)
                            dve.tensor_tensor(mpt_lo[:, 2 * i:2 * i + 2, :].rearrange("p a b -> p (a b)"), aux[x % AUX][:, :],
                                              mpt_hi[:, 2 * i:2 * i + 2, :].rearrange("p a b -> p (a b)").bitcast(F32),
                                              ALU.subtract).then_inc(s("mla_pt_lo"), 1)
                        if h % 2:
                            m = h // 2
                            dve.wait_ge(s("mla_o_hi"), m + 1)
                            dve.tensor_tensor(G_lo[:, m, 0:LAT], pv_ps[:, (m % 2) * LAT:(m % 2 + 1) * LAT],
                                              G_hi[:, m, 0:LAT].bitcast(F32), ALU.subtract).then_inc(s("mla_o_lo"), 1)
                split_lo_at(p0 + 8)

            norm_rest("mix2", TOK)
            for j in range(2):
                dve.memset(mv_hi[j][:, :, :].bitcast(F32), 0.0)
                ins = dve.memset(mv_lo[j][:, :, :].bitcast(F32), 0.0)
            ins.then_inc(s("mv_zero"), 1)
            dve.wait_ge(s("mv_zero"), 1)
            down_outputs()
            mla_attention()
            output_added("mlao", 2, 1)
            norm_rest("mlp2", LAT)
            mlp(2, 1, True, ("mix3", LAT))
            dve.wait_ge(s("dft_hi"), 2)
            dve.tensor_tensor(dft_lo[:, :, :], dft[:, :, :], dft_hi[:, :, :].bitcast(F32), ALU.subtract).then_inc(s("dft_lo"), 1)
            norm_rest("mix3", LAT)
            fourier("four3", 3, 1)
            norm_rest("mlp3", LAT)
            mlp(3, 1, False, ("final", LAT))
            norm_rest("final", LAT)
            dve.wait_ge(s("small_in"), 16 * 7)
            dve.memset(chunk_mask[:, :], 1.0).then_inc(s("mask"), 1)
            dve.wait_ge(s("mask"), 1)
            for c0, _ in CHUNKS:
                ins = dve.memset(chunk_mask[:, c0:c0 + 1], 0.0)
            ins.then_inc(s("mask"), 1)
            norm("mix_2", TOK2)

            def gates():
                dve.wait_ge(s("z_ln"), 1)
                dve.scalar_tensor_tensor(log_a[:, :, :], z_f[:, :, :], 0.0, z_abs[:, :, :], ALU.min,
                                         ALU.subtract).then_inc(s("log_a"), 1)
                dve.wait_ge(s("log_a"), 1)
                dve.wait_ge(s("mask"), 2)
                for j in range(2):
                    ins = dve.tensor_tensor_scan(b_cum[:, j, :], chunk_mask[:, :], log_a[:, j, :], 0.0, ALU.mult, ALU.add)
                ins.then_inc(s("b_cum"), 1)
                dve.wait_ge(s("b_cum"), 1)
                for n in range(4):
                    end = CHUNKS[n][0] + CHUNKS[n][1] - 1
                    ins = dve.tensor_scalar(b_last[:, :, n:n + 1], b_cum[:, :, end:end + 1], 1.0 / 16, None, ALU.mult)
                ins.then_inc(s("b_last"), 1)

            def gated_qk():
                for j in range(2):
                    dve.memset(q_pad[j][:, :, :], 0.0).then_inc(s("mask"), 1)
                dve.wait_ge(s("mask"), 4)
                dve.wait_ge(s("e_end"), 1)
                dve.wait_ge(s("proj"), 5)
                dve.tensor_tensor(k_end[:, :, 0:CHUNKS[4][0]], proj[:, K_AT:K_AT + 2, 0:CHUNKS[4][0]],
                                  e_end[:, :, 0:CHUNKS[4][0]], ALU.mult).then_inc(s("k_end"), 1)
                for j in range(2):
                    half = slice(j * HALF, (j + 1) * HALF)
                    dve.scalar_tensor_tensor(q_pad[j][half, :, :], proj[half, Q_AT:Q_AT + 2, META:], HALF ** -0.5,
                                             e_pos[half, :, META:], ALU.mult, ALU.mult)
                dve.tensor_tensor(k_t[:, :, :], proj[:, K_AT:K_AT + 2, META:], e_neg[:, :, :], ALU.mult).then_inc(s("qk_t"), 1)

            def pooling():
                dve.wait_ge(s("proj"), 13)
                u = proj[:, POOL_AT:POOL_AT + 4, :]
                src, width = u, 1
                for g, dst in enumerate((win_a, win_b, win_a, win_b)):
                    lo = 2 * width - 1
                    dve.tensor_tensor(dst[:, g:, lo:], src[:, g:, lo:], src[:, g:, lo - width:TOK2 - width],
                                      ALU.add).then_inc(s("window"), 1)
                    dve.wait_ge(s("window"), g + 1)
                    width *= 2
                    dve.scalar_tensor_tensor(pooled[:, g, :], dst[:, g, META:], 1.0 / width, u[:, g, META:], ALU.mult,
                                             ALU.subtract).then_inc(s("pooled"), 1)
                    if g < 3:
                        dve.wait_ge(s("pooled"), g + 1)
                    src = dst

            def mixer_rest():
                dve.wait_ge(s("r_exp"), 1)
                dve.tensor_scalar(r_silu[:, :, :], r_silu[:, :, :], 1.0, None, ALU.add).then_inc(s("r_step"), 1)
                dve.wait_ge(s("r_step"), 1)
                dve.reciprocal(r_silu[:, :, :], r_silu[:, :, :]).then_inc(s("r_step"), 1)
                dve.wait_ge(s("r_step"), 2)
                dve.tensor_tensor(r_silu[:, :, :], r_silu[:, :, :], proj[:, R_AT:R_AT + 4, META:], ALU.mult).then_inc(s("r_step"), 1)
                dve.wait_ge(s("y_hi"), 1)
                dve.tensor_tensor(Y_lo[:, 0:4, :], y_f[:, :, :], Y_hi[:, 0:4, :].bitcast(F32), ALU.subtract).then_inc(s("y_lo"), 1)
                for i in range(2):
                    n = MIX_AT["state", i]
                    ps = mix_ps[n % 4]
                    dve.wait_ge(s("mix_done_ps"), n + 1)
                    dve.tensor_copy(S_all[:, i, 0, :], ps[:, 0:P]).then_inc(s("states"), 1)
                    for c in range(1, 4):
                        dve.wait_ge(s("states"), 4 * i + c)
                        dve.scalar_tensor_tensor(S_all[:, i, c, :], S_all[:, i, c - 1, :], decay[:, i, c:c + 1],
                                                 ps[:, c * P:(c + 1) * P], ALU.mult, ALU.add).then_inc(s("states"), 1)
                dve.wait_ge(s("go_root"), 2)
                dve.reciprocal(go_inv, go_inv).then_inc(s("go_step"), 1)
                dve.wait_ge(s("go_step"), 1)
                dve.tensor_tensor(go_inv, go_inv, r_silu[:, :, :], ALU.mult).then_inc(s("go_step"), 1)
                dve.wait_ge(s("go_step"), 2)
                dve.tensor_tensor(go_f[:, :, :], go_f[:, :, :], go_inv, ALU.mult).then_inc(s("go_t"), 1)
                dve.wait_ge(s("y_hi"), 2)
                dve.tensor_tensor(Y_lo[:, 4:8, :], y_f[:, :, :], Y_hi[:, 4:8, :].bitcast(F32), ALU.subtract).then_inc(s("y_lo"), 1)

            for i in range(len(WIN_ORDER)):
                split_lo_at(PLAN.at["win"]["panel"] + i + AHEAD)
                if i == 3:
                    gates()
                if i == 6:
                    gated_qk()
                if i == 13:
                    pooling()
            mixer_rest()
            for m in range(KT):
                split_lo_at(PLAN.at["wout"]["panel"] + m + AHEAD)
                t = PLAN.at["wout"]["tile"] + m
                dve.wait_ge(s("tile_done"), t + 1)
                dve.tensor_tensor(X[:, m, 0:LAT], X[:, m, 0:LAT], bank[t % BANKS][:, 0:LAT], ALU.add).then_inc(s("x_done"), 1)
                if m:
                    add_square("ffn_2", LAT, m - 1)
            add_square("ffn_2", LAT, KT - 1)
            dve.memset(zero_row[:, :], 0.0).then_inc(s("zero_row"), 1)
            norm_rest("ffn_2", LAT)

            steps = [0]

            def step(ins):
                ins.then_inc(s("route"), 1)
                steps[0] += 1
                dve.wait_ge(s("route"), steps[0])

            def spread(x, n=4):
                return x[:, :].rearrange("p (t o) -> p t o", o=1).to_broadcast([P, 2, n])

            def first_largest(choice, top, values, scratch):
                step(dve.tensor_reduce(top[:, :], values, AX.X, ALU.max))
                step(dve.tensor_tensor(choice, values, spread(top), ALU.is_equal))
                step(dve.tensor_tensor(choice, choice, rank[:, :, :], ALU.mult))
                step(dve.tensor_reduce(scratch[:, :], choice, AX.X, ALU.max))
                step(dve.tensor_tensor(choice, choice, spread(scratch), ALU.is_equal))

            def router():
                for j in range(4):
                    step(dve.memset(rank[:, :, j:j + 1], float(4 - j)))
                dve.wait_ge(s("logits"), 1)
                groups = logits[:, :, 0:4]
                g_one, e_sel, e_one, e_two = r4[2][:, :, :], r4[3][:, :, :], r4[6][:, :, :], r4[7][:, :, :]
                first_largest(g_one, r1[0], groups, r1[1])
                dve.tensor_tensor(r4[0][:, :, :], groups, spread(r1[0]), ALU.subtract).then_inc(s("shifted"), 1)
                experts = logits[:, :, 4:].rearrange("p t (g j) -> p t g j", g=4)
                for t in range(2):
                    dve.tensor_tensor(r16[:, t, :, :], experts[:, t, :, :],
                                      r4[2][:, t, :].rearrange("p (g o) -> p g o", o=1).to_broadcast([P, 4, 4]), ALU.mult)
                step(dve.memset(r1[7][:, :], 0.0))
                step(dve.tensor_tensor(r4[8][:, :, :], r16[:, :, 0, :], r16[:, :, 1, :], ALU.add))
                step(dve.tensor_tensor(r4[9][:, :, :], r16[:, :, 2, :], r16[:, :, 3, :], ALU.add))
                step(dve.tensor_tensor(e_sel, r4[8][:, :, :], r4[9][:, :, :], ALU.add))
                first_largest(e_one, r1[2], e_sel, r1[3])
                dve.tensor_tensor(r4[4][:, :, :], e_sel, spread(r1[2]), ALU.subtract).then_inc(s("shifted"), 1)
                step(dve.scalar_tensor_tensor(r4[8][:, :, :], e_one, -3e38, e_sel, ALU.mult, ALU.add))
                first_largest(e_two, r1[4], r4[8][:, :, :], r1[5])
                step(dve.tensor_tensor(e_one, e_one, e_two, ALU.add))
                dve.wait_ge(s("route_exp"), 2)
                step(dve.tensor_reduce(r1[0][:, :], r4[1][:, :, :], AX.X, ALU.add))
                step(dve.tensor_tensor(r4[9][:, :, :], r4[5][:, :, :], e_one, ALU.mult))
                step(dve.tensor_reduce(r1[1][:, :], r4[9][:, :, :], AX.X, ALU.add))
                step(dve.tensor_tensor(r1[2][:, :], r1[0][:, :], r1[1][:, :], ALU.mult))
                step(dve.reciprocal(r1[3][:, :], r1[2][:, :]))
                step(dve.tensor_tensor(r4[9][:, :, :], r4[9][:, :, :], spread(r1[3]), ALU.mult))
                for g in range(4):
                    step(dve.tensor_tensor(combine[:, :, 4 * g:4 * g + 4], r4[9][:, :, :],
                                           r4[2][:, :, g:g + 1].to_broadcast([P, 2, 4]), ALU.mult))

            p0 = PLAN.at["moe"]["panel"]

            def expert_split(n, i=None):
                if n < 6 * EXPERTS:
                    dve.wait_ge(s("w_hi"), later(p0 + n + 1, i, 6 * EXPERT_TURNS))
                    split_lo(p0 + n)

            def diagonal(x, i=None):
                if x >= 2:
                    dve.wait_ge(s("weight_row"), later(x - 1, i, EXPERT_TURNS))
                for tt in range(2):
                    col = combine[:, tt, x:x + 1] if i is None else combine[:, tt, bass.ds(i * EXPERT_TURNS + x, 1)]
                    ins = dve.tensor_scalar(diag[x % 2][:, tt, :], ident[:, :], col, None, ALU.mult)
                ins.then_inc(s("diag"), 1)

            def gated(x, i=None):
                st = EXPERT_TURNS
                h = e_hid[x % 2]
                flat = lambda v: v[:, :, :].rearrange("p m c -> p (m c)")
                dve.wait_ge(s("e_exp"), later(x + 1, i, st))
                dve.tensor_scalar(e_inv[:, :, :], e_exp[:, :, :], 1.0, None, ALU.add).then_inc(s("e_step"), 1)
                dve.wait_ge(s("e_step"), later(4 * x + 1, i, 4 * st))
                dve.reciprocal(e_inv[:, :, :], e_inv[:, :, :]).then_inc(s("e_step"), 1)
                dve.wait_ge(s("e_step"), later(4 * x + 2, i, 4 * st))
                dve.tensor_tensor(flat(e_inv), flat(e_inv), psum[3 * (x % 2)][:, :], ALU.mult).then_inc(s("e_step"), 1)
                dve.wait_ge(s("e_step"), later(4 * x + 3, i, 4 * st))
                dve.wait_ge(s("expert_done"), later(6 * x + 2 if x else 4, i, 6 * st))
                dve.tensor_tensor(flat(e_inv), flat(e_inv), psum[1][:, :], ALU.mult).then_inc(s("e_step"), 1)
                dve.wait_ge(s("e_step"), later(4 * x + 4, i, 4 * st))
                dve.wait_ge(s("weight_row"), later(x + 1, i, st))
                row = psum[2][:, 0:LAT].rearrange("p (o c) -> p o c", o=1).to_broadcast([P, 2, LAT])
                dve.tensor_tensor(h[:, :, :], e_inv[:, :, :], row, ALU.mult).then_inc(s("e_hid"), 1)
                dve.wait_ge(s("e_hi"), later(x + 1, i, st))
                dve.tensor_tensor(E_lo[x % 2][:, :, :], h[:, :, :], E_hi[x % 2][:, :, :].bitcast(F32),
                                  ALU.subtract).then_inc(s("e_lo"), 1)

            def expert_turn(x, i=None):
                n = 6 * x - 2 if x else 0
                diagonal(x, i)
                for j in range(4):
                    expert_split(n + j + AHEAD, i)
                gated(x, i)
                if x:
                    for j in range(4, 6):
                        expert_split(n + j + AHEAD, i)

            router()
            expert_turn(0)
            with dve.Fori(0, 3) as i:
                for j in range(EXPERT_TURNS):
                    expert_turn(1 + j, i)
            for x in range(1 + 3 * EXPERT_TURNS, EXPERTS):
                expert_turn(x)
            dve.wait_ge(s("expert_done"), 6 * EXPERTS)
            for b in range(4):
                ins = dve.tensor_tensor(X[:, 2 * b:2 * b + 2, 0:LAT], X[:, 2 * b:2 * b + 2, 0:LAT],
                                        psum[4 + b][:, :].rearrange("p (m c) -> p m c", m=2), ALU.add)
            ins.then_inc(s("y_added"), 1)
            norm("final_2", LAT)


DFT_N = 256


def tables():
    n = np.arange(DFT_N)
    angle = 2 * np.pi * ((n[:, None] * n[None, :]) % DFT_N) / DFT_N
    dft = np.concatenate([np.cos(angle), np.sin(angle)], axis=1) / np.sqrt(DFT_N)
    def rope(width, reps):
        n_freq = width // 4
        inv_freq = (np.float32(10000.0) ** (-np.arange(n_freq, dtype=np.float32) / n_freq)).astype(np.float32)
        t = np.arange(LAT)
        where = np.stack([t // 64, t % 64]).astype(np.float32)
        f = np.arange(width)
        turn = where[f // (2 * n_freq)] * inv_freq[f % n_freq][:, None]
        sign = np.where(f // n_freq % 2 == 0, -1.0, 1.0)[:, None]
        both = np.stack([np.cos(turn), np.sin(turn) * sign], axis=1)
        return np.tile(both, (reps, 1, 1)).astype(np.float32)

    return {"dft": dft.astype(np.float32), "rope_diff": rope(HALF, 2), "rope_mla": rope(ROPE, 1)}


def kernel(**inputs):
    import concourse.bacc as bacc
    from concourse.bass_utils import run_bass_kernel_spmd

    nc = bacc.Bacc("TRN2", target_bir_lowering=False, num_devices=1)
    arrays = {f"in_{name}": np.ascontiguousarray(value) for name, value in {**inputs, **tables()}.items()}
    aps = {name[3:]: nc.dram_tensor(name, v.shape, mybir.dt.from_np(v.dtype), kind="ExternalInput").ap()
           for name, v in arrays.items()}
    out = nc.dram_tensor("out", (1, LAT, D), F32, kind="ExternalOutput").ap()
    build_program(nc, aps, out)
    result = run_bass_kernel_spmd(nc, [arrays], core_ids=[0])
    return result.results[0]["out"]
```

```python
from contextlib import ExitStack

import numpy as np
import concourse.bass as bass
from concourse import mybir

F32 = mybir.dt.float32
F32R = mybir.dt.float32r
ACT = mybir.ActivationFunctionType
ALU = mybir.AluOpType
AX = mybir.AxisListType

P = 128
D = 1024
KT = D // P
LAT = 256
CTX = 256
TOK = LAT + CTX
META = 16
TOK2 = LAT + META
DEPTH = 4
FF = 4 * D
FF_BLOCK = 1024
BLOCKS = FF // FF_BLOCK
MOD_TILES = 6 * KT
EPS = 1e-6
LAM_INIT = 0.8 - 0.6 * float(np.exp(-0.3))
HEADS = 8
HALF = 64
O_BATCH = 4
MLA_HEADS = 16
NOPE, ROPE = 64, 32
QD = NOPE + ROPE
Q_RANK, KV_RANK = 256, 128
GLA_HEADS = 4
CHUNK = 64
EXPERTS = 16

RING = 4
RAW = 4
AHEAD = RING - 1
BANKS = 4
ATTENTION_BANKS = {"diff": (4, 5, 6, 7), "mla": (5, 6, 7)}
PANEL = KT * P

VEC_ROWS = {}
VEC_TILES = 3


def place_vectors():
    rows = [0] * VEC_TILES
    plan = [("mod_b_lo", 0, 96), ("c", 0, 8), ("c_ctx", 0, 8), ("mod_b_hi", 1, 96),
            ("norm_mix_g", 2, 32), ("norm_mlp_g", 2, 32), ("final_g", 2, 8), ("fourier_b", 2, 16),
            ("norm_mix_w_2", 2, 8), ("norm_ffn_w_2", 2, 8), ("final_norm_w_2", 2, 8),
            ("pool_scale_2", 2, 4), ("gla_norm_w_2", 2, 1), ("b_gate_2", 2, 2), ("diff_subln_g", 2, 1),
            ("mla_q_norm_g", 2, 2), ("mla_kv_norm_g", 2, 1)]
    for name, tile, n in plan:
        VEC_ROWS[name] = (tile, rows[tile], n)
        rows[tile] += n
    return rows


VEC_COUNT = place_vectors()
FIRST_VECTORS = sum(tile == 0 for tile, _, _ in VEC_ROWS.values())


class Plan:

    def __init__(self):
        self.tiles = []
        self.aux = []
        self.loaded = [0] * RAW
        self.at = {}
        self.units = []
        self.panels = []

    def phase(self, name, units=(), tiles=(), aux=(), frees=()):
        self.at[name] = {"unit": len(self.units), "panel": len(self.panels), "tile": len(self.tiles), "aux": len(self.aux)}
        k = 0
        first = len(self.panels)
        self.panels += [None] * len(frees)
        for panels, dmas in units:
            if isinstance(panels, int):
                panels = range(k, k + panels)
            slot = len(self.units) % RAW
            self.loaded[slot] += 16 * dmas
            for place, panel in enumerate(panels):
                free = frees[panel]
                if isinstance(free, int):
                    free = ("tile_done", len(self.tiles) + free + 1)
                self.panels[first + panel] = (len(self.units), place, free)
                k += 1
            self.units.append((first + max(panels) + 1, slot, self.loaded[slot]))
        assert k == len(frees)
        self.tiles += tiles
        self.aux += aux


AUX_AT = {}


def diff_aux():
    tiles = []

    def add(what, h, i, signal, value):
        AUX_AT["diff", what, h, i] = len(tiles)
        tiles.append((signal, value))

    for turn in range(HEADS + 1 + O_BATCH):
        h = turn - 1
        on = 0 <= h < HEADS
        if on:
            for i in range(4):
                add("score", h, i, "p_exp", 8 * h + i + 1)
        if on:
            for i in range(4, 8):
                add("score", h, i, "p_exp", 8 * h + i + 1)
            for i in range(3):
                add("turn_p", h, i, "pt_lo", 3 * h + i + 1)
        if h >= O_BATCH:
            add("turn_o", h - O_BATCH, 0, "o_g", h - O_BATCH + 1)
        if on:
            add("pv", h, 0, "o_sq", h + 1)
        if turn < HEADS:
            add("turn_v", turn, 0, "v_lo", turn + 1)
    return tiles


def mla_aux():
    tiles = []

    def add(what, h, i, signal, value):
        AUX_AT["mla", what, h, i] = len(tiles)
        tiles.append((signal, value))

    for turn in range(MLA_HEADS + 2):
        h = turn - 1
        for i in range(2):
            if h >= 1:
                add("turn_p", h - 1, i, "mla_pt_lo", 2 * (h - 1) + i + 1)
            if 0 <= h < MLA_HEADS:
                add("score", h, i, "mla_exp", 2 * h + i + 1)
        if turn < MLA_HEADS:
            add("turn_v", turn, 0, "mla_v_lo", turn + 1)
    return tiles


EXPERT_TURNS = 4
WIN_ORDER = [16, 4, 5, 6, 7, 8, 9, 10, 11, 0, 1, 2, 3, 12, 13, 14, 15]
POOL_AT, Q_AT, K_AT, V_AT, R_AT, GATE_AT = 0, 4, 6, 8, 12, 16
GATE_RANK = 16
CHUNKS = [(0, META)] + [(META + CHUNK * n, CHUNK) for n in range(LAT // CHUNK)]
MLP_TILES = 2 * KT


def signals(name, first, n):
    return [(name, first + i + 1) for i in range(n)]


X_AT = {"four0": 0, "mlp0": 8, "diffo": 40, "mlp1": 48, "mlao": 80, "mlp2": 88, "four3": 120,
        "mlp3": 128, "wout": 160, "moe": 168}


def mlp_tiles(layer):
    tiles = []
    for b in range(BLOCKS):
        tiles += signals("relu", KT * (BLOCKS * layer + b), KT)
        tiles += signals("x_done", X_AT[f"mlp{layer}"] + KT * b, KT)
    return tiles


def make_plan():
    p = Plan()
    p.phase("vec", tiles=[("vec", 1)])
    p.phase("xin", tiles=signals("x_cols", 0, KT))
    p.phase("vecs", tiles=[("vec", 2), ("lam_col", 1)])
    p.phase("four0", [(2, 1)] * 4, signals("four_lo", 0, 24) + signals("x_done", 0, KT), frees=[24 + m for m in range(KT)])
    p.phase("mlp0", [(2, 1)] * 32, mlp_tiles(0), frees=range(64))
    pairs = [([h + j, h + j + 3], 1) for h in range(0, 3 * HEADS, 6) for j in range(3)]
    p.phase("diff", pairs, signals("qkv", 0, 24), diff_aux(), frees=range(24))
    p.phase("diffo", [(2, 1)] * 4, signals("x_done", X_AT["diffo"], KT), frees=range(8))
    p.phase("mlp1", [(2, 1)] * 32, mlp_tiles(1), frees=range(64))
    p.phase("mlad", [(2, 1), (1, 1), (1, 1)], signals("down_out", 0, 4), frees=range(4))
    p.phase("mla", [(2, 4), (2, 2), (2, 4)], signals("mla_qkv", 0, 2 * MLA_HEADS), mla_aux(),
            frees=[6, 14, 15, 31, 22, 30])
    p.phase("mlao", [(2, 1)] * 4, signals("x_done", X_AT["mlao"], KT), frees=range(8))
    p.phase("mlp2", [(2, 1)] * 32, mlp_tiles(2), frees=range(64))
    p.phase("four3", [(2, 1)] * 4, signals("four_lo", 24, 16) + signals("x_done", X_AT["four3"], KT),
            frees=[16 + m for m in range(KT)])
    p.phase("mlp3", [(2, 1)] * 32, mlp_tiles(3), frees=range(64))
    p.phase("meta", tiles=[("meta_cols", 1)])
    p.phase("win", [(1, 1)] + [(2, 1)] * 8, signals("proj", 0, 17), frees=range(17))
    p.phase("wout", [(2, 1)] * 4, signals("x_done", X_AT["wout"], KT), frees=range(8))
    panels = 6 * EXPERTS
    p.phase("moe", [(2, 1)] * (panels // 2), frees=[("expert_done", i + 1) for i in range(panels)])
    return p


PLAN = make_plan()

MIX_TILES = []
MIX_AT = {}
for _what, _n, _signal in (("gate", 2, "z_in"), ("turn_v", 5, "v_rows"), ("turn_k", 2, "k_rows"),
                           ("pool", 2, "pool_in"), ("score", 2, "sc_in"), ("state", 2, "states"),
                           ("out", 2, "go_in"), ("square", 2, "go_root")):
    for _i in range(_n):
        MIX_AT[_what, _i] = len(MIX_TILES)
        MIX_TILES.append((_signal, _i + 1 if _signal != "states" else 4 * (_i + 1)))



NORMS = [("mix0", True, TOK), ("mlp0", True, TOK), ("mix1", True, TOK), ("mlp1", True, TOK),
         ("mix2", True, TOK), ("mlp2", True, LAT), ("mix3", True, LAT), ("mlp3", True, LAT),
         ("final", False, LAT), ("mix_2", True, TOK2), ("ffn_2", True, LAT), ("final_2", False, LAT)]
SPLIT_NORMS = {name for name, split, _ in NORMS if split}
NORM_AT = {name: i for i, (name, _, _) in enumerate(NORMS)}
SPLIT_AT = {name: sum(s for _, s, _ in NORMS[:i]) for i, (name, _, _) in enumerate(NORMS)}
MOD_RING = 4
MOD_COLS = 6 * D // BLOCKS
MOD_UNITS = KT
MOD_PART = MOD_COLS // 4
MOD_AFTER = {1: 0, 2: 1, 4: 2, 5: 3, 7: 4, 8: 5, 10: 6, 11: 7}
MOD_ROWS_AT, MOD_TURN_AT = 12, 14


def build_program(nc, a, out):
    ctx = ExitStack()
    sems = {}

    def s(name):
        if name not in sems:
            sems[name] = ctx.enter_context(nc.semaphore(name))
        return sems[name]

    with ctx:
        base = 16512
        at = {}

        def sb(name, shape, dtype=F32, over=None):
            nonlocal base
            size = int(np.prod(shape[1:])) * 4
            size = (size + 31) // 32 * 32
            if over is None:
                place, base = base, base + size
            else:
                place = over
            at[name] = place
            return nc.alloc_sbuf_tensor_at(name, list(shape), dtype, offset=place)

        X = sb("x", [P, KT, TOK])
        H_hi = sb("h_hi", [P, KT, TOK], F32R)
        H_lo = sb("h_lo", [P, KT, TOK], F32R)
        G_hi = sb("g_hi", [P, KT, TOK], F32R)
        G_lo = sb("g_lo", [P, KT, TOK], F32R)
        x_rows = sb("x_rows", [P, 4, D], over=at["g_hi"])
        W_hi = [sb(f"w_hi{r}", [P, PANEL], F32R) for r in range(RING)]
        W_lo = [sb(f"w_lo{r}", [P, PANEL], F32R) for r in range(RING)]
        w_raw = [sb(f"w_raw{r}", [P, KT, 2, P]) for r in range(RAW)]
        ident = sb("ident", [P, P])
        ones = sb("ones", [P, P])
        eps = sb("eps", [P, 1])
        vec_rows = sb("vec_rows", [P, VEC_TILES, P])
        vec = sb("vec", [P, VEC_TILES, P])
        lam_in = sb("lam_in", [1, 4, HALF])
        lam_prod = sb("lam_prod", [1, 2, HALF])
        lam_row = sb("lam_row", [1, 4])
        lam_col = sb("lam_col", [P, 2])
        subln = sb("subln", [P, 1])
        silu_c = sb("silu_c", [P, KT, 32])
        silu_t = sb("silu_t", [P, 2, KT])
        mod = [sb(f"mod{r}", [P, MOD_TILES, 2]) for r in range(2)]
        scale_mix = sb("scale_mix", [P, KT, 2])
        scale_mlp = sb("scale_mlp", [P, KT, 2])
        gated_b = sb("gated_b", [P, KT, 2])
        norm_buf = [sb(f"norm{r}", [P, TOK]) for r in range(6)]
        work = base
        mod_raw = [sb(f"mod_raw{r}", [P, MOD_COLS]) for r in range(MOD_RING)]
        mod_rows = sb("mod_rows", [P, MOD_PART])
        mlp_work = base
        relu = [sb(f"relu{r}", [P, TOK]) for r in range(2)]
        square = [sb(f"square{r}", [P, TOK]) for r in range(2)]
        base = mlp_work
        dft = sb("dft", [P, 2, 2 * 256])
        dft_hi = sb("dft_hi", [P, 2, 2 * 256], F32R)
        dft_lo = sb("dft_lo", [P, 2, 2 * 256], F32R)
        base = work
        rope = sb("rope", [P, 2, LAT])
        q_f = sb("q_f", [P, TOK])
        k_f = sb("k_f", [P, TOK])
        v_f = q_f
        q_hi, q_lo = sb("q_hi", [P, TOK], F32R), sb("q_lo", [P, TOK], F32R)
        k_hi, k_lo = sb("k_hi", [P, TOK], F32R), sb("k_lo", [P, TOK], F32R)
        v_hi, v_lo = sb("v_hi", [P, 4, P], F32R), sb("v_lo", [P, 4, P], F32R)
        p_raw = [[sb(f"p_raw{r}{j}", [P, TOK]) for j in range(2)] for r in range(2)]
        p_all = sb("p_all", [P, 2 * TOK + 2 * CTX])
        pt_hi, pt_lo = sb("pt_hi", [P, 6, LAT], F32R), sb("pt_lo", [P, 6, LAT], F32R)
        neg_max = sb("neg_max", [P, 8])
        z = sb("z", [P, 8])
        z_inv = sb("z_inv", [P, 8])
        z_mix = sb("z_mix", [P, 8])
        o_rows, o_g = norm_buf[:O_BATCH], norm_buf[4]
        o_sum = sb("o_sum", [P, 4 * HEADS], over=at["lam_in"])
        o_inv = sb("o_inv", [P, 4 * HEADS], over=at["lam_prod"])
        squares = p_raw[0][0]
        turned, straight = norm_buf[5][:, 0:LAT], norm_buf[5][:, LAT:TOK]
        assert base <= 229344, base
        base = work
        rope32 = sb("rope32", [P, 2, LAT])
        cq_f = sb("cq_f", [P, 2, LAT])
        ckv_f = sb("ckv_f", [P, TOK])
        cq_hi, cq_lo = sb("cq_hi", [P, 2, LAT], F32R), sb("cq_lo", [P, 2, LAT], F32R)
        ckv_hi, ckv_lo = sb("ckv_hi", [P, TOK], F32R), sb("ckv_lo", [P, TOK], F32R)
        mq_f = sb("mq_f", [P, LAT])
        kv_f = sb("kv_f", [P, TOK])
        mq_hi, mq_lo = sb("mq_hi", [P, LAT], F32R), sb("mq_lo", [P, LAT], F32R)
        mk_hi, mk_lo = sb("mk_hi", [P, TOK], F32R), sb("mk_lo", [P, TOK], F32R)
        mv_hi = [sb(f"mv_hi{j}", [P, 4, P], F32R) for j in range(2)]
        mv_lo = [sb(f"mv_lo{j}", [P, 4, P], F32R) for j in range(2)]
        mp_raw = [sb(f"mp_raw{r}", [P, TOK], over=at[("cq_f", "ckv_f")[r]]) for r in range(2)]
        mp_all = sb("mp_all", [P, 2, TOK])
        mpt_hi, mpt_lo = sb("mpt_hi", [P, 4, LAT], F32R), sb("mpt_lo", [P, 4, LAT], F32R)
        m_max = sb("m_max", [P, 2])
        m_z = sb("m_z", [P, 2])
        m_zinv = sb("m_zinv", [P, 2])
        assert base <= 229344, base

        base = work
        meta_rows = sb("meta_rows", [META, D])
        pool_w = sb("pool_w", [P, 4, P])
        gate_up = sb("gate_up", [GATE_RANK, 2 * P])
        route_w = sb("route_w", [P, KT, 4 + EXPERTS])
        route_b = sb("route_b", [1, 4 + EXPERTS])
        chunk_mask = sb("chunk_mask", [P, TOK2])
        S_all = sb("S_all", [P, 2, 4, P])
        second_work = base
        base = at["g_hi"]
        proj = sb("proj", [P, 17, TOK2])
        pooled = sb("pooled", [P, 4, LAT])
        win_a = sb("win_a", [P, 4, TOK2])
        win_b = sb("win_b", [P, 4, TOK2])
        assert base <= at["w_hi0"]
        base = at["h_hi"]
        Y_hi, Y_lo = sb("Y_hi", [P, KT, LAT], F32R), sb("Y_lo", [P, KT, LAT], F32R)
        go_f = sb("go_f", [P, GLA_HEADS, LAT])
        r_silu = sb("r_silu", [P, GLA_HEADS, LAT])
        y_f = sb("y_f", [P, 4, LAT])
        sc = sb("sc", [CHUNK, GLA_HEADS, 4, CHUNK])
        assert base <= at["g_hi"]
        base = at["norm0"]
        z_f = sb("z_f", [P, 2, TOK2])
        z_abs = sb("z_abs", [P, 2, TOK2])
        log_a = sb("log_a", [P, 2, TOK2])
        b_cum = sb("b_cum", [P, 2, TOK2])
        e_pos = sb("e_pos", [P, 2, TOK2])
        assert base <= work
        base = second_work
        e_neg = sb("e_neg", [P, 2, LAT])
        e_end = sb("e_end", [P, 2, TOK2])
        q_pad = [sb(f"q_pad{j}", [P, 2, LAT]) for j in range(2)]
        k_t = sb("k_t", [P, 2, LAT])
        k_end = sb("k_end", [P, 2, TOK2])
        v_rows_m = sb("v_rows_m", [META, GLA_HEADS, P])
        k_rows_m = sb("k_rows_m", [META, 2, P])
        b_last = sb("b_last", [P, 2, 4])
        decay = sb("decay", [P, 2, 4])
        v_rows = sb("v_rows", [CHUNK, GLA_HEADS, 4, P])
        k_rows = sb("k_rows", [CHUNK, 2, 3, P])
        go_sq, go_inv = win_a[:, :, 0:LAT], win_b[:, :, 0:LAT]
        assert base <= 229344, base
        base = second_work
        logits = sb("logits", [P, 2, 4 + EXPERTS])
        r4 = [sb(f"r4_{i}", [P, 2, 4]) for i in range(12)]
        r1 = [sb(f"r1_{i}", [P, 2]) for i in range(8)]
        r16 = sb("r16", [P, 2, 4, 4])
        rank = sb("rank", [P, 2, 4])
        combine = sb("combine", [P, 2, EXPERTS])
        diag = [sb(f"diag{j}", [P, 2, P]) for j in range(2)]
        e_silu = sb("e_silu", [P, 2, LAT])
        e_up = sb("e_up", [P, 2, LAT])
        e_hid = [sb(f"e_hid{j}", [P, 2, LAT]) for j in range(2)]
        E_hi = [sb(f"E_hi{j}", [P, 2, LAT], F32R) for j in range(2)]
        E_lo = [sb(f"E_lo{j}", [P, 2, LAT], F32R) for j in range(2)]
        zero_row = sb("zero_row", [1, TOK])
        out_rows = sb("out_rows", [P, 2, D])
        assert base <= 229344, base

        psum = [ctx.enter_context(nc.psum_tensor(f"bank{b}", [P, 512], F32)) for b in range(8)]
        bank = psum[:BANKS]
        mod_ps = psum[4]
        pv_ps = psum[4]
        mix_ps = psum[4:8]
        sum_ps = psum[7]

        def vcol(name, k=0):
            tile, row, _ = VEC_ROWS[name]
            return vec[:, tile, row + k:row + k + 1]

        def vcols(name, first=0, n=None):
            tile, row, count = VEC_ROWS[name]
            n = count if n is None else n
            return vec[:, tile, row + first:row + first + n]

        def later(value, i, step):
            return value if i is None else value + i * step

        def attention_tile(phase, what, h, i=0):
            n, ring = AUX_AT[phase, what, h, i], ATTENTION_BANKS[phase]
            return PLAN.at[phase]["aux"] + n + 1, psum[ring[n % len(ring)]]

        w1 = a["mlp_w1"].rearrange("l (k p) (b u c) -> l b u p k c", p=P, b=BLOCKS, u=4)
        w2 = a["mlp_w2"].rearrange("l (b k p) (u c) -> l b u p k c", p=P, b=BLOCKS, u=4)
        mod_w = a["mod_w"].rearrange("l (k p) (b c) -> l b k p c", p=P, b=BLOCKS)

        block = ctx.enter_context(nc.Block())

        @block.sync
        def _(sp):
            def wait_raw_free(u, i=None, step=0):
                if u >= RAW:
                    sp.wait_ge(s("panel_ready"), later(PLAN.units[u - RAW][0], i, step))

            def load_unit(u, parts, i=None, step=0):
                wait_raw_free(u, i, step)
                slot = PLAN.units[u][1]
                for dst, src in parts:
                    sp.dma_start(dst(w_raw[slot]), src).then_inc(s(f"raw_in{slot}"), 16)

            def whole(raw):
                return raw[:, :, :, :].rearrange("p k j c -> p k (j c)")

            def load_square(name, w):
                v = w.rearrange("(k p) (u c) -> u p k c", p=P, c=2 * P)
                for u in range(4):
                    load_unit(PLAN.at[name]["unit"] + u, [(whole, v[u])])

            def load_mod(layer, block, u, n0, i=None):
                n = n0 + u
                if n >= MOD_RING:
                    sp.wait_ge(s("mod_used"), later(n - MOD_RING + 1, i, MOD_UNITS))
                sp.dma_start(mod_raw[u % MOD_RING][:, :], mod_w[layer, block, u]).then_inc(s(f"mod_in{u % MOD_RING}"), 16)

            def load_mlp(layer, with_mod):
                u0 = PLAN.at[f"mlp{layer}"]["unit"]
                n0 = BLOCKS * MOD_UNITS * (layer + 1)

                def weights(u, b, i):
                    w = w1[layer, b, u] if u < 4 else w2[layer, b, u - 4]
                    load_unit(u0 + u, [(whole, w)], i, 2 * KT)

                def block(b, order, i):
                    for what, u in order:
                        if what == "w":
                            weights(u, b, i)
                        elif what == "M":
                            load_mod(layer + 1, 0, u, n0)
                        else:
                            load_mod(layer + 1, b + 1, u, n0 + MOD_UNITS, i)

                def order(text):
                    return [(x[0], int(x[1])) for x in text.split()]

                if with_mod:
                    block(0, order("M0 M1 M2 M3 w0 w1 w2 w3 w4 M4 M5 M6 M7 m0 w5 m1 w6 m2 m3 w7 m4 m5 m6 m7"), None)
                    with sp.Fori(1, BLOCKS - 1) as b:
                        block(b, order("w0 m0 w1 m1 w2 m2 m3 w3 w4 w5 m4 w6 m5 m6 w7 m7"), b)
                    with sp.Fori(BLOCKS - 1, BLOCKS) as b:
                        block(b, order("w0 w1 w2 w3 w4 w5 w6 w7"), b)
                else:
                    with sp.Fori(0, BLOCKS) as b:
                        block(b, order("w0 w1 w2 w3 w4 w5 w6 w7"), b)

            mod_b = a["mod_b"].rearrange("l (r c) -> (l r) c", c=P)
            rows = {"mod_b_lo": mod_b[0:96], "mod_b_hi": mod_b[96:192],
                    "c": a["c"].rearrange("o (r c) -> (o r) c", c=P),
                    "c_ctx": a["c_ctx"].rearrange("(r c) -> r c", c=P),
                    "final_g": a["final_g"].rearrange("(r c) -> r c", c=P),
                    "final_norm_w_2": a["final_norm_w_2"].rearrange("(r c) -> r c", c=P)}

            def load_vectors(tiles):
                for name, (tile, row, n) in VEC_ROWS.items():
                    if tile in tiles:
                        src = rows[name] if name in rows else a[name].rearrange("l (r c) -> (l r) c", c=P)
                        sp.dma_start(vec_rows[row:row + n, tile, :], src).then_inc(s("vec_in" if tile else "first_vec_in"), 16)

            load_vectors([0])
            for u in range(MOD_RING):
                load_mod(0, 0, u, 0)
            sp.dma_start(x_rows[:, 0:2, :], a["x"][0].rearrange("(t p) d -> p t d", p=P)).then_inc(s("x_in"), 16)
            sp.dma_start(x_rows[:, 2:4, :], a["ctx"][0].rearrange("(t p) d -> p t d", p=P)).then_inc(s("x_in"), 16)
            load_vectors([1, 2])
            for n, name in enumerate(["diff_lambda_q1", "diff_lambda_q2", "diff_lambda_k1", "diff_lambda_k2"]):
                sp.dma_start(lam_in[:, n, :], a[name]).then_inc(s("vec_in"), 16)
            sp.dma_start(dft[:, :, :], a["dft"].rearrange("(k p) c -> p k c", p=P)).then_inc(s("dft_in"), 16)

            for b in range(BLOCKS):
                if b == 2:
                    load_square("four0", a["fourier_w"][0])
                for u in range(MOD_RING if b == 0 else 0, MOD_UNITS):
                    load_mod(0, b, u, MOD_UNITS * b)
            load_mlp(0, True)
            w_qkv = a["diff_w_qkv"][0].rearrange("(k p) (three m c) -> m three p k c", p=P, three=3, c=2 * P)
            sp.wait_ge(s("mod_used"), 2 * BLOCKS * MOD_UNITS)
            sp.dma_start(rope[:, :, :], a["rope_diff"]).then_inc(s("rope_in"), 16)
            for h in range(HEADS // 2):
                for j in range(3):
                    load_unit(PLAN.at["diff"]["unit"] + 3 * h + j, [(whole, w_qkv[h, j])])
            load_square("diffo", a["diff_w_o"][0])
            sp.wait_ge(s("o_lo"), KT)
            load_mlp(1, True)
            sp.wait_ge(s("mod_used"), 3 * BLOCKS * MOD_UNITS)
            sp.dma_start(rope32[HALF:HALF + ROPE, :, :], a["rope_mla"]).then_inc(s("rope_in"), 16)
            down = a["mla_w_down"][0].rearrange("(k p) c -> p k c", p=P)
            u = PLAN.at["mlad"]["unit"]
            load_unit(u, [(whole, down[:, :, 0:Q_RANK])])
            load_unit(u + 1, [(lambda raw: raw[:, :, 0, :], down[:, :, Q_RANK:Q_RANK + KV_RANK])])
            load_unit(u + 2, [(lambda raw: raw[:, :, 0, 0:QD], down[:, :, Q_RANK + KV_RANK - NOPE:])])
            uq = a["mla_w_uq"][0].rearrange("(k p) (g h c) -> g k p h c", p=P, g=4, c=QD)
            ukv = a["mla_w_ukv"][0].rearrange("p (j h c) -> j p h c", j=2, c=P)
            u = PLAN.at["mla"]["unit"]

            def load_uq(u, g0):
                load_unit(u, [(lambda raw, j=j, k=k: raw[:, 4 * k:4 * k + 4, j, 0:QD], uq[g0 + j, k])
                              for j in range(2) for k in range(2)])

            load_uq(u, 0)
            load_unit(u + 1, [(lambda raw, j=j: raw[:, :, j, :], ukv[j]) for j in range(2)])
            load_uq(u + 2, 2)
            load_square("mlao", a["mla_w_o"][0])
            sp.wait_ge(s("mla_o_lo"), KT)
            load_mlp(2, True)
            sp.wait_ge(s("g_lo"), 3 * KT * BLOCKS)
            sp.dma_start(dft[:, :, :], a["dft"].rearrange("(k p) c -> p k c", p=P)).then_inc(s("dft_in"), 16)
            load_square("four3", a["fourier_w"][1])
            load_mlp(3, False)
            sp.wait_ge(s("mod_used"), DEPTH * BLOCKS * MOD_UNITS)
            small = [(meta_rows[:, :], a["meta_tokens_2"]),
                     (pool_w[:, :, :], a["pool_w_2"][0].rearrange("g c d -> c g d")),
                     (gate_up[:, :], a["w_gate_up_2"][0]),
                     (route_w[:, :, 0:4], a["w_router_group_2"][0].rearrange("(k p) c -> p k c", p=P)),
                     (route_w[:, :, 4:], a["w_router_expert_2"][0].rearrange("(k p) c -> p k c", p=P)),
                     (route_b[:, 0:4], a["b_router_group_2"]),
                     (route_b[:, 4:], a["b_router_expert_2"])]
            for dst, src in small:
                sp.dma_start(dst, src).then_inc(s("small_in"), 16)
            w_in = a["w_in_2"][0].rearrange("(k p) c -> p k c", p=P)
            u = PLAN.at["win"]["unit"]
            load_unit(u, [(lambda raw: raw[:, :, 0, 0:GATE_RANK], w_in[:, :, GATE_AT * P:])])
            for i in range(8):
                c = WIN_ORDER[1 + 2 * i] * P
                load_unit(u + 1 + i, [(whole, w_in[:, :, c:c + 2 * P])])
            load_square("wout", a["w_out_2"][0])
            w_gate = a["w_expert_gate_2"][0].rearrange("e (k p) c -> e p k c", p=P)
            w_up = a["w_expert_up_2"][0].rearrange("e (k p) c -> e p k c", p=P)
            w_down = a["w_expert_down_2"][0].rearrange("e (k p) c -> e p k c", p=P)

            def down_rows(raw):
                return raw[:, :, :, :].rearrange("p (k a) j c -> p k (a j c)", k=2)

            u = PLAN.at["moe"]["unit"]

            def load_experts(x, place, i=None):
                first = u + 3 * place - 1 if place else u
                step = 6 * EXPERT_TURNS
                load_unit(first, [(whole, w_gate[x])], i, step)
                load_unit(first + 1, [(whole, w_up[x])], i, step)
                if place:
                    load_unit(first + 2, [(down_rows, w_down[x - 1])], i, step)

            load_experts(0, 0)
            with sp.Fori(0, 3) as i:
                for j in range(EXPERT_TURNS):
                    load_experts(i * EXPERT_TURNS + (1 + j), 1 + j, i)
            for x in range(1 + 3 * EXPERT_TURNS, EXPERTS):
                load_experts(x, x)
            load_unit(u + 3 * EXPERTS - 1, [(down_rows, w_down[EXPERTS - 1])])
            out_v = out[0].rearrange("(t p) d -> p t d", p=P)
            for tt in range(2):
                sp.wait_ge(s("out_rows"), 2 * tt + 2)
                sp.dma_start(out_v[:, tt, :], out_rows[:, tt, :]).then_inc(s("out"), 16)
            sp.wait_ge(s("out"), 32)

        @block.gpsimd
        def _(pool):
            pool.memset(ident[:, :], 0.0).then_inc(s("const"), 1)
            pool.memset(ones[:, :], 1.0).then_inc(s("const"), 1)
            pool.memset(eps[:, :], EPS).then_inc(s("const"), 1)
            pool.memset(silu_c[:, :, :], 0.0).then_inc(s("const"), 1)
            pool.wait_ge(s("const"), 4)
            pool.affine_select(out=ident[:, :], in_=ident[:, :], compare_op=ALU.not_equal, fill=1.0,
                               base=0, pattern=[[-1, P]], channel_multiplier=1).then_inc(s("const"), 1)

            for h in range(MLA_HEADS):
                pool.wait_ge(s("mla_k_hi"), h + 1)
                pool.tensor_tensor(mk_lo[0:NOPE, :], kv_f[0:NOPE, :], mk_hi[0:NOPE, :].bitcast(F32),
                                   ALU.subtract).then_inc(s("mla_k_lo"), 1)
            for i in range(2):
                pool.wait_ge(s("sc_in"), i + 1)
                pool.affine_select(out=sc[:, 2 * i:2 * i + 2, :, :].rearrange("p h n c -> p (h n) c"),
                                   in_=sc[:, 2 * i:2 * i + 2, :, :].rearrange("p h n c -> p (h n) c"),
                                   compare_op=ALU.is_ge, fill=0.0, base=0, pattern=[[0, 8], [1, CHUNK]],
                                   channel_multiplier=-1).then_inc(s("sc_masked"), 1)

        @block.scalar
        def _(act):
            def split_hi(n, i=None, tiles=0, raws=0):
                if isinstance(i, int):
                    n, i = n + i * MLP_TILES, None
                unit, place, _ = PLAN.panels[n]
                _, slot, value = PLAN.units[unit]
                act.wait_ge(s(f"raw_in{slot}"), later(value, i, raws))
                if n >= RING:
                    name, freed = PLAN.panels[n - RING][2]
                    act.wait_ge(s(name), later(freed, i, tiles))
                act.activation(W_hi[n % RING][:, :].rearrange("p (k c) -> p k c", c=P),
                               w_raw[slot][:, :, place, :], ACT.Copy).then_inc(s("w_hi"), 1)

            def square(name, n_cols, k, x_done=None):
                ni, c = NORM_AT[name], slice(0, n_cols)
                if x_done is not None:
                    act.wait_ge(s("x_done"), x_done)
                if k >= 2:
                    act.wait_ge(s("sq_added"), KT * ni + k - 1)
                elif ni:
                    act.wait_ge(s("h"), KT * ni)
                act.activation(norm_buf[k % 2][:, c], X[:, k, c], ACT.Square).then_inc(s("sq"), 1)

            def root(name, n_cols):
                ni, c = NORM_AT[name], slice(0, n_cols)
                act.wait_ge(s("sum"), ni + 1)
                act.activation(norm_buf[3][:, c], sum_ps[:, c], ACT.Sqrt, bias=eps[:, 0:1],
                               scale=1.0 / D).then_inc(s("root"), 1)

            def apply(name, n_cols, segments, pairs):
                ni, c = NORM_AT[name], slice(0, n_cols)
                for k in range(KT):
                    act.wait_ge(s("t"), KT * ni + k + 1)
                    if pairs is not None and k >= 2:
                        act.wait_ge(s("h_lo"), KT * pairs + k - 1)
                    for c0, cn, scale, shift, *to in segments:
                        d0 = to[0] if to else c0
                        dst = norm_buf[4 + k % 2][:, d0:d0 + cn] if pairs is not None else X[:, k, c0:c0 + cn]
                        ins = act.activation(dst, norm_buf[k % 2][:, c0:c0 + cn], ACT.Identity,
                                             bias=shift(k) if shift else 0.0, scale=scale(k))
                    ins.then_inc(s("h"), 1)
                    if pairs is not None:
                        act.wait_ge(s("h"), KT * ni + k + 1)
                        act.activation(H_hi[:, k, c], norm_buf[4 + k % 2][:, c], ACT.Copy).then_inc(s("h_hi"), 1)

            def mod_apply(name, layer, n_cols):
                m = mod[layer % 2]
                mix = name.startswith("mix")
                act.wait_ge(s("scales_mix" if mix else "scales_mlp"), layer + 1)
                shift_at = 0 if mix else 3 * KT
                scales = scale_mix if mix else scale_mlp
                segs = [(st * LAT, LAT, lambda k, st=st: scales[:, k, st:st + 1],
                         lambda k, st=st: m[:, shift_at + k, st:st + 1]) for st in range(n_cols // LAT)]
                apply(name, n_cols, segs, SPLIT_AT[name])

            def mod_norm(name, layer, n_cols):
                root(name, n_cols)
                mod_apply(name, layer, n_cols)

            def copy_mod_rows(g, i=None):
                act.wait_ge(s("mod_used"), later(MOD_UNITS * (g + 1), i, MOD_UNITS))
                act.activation(mod_rows[:, :], mod_ps[:, 0:MOD_PART], ACT.Copy).then_inc(s("mod_rows_in"), 1)

            def output_splits(name, norm_name, n_cols):
                for m in range(KT):
                    split_hi(PLAN.at[name]["panel"] + m + AHEAD)
                    if m:
                        square(norm_name, n_cols, m - 1, X_AT[name] + m)
                square(norm_name, n_cols, KT - 1, X_AT[name] + KT)

            def fourier(name, streams):
                t = PLAN.at[name]["tile"]
                n_tok = 2 * streams
                for g in range(4):
                    if name == "four0" and g == 3:
                        for n in range(AHEAD):
                            split_hi(PLAN.at[name]["panel"] + n)
                    for tt in range(n_tok):
                        act.wait_ge(s("tile_done"), t + 1)
                        act.activation(G_hi[:, 4 * (g % 2) + tt, 0:256], bank[t % BANKS][:, 0:256], ACT.Copy)
                        act.activation(G_hi[:, 4 * (g % 2) + tt, 256:512], bank[t % BANKS][:, 256:512],
                                       ACT.Copy, scale=-1.0).then_inc(s("four_hi"), 1)
                        t += 1
                    if name == "four0" and g % 2:
                        copy_mod_rows(2 + g // 2)
                    for m in range(2):
                        act.wait_ge(s("tile_done"), t + 1)
                        act.activation(H_hi[:, 2 * g + m, 0:streams * LAT], bank[t % BANKS][:, 0:streams * LAT],
                                       ACT.Copy).then_inc(s("four_hi"), 1)
                        t += 1

            def mlp(layer, n_cols, with_mod, next_norm):
                at0 = PLAN.at[f"mlp{layer}"]
                p0, t0 = at0["panel"], at0["tile"]
                h0 = KT * BLOCKS * layer
                def hidden_block(b, last=False):
                    for j in range(MLP_TILES):
                        split_hi(p0 + j + AHEAD, b, MLP_TILES, 2 * 16)
                        if with_mod and not last and j == MOD_ROWS_AT:
                            copy_mod_rows(BLOCKS * (layer + 1) + 1, b)
                        if last and j > KT:
                            square(*next_norm, j - KT - 1, X_AT[f"mlp{layer}"] + KT * (BLOCKS - 2) + j)
                        if j < KT:
                            act.wait_ge(s("tile_done"), later(t0 + j + 1, b, MLP_TILES))
                            if layer or j >= 2:
                                act.wait_ge(s("g_sq"), later(h0 + j - 1, b, KT))
                            act.activation(relu[j % 2][:, 0:n_cols], bank[(t0 + j) % BANKS][:, 0:n_cols],
                                           ACT.Relu).then_inc(s("relu"), 1)
                            act.wait_ge(s("relu"), later(h0 + j + 1, b, KT))
                            act.activation(G_hi[:, j, 0:n_cols], relu[j % 2][:, 0:n_cols],
                                           ACT.Square).then_inc(s("g_hi"), 1)

                if with_mod:
                    copy_mod_rows(BLOCKS * (layer + 1))
                with act.Fori(0, BLOCKS - 1) as b:
                    hidden_block(b)
                hidden_block(BLOCKS - 1, True)
                square(*next_norm, KT - 1, X_AT[f"mlp{layer}"] + KT * BLOCKS)

            act.wait_ge(s("tile_done"), 1)
            act.activation(vec[:, 0, 0:VEC_COUNT[0]], bank[0][:, 0:VEC_COUNT[0]], ACT.Copy).then_inc(s("vec"), 1)
            act.wait_ge(s("vec"), 1)
            act.activation(silu_t[:, :, :], vcols("c", 0, 16).rearrange("p (s k) -> p s k", s=2),
                           ACT.Exp, scale=-1.0).then_inc(s("silu_exp"), 1)
            t0 = PLAN.at["xin"]["tile"]
            for k in range(KT):
                act.wait_ge(s("tile_done"), t0 + k + 1)
                act.activation(X[:, k, :], bank[(t0 + k) % BANKS][:, :], ACT.Copy).then_inc(s("x_cols"), 1)
            t0 = PLAN.at["vecs"]["tile"]
            act.wait_ge(s("tile_done"), t0 + 1)
            for v in range(1, VEC_TILES):
                ins = act.activation(vec[:, v, 0:VEC_COUNT[v]], bank[t0 % BANKS][:, v * P:v * P + VEC_COUNT[v]], ACT.Copy)
            ins.then_inc(s("vec"), 1)
            copy_mod_rows(0)
            act.wait_ge(s("lam"), 2)
            act.activation(lam_row[:, 2:4], lam_row[:, 0:2], ACT.Exp).then_inc(s("lam_exp"), 1)
            act.wait_ge(s("dft_in"), 16)
            act.activation(dft_hi[:, :, :], dft[:, :, :], ACT.Copy).then_inc(s("dft_hi"), 1)
            act.wait_ge(s("x_cols"), KT)
            for k in range(KT):
                square("mix0", TOK, k)
            root("mix0", TOK)
            copy_mod_rows(1)
            mod_apply("mix0", 0, TOK)
            fourier("four0", 2)
            output_splits("four0", "mlp0", TOK)
            mod_norm("mlp0", 0, TOK)
            mlp(0, TOK, True, ("mix1", TOK))
            def exps(h, tiles):
                def scaled(qt):
                    n = TOK if qt < 2 else CTX
                    act.wait_ge(s("z_mix"), 4 * h + qt + 1)
                    act.activation(p_raw[qt % 2][1][:, 0:n], p_raw[qt % 2][1][:, 0:n], ACT.Identity,
                                   scale=z_mix[:, 2 * qt + 1:2 * qt + 2]).then_inc(s("p_scaled"), 1)

                for qt in tiles:
                    n = TOK if qt < 2 else CTX
                    for j in range(2):
                        i = 2 * qt + j
                        act.wait_ge(s("neg_max"), 8 * h + i + 1)
                        if 4 * h + qt >= 2:
                            act.wait_ge(s("p_mix"), 4 * h + qt - 1)
                        _, ps = attention_tile("diff", "score", h, i)
                        act.activation(p_raw[qt % 2][j][:, 0:n], ps[:, 0:n], ACT.Exp,
                                       bias=neg_max[:, i:i + 1], accum_out=z[:, i:i + 1]).then_inc(s("p_exp"), 1)
                    if qt > tiles[0]:
                        scaled(qt - 1)
                scaled(tiles[-1])

            def diff_attention():
                t0, p0 = PLAN.at["diff"]["tile"], PLAN.at["diff"]["panel"]

                def take(turn, j, dst, scale=1.0):
                    t = t0 + 3 * turn + j
                    act.wait_ge(s("tile_done"), t + 1)
                    if j == 2:
                        act.wait_ge(s("qk_lo"), 2 * turn + 1)
                    elif turn:
                        act.wait_ge(s("qk_lo"), 2 * turn - 1 + j)
                    act.activation(dst[:, :], bank[t % BANKS][:, :], ACT.Copy, scale=scale).then_inc(s("qkv"), 1)

                for turn in range(HEADS + 1 + O_BATCH):
                    h = turn - 1
                    on = 0 <= h < HEADS
                    ready = h - O_BATCH
                    if turn < HEADS:
                        split_hi(p0 + 3 * turn + AHEAD)
                    if on:
                        exps(h, (0, 1))
                    if turn < HEADS:
                        take(turn, 0, q_f, HALF ** -0.5)
                    if on:
                        exps(h, (2, 3))
                    if turn < HEADS:
                        split_hi(p0 + 3 * turn + 1 + AHEAD)
                        take(turn, 1, k_f)
                    if on:
                        for i in range(3):
                            done, ps = attention_tile("diff", "turn_p", h, i)
                            act.wait_ge(s("aux_done"), done)
                            act.activation(pt_hi[:, 2 * i:2 * i + 2, :].rearrange("p a b -> p (a b)"), ps[:, :],
                                           ACT.Copy).then_inc(s("pt_hi"), 1)
                    if turn < HEADS:
                        for j, (dst, src) in enumerate(((q_hi, q_f), (k_hi, k_f))):
                            act.wait_ge(s("roped"), 2 * turn + j + 1)
                            act.activation(dst[:, :], src[:, :], ACT.Copy).then_inc(s("qk_hi"), 1)
                        split_hi(p0 + 3 * turn + 2 + AHEAD)
                    if ready >= 0 and ready % O_BATCH == 0:
                        c = slice(4 * ready, 4 * (ready + O_BATCH))
                        act.wait_ge(s("o_sq"), h)
                        act.activation(o_inv[:, c], o_sum[:, c], ACT.Sqrt, bias=eps[:, 0:1],
                                       scale=1.0 / P).then_inc(s("o_root"), 1)
                    if turn < HEADS:
                        take(turn, 2, v_f)
                    if ready >= 0:
                        done, ps = attention_tile("diff", "turn_o", ready)
                        act.wait_ge(s("aux_done"), done)
                        if ready:
                            act.wait_ge(s("o_lo"), ready)
                        act.activation(o_g[:, :], ps[:, :], ACT.Identity, scale=subln[:, 0:1]).then_inc(s("o_g"), 1)
                        act.wait_ge(s("o_g"), ready + 1)
                        act.activation(G_hi[:, ready, :], o_g[:, :], ACT.Copy).then_inc(s("o_hi"), 1)
                    if on:
                        done, ps = attention_tile("diff", "pv", h)
                        act.wait_ge(s("aux_done"), done)
                        act.activation(o_rows[h % O_BATCH][:, :], ps[:, :], ACT.Copy)
                        if h:
                            act.wait_ge(s("o_sq"), h)
                        for tt in range(4):
                            c = slice(tt * P, (tt + 1) * P)
                            ins = act.activation(squares[:, c], ps[:, c], ACT.Square,
                                                 accum_out=o_sum[:, 4 * h + tt:4 * h + tt + 1])
                        ins.then_inc(s("o_sq"), 1)
                    if turn < HEADS:
                        done, ps = attention_tile("diff", "turn_v", turn)
                        act.wait_ge(s("aux_done"), done)
                        act.activation(v_hi[:, :, :].rearrange("p a b -> p (a b)"), ps[:, :],
                                       ACT.Copy).then_inc(s("v_hi"), 1)

            mod_norm("mix1", 1, TOK)
            diff_attention()
            output_splits("diffo", "mlp1", TOK)
            mod_norm("mlp1", 1, TOK)
            mlp(1, TOK, True, ("mix2", TOK))
            def down_outputs():
                t0, p0 = PLAN.at["mlad"]["tile"], PLAN.at["mlad"]["panel"]
                rotary = slice(HALF, HALF + ROPE)

                def take(j, dst):
                    b = bank[(t0 + j) % BANKS]
                    act.wait_ge(s("tile_done"), t0 + j + 1)
                    src = b[:, 0:LAT] if j < 2 else b[:, :] if j == 2 else b[rotary, :]
                    act.activation(dst, src, ACT.Copy).then_inc(s("down_out"), 1)

                split_hi(p0 + AHEAD)
                for j, dst in enumerate((cq_f[:, 0, :], cq_f[:, 1, :], ckv_f[:, :])):
                    take(j, dst)
                act.wait_ge(s("down_out"), 3)
                act.activation(norm_buf[0][:, :], cq_f[:, :, :].rearrange("p a b -> p (a b)"), ACT.Square).then_inc(s("down_sq"), 1)
                act.activation(norm_buf[1][:, :], ckv_f[:, :], ACT.Square).then_inc(s("down_sq"), 1)
                act.wait_ge(s("down_sum"), 1)
                act.activation(norm_buf[2][:, 0:LAT], pv_ps[:, 0:LAT], ACT.Sqrt, bias=eps[:, 0:1],
                               scale=1.0 / Q_RANK).then_inc(s("down_root"), 1)
                act.wait_ge(s("down_sum"), 2)
                act.activation(norm_buf[3][:, :], sum_ps[:, :], ACT.Sqrt, bias=eps[:, 0:1],
                               scale=1.0 / KV_RANK).then_inc(s("down_root"), 1)
                for j in range(1, 4):
                    split_hi(p0 + j + AHEAD)
                act.wait_ge(s("down_t"), 1)
                for k in range(2):
                    ins = act.activation(cq_f[:, k, :], norm_buf[4][:, k * LAT:(k + 1) * LAT], ACT.Identity,
                                         scale=vcol("mla_q_norm_g", k))
                ins.then_inc(s("down_g"), 1)
                act.wait_ge(s("down_g"), 1)
                act.activation(cq_hi[:, :, :], cq_f[:, :, :], ACT.Copy).then_inc(s("down_hi"), 1)
                take(3, kv_f[rotary, :])
                act.wait_ge(s("down_t"), 2)
                act.activation(ckv_f[:, :], norm_buf[5][:, :], ACT.Identity,
                               scale=vcol("mla_kv_norm_g")).then_inc(s("down_g"), 1)
                act.wait_ge(s("down_g"), 2)
                act.activation(ckv_hi[:, :], ckv_f[:, :], ACT.Copy).then_inc(s("down_hi"), 1)
                act.wait_ge(s("rope32_done"), 1)
                act.activation(mk_hi[rotary, :], kv_f[rotary, :], ACT.Copy).then_inc(s("key_hi"), 1)

            def mla_attention():
                t0, p0 = PLAN.at["mla"]["tile"], PLAN.at["mla"]["panel"]
                split_after = {0: [3], 3: [4], 7: [5, 6], 11: [], 15: [7]}
                for turn in range(MLA_HEADS + 2):
                    h = turn - 1
                    if h >= 1:
                        for i in range(2):
                            done, ps = attention_tile("mla", "turn_p", h - 1, i)
                            act.wait_ge(s("aux_done"), done)
                            act.activation(mpt_hi[:, 2 * i:2 * i + 2, :].rearrange("p a b -> p (a b)"), ps[:, :],
                                           ACT.Copy).then_inc(s("mla_pt_hi"), 1)
                    for i in range(2):
                        if 0 <= h < MLA_HEADS:
                            _, ps = attention_tile("mla", "score", h, i)
                            act.wait_ge(s("mla_max"), 2 * h + i + 1)
                            if h:
                                act.wait_ge(s("mla_mix"), 2 * h + i - 1)
                            act.activation(mp_raw[i][:, :], ps[:, :], ACT.Exp, bias=m_max[:, i:i + 1],
                                           accum_out=m_z[:, i:i + 1]).then_inc(s("mla_exp"), 1)
                        if turn < MLA_HEADS and i == 0:
                            t = t0 + 2 * turn
                            act.wait_ge(s("tile_done"), t + 1)
                            if turn:
                                act.wait_ge(s("mla_q_lo"), turn)
                            act.activation(mq_f[0:QD, :], bank[t % BANKS][0:QD, 0:LAT], ACT.Copy,
                                           scale=QD ** -0.5).then_inc(s("mla_qkv"), 1)
                    if turn < MLA_HEADS:
                        act.wait_ge(s("tile_done"), t + 2)
                        act.wait_ge(s("mla_k_lo"), turn + 1)
                        act.activation(kv_f[:, :], bank[(t + 1) % BANKS][:, :], ACT.Copy).then_inc(s("mla_qkv"), 1)
                        act.wait_ge(s("mla_qkv"), 2 * turn + 2)
                        act.activation(mk_hi[0:NOPE, :], kv_f[0:NOPE, :], ACT.Copy).then_inc(s("mla_k_hi"), 1)
                        act.wait_ge(s("rope32_done"), turn + 2)
                        act.activation(mq_hi[0:QD, :], mq_f[0:QD, :], ACT.Copy).then_inc(s("mla_q_hi"), 1)
                        for n in split_after.get(turn, []):
                            split_hi(p0 + n)
                    if h >= 1 and (h - 1) % 2:
                        m = (h - 1) // 2
                        act.wait_ge(s("pv_done"), m + 1)
                        act.activation(G_hi[:, m, 0:LAT], pv_ps[:, (m % 2) * LAT:(m % 2 + 1) * LAT],
                                       ACT.Copy).then_inc(s("mla_o_hi"), 1)
                    if turn < MLA_HEADS:
                        j = turn % 2
                        done, ps = attention_tile("mla", "turn_v", turn)
                        act.wait_ge(s("aux_done"), done)
                        act.activation(mv_hi[j][:, :, j * HALF:(j + 1) * HALF],
                                       ps[:, :].rearrange("p (t c) -> p t c", c=P)[:, :, HALF:P],
                                       ACT.Copy).then_inc(s("mla_v_hi"), 1)
                split_hi(p0 + 8)

            mod_norm("mix2", 2, TOK)
            down_outputs()
            mla_attention()
            output_splits("mlao", "mlp2", LAT)
            mod_norm("mlp2", 2, LAT)
            mlp(2, LAT, True, ("mix3", LAT))
            act.wait_ge(s("dft_in"), 32)
            act.activation(dft_hi[:, :, :], dft[:, :, :], ACT.Copy).then_inc(s("dft_hi"), 1)
            mod_norm("mix3", 3, LAT)
            fourier("four3", 1)
            output_splits("four3", "mlp3", LAT)
            mod_norm("mlp3", 3, LAT)
            mlp(3, LAT, False, ("final", LAT))
            act.wait_ge(s("tile_done"), PLAN.at["meta"]["tile"] + 1)
            b = bank[PLAN.at["meta"]["tile"] % BANKS]
            act.activation(X[:, :, LAT:TOK2], b[:, 0:KT * META].rearrange("p (k t) -> p k t", t=META),
                           ACT.Copy).then_inc(s("meta_cols"), 1)
            root("final", LAT)
            act.wait_ge(s("meta_cols"), 1)
            for k in range(KT):
                done = KT * NORM_AT["final"] + k + 1
                act.wait_ge(s("t"), done)
                act.activation(X[:, k, 0:LAT], norm_buf[4 + k % 2][:, 0:LAT], ACT.Identity,
                               scale=vcol("final_g", k)).then_inc(s("h"), 1)
                act.wait_ge(s("h"), done)
                if k >= 2:
                    act.wait_ge(s("sq_added"), KT * NORM_AT["mix_2"] + k - 1)
                act.activation(norm_buf[k % 2][:, 0:TOK2], X[:, k, 0:TOK2], ACT.Square).then_inc(s("sq"), 1)
            w = lambda k: vcol("norm_mix_w_2", k)
            root("mix_2", TOK2)
            apply("mix_2", TOK2, [(0, LAT, w, None, META), (LAT, META, w, None, 0)], SPLIT_AT["mix_2"])

            def projections():
                t0, p0 = PLAN.at["win"]["tile"], PLAN.at["win"]["panel"]
                for i, col in enumerate(WIN_ORDER):
                    split_hi(p0 + i + AHEAD)
                    act.wait_ge(s("tile_done"), t0 + i + 1)
                    rows = slice(0, GATE_RANK if col == GATE_AT else P)
                    act.activation(proj[rows, col, :], bank[(t0 + i) % BANKS][rows, 0:TOK2], ACT.Copy).then_inc(s("proj"), 1)
                    if i == 3:
                        gates()
                    if i == 10:
                        turned_values()
                    if i == 14:
                        turned_keys()

            def mix_tile(what, i):
                n = MIX_AT[what, i]
                act.wait_ge(s("mix_done_ps"), n + 1)
                return mix_ps[n % 4]

            def gates():
                for j in range(2):
                    ps = mix_tile("gate", j)
                    act.activation(z_f[:, j, :], ps[:, 0:TOK2], ACT.Identity, bias=vcol("b_gate_2", j)).then_inc(s("z_in"), 1)
                act.wait_ge(s("z_in"), 2)
                act.activation(z_abs[:, :, :], z_f[:, :, :], ACT.Abs).then_inc(s("z_step"), 1)
                act.wait_ge(s("z_step"), 1)
                act.activation(z_abs[:, :, :], z_abs[:, :, :], ACT.Exp, scale=-1.0).then_inc(s("z_step"), 1)
                act.wait_ge(s("z_step"), 2)
                act.activation(z_abs[:, :, :], z_abs[:, :, :], ACT.Ln, bias=1.0).then_inc(s("z_ln"), 1)
                act.wait_ge(s("b_last"), 1)
                act.activation(e_pos[:, :, :], b_cum[:, :, :], ACT.Exp, scale=1.0 / 16)
                act.activation(e_neg[:, :, :], b_cum[:, :, META:], ACT.Exp, scale=-1.0 / 16)
                for j in range(2):
                    for n in range(4):
                        c0, cn = CHUNKS[n]
                        act.activation(e_end[:, j, c0:c0 + cn], b_cum[:, j, c0:c0 + cn], ACT.Exp,
                                       bias=b_last[:, j, n:n + 1], scale=-1.0 / 16)
                act.activation(decay[:, :, :], b_last[:, :, :], ACT.Exp).then_inc(s("e_end"), 1)

            def turned_values():
                for i in range(5):
                    ps = mix_tile("turn_v", i)
                    if i < 4:
                        act.activation(v_rows[:, i, :, :].rearrange("p n c -> p (n c)"), ps[0:CHUNK, :], ACT.Copy).then_inc(s("v_rows"), 1)
                    else:
                        act.activation(v_rows_m[:, :, :].rearrange("p n c -> p (n c)"), ps[0:META, :], ACT.Copy).then_inc(s("v_rows"), 1)

            def turned_keys():
                for j in range(2):
                    ps = mix_tile("turn_k", j)
                    act.activation(k_rows[:, j, :, :].rearrange("p n c -> p (n c)"), ps[0:CHUNK, 0:3 * P], ACT.Copy)
                    act.activation(k_rows_m[:, j, :], ps[0:META, 3 * P:4 * P], ACT.Copy).then_inc(s("k_rows"), 1)

            def mixer_rest():
                for i in range(2):
                    ps = mix_tile("pool", i)
                    for g in range(2):
                        ins = act.activation(y_f[:, 2 * i + g, :], ps[:, g * LAT:(g + 1) * LAT], ACT.Identity,
                                             scale=vcol("pool_scale_2", 2 * i + g))
                    ins.then_inc(s("pool_in"), 1)
                act.wait_ge(s("proj"), 17)
                act.activation(r_silu[:, :, :], proj[:, R_AT:R_AT + 4, META:], ACT.Silu).then_inc(s("r_silu"), 1)
                act.wait_ge(s("pool_in"), 2)
                act.activation(Y_hi[:, 0:4, :], y_f[:, :, :], ACT.Copy).then_inc(s("y_hi"), 1)
                for i in range(2):
                    ps = mix_tile("score", i)
                    act.activation(sc[:, 2 * i:2 * i + 2, :, :].rearrange("p h n c -> p (h n c)"), ps[0:CHUNK, :],
                                   ACT.Copy).then_inc(s("sc_in"), 1)
                for i in range(2):
                    ps = mix_tile("out", i)
                    act.activation(go_f[:, 2 * i:2 * i + 2, :], ps[:, :].rearrange("p (h c) -> p h c", h=2), ACT.Copy).then_inc(s("go_in"), 1)
                act.wait_ge(s("go_in"), 2)
                act.activation(go_sq, go_f[:, :, :], ACT.Square).then_inc(s("go_sq"), 1)
                for i in range(2):
                    ps = mix_tile("square", i)
                    act.activation(go_inv[:, 2 * i:2 * i + 2, :], ps[:, :].rearrange("p (h c) -> p h c", h=2), ACT.Sqrt,
                                   bias=eps[:, 0:1], scale=1.0 / P).then_inc(s("go_root"), 1)
                act.wait_ge(s("y_lo"), 1)
                for i in range(2):
                    pair = slice(2 * i, 2 * i + 2)
                    act.wait_ge(s("go_t"), i + 1)
                    act.activation(y_f[:, pair, :], r_silu[:, pair, :], ACT.Identity, scale=vcol("gla_norm_w_2")).then_inc(s("go_g"), 1)
                    act.wait_ge(s("go_g"), i + 1)
                    act.activation(Y_hi[:, 4 + 2 * i:6 + 2 * i, :], y_f[:, pair, :], ACT.Copy).then_inc(s("y_hi"), 1)

            projections()
            mixer_rest()
            output_splits("wout", "ffn_2", LAT)
            root("ffn_2", LAT)
            apply("ffn_2", LAT, [(0, LAT, lambda k: vcol("norm_ffn_w_2", k), None)], SPLIT_AT["ffn_2"])

            def router():
                act.wait_ge(s("logit_done"), 1)
                act.activation(logits[:, :, :], psum[2][:, 0:2 * (4 + EXPERTS)].rearrange("p (t c) -> p t c", t=2),
                               ACT.Copy).then_inc(s("logits"), 1)
                for i in range(2):
                    act.wait_ge(s("shifted"), i + 1)
                    act.activation(r4[4 * i + 1][:, :, :], r4[4 * i][:, :, :], ACT.Exp).then_inc(s("route_exp"), 1)

            def gated(x, i=None, step=0):
                done = 6 * x + 2
                act.wait_ge(s("expert_done"), later(done, i, 6 * step))
                if x:
                    act.wait_ge(s("e_hid"), later(x, i, step))
                act.activation(e_silu[:, :, :].rearrange("p m c -> p (m c)"), psum[3 * (x % 2)][:, :],
                               ACT.Silu).then_inc(s("e_silu"), 1)
                act.wait_ge(s("e_hid"), later(x + 1, i, step))
                act.activation(E_hi[x % 2][:, :, :], e_hid[x % 2][:, :, :], ACT.Copy).then_inc(s("e_hi"), 1)

            p0 = PLAN.at["moe"]["panel"]

            def expert_split(n, i=None):
                if n < 6 * EXPERTS:
                    step = 6 * EXPERT_TURNS
                    split_hi(p0 + n, i, step, 16 * 3)

            def expert_turn(x, i=None):
                n = 6 * x - 2 if x else 0
                for j in range(0 if x else 1, 4):
                    expert_split(n + j + AHEAD, i)
                gated(x, i, EXPERT_TURNS)
                if x:
                    for j in range(4, 6):
                        expert_split(n + j + AHEAD, i)

            expert_split(AHEAD)
            router()
            expert_turn(0)
            with act.Fori(0, 3) as i:
                for j in range(EXPERT_TURNS):
                    expert_turn(1 + j, i)
            for x in range(1 + 3 * EXPERT_TURNS, EXPERTS):
                expert_turn(x)
            for k in range(KT):
                if k % 2 == 0:
                    act.wait_ge(s("y_added"), k // 2 + 1)
                square("final_2", LAT, k)
            root("final_2", LAT)
            apply("final_2", LAT, [(0, LAT, lambda k: vcol("final_norm_w_2", k), None)], None)
            for n in range(4):
                act.wait_ge(s("out_turned"), n + 1)
                act.activation(out_rows[:, n // 2, 512 * (n % 2):512 * (n % 2 + 1)], psum[n][:, :], ACT.Copy).then_inc(s("out_rows"), 1)

        @block.tensor
        def _(pe):
            def split_product(dst, w_hi, w_lo, r_hi, r_lo, start, stop):
                pe.matmul(dst, w_hi, r_hi, start=start, stop=False)
                pe.matmul(dst, w_hi, r_lo, start=False, stop=False)
                return pe.matmul(dst, w_lo, r_hi, start=False, stop=stop)

            def wait_bank(t, i=None, step=KT):
                if t >= BANKS:
                    name, value = PLAN.tiles[t - BANKS]
                    pe.wait_ge(s(name), later(value, i, step))

            def panel_product(n, t, r_hi, r_lo, c, i=None, ready=None, rows=P):
                if isinstance(i, int):
                    n, t, i = n + i * MLP_TILES, t + i * MLP_TILES, None
                pe.wait_ge(s("panel_ready"), later(n + 1, i, MLP_TILES))
                wait_bank(t, i)
                dst = bank[t % BANKS][0:rows, 0:c.stop - c.start]
                for k in range(KT):
                    if ready:
                        ready(k)
                    w = slice(k * P, k * P + rows)
                    ins = split_product(dst, W_hi[n % RING][:, w], W_lo[n % RING][:, w], r_hi[:, k, c],
                                        r_lo[:, k, c], k == 0, k == KT - 1)
                ins.then_inc(s("tile_done"), 1)

            def first_products(panels, t, r_hi, r_lo, c, ready, rows=P):
                for j, n in enumerate(panels):
                    pe.wait_ge(s("panel_ready"), n + 1)
                    wait_bank(t + j)
                for k in range(KT):
                    ready(k)
                    for j, n in enumerate(panels):
                        m = rows[j] if isinstance(rows, list) else rows
                        cols = c[j] if isinstance(c, list) else c
                        w = slice(k * P, k * P + m)
                        ins = split_product(bank[(t + j) % BANKS][0:m, 0:cols.stop], W_hi[n % RING][:, w], W_lo[n % RING][:, w],
                                            r_hi[:, k, cols], r_lo[:, k, cols], k == 0, k == KT - 1)
                        if k == KT - 1:
                            ins.then_inc(s("tile_done"), 1)

            def mod_unit(u, g, i=None):
                if u == 0 and (g or i is not None):
                    pe.wait_ge(s("mod_read"), later(g, i, 1))
                uses = MOD_UNITS // MOD_RING
                pe.wait_ge(s(f"mod_in{u % MOD_RING}"), later(16 * (uses * g + u // MOD_RING + 1), i, 16 * uses))
                for j in range(4):
                    ins = pe.matmul(mod_ps[32 * j:32 * (j + 1), 0:MOD_PART], silu_c[:, u, :],
                                    mod_raw[u % MOD_RING][:, j * MOD_PART:(j + 1) * MOD_PART],
                                    start=(u == 0), stop=(u == MOD_UNITS - 1))
                ins.then_inc(s("mod_used"), 1)

            def turn_mod(g, i=None):
                pe.wait_ge(s("mod_rows_in"), later(g + 1, i, 1))
                for j in range(MOD_PART // P):
                    ins = pe.transpose(mod_ps[:, j * P:(j + 1) * P], mod_rows[:, j * P:(j + 1) * P], ident[:, :])
                ins.then_inc(s("mod_turned"), 1)

            def norm_sum(name, n_cols):
                ni = NORM_AT[name]
                pe.wait_ge(s("sq_added"), KT * ni + KT)
                pe.matmul(sum_ps[:, 0:n_cols], ones[:, :], norm_buf[2][:, 0:n_cols], start=True,
                          stop=True).then_inc(s("sum"), 1)

            def h_ready(name):
                split = SPLIT_AT[name]
                return lambda k: pe.wait_ge(s("h_lo"), KT * split + k + 1)

            def fourier(name, streams, norm_name):
                t = PLAN.at[name]["tile"]
                f0 = 0 if name == "four0" else 24
                n_tok = 2 * streams
                for g in range(4):
                    for tt in range(n_tok):
                        wait_bank(t)
                        if g >= 2:
                            pe.wait_ge(s("tile_done"), t - tt - (n_tok + 2))
                        tok = slice(tt * P, (tt + 1) * P)
                        for k in range(2):
                            h_ready(norm_name)(2 * g + k)
                            ins = split_product(bank[t % BANKS][:, :], H_hi[:, 2 * g + k, tok], H_lo[:, 2 * g + k, tok],
                                                dft_hi[:, k, :], dft_lo[:, k, :], k == 0, k == 1)
                        ins.then_inc(s("tile_done"), 1)
                        if name == "four0":
                            mod_unit((4 * g + tt) % MOD_UNITS, 2 + g // 2)
                        t += 1
                    for m in range(2):
                        wait_bank(t)
                        for st in range(streams):
                            for q in range(4):
                                part, k = q // 2, q % 2
                                if m == 0:
                                    pe.wait_ge(s("four_lo"), f0 + (n_tok + 2) * g + 2 * st + k + 1)
                                col = slice(part * 256 + m * P, part * 256 + (m + 1) * P)
                                row = 4 * (g % 2) + 2 * st + k
                                trig = slice(part * 256, part * 256 + 256)
                                ins = split_product(bank[t % BANKS][:, st * LAT:(st + 1) * LAT],
                                                    G_hi[:, row, col], G_lo[:, row, col], dft_hi[:, k, trig],
                                                    dft_lo[:, k, trig], q == 0, q == 3)
                        ins.then_inc(s("tile_done"), 1)
                        t += 1
                    if name == "four0" and g % 2:
                        turn_mod(2 + g // 2)
                for m in range(KT):
                    n = PLAN.at[name]["panel"] + m
                    panel_product(n, t + m, H_hi, H_lo, slice(0, streams * LAT),
                                  ready=lambda k: pe.wait_ge(s("four_lo"), f0 + (n_tok + 2) * (k // 2) + n_tok + k % 2 + 1))

            def mlp(layer, n_cols, with_mod):
                at0 = PLAN.at[f"mlp{layer}"]
                p0, t0 = at0["panel"], at0["tile"]
                h0 = KT * BLOCKS * layer
                ready = h_ready(f"mlp{layer}")
                for u in range(MOD_UNITS):
                    if u == MOD_UNITS // 2 - 1:
                        norm_sum(f"mlp{layer}", n_cols)
                    if with_mod:
                        mod_unit(u, BLOCKS * (layer + 1))

                def hidden_block(b, first=False, last=False):
                    if first:
                        first_products([p0, p0 + 1], t0, H_hi, H_lo, slice(0, n_cols), ready)
                        if with_mod:
                            turn_mod(BLOCKS * (layer + 1))
                    for j in range(MLP_TILES):
                        if j < KT:
                            if not first or j >= 2:
                                panel_product(p0 + j, t0 + j, H_hi, H_lo, slice(0, n_cols), b)
                        else:
                            panel_product(p0 + j, t0 + j, G_hi, G_lo, slice(0, n_cols), b,
                                          (lambda k: pe.wait_ge(s("g_lo"), later(h0 + k + 1, b, KT))) if j == KT else None)
                        if with_mod and not last and j in MOD_AFTER:
                            mod_unit(MOD_AFTER[j], BLOCKS * (layer + 1) + 1, b)
                        if with_mod and not last and j == MOD_TURN_AT:
                            turn_mod(BLOCKS * (layer + 1) + 1, b)

                hidden_block(0, first=True)
                with pe.Fori(1, BLOCKS - 1) as b:
                    hidden_block(b)
                hidden_block(BLOCKS - 1, last=True)

            pe.wait_ge(s("const"), 5)
            pe.wait_ge(s("first_vec_in"), 16 * FIRST_VECTORS)
            pe.transpose(bank[0][:, 0:VEC_COUNT[0]], vec_rows[0:VEC_COUNT[0], 0, :],
                         ident[0:VEC_COUNT[0], 0:VEC_COUNT[0]]).then_inc(s("tile_done"), 1)
            pe.wait_ge(s("silu_c"), 1)
            for u in range(MOD_RING):
                mod_unit(u, 0)
            pe.wait_ge(s("x_in"), 32)
            t0 = PLAN.at["xin"]["tile"]
            for k in range(KT):
                wait_bank(t0 + k)
                for tt in range(4):
                    ins = pe.transpose(bank[(t0 + k) % BANKS][:, tt * P:(tt + 1) * P],
                                       x_rows[:, tt, k * P:(k + 1) * P], ident[:, :])
                ins.then_inc(s("tile_done"), 1)
            for u in range(MOD_RING, MOD_UNITS):
                mod_unit(u, 0)
            pe.wait_ge(s("vec_in"), 16 * (len(VEC_ROWS) - FIRST_VECTORS + 4))
            t0 = PLAN.at["vecs"]["tile"]
            wait_bank(t0)
            for v in range(1, VEC_TILES):
                ins = pe.transpose(bank[t0 % BANKS][:, v * P:v * P + VEC_COUNT[v]], vec_rows[0:VEC_COUNT[v], v, :],
                                   ident[0:VEC_COUNT[v], 0:VEC_COUNT[v]])
            ins.then_inc(s("tile_done"), 1)
            turn_mod(0)
            wait_bank(t0 + 1)
            pe.wait_ge(s("lam"), 3)
            pe.matmul(bank[(t0 + 1) % BANKS][:, 0:2], ones[0:1, :], lam_row[:, 0:2], start=True, stop=True).then_inc(s("tile_done"), 1)
            for u in range(MOD_UNITS):
                if u == 5:
                    norm_sum("mix0", TOK)
                mod_unit(u, 1)
            turn_mod(1)
            pe.wait_ge(s("dft_lo"), 1)
            fourier("four0", 2, "mix0")
            mlp(0, TOK, True)
            def take_aux(phase, what, h, i=0):
                n, banks = AUX_AT[phase, what, h, i], len(ATTENTION_BANKS[phase])
                if n >= banks:
                    name, value = PLAN.aux[PLAN.at[phase]["aux"] + n - banks]
                    pe.wait_ge(s(name), value)
                return attention_tile(phase, what, h, i)[1]

            def diff_attention():
                t0, p0 = PLAN.at["diff"]["tile"], PLAN.at["diff"]["panel"]
                full = slice(0, TOK)

                def scores(h, tiles):
                    for i in tiles:
                        qt, j = i // 2, i % 2
                        dst = take_aux("diff", "score", h, i)
                        half = slice(j * HALF, (j + 1) * HALF)
                        keys = full if qt < 2 else slice(LAT, TOK)
                        q = slice(qt * P, (qt + 1) * P)
                        split_product(dst[:, 0:keys.stop - keys.start], q_hi[half, q], q_lo[half, q], k_hi[half, keys],
                                      k_lo[half, keys], True, True).then_inc(s("aux_done"), 1)

                for turn in range(HEADS + 1 + O_BATCH):
                    h = turn - 1
                    on = 0 <= h < HEADS
                    ready = h - O_BATCH
                    if on:
                        pe.wait_ge(s("qk_lo"), 2 * h + 2)
                        scores(h, range(4))
                    if turn == 0:
                        first_products([p0, p0 + 1], t0, H_hi, H_lo, full, h_ready("mix1"))
                    elif turn < HEADS:
                        panel_product(p0 + 3 * turn, t0 + 3 * turn, H_hi, H_lo, full)
                    if on:
                        scores(h, range(4, 8))
                    if 0 < turn < HEADS:
                        panel_product(p0 + 3 * turn + 1, t0 + 3 * turn + 1, H_hi, H_lo, full)
                    if on:
                        pe.wait_ge(s("p_mix"), 4 * h + 4)
                        for i in range(3):
                            dst = take_aux("diff", "turn_p", h, i)
                            for j in range(2):
                                for q in range(2):
                                    key = q * TOK + (2 * i + j) * P if i < 2 else 2 * TOK + q * CTX + j * P
                                    ins = pe.transpose(dst[:, j * LAT + q * P:j * LAT + (q + 1) * P],
                                                       p_all[:, key:key + P], ident[:, :])
                            ins.then_inc(s("aux_done"), 1)
                    if turn < HEADS:
                        panel_product(p0 + 3 * turn + 2, t0 + 3 * turn + 2, H_hi, H_lo, full)
                    if ready >= 0:
                        dst = take_aux("diff", "turn_o", ready)
                        pe.wait_ge(s("o_scaled"), ready + 1)
                        for tt in range(4):
                            c = slice(tt * P, (tt + 1) * P)
                            ins = pe.transpose(dst[:, c], o_rows[ready % O_BATCH][:, c], ident[:, :])
                        ins.then_inc(s("aux_done"), 1)
                    if on:
                        dst = take_aux("diff", "pv", h)
                        pe.wait_ge(s("v_lo"), h + 1)
                        pe.wait_ge(s("pt_lo"), 3 * h + 3)
                        for tt in range(4):
                            q = slice(tt % 2 * P, (tt % 2 + 1) * P)
                            keys = [(kt, kt) for kt in range(4)] if tt < 2 else [(4, 2), (5, 3)]
                            for i, (kp, kv) in enumerate(keys):
                                ins = split_product(dst[:, tt * P:(tt + 1) * P], pt_hi[:, kp, q], pt_lo[:, kp, q],
                                                    v_hi[:, kv, :], v_lo[:, kv, :], i == 0, i == len(keys) - 1)
                        ins.then_inc(s("aux_done"), 1)
                    if turn < HEADS:
                        dst = take_aux("diff", "turn_v", turn)
                        pe.wait_ge(s("qkv"), 3 * turn + 3)
                        for tt in range(4):
                            ins = pe.transpose(dst[:, tt * P:(tt + 1) * P], v_f[:, tt * P:(tt + 1) * P], ident[:, :])
                        ins.then_inc(s("aux_done"), 1)

            def output_product(name, signal, c):
                p0, t0 = PLAN.at[name]["panel"], PLAN.at[name]["tile"]
                first_products([p0, p0 + 1], t0, G_hi, G_lo, c, lambda k: pe.wait_ge(s(signal), k + 1))
                for m in range(2, KT):
                    panel_product(p0 + m, t0 + m, G_hi, G_lo, c)

            norm_sum("mix1", TOK)
            diff_attention()
            output_product("diffo", "o_lo", slice(0, TOK))
            mlp(1, TOK, True)
            def down_products():
                t0, p0 = PLAN.at["mlad"]["tile"], PLAN.at["mlad"]["panel"]
                first_products([p0, p0 + 1, p0 + 2], t0, H_hi, H_lo, [slice(0, LAT), slice(0, LAT), slice(0, TOK)],
                               h_ready("mix2"))
                pe.wait_ge(s("down_sq"), 1)
                for k in range(2):
                    ins = pe.matmul(pv_ps[:, 0:LAT], ones[:, :], norm_buf[0][:, k * LAT:(k + 1) * LAT], start=(k == 0), stop=(k == 1))
                ins.then_inc(s("down_sum"), 1)
                pe.wait_ge(s("down_sq"), 2)
                pe.matmul(sum_ps[:, :], ones[:, :], norm_buf[1][:, :], start=True, stop=True).then_inc(s("down_sum"), 1)
                panel_product(p0 + 3, t0 + 3, H_hi, H_lo, slice(0, TOK), rows=QD)

            def mla_attention():
                t0, p0 = PLAN.at["mla"]["tile"], PLAN.at["mla"]["panel"]
                pe.wait_ge(s("mv_zero"), 1)
                for turn in range(MLA_HEADS + 2):
                    h = turn - 1
                    for i in range(2):
                        if h >= 1:
                            pe.wait_ge(s("mla_mix"), 2 * h)
                            dst = take_aux("mla", "turn_p", h - 1, i)
                            for j in range(2):
                                for q in range(2):
                                    ins = pe.transpose(dst[:, j * LAT + q * P:j * LAT + (q + 1) * P],
                                                       mp_all[:, q, (2 * i + j) * P:(2 * i + j + 1) * P], ident[:, :])
                            ins.then_inc(s("aux_done"), 1)
                        if 0 <= h < MLA_HEADS:
                            pe.wait_ge(s("mla_q_lo"), h + 1)
                            pe.wait_ge(s("mla_k_lo"), h + 2)
                            dst = take_aux("mla", "score", h, i)
                            q = slice(i * P, (i + 1) * P)
                            split_product(dst[:, :], mq_hi[0:QD, q], mq_lo[0:QD, q], mk_hi[0:QD, :], mk_lo[0:QD, :],
                                          True, True).then_inc(s("aux_done"), 1)
                    if turn < MLA_HEADS:
                        t = t0 + 2 * turn
                        n = p0 + [0, 1, 4, 5][turn // 4]
                        pe.wait_ge(s("panel_ready"), n + 1)
                        pe.wait_ge(s("down_lo"), 1)
                        wait_bank(t)
                        for k in range(2):
                            w = slice((4 * k + turn % 4) * P, (4 * k + turn % 4) * P + QD)
                            ins = split_product(bank[t % BANKS][0:QD, 0:LAT], W_hi[n % RING][:, w], W_lo[n % RING][:, w],
                                                cq_hi[:, k, :], cq_lo[:, k, :], k == 0, k == 1)
                        ins.then_inc(s("tile_done"), 1)
                        n = p0 + 2 + turn // 8
                        pe.wait_ge(s("panel_ready"), n + 1)
                        pe.wait_ge(s("down_lo"), 2)
                        wait_bank(t + 1)
                        w = slice(turn % 8 * P, (turn % 8 + 1) * P)
                        split_product(bank[(t + 1) % BANKS][:, :], W_hi[n % RING][:, w], W_lo[n % RING][:, w], ckv_hi[:, :],
                                      ckv_lo[:, :], True, True).then_inc(s("tile_done"), 1)
                    if h >= 1:
                        m, j = (h - 1) // 2, (h - 1) % 2
                        if j == 0 and m >= 2:
                            pe.wait_ge(s("mla_o_lo"), m - 1)
                        pe.wait_ge(s("mla_v_lo"), h)
                        pe.wait_ge(s("mla_pt_lo"), 2 * h)
                        for kt in range(4):
                            ins = split_product(pv_ps[:, (m % 2) * LAT:(m % 2 + 1) * LAT], mv_hi[j][:, kt, :], mv_lo[j][:, kt, :],
                                                mpt_hi[:, kt, :], mpt_lo[:, kt, :], j == 0 and kt == 0, j == 1 and kt == 3)
                        if j:
                            ins.then_inc(s("pv_done"), 1)
                    if turn < MLA_HEADS:
                        dst = take_aux("mla", "turn_v", turn)
                        pe.wait_ge(s("mla_qkv"), 2 * turn + 2)
                        for tt in range(4):
                            ins = pe.transpose(dst[:, tt * P:(tt + 1) * P], kv_f[:, tt * P:(tt + 1) * P], ident[:, :])
                        ins.then_inc(s("aux_done"), 1)

            norm_sum("mix2", TOK)
            down_products()
            mla_attention()
            output_product("mlao", "mla_o_lo", slice(0, LAT))
            mlp(2, LAT, True)
            norm_sum("mix3", LAT)
            pe.wait_ge(s("dft_lo"), 2)
            fourier("four3", 1, "mix3")
            mlp(3, LAT, False)
            pe.wait_ge(s("small_in"), 16 * 7)
            t = PLAN.at["meta"]["tile"]
            wait_bank(t)
            for k in range(KT):
                ins = pe.transpose(bank[t % BANKS][:, k * META:(k + 1) * META], meta_rows[:, k * P:(k + 1) * P],
                                   ident[0:META, 0:META])
            ins.then_inc(s("tile_done"), 1)
            norm_sum("final", LAT)
            norm_sum("mix_2", TOK2)

            def mix_tile(what, i):
                n = MIX_AT[what, i]
                if n >= 4:
                    name, value = MIX_TILES[n - 4]
                    pe.wait_ge(s(name), value)
                return mix_ps[n % 4]

            def done(ins):
                ins.then_inc(s("mix_done_ps"), 1)

            def gates():
                pe.wait_ge(s("proj"), 1)
                for j in range(2):
                    ps = mix_tile("gate", j)
                    done(pe.matmul(ps[:, 0:TOK2], gate_up[:, j * P:(j + 1) * P], proj[0:GATE_RANK, GATE_AT, :],
                                   start=True, stop=True))

            def turned_values():
                pe.wait_ge(s("proj"), 9)
                for h in range(GLA_HEADS):
                    ps = mix_tile("turn_v", h)
                    for n in range(4):
                        c0, cn = CHUNKS[n + 1]
                        ins = pe.transpose(ps[0:cn, n * P:(n + 1) * P], proj[:, V_AT + h, c0:c0 + cn], ident[:, :])
                    done(ins)
                ps = mix_tile("turn_v", 4)
                for h in range(GLA_HEADS):
                    ins = pe.transpose(ps[0:META, h * P:(h + 1) * P], proj[:, V_AT + h, 0:META], ident[:, :])
                done(ins)

            def turned_keys():
                pe.wait_ge(s("k_end"), 1)
                for j in range(2):
                    ps = mix_tile("turn_k", j)
                    for n in range(3):
                        c0, cn = CHUNKS[n + 1]
                        pe.transpose(ps[0:cn, n * P:(n + 1) * P], k_end[:, j, c0:c0 + cn], ident[:, :])
                    done(pe.transpose(ps[0:META, 3 * P:4 * P], k_end[:, j, 0:META], ident[:, :]))

            def mixer_rest():
                for i in range(2):
                    ps = mix_tile("pool", i)
                    pe.wait_ge(s("pooled"), 2 * i + 2)
                    for g in range(2):
                        ins = pe.matmul(ps[:, g * LAT:(g + 1) * LAT], pool_w[:, 2 * i + g, :], pooled[:, 2 * i + g, :],
                                        start=True, stop=True)
                    done(ins)
                pe.wait_ge(s("qk_t"), 1)
                for i in range(2):
                    ps = mix_tile("score", i)
                    for j in range(2):
                        for n in range(4):
                            c = slice(n * CHUNK, (n + 1) * CHUNK)
                            ins = pe.matmul(ps[0:CHUNK, j * LAT + n * CHUNK:j * LAT + (n + 1) * CHUNK], k_t[:, i, c],
                                            q_pad[j][:, i, c], start=True, stop=True)
                    done(ins)
                pe.wait_ge(s("v_rows"), 5)
                pe.wait_ge(s("k_rows"), 2)
                for i in range(2):
                    ps = mix_tile("state", i)
                    for n in range(4):
                        for j in range(2):
                            half = slice(j * HALF, (j + 1) * HALF)
                            h = 2 * i + j
                            keys = k_rows_m[:, i, half] if n == 0 else k_rows[:, i, n - 1, half]
                            values = v_rows_m[:, h, :] if n == 0 else v_rows[:, h, n - 1, :]
                            ins = pe.matmul(ps[half, n * P:(n + 1) * P], keys, values, start=True, stop=True)
                    done(ins)
                for i in range(2):
                    ps = mix_tile("out", i)
                    pe.wait_ge(s("sc_masked"), i + 1)
                    pe.wait_ge(s("states"), 4 * i + 4)
                    for j in range(2):
                        h = 2 * i + j
                        for n in range(4):
                            dst = ps[:, j * LAT + n * CHUNK:j * LAT + (n + 1) * CHUNK]
                            pe.matmul(dst, v_rows[:, h, n, :], sc[:, h, n, :], start=True, stop=False)
                            ins = pe.matmul(dst, S_all[:, i, n, :], q_pad[j][:, i, n * CHUNK:(n + 1) * CHUNK],
                                            start=False, stop=True)
                    done(ins)
                pe.wait_ge(s("go_sq"), 1)
                for i in range(2):
                    ps = mix_tile("square", i)
                    for j in range(2):
                        ins = pe.matmul(ps[:, j * LAT:(j + 1) * LAT], ones[:, :], go_sq[:, 2 * i + j, :], start=True, stop=True)
                    done(ins)

            p0, t0 = PLAN.at["win"]["panel"], PLAN.at["win"]["tile"]
            first_products([p0, p0 + 1, p0 + 2], t0, H_hi, H_lo, slice(0, TOK2), h_ready("mix_2"), [GATE_RANK, P, P])
            for i in range(2, len(WIN_ORDER)):
                if i > 2:
                    panel_product(p0 + i, t0 + i, H_hi, H_lo, slice(0, TOK2))
                if i == 2:
                    gates()
                if i == 10:
                    turned_values()
                if i == 14:
                    turned_keys()
            mixer_rest()
            p0, t0 = PLAN.at["wout"]["panel"], PLAN.at["wout"]["tile"]
            first_products([p0, p0 + 1, p0 + 2], t0, Y_hi, Y_lo, slice(0, LAT),
                           lambda k: pe.wait_ge(s("y_lo"), max(1, k // 2)))
            for m in range(3, KT):
                panel_product(p0 + m, t0 + m, Y_hi, Y_lo, slice(0, LAT))
            norm_sum("ffn_2", LAT)
            p0 = PLAN.at["moe"]["panel"]

            def expert_panel(n, i):
                pe.wait_ge(s("panel_ready"), later(p0 + n + 1, i, 6 * EXPERT_TURNS))
                r = (p0 + n) % RING
                return W_hi[r], W_lo[r]

            def expert_in(x, n, what, i=None, ready=None):
                if what == 0 and x >= 2:
                    pe.wait_ge(s("e_hid"), later(x - 1, i, EXPERT_TURNS))
                if what == 1 and x >= 1:
                    pe.wait_ge(s("e_hid"), later(x, i, EXPERT_TURNS))
                ps = psum[3 * (x % 2)] if what == 0 else psum[1]
                for j in range(2):
                    hi, lo = expert_panel(n + j, i)
                    for k in range(KT):
                        if ready and j == 0:
                            ready(k)
                        w = slice(k * P, (k + 1) * P)
                        ins = split_product(ps[:, j * LAT:(j + 1) * LAT], hi[:, w], lo[:, w], H_hi[:, k, 0:LAT],
                                            H_lo[:, k, 0:LAT], k == 0, k == KT - 1)
                    ins.then_inc(s("expert_done"), 1)

            def weight_row(x, i=None):
                pe.wait_ge(s("diag"), later(x + 1, i, EXPERT_TURNS))
                if x:
                    pe.wait_ge(s("e_hid"), later(x, i, EXPERT_TURNS))
                else:
                    pe.wait_ge(s("logits"), 1)
                for tt in range(2):
                    ins = pe.matmul(psum[2][:, tt * P:(tt + 1) * P], ones[:, :], diag[x % 2][:, tt, :], start=True, stop=True)
                ins.then_inc(s("weight_row"), 1)

            def expert_out(x, n, i=None):
                pe.wait_ge(s("e_lo"), later(x + 1, i, EXPERT_TURNS))
                for j in range(2):
                    hi, lo = expert_panel(n + j, i)
                    for a4 in range(4):
                        m = 2 * a4 + j
                        dst = psum[4 + m // 2][:, (m % 2) * LAT:(m % 2 + 1) * LAT]
                        for k in range(2):
                            w = slice((4 * k + a4) * P, (4 * k + a4 + 1) * P)
                            last = x == EXPERTS - 1 and k == 1
                            for q, (wp, rp) in enumerate(((hi, E_hi), (hi, E_lo), (lo, E_hi))):
                                ins = pe.matmul(dst, wp[:, w], rp[x % 2][:, k, :], start=False,
                                                stop=last and q == 2, skip_group_check=True)
                    ins.then_inc(s("expert_done"), 1)

            def expert_turn(x, i=None):
                n = 6 * x - 2 if x else 0
                expert_in(x, n, 0, i)
                expert_in(x, n + 2, 1, i)
                weight_row(x, i)
                if x:
                    expert_out(x - 1, n + 4, i)

            def router_products():
                for tt in range(2):
                    dst = psum[2][:, tt * (4 + EXPERTS):(tt + 1) * (4 + EXPERTS)]
                    pe.matmul(dst, ones[0:1, :], route_b[:, :], start=True, stop=False)
                    for k in range(KT):
                        tok = slice(tt * P, (tt + 1) * P)
                        pe.matmul(dst, H_hi[:, k, tok].bitcast(F32), route_w[:, k, :], start=False, stop=False)
                        ins = pe.matmul(dst, H_lo[:, k, tok].bitcast(F32), route_w[:, k, :], start=False, stop=(k == KT - 1))
                ins.then_inc(s("logit_done"), 1)

            pe.wait_ge(s("x_done"), X_AT["moe"])
            expert_in(0, 0, 0, ready=h_ready("ffn_2"))
            router_products()
            pe.wait_ge(s("zero_row"), 1)
            for b in range(4):
                pe.matmul(psum[4 + b][:, :], ones[0:1, :], zero_row[:, :], start=True, stop=False, skip_group_check=True)
            expert_in(0, 2, 1)
            weight_row(0)
            with pe.Fori(0, 3) as i:
                for j in range(EXPERT_TURNS):
                    expert_turn(1 + j, i)
            for x in range(1 + 3 * EXPERT_TURNS, EXPERTS):
                expert_turn(x)
            expert_out(EXPERTS - 1, 6 * EXPERTS - 2)
            norm_sum("final_2", LAT)
            for tt in range(2):
                for half in range(2):
                    n = 2 * tt + half
                    for k in range(4):
                        pe.wait_ge(s("h"), KT * NORM_AT["final_2"] + 4 * half + k + 1)
                        ins = pe.transpose(psum[n][:, k * P:(k + 1) * P], X[:, 4 * half + k, tt * P:(tt + 1) * P], ident[:, :])
                    ins.then_inc(s("out_turned"), 1)

        @block.vector
        def _(dve):
            def split_lo(n):
                unit, place, _ = PLAN.panels[n]
                slot = PLAN.units[unit][1]
                dve.tensor_tensor(W_lo[n % RING][:, :].rearrange("p (k c) -> p k c", c=P), w_raw[slot][:, :, place, :],
                                  W_hi[n % RING][:, :].bitcast(F32).rearrange("p (k c) -> p k c", c=P),
                                  ALU.subtract).then_inc(s("panel_ready"), 1)

            def split_lo_at(n, i=None):
                if isinstance(i, int):
                    n, i = n + i * MLP_TILES, None
                dve.wait_ge(s("w_hi"), later(n + 1, i, MLP_TILES))
                split_lo(n)

            def add_square(name, n_cols, k):
                ni, c = NORM_AT[name], slice(0, n_cols)
                dve.wait_ge(s("sq"), KT * ni + k + 1)
                if k == 0:
                    dve.tensor_copy(norm_buf[2][:, c], norm_buf[0][:, c]).then_inc(s("sq_added"), 1)
                else:
                    dve.wait_ge(s("sq_added"), KT * ni + k)
                    dve.tensor_tensor(norm_buf[2][:, c], norm_buf[2][:, c], norm_buf[k % 2][:, c],
                                      ALU.add).then_inc(s("sq_added"), 1)

            def invert(name, n_cols):
                ni, c = NORM_AT[name], slice(0, n_cols)
                dve.wait_ge(s("root"), ni + 1)
                dve.reciprocal(norm_buf[3][:, c], norm_buf[3][:, c]).then_inc(s("rstd"), 1)

            def apply(name, n_cols, pairs):
                ni, c = NORM_AT[name], slice(0, n_cols)
                dve.wait_ge(s("rstd"), ni + 1)

                def lo(k):
                    dve.wait_ge(s("h_hi"), KT * pairs + k + 1)
                    dve.tensor_tensor(H_lo[:, k, c], norm_buf[4 + k % 2][:, c], H_hi[:, k, c].bitcast(F32),
                                      ALU.subtract).then_inc(s("h_lo"), 1)

                for k in range(KT):
                    if k >= 2:
                        dve.wait_ge(s("h"), KT * ni + k - 1)
                    dve.tensor_tensor(norm_buf[k % 2][:, c], X[:, k, c], norm_buf[3][:, c], ALU.mult).then_inc(s("t"), 1)
                    if pairs is not None and k >= 1:
                        lo(k - 1)
                if pairs is not None:
                    lo(KT - 1)

            def norm_rest(name, n_cols):
                invert(name, n_cols)
                apply(name, n_cols, SPLIT_AT[name] if name in SPLIT_NORMS else None)

            def mod_read(layer, g, i=None):
                dve.wait_ge(s("mod_turned"), later(g + 1, i, 1))
                turned_tiles = mod_ps[:, 0:MOD_PART].rearrange("p (t j r) -> p j t r", t=MOD_PART // P, j=4)
                b = g % BLOCKS if i is None else i + g % BLOCKS
                dst = mod[layer % 2][:, bass.ds(b * (MOD_TILES // BLOCKS), MOD_TILES // BLOCKS), :] if i is not None else \
                    mod[layer % 2][:, b * (MOD_TILES // BLOCKS):(b + 1) * (MOD_TILES // BLOCKS), :]
                dve.tensor_copy(dst.rearrange("p (j t) s -> p j t s", j=4), turned_tiles[:, :, :, 0:2]).then_inc(s("mod_read"), 1)

            def mod_finish(layer, half):
                n = MOD_TILES // 2
                m = mod[layer % 2][:, half * n:(half + 1) * n, :]
                tile, row = ("mod_b_lo", 48 * layer) if layer < 2 else ("mod_b_hi", 48 * (layer - 2))
                dve.wait_ge(s("mod_read"), BLOCKS * layer + 2 * (half + 1))
                bias = vcols(tile, row + half * n, n).rearrange("p (m o) -> p m o", o=1).to_broadcast([P, n, 2])
                dve.tensor_tensor(m, m, bias, ALU.add).then_inc(s("mod_sum"), 1)
                dve.wait_ge(s("mod_sum"), 2 * layer + half + 1)
                name, scales = (("norm_mix_g", scale_mix), ("norm_mlp_g", scale_mlp))[half]
                g = vcols(name, KT * layer, KT).rearrange("p (m o) -> p m o", o=1).to_broadcast([P, KT, 2])
                dve.scalar_tensor_tensor(scales[:, :, :], m[:, KT:2 * KT, :], 1.0, g, ALU.add,
                                         ALU.mult).then_inc(s(("scales_mix", "scales_mlp")[half]), 1)

            def add_gated(m, t, xn, layer, gate_at, streams, i=None, step=0):
                dve.wait_ge(s("tile_done"), later(t + 1, i, MLP_TILES))
                if xn:
                    dve.wait_ge(s("x_done"), later(xn, i, step))
                for st in range(streams):
                    c = slice(st * LAT, (st + 1) * LAT)
                    ins = dve.scalar_tensor_tensor(X[:, m, c], bank[t % BANKS][:, c],
                                                   mod[layer % 2][:, gate_at + m, st:st + 1], X[:, m, c],
                                                   ALU.mult, ALU.add)
                ins.then_inc(s("x_done"), 1)

            def fourier(name, layer, streams):
                t = PLAN.at[name]["tile"]
                p0 = PLAN.at[name]["panel"]
                f0 = 0 if name == "four0" else 24
                n_tok = 2 * streams
                for g in range(4):
                    if name == "four0" and g == 3:
                        for n in range(AHEAD):
                            split_lo_at(p0 + n)
                    for tt in range(n_tok):
                        row = 4 * (g % 2) + tt
                        dve.wait_ge(s("four_hi"), f0 + t - PLAN.at[name]["tile"] + 1)
                        dve.tensor_tensor(G_lo[:, row, 0:256], bank[t % BANKS][:, 0:256],
                                          G_hi[:, row, 0:256].bitcast(F32), ALU.subtract)
                        dve.scalar_tensor_tensor(G_lo[:, row, 256:512], bank[t % BANKS][:, 256:512], -1.0,
                                                 G_hi[:, row, 256:512].bitcast(F32), ALU.mult,
                                                 ALU.subtract).then_inc(s("four_lo"), 1)
                        t += 1
                    for m in range(2):
                        c = slice(0, streams * LAT)
                        dve.wait_ge(s("four_hi"), f0 + t - PLAN.at[name]["tile"] + 1)
                        dve.tensor_tensor(H_lo[:, 2 * g + m, c], bank[t % BANKS][:, c],
                                          H_hi[:, 2 * g + m, c].bitcast(F32), ALU.subtract).then_inc(s("four_lo"), 1)
                        t += 1
                    if name == "four0" and g % 2:
                        mod_read(0, 2 + g // 2)
                if name == "four0":
                    mod_finish(0, 1)
                bias = vcols("fourier_b", KT * (layer // 3), KT).rearrange("p (m o) -> p m o", o=1).to_broadcast([P, KT, 2])
                dve.tensor_tensor(gated_b[:, :, :], mod[layer % 2][:, 2 * KT:3 * KT, :], bias,
                                  ALU.mult).then_inc(s("gated_b"), 1)
                dve.wait_ge(s("gated_b"), layer // 3 + 1)
                for m in range(KT):
                    for st in range(streams):
                        c = slice(st * LAT, (st + 1) * LAT)
                        ins = dve.tensor_scalar(X[:, m, c], X[:, m, c], gated_b[:, m, st:st + 1], None, ALU.add)
                ins.then_inc(s("x_bias"), 1)
                dve.wait_ge(s("x_bias"), layer // 3 + 1)
                for m in range(KT):
                    split_lo_at(p0 + m + AHEAD)
                    add_gated(m, t + m, 0, layer, 2 * KT, streams)
                    if m:
                        add_square(f"mlp{layer}", streams * LAT, m - 1)
                add_square(f"mlp{layer}", streams * LAT, KT - 1)

            def mlp(layer, streams, with_mod, next_norm):
                at0 = PLAN.at[f"mlp{layer}"]
                p0, t0 = at0["panel"], at0["tile"]
                h0 = KT * BLOCKS * layer
                xn = X_AT[f"mlp{layer}"]
                c = slice(0, streams * LAT)

                def lo(j, b):
                    dve.wait_ge(s("g_hi"), later(h0 + j + 1, b, KT))
                    dve.wait_ge(s("g_sq"), later(h0 + j + 1, b, KT))
                    dve.tensor_tensor(G_lo[:, j, c], square[j % 2][:, c], G_hi[:, j, c].bitcast(F32),
                                      ALU.subtract).then_inc(s("g_lo"), 1)

                def hidden_block(b, last=False):
                    for j in range(MLP_TILES):
                        split_lo_at(p0 + j + AHEAD, b)
                        if j < KT:
                            dve.wait_ge(s("relu"), later(h0 + j + 1, b, KT))
                            dve.tensor_tensor(square[j % 2][:, c], relu[j % 2][:, c], relu[j % 2][:, c],
                                              ALU.mult).then_inc(s("g_sq"), 1)
                            lo(j, b)
                        else:
                            add_gated(j - KT, t0 + j, xn + j - KT, layer, 5 * KT, streams, b, KT)
                        if with_mod and not last and j == MOD_TURN_AT:
                            mod_read(layer + 1, BLOCKS * (layer + 1) + 1, b)
                        if last and j > KT:
                            add_square(*next_norm, j - KT - 1)

                if with_mod:
                    mod_read(layer + 1, BLOCKS * (layer + 1))
                with dve.Fori(0, BLOCKS - 1) as b:
                    hidden_block(b)
                if with_mod:
                    for half in range(2):
                        mod_finish(layer + 1, half)
                hidden_block(BLOCKS - 1, last=True)
                add_square(*next_norm, KT - 1)

            dve.wait_ge(s("silu_exp"), 1)
            dve.tensor_scalar(silu_t[:, :, :], silu_t[:, :, :], 1.0, None, ALU.add).then_inc(s("silu_add"), 1)
            dve.wait_ge(s("silu_add"), 1)
            dve.reciprocal(silu_t[:, :, :], silu_t[:, :, :]).then_inc(s("silu_add"), 1)
            dve.wait_ge(s("silu_add"), 2)
            dve.wait_ge(s("const"), 5)
            dve.tensor_tensor(silu_c[:, :, 0:2].rearrange("p k s -> p s k"), silu_t[:, :, :],
                              vcols("c", 0, 16).rearrange("p (s k) -> p s k", s=2), ALU.mult).then_inc(s("silu_c"), 1)
            mod_read(0, 0)
            dve.wait_ge(s("vec_in"), 16 * (len(VEC_ROWS) - FIRST_VECTORS + 4))
            dve.tensor_tensor(lam_prod[:, :, :], lam_in[:, 0:2, :], lam_in[:, 2:4, :], ALU.mult).then_inc(s("lam"), 1)
            dve.wait_ge(s("lam"), 1)
            dve.tensor_reduce(lam_row[:, 0:2], lam_prod[:, :, :], AX.X, ALU.add).then_inc(s("lam"), 1)
            dve.wait_ge(s("lam_exp"), 1)
            dve.scalar_tensor_tensor(lam_row[:, 1:2], lam_row[:, 3:4], LAM_INIT, lam_row[:, 2:3], ALU.subtract,
                                     ALU.subtract)
            dve.memset(lam_row[:, 0:1], 1.0).then_inc(s("lam"), 1)
            dve.wait_ge(s("tile_done"), PLAN.at["vecs"]["tile"] + 2)
            dve.tensor_copy(lam_col[:, :], bank[(PLAN.at["vecs"]["tile"] + 1) % BANKS][:, 0:2]).then_inc(s("lam_col"), 1)
            dve.wait_ge(s("dft_hi"), 1)
            dve.tensor_tensor(dft_lo[:, :, :], dft[:, :, :], dft_hi[:, :, :].bitcast(F32), ALU.subtract).then_inc(s("dft_lo"), 1)
            for k in range(KT):
                add_square("mix0", TOK, k)
            invert("mix0", TOK)
            mod_read(0, 1)
            dve.wait_ge(s("vec"), 2)
            mod_finish(0, 0)
            apply("mix0", TOK, SPLIT_AT["mix0"])
            fourier("four0", 0, 2)
            norm_rest("mlp0", TOK)
            mlp(0, 2, True, ("mix1", TOK))

            def mixes(h, tiles):
                def mix(qt):
                    n = TOK if qt < 2 else CTX
                    pair = slice(2 * qt, 2 * qt + 2)
                    dve.wait_ge(s("p_exp"), 8 * h + 2 * qt + 2)
                    dve.reciprocal(z_inv[:, pair], z[:, pair]).then_inc(s("z_inv"), 1)
                    dve.wait_ge(s("z_inv"), 4 * h + qt + 1)
                    dve.tensor_tensor(z_mix[:, pair], z_inv[:, pair], lam_col[:, :], ALU.mult).then_inc(s("z_mix"), 1)
                    dve.wait_ge(s("p_scaled"), 4 * h + qt + 1)
                    first = qt * TOK if qt < 2 else 2 * TOK + (qt - 2) * CTX
                    dve.scalar_tensor_tensor(p_all[:, first:first + n], p_raw[qt % 2][0][:, 0:n],
                                             z_mix[:, 2 * qt:2 * qt + 1], p_raw[qt % 2][1][:, 0:n], ALU.mult,
                                             ALU.add).then_inc(s("p_mix"), 1)

                for qt in tiles:
                    n = TOK if qt < 2 else CTX
                    for j in range(2):
                        done, ps = attention_tile("diff", "score", h, 2 * qt + j)
                        dve.wait_ge(s("aux_done"), done)
                        dve.tensor_reduce(neg_max[:, 2 * qt + j:2 * qt + j + 1], ps[:, 0:n], AX.X, ALU.max,
                                          negate=True).then_inc(s("neg_max"), 1)
                    if qt > tiles[0]:
                        mix(qt - 1)
                mix(tiles[-1])

            swap16 = [i ^ 16 for i in range(32)]

            def diff_attention():
                p0 = PLAN.at["diff"]["panel"]

                def rotate_latents(turn, j, f):
                    dve.wait_ge(s("qkv"), 3 * turn + j + 1)
                    r = 2 * turn + j
                    if r:
                        dve.wait_ge(s("roped"), r)
                    dve.stream_shuffle(turned, f[:, 0:LAT], swap16).then_inc(s("rope_step"), 1)
                    dve.tensor_tensor(straight, f[:, 0:LAT], rope[:, 0, :], ALU.mult)
                    dve.wait_ge(s("rope_step"), 2 * r + 1)
                    dve.tensor_tensor(turned, turned, rope[:, 1, :], ALU.mult).then_inc(s("rope_step"), 1)
                    dve.wait_ge(s("rope_step"), 2 * r + 2)
                    dve.tensor_tensor(f[:, 0:LAT], straight, turned, ALU.add).then_inc(s("roped"), 1)

                def scale_output(h):
                    rows = o_rows[h % O_BATCH][:, :].rearrange("p (t c) -> p t c", c=P)
                    inv = o_inv[:, 4 * h:4 * h + 4].rearrange("p (t o) -> p t o", o=1).to_broadcast([P, 4, P])
                    dve.tensor_tensor(rows, rows, inv, ALU.mult).then_inc(s("o_scaled"), 1)

                for turn in range(HEADS + 1 + O_BATCH):
                    h = turn - 1
                    on = 0 <= h < HEADS
                    ready = h - O_BATCH
                    if turn < HEADS:
                        split_lo_at(p0 + 3 * turn + AHEAD)
                    if on:
                        mixes(h, (0, 1))
                    if on:
                        mixes(h, (2, 3))
                    if turn < HEADS:
                        rotate_latents(turn, 0, q_f)
                        split_lo_at(p0 + 3 * turn + 1 + AHEAD)
                        rotate_latents(turn, 1, k_f)
                    if on:
                        for i in range(3):
                            _, ps = attention_tile("diff", "turn_p", h, i)
                            dve.wait_ge(s("pt_hi"), 3 * h + i + 1)
                            dve.tensor_tensor(pt_lo[:, 2 * i:2 * i + 2, :].rearrange("p a b -> p (a b)"), ps[:, :],
                                              pt_hi[:, 2 * i:2 * i + 2, :].rearrange("p a b -> p (a b)").bitcast(F32),
                                              ALU.subtract).then_inc(s("pt_lo"), 1)
                    if turn < HEADS:
                        for j, (lo, hi, f) in enumerate(((q_lo, q_hi, q_f), (k_lo, k_hi, k_f))):
                            dve.wait_ge(s("qk_hi"), 2 * turn + j + 1)
                            dve.tensor_tensor(lo[:, :], f[:, :], hi[:, :].bitcast(F32), ALU.subtract).then_inc(s("qk_lo"), 1)
                        split_lo_at(p0 + 3 * turn + 2 + AHEAD)
                    if ready >= 0 and ready % O_BATCH == 0:
                        batch = ready // O_BATCH
                        c = slice(4 * ready, 4 * (ready + O_BATCH))
                        dve.wait_ge(s("o_root"), batch + 1)
                        dve.reciprocal(o_inv[:, c], o_inv[:, c]).then_inc(s("o_inv"), 1)
                        dve.wait_ge(s("o_inv"), batch + 1)
                        for i in range(O_BATCH):
                            scale_output(ready + i)
                    if ready >= 0:
                        dve.wait_ge(s("o_hi"), ready + 1)
                        dve.tensor_tensor(G_lo[:, ready, :], o_g[:, :], G_hi[:, ready, :].bitcast(F32),
                                          ALU.subtract).then_inc(s("o_lo"), 1)
                    if turn < HEADS:
                        _, ps = attention_tile("diff", "turn_v", turn)
                        dve.wait_ge(s("v_hi"), turn + 1)
                        dve.tensor_tensor(v_lo[:, :, :].rearrange("p a b -> p (a b)"), ps[:, :],
                                          v_hi[:, :, :].rearrange("p a b -> p (a b)").bitcast(F32),
                                          ALU.subtract).then_inc(s("v_lo"), 1)

            def output_added(name, layer, streams):
                for m in range(KT):
                    split_lo_at(PLAN.at[name]["panel"] + m + AHEAD)
                    add_gated(m, PLAN.at[name]["tile"] + m, 0, layer, 2 * KT, streams)
                    if m:
                        add_square(f"mlp{layer}", streams * LAT, m - 1)
                add_square(f"mlp{layer}", streams * LAT, KT - 1)

            dve.tensor_scalar(subln[:, :], vcol("diff_subln_g"), 1.0 - LAM_INIT, None, ALU.mult)
            norm_rest("mix1", TOK)
            dve.wait_ge(s("rope_in"), 16)
            diff_attention()
            output_added("diffo", 1, 2)
            norm_rest("mlp1", TOK)
            mlp(1, 2, True, ("mix2", TOK))

            def down_outputs():
                p0 = PLAN.at["mlad"]["panel"]
                rotary = slice(HALF, HALF + ROPE)
                split_lo_at(p0 + AHEAD)
                dve.wait_ge(s("down_root"), 1)
                dve.reciprocal(norm_buf[2][:, 0:LAT], norm_buf[2][:, 0:LAT]).then_inc(s("down_inv"), 1)
                dve.wait_ge(s("down_inv"), 1)
                for k in range(2):
                    ins = dve.tensor_tensor(norm_buf[4][:, k * LAT:(k + 1) * LAT], cq_f[:, k, :], norm_buf[2][:, 0:LAT], ALU.mult)
                ins.then_inc(s("down_t"), 1)
                dve.wait_ge(s("down_root"), 2)
                dve.reciprocal(norm_buf[3][:, :], norm_buf[3][:, :]).then_inc(s("down_inv"), 1)
                dve.wait_ge(s("down_inv"), 2)
                dve.tensor_tensor(norm_buf[5][:, :], ckv_f[:, :], norm_buf[3][:, :], ALU.mult).then_inc(s("down_t"), 1)
                dve.wait_ge(s("down_hi"), 1)
                dve.tensor_tensor(cq_lo[:, :, :], cq_f[:, :, :], cq_hi[:, :, :].bitcast(F32), ALU.subtract).then_inc(s("down_lo"), 1)
                for j in range(1, 4):
                    split_lo_at(p0 + j + AHEAD)
                dve.wait_ge(s("down_hi"), 2)
                dve.tensor_tensor(ckv_lo[:, :], ckv_f[:, :], ckv_hi[:, :].bitcast(F32), ALU.subtract).then_inc(s("down_lo"), 1)
                dve.wait_ge(s("rope_in"), 32)
                dve.wait_ge(s("down_out"), 4)
                rotate(kv_f[rotary, 0:LAT], rotary, 0, mp_all[:, 0, :])
                dve.wait_ge(s("key_hi"), 1)
                dve.tensor_tensor(mk_lo[rotary, :], kv_f[rotary, :], mk_hi[rotary, :].bitcast(F32),
                                  ALU.subtract).then_inc(s("mla_k_lo"), 1)

            swap8 = [i ^ 8 for i in range(32)]

            def rotate(x, rows, r, buf):
                m_turned, m_straight = buf[:, 0:LAT], buf[:, LAT:TOK]
                if r:
                    dve.wait_ge(s("rope32_done"), r)
                dve.stream_shuffle(m_turned[rows, 0:LAT], x, swap8).then_inc(s("rope32_step"), 1)
                dve.tensor_tensor(m_straight[rows, 0:LAT], x, rope32[rows, 0, :], ALU.mult)
                dve.wait_ge(s("rope32_step"), 2 * r + 1)
                dve.tensor_tensor(m_turned[rows, 0:LAT], m_turned[rows, 0:LAT], rope32[rows, 1, :],
                                  ALU.mult).then_inc(s("rope32_step"), 1)
                dve.wait_ge(s("rope32_step"), 2 * r + 2)
                dve.tensor_tensor(x, m_straight[rows, 0:LAT], m_turned[rows, 0:LAT], ALU.add).then_inc(s("rope32_done"), 1)

            def mla_attention():
                p0 = PLAN.at["mla"]["panel"]
                split_after = {0: [3], 3: [4], 7: [5, 6], 11: [], 15: [7]}
                rotary = slice(HALF, HALF + ROPE)
                for turn in range(MLA_HEADS + 2):
                    h = turn - 1
                    on = 0 <= h < MLA_HEADS
                    for i in range(2):
                        if h >= 1:
                            _, ps = attention_tile("mla", "turn_p", h - 1, i)
                            dve.wait_ge(s("mla_pt_hi"), 2 * (h - 1) + i + 1)
                            dve.tensor_tensor(mpt_lo[:, 2 * i:2 * i + 2, :].rearrange("p a b -> p (a b)"), ps[:, :],
                                              mpt_hi[:, 2 * i:2 * i + 2, :].rearrange("p a b -> p (a b)").bitcast(F32),
                                              ALU.subtract).then_inc(s("mla_pt_lo"), 1)
                        if on:
                            done, ps = attention_tile("mla", "score", h, i)
                            dve.wait_ge(s("aux_done"), done)
                            dve.tensor_reduce(m_max[:, i:i + 1], ps[:, :], AX.X, ALU.max,
                                              negate=True).then_inc(s("mla_max"), 1)
                    if turn < MLA_HEADS:
                        dve.wait_ge(s("mla_qkv"), 2 * turn + 1)
                        rotate(mq_f[rotary, :], rotary, turn + 1, norm_buf[0])
                    if on:
                        dve.wait_ge(s("mla_exp"), 2 * h + 2)
                        dve.reciprocal(m_zinv[:, :], m_z[:, :]).then_inc(s("mla_zinv"), 1)
                        dve.wait_ge(s("mla_zinv"), h + 1)
                        for i in range(2):
                            dve.tensor_scalar(mp_all[:, i, :], mp_raw[i][:, :], m_zinv[:, i:i + 1], None,
                                              ALU.mult).then_inc(s("mla_mix"), 1)
                    if turn < MLA_HEADS:
                        dve.wait_ge(s("mla_q_hi"), turn + 1)
                        dve.tensor_tensor(mq_lo[0:QD, :], mq_f[0:QD, :], mq_hi[0:QD, :].bitcast(F32),
                                          ALU.subtract).then_inc(s("mla_q_lo"), 1)
                        for n in split_after.get(turn, []):
                            split_lo_at(p0 + n)
                    if h >= 1 and (h - 1) % 2:
                        m = (h - 1) // 2
                        dve.wait_ge(s("mla_o_hi"), m + 1)
                        dve.tensor_tensor(G_lo[:, m, 0:LAT], pv_ps[:, (m % 2) * LAT:(m % 2 + 1) * LAT],
                                          G_hi[:, m, 0:LAT].bitcast(F32), ALU.subtract).then_inc(s("mla_o_lo"), 1)
                    if turn < MLA_HEADS:
                        j = turn % 2
                        half = slice(j * HALF, (j + 1) * HALF)
                        _, ps = attention_tile("mla", "turn_v", turn)
                        dve.wait_ge(s("mla_v_hi"), turn + 1)
                        dve.tensor_tensor(mv_lo[j][:, :, half], ps[:, :].rearrange("p (t c) -> p t c", c=P)[:, :, HALF:P],
                                          mv_hi[j][:, :, half].bitcast(F32), ALU.subtract).then_inc(s("mla_v_lo"), 1)
                split_lo_at(p0 + 8)

            norm_rest("mix2", TOK)
            for j in range(2):
                dve.memset(mv_hi[j][:, :, :].bitcast(F32), 0.0)
                ins = dve.memset(mv_lo[j][:, :, :].bitcast(F32), 0.0)
            ins.then_inc(s("mv_zero"), 1)
            dve.wait_ge(s("mv_zero"), 1)
            down_outputs()
            mla_attention()
            output_added("mlao", 2, 1)
            norm_rest("mlp2", LAT)
            mlp(2, 1, True, ("mix3", LAT))
            dve.wait_ge(s("dft_hi"), 2)
            dve.tensor_tensor(dft_lo[:, :, :], dft[:, :, :], dft_hi[:, :, :].bitcast(F32), ALU.subtract).then_inc(s("dft_lo"), 1)
            norm_rest("mix3", LAT)
            fourier("four3", 3, 1)
            norm_rest("mlp3", LAT)
            mlp(3, 1, False, ("final", LAT))
            dve.wait_ge(s("small_in"), 16 * 7)
            dve.memset(chunk_mask[:, :], 1.0).then_inc(s("mask"), 1)
            dve.wait_ge(s("mask"), 1)
            for c0, _ in CHUNKS:
                ins = dve.memset(chunk_mask[:, c0:c0 + 1], 0.0)
            ins.then_inc(s("mask"), 1)
            invert("final", LAT)
            dve.wait_ge(s("rstd"), NORM_AT["final"] + 1)
            for k in range(KT):
                if k >= 2:
                    dve.wait_ge(s("h"), KT * NORM_AT["final"] + k - 1)
                dve.tensor_tensor(norm_buf[4 + k % 2][:, 0:LAT], X[:, k, 0:LAT], norm_buf[3][:, 0:LAT],
                                  ALU.mult).then_inc(s("t"), 1)
                if k:
                    add_square("mix_2", TOK2, k - 1)
            add_square("mix_2", TOK2, KT - 1)
            norm_rest("mix_2", TOK2)

            def gates():
                dve.wait_ge(s("z_ln"), 1)
                dve.scalar_tensor_tensor(log_a[:, :, :], z_f[:, :, :], 0.0, z_abs[:, :, :], ALU.min,
                                         ALU.subtract).then_inc(s("log_a"), 1)
                dve.wait_ge(s("log_a"), 1)
                dve.wait_ge(s("mask"), 2)
                for j in range(2):
                    ins = dve.tensor_tensor_scan(b_cum[:, j, :], chunk_mask[:, :], log_a[:, j, :], 0.0, ALU.mult, ALU.add)
                ins.then_inc(s("b_cum"), 1)
                dve.wait_ge(s("b_cum"), 1)
                for n in range(4):
                    end = CHUNKS[n][0] + CHUNKS[n][1] - 1
                    ins = dve.tensor_scalar(b_last[:, :, n:n + 1], b_cum[:, :, end:end + 1], 1.0 / 16, None, ALU.mult)
                ins.then_inc(s("b_last"), 1)

            def gated_qk():
                for j in range(2):
                    dve.memset(q_pad[j][:, :, :], 0.0).then_inc(s("mask"), 1)
                dve.wait_ge(s("mask"), 4)
                dve.wait_ge(s("e_end"), 1)
                dve.wait_ge(s("proj"), 5)
                dve.tensor_tensor(k_end[:, :, 0:CHUNKS[4][0]], proj[:, K_AT:K_AT + 2, 0:CHUNKS[4][0]],
                                  e_end[:, :, 0:CHUNKS[4][0]], ALU.mult).then_inc(s("k_end"), 1)
                for j in range(2):
                    half = slice(j * HALF, (j + 1) * HALF)
                    dve.scalar_tensor_tensor(q_pad[j][half, :, :], proj[half, Q_AT:Q_AT + 2, META:], HALF ** -0.5,
                                             e_pos[half, :, META:], ALU.mult, ALU.mult)
                dve.tensor_tensor(k_t[:, :, :], proj[:, K_AT:K_AT + 2, META:], e_neg[:, :, :], ALU.mult).then_inc(s("qk_t"), 1)

            def pooling():
                dve.wait_ge(s("proj"), 13)
                u = proj[:, POOL_AT:POOL_AT + 4, :]
                src, width = u, 1
                for g, dst in enumerate((win_a, win_b, win_a, win_b)):
                    lo = 2 * width - 1
                    dve.tensor_tensor(dst[:, g:, lo:], src[:, g:, lo:], src[:, g:, lo - width:TOK2 - width],
                                      ALU.add).then_inc(s("window"), 1)
                    dve.wait_ge(s("window"), g + 1)
                    width *= 2
                    dve.scalar_tensor_tensor(pooled[:, g, :], dst[:, g, META:], 1.0 / width, u[:, g, META:], ALU.mult,
                                             ALU.subtract).then_inc(s("pooled"), 1)
                    if g < 3:
                        dve.wait_ge(s("pooled"), g + 1)
                    src = dst

            def mixer_rest():
                for i in range(2):
                    n = MIX_AT["state", i]
                    ps = mix_ps[n % 4]
                    dve.wait_ge(s("mix_done_ps"), n + 1)
                    dve.tensor_copy(S_all[:, i, 0, :], ps[:, 0:P]).then_inc(s("states"), 1)
                    for c in range(1, 4):
                        dve.wait_ge(s("states"), 4 * i + c)
                        dve.scalar_tensor_tensor(S_all[:, i, c, :], S_all[:, i, c - 1, :], decay[:, i, c:c + 1],
                                                 ps[:, c * P:(c + 1) * P], ALU.mult, ALU.add).then_inc(s("states"), 1)
                dve.wait_ge(s("y_hi"), 1)
                dve.tensor_tensor(Y_lo[:, 0:4, :], y_f[:, :, :], Y_hi[:, 0:4, :].bitcast(F32), ALU.subtract).then_inc(s("y_lo"), 1)
                dve.wait_ge(s("r_silu"), 1)
                dve.wait_ge(s("go_in"), 2)
                dve.tensor_tensor(r_silu[:, :, :], r_silu[:, :, :], go_f[:, :, :], ALU.mult).then_inc(s("go_step"), 1)
                for i in range(2):
                    pair = slice(2 * i, 2 * i + 2)
                    dve.wait_ge(s("go_root"), i + 1)
                    dve.reciprocal(go_inv[:, pair, :], go_inv[:, pair, :]).then_inc(s("go_step"), 1)
                    dve.wait_ge(s("go_step"), i + 2)
                    dve.tensor_tensor(r_silu[:, pair, :], r_silu[:, pair, :], go_inv[:, pair, :], ALU.mult).then_inc(s("go_t"), 1)
                for i in range(2):
                    c = slice(4 + 2 * i, 6 + 2 * i)
                    dve.wait_ge(s("y_hi"), i + 2)
                    dve.tensor_tensor(Y_lo[:, c, :], y_f[:, 2 * i:2 * i + 2, :], Y_hi[:, c, :].bitcast(F32),
                                      ALU.subtract).then_inc(s("y_lo"), 1)

            for i in range(len(WIN_ORDER)):
                split_lo_at(PLAN.at["win"]["panel"] + i + AHEAD)
                if i == 3:
                    gates()
                if i == 6:
                    gated_qk()
                if i == 13:
                    pooling()
            mixer_rest()
            for m in range(KT):
                split_lo_at(PLAN.at["wout"]["panel"] + m + AHEAD)
                t = PLAN.at["wout"]["tile"] + m
                dve.wait_ge(s("tile_done"), t + 1)
                dve.tensor_tensor(X[:, m, 0:LAT], X[:, m, 0:LAT], bank[t % BANKS][:, 0:LAT], ALU.add).then_inc(s("x_done"), 1)
                if m:
                    add_square("ffn_2", LAT, m - 1)
            add_square("ffn_2", LAT, KT - 1)
            dve.memset(zero_row[:, :], 0.0).then_inc(s("zero_row"), 1)
            norm_rest("ffn_2", LAT)

            steps = [0]

            def step(ins):
                ins.then_inc(s("route"), 1)
                steps[0] += 1
                dve.wait_ge(s("route"), steps[0])

            def spread(x, n=4):
                return x[:, :].rearrange("p (t o) -> p t o", o=1).to_broadcast([P, 2, n])

            def first_largest(choice, top, values, scratch):
                step(dve.tensor_reduce(top[:, :], values, AX.X, ALU.max))
                step(dve.tensor_tensor(choice, values, spread(top), ALU.is_equal))
                step(dve.tensor_tensor(choice, choice, rank[:, :, :], ALU.mult))
                step(dve.tensor_reduce(scratch[:, :], choice, AX.X, ALU.max))
                step(dve.tensor_tensor(choice, choice, spread(scratch), ALU.is_equal))

            def router():
                for j in range(4):
                    step(dve.memset(rank[:, :, j:j + 1], float(4 - j)))
                dve.wait_ge(s("logits"), 1)
                groups = logits[:, :, 0:4]
                g_one, e_sel, e_one, e_two = r4[2][:, :, :], r4[3][:, :, :], r4[6][:, :, :], r4[7][:, :, :]
                first_largest(g_one, r1[0], groups, r1[1])
                dve.tensor_tensor(r4[0][:, :, :], groups, spread(r1[0]), ALU.subtract).then_inc(s("shifted"), 1)
                experts = logits[:, :, 4:].rearrange("p t (g j) -> p t g j", g=4)
                for t in range(2):
                    dve.tensor_tensor(r16[:, t, :, :], experts[:, t, :, :],
                                      r4[2][:, t, :].rearrange("p (g o) -> p g o", o=1).to_broadcast([P, 4, 4]), ALU.mult)
                step(dve.memset(r1[7][:, :], 0.0))
                step(dve.tensor_tensor(r4[8][:, :, :], r16[:, :, 0, :], r16[:, :, 1, :], ALU.add))
                step(dve.tensor_tensor(r4[9][:, :, :], r16[:, :, 2, :], r16[:, :, 3, :], ALU.add))
                step(dve.tensor_tensor(e_sel, r4[8][:, :, :], r4[9][:, :, :], ALU.add))
                first_largest(e_one, r1[2], e_sel, r1[3])
                dve.tensor_tensor(r4[4][:, :, :], e_sel, spread(r1[2]), ALU.subtract).then_inc(s("shifted"), 1)
                step(dve.scalar_tensor_tensor(r4[8][:, :, :], e_one, -3e38, e_sel, ALU.mult, ALU.add))
                first_largest(e_two, r1[4], r4[8][:, :, :], r1[5])
                step(dve.tensor_tensor(e_one, e_one, e_two, ALU.add))
                dve.wait_ge(s("route_exp"), 2)
                step(dve.tensor_reduce(r1[0][:, :], r4[1][:, :, :], AX.X, ALU.add))
                step(dve.tensor_tensor(r4[9][:, :, :], r4[5][:, :, :], e_one, ALU.mult))
                step(dve.tensor_reduce(r1[1][:, :], r4[9][:, :, :], AX.X, ALU.add))
                step(dve.tensor_tensor(r1[2][:, :], r1[0][:, :], r1[1][:, :], ALU.mult))
                step(dve.reciprocal(r1[3][:, :], r1[2][:, :]))
                step(dve.tensor_tensor(r4[9][:, :, :], r4[9][:, :, :], spread(r1[3]), ALU.mult))
                for g in range(4):
                    step(dve.tensor_tensor(combine[:, :, 4 * g:4 * g + 4], r4[9][:, :, :],
                                           r4[2][:, :, g:g + 1].to_broadcast([P, 2, 4]), ALU.mult))

            p0 = PLAN.at["moe"]["panel"]

            def expert_split(n, i=None):
                if n < 6 * EXPERTS:
                    dve.wait_ge(s("w_hi"), later(p0 + n + 1, i, 6 * EXPERT_TURNS))
                    split_lo(p0 + n)

            def diagonal(x, i=None):
                if x >= 2:
                    dve.wait_ge(s("weight_row"), later(x - 1, i, EXPERT_TURNS))
                for tt in range(2):
                    col = combine[:, tt, x:x + 1] if i is None else combine[:, tt, bass.ds(i * EXPERT_TURNS + x, 1)]
                    ins = dve.tensor_scalar(diag[x % 2][:, tt, :], ident[:, :], col, None, ALU.mult)
                ins.then_inc(s("diag"), 1)

            def gated(x, i=None):
                st = EXPERT_TURNS
                h = e_hid[x % 2]
                flat = lambda v: v[:, :, :].rearrange("p m c -> p (m c)")
                dve.wait_ge(s("e_silu"), later(x + 1, i, st))
                dve.wait_ge(s("expert_done"), later(6 * x + 2 if x else 4, i, 6 * st))
                dve.tensor_tensor(flat(e_up), flat(e_silu), psum[1][:, :], ALU.mult).then_inc(s("e_step"), 1)
                dve.wait_ge(s("e_step"), later(x + 1, i, st))
                dve.wait_ge(s("weight_row"), later(x + 1, i, st))
                row = psum[2][:, 0:LAT].rearrange("p (o c) -> p o c", o=1).to_broadcast([P, 2, LAT])
                dve.tensor_tensor(h[:, :, :], e_up[:, :, :], row, ALU.mult).then_inc(s("e_hid"), 1)
                dve.wait_ge(s("e_hi"), later(x + 1, i, st))
                dve.tensor_tensor(E_lo[x % 2][:, :, :], h[:, :, :], E_hi[x % 2][:, :, :].bitcast(F32),
                                  ALU.subtract).then_inc(s("e_lo"), 1)

            def expert_turn(x, i=None):
                n = 6 * x - 2 if x else 0
                diagonal(x, i)
                for j in range(0 if x else 1, 4):
                    expert_split(n + j + AHEAD, i)
                gated(x, i)
                if x:
                    for j in range(4, 6):
                        expert_split(n + j + AHEAD, i)

            expert_split(AHEAD)
            router()
            expert_turn(0)
            with dve.Fori(0, 3) as i:
                for j in range(EXPERT_TURNS):
                    expert_turn(1 + j, i)
            for x in range(1 + 3 * EXPERT_TURNS, EXPERTS):
                expert_turn(x)
            dve.wait_ge(s("expert_done"), 6 * EXPERTS)
            for b in range(4):
                dve.tensor_tensor(X[:, 2 * b:2 * b + 2, 0:LAT], X[:, 2 * b:2 * b + 2, 0:LAT],
                                  psum[4 + b][:, :].rearrange("p (m c) -> p m c", m=2), ALU.add).then_inc(s("y_added"), 1)
                if b:
                    for k in range(2 * b - 2, 2 * b):
                        add_square("final_2", LAT, k)
            for k in range(KT - 2, KT):
                add_square("final_2", LAT, k)
            norm_rest("final_2", LAT)


DFT_N = 256


def tables():
    n = np.arange(DFT_N)
    angle = 2 * np.pi * ((n[:, None] * n[None, :]) % DFT_N) / DFT_N
    dft = np.concatenate([np.cos(angle), np.sin(angle)], axis=1) / np.sqrt(DFT_N)
    def rope(width, reps):
        n_freq = width // 4
        inv_freq = (np.float32(10000.0) ** (-np.arange(n_freq, dtype=np.float32) / n_freq)).astype(np.float32)
        t = np.arange(LAT)
        where = np.stack([t // 64, t % 64]).astype(np.float32)
        f = np.arange(width)
        turn = where[f // (2 * n_freq)] * inv_freq[f % n_freq][:, None]
        sign = np.where(f // n_freq % 2 == 0, -1.0, 1.0)[:, None]
        both = np.stack([np.cos(turn), np.sin(turn) * sign], axis=1)
        return np.tile(both, (reps, 1, 1)).astype(np.float32)

    return {"dft": dft.astype(np.float32), "rope_diff": rope(HALF, 2), "rope_mla": rope(ROPE, 1)}


def kernel(**inputs):
    import concourse.bacc as bacc
    from concourse.bass_utils import run_bass_kernel_spmd

    nc = bacc.Bacc("TRN2", target_bir_lowering=False, num_devices=1)
    arrays = {f"in_{name}": np.ascontiguousarray(value) for name, value in {**inputs, **tables()}.items()}
    aps = {name[3:]: nc.dram_tensor(name, v.shape, mybir.dt.from_np(v.dtype), kind="ExternalInput").ap()
           for name, v in arrays.items()}
    out = nc.dram_tensor("out", (1, LAT, D), F32, kind="ExternalOutput").ap()
    build_program(nc, aps, out)
    result = run_bass_kernel_spmd(nc, [arrays], core_ids=[0])
    return result.results[0]["out"]
```
